# Optimizing a Trainium2 kernel written in Bass

```python
import math
import jax, jax.numpy as jnp
from jax import lax
import numpy as np

D_MODEL = 1024
BATCH = 1
SEQ = 512
DEPTH = 1

N_MEM = 256
EPS = 1e-6

SSD_D_INNER = D_MODEL
SSD_HEAD_DIM = 64
SSD_HEADS = SSD_D_INNER // SSD_HEAD_DIM
SSD_GROUPS = 4
SSD_HEADS_PER_GROUP = SSD_HEADS // SSD_GROUPS
SSD_STATE = 128
SSD_CONV = 4
SSD_CHUNK = 128
SSD_CONV_DIM = SSD_D_INNER + 2 * SSD_GROUPS * SSD_STATE

DIL_PAIRS = ((128, 1), (512, 4), (2048, 16))
DIL_HEADS_PER_GROUP = 4
DIL_HEAD_DIM = 64
DIL_HEADS = len(DIL_PAIRS) * DIL_HEADS_PER_GROUP
DIL_WIDTH = DIL_HEADS * DIL_HEAD_DIM
DIL_OUT_WIDTH = DIL_HEADS_PER_GROUP * DIL_HEAD_DIM

MEM_HEADS = 4
MEM_HEAD_DIM = 192
MEM_WIDTH = MEM_HEADS * MEM_HEAD_DIM

ROPE_THETA = 500000.0
ROPE_FRACTION = 4

PEER_HEADS = 8
PEER_N_KEYS = 128
PEER_EXPERTS = PEER_N_KEYS * PEER_N_KEYS
PEER_QUERY_DIM = 256
PEER_TOPK = 16
PEER_BLOCK = 64

N_BRANCHES = 3

OFF_Z = 0
OFF_XBC = OFF_Z + SSD_D_INNER
OFF_DT = OFF_XBC + SSD_CONV_DIM
OFF_DQ = OFF_DT + SSD_HEADS
OFF_DK = OFF_DQ + DIL_WIDTH
OFF_DV = OFF_DK + DIL_WIDTH
OFF_MQ = OFF_DV + DIL_WIDTH
OFF_GATE = OFF_MQ + MEM_WIDTH
IN_PROJ_WIDTH = OFF_GATE + N_BRANCHES * D_MODEL


F32 = jnp.float32

def _rms_norm(t, w):
    tf = t.astype(F32)
    tf = tf * lax.rsqrt(jnp.mean(tf * tf, axis=-1, keepdims=True) + EPS)
    return (tf * w.astype(F32)).astype(t.dtype)

def _partial_rope(t, positions):
    hd = t.shape[-1]
    rot = hd // ROPE_FRACTION
    half = rot // 2
    inv = jnp.exp(-math.log(ROPE_THETA) * (2.0 / rot) * jnp.arange(half, dtype=F32))
    ang = positions.astype(F32)[..., None] * inv
    cos = jnp.cos(ang)[:, :, None, :]
    sin = jnp.sin(ang)[:, :, None, :]
    tf = t.astype(F32)
    t1 = tf[..., :half]
    t2 = tf[..., half:rot]
    out = jnp.concatenate([t1 * cos - t2 * sin, t2 * cos + t1 * sin, tf[..., rot:]], axis=-1)
    return out.astype(t.dtype)

def _causal_depthwise_conv(t, w, bias):
    c = t.shape[-1]
    y = lax.conv_general_dilated(
        t, w[:, None, :].astype(t.dtype), window_strides=(1,),
        padding=[(w.shape[0] - 1, 0)],
        dimension_numbers=('NWC', 'WIO', 'NWC'),
        feature_group_count=c)
    return y + bias.astype(t.dtype)

def _ssd_chunked(xh, dt, a, bmat, cmat):
    b, s, g, r, p = xh.shape
    n = bmat.shape[-1]
    nc = s // SSD_CHUNK
    x_dt = xh.astype(F32) * dt[..., None]
    da = dt * a

    def chunks(t):
        return jnp.moveaxis(t.reshape(b, nc, SSD_CHUNK, *t.shape[2:]), 1, 0)

    tril = jnp.tril(jnp.ones((SSD_CHUNK, SSD_CHUNK), dtype=bool))
    strict = jnp.tril(jnp.ones((SSD_CHUNK, SSD_CHUNK), dtype=bool), k=-1)

    def step(state, inp):
        xc, dac, bc, cc = inp
        dat = jnp.moveaxis(dac, 1, -1)
        acum = jnp.cumsum(dat, axis=-1)
        seg = jnp.cumsum(jnp.where(strict, dat[..., :, None], 0.0), axis=-2)
        lmat = jnp.exp(jnp.where(tril, seg, -jnp.inf))
        cb = jnp.einsum('bsgn,btgn->bgst', cc, bc)
        y_diag = jnp.einsum('bgst,bgrst,btgrp->bsgrp', cb, lmat, xc)
        y_off = jnp.einsum('bsgn,bgrpn,bgrs->bsgrp', cc, state, jnp.exp(acum))
        decay = jnp.exp(acum[..., -1:] - acum)
        new_state = (state * jnp.exp(acum[..., -1])[..., None, None]
                     + jnp.einsum('btgn,bgrt,btgrp->bgrpn', bc, decay, xc))
        return new_state, y_diag + y_off

    state0 = jnp.zeros((b, g, r, p, n), F32)
    _, ys = lax.scan(step, state0, (chunks(x_dt), chunks(da),
                                    chunks(bmat.astype(F32)), chunks(cmat.astype(F32))))
    return jnp.moveaxis(ys, 0, 1).reshape(b, s, g, r, p)

def _dilated_group_attention(q, k, v, dilation, n_back):
    b, s, h, hd = q.shape
    m = s // dilation
    blk = n_back
    nb = -(-m // blk)
    mp = nb * blk

    def to_sub(t):
        t = t.reshape(b, m, dilation, h, hd)
        t = jnp.pad(t, ((0, 0), (0, mp - m), (0, 0), (0, 0), (0, 0)))
        return t.reshape(b, nb, blk, dilation, h, hd)

    def with_prev(t):
        prev = jnp.pad(t[:, :-1], ((0, 0), (1, 0), (0, 0), (0, 0), (0, 0), (0, 0)))
        return jnp.concatenate([prev, t], axis=2)

    qs = to_sub(q)
    kk = with_prev(to_sub(k))
    vv = with_prev(to_sub(v))
    scores = jnp.einsum('bnqrhd,bnkrhd->bnrhqk', qs, kk).astype(F32) * (hd ** -0.5)
    qi = jnp.arange(blk)[:, None]
    ki = jnp.arange(2 * blk)[None, :]
    dist = qi + blk - ki
    band = (dist >= 0) & (dist <= n_back)
    valid = band[None] & ((jnp.arange(nb)[:, None, None] > 0) | (ki >= blk)[None])
    scores = jnp.where(valid[None, :, None, None], scores, -jnp.inf)
    lse = jax.nn.logsumexp(scores, axis=-1)
    probs = jnp.exp(scores - lse[..., None]).astype(v.dtype)
    out = jnp.einsum('bnrhqk,bnkrhd->bnqrhd', probs, vv)
    out = out.reshape(b, mp, dilation, h, hd)[:, :m].reshape(b, s, h, hd)
    lse = lse.transpose(0, 1, 4, 2, 3).reshape(b, mp, dilation, h)[:, :m].reshape(b, s, h)
    return out, lse

def _peer(hn, w_query, sub_keys, expert_down, expert_up):
    b, s, d = hn.shape
    q = (hn @ w_query).reshape(b, s, PEER_HEADS, 2, PEER_QUERY_DIM // 2)
    sc = jnp.einsum('bshcd,hckd->bshck', q, sub_keys).astype(F32)
    v1, i1 = lax.top_k(sc[..., 0, :], PEER_TOPK)
    v2, i2 = lax.top_k(sc[..., 1, :], PEER_TOPK)
    cand = (v1[..., :, None] + v2[..., None, :]).reshape(b, s, PEER_HEADS, PEER_TOPK * PEER_TOPK)
    cidx = (i1[..., :, None] * PEER_N_KEYS + i2[..., None, :]).reshape(b, s, PEER_HEADS, PEER_TOPK * PEER_TOPK)
    top, pos = lax.top_k(cand, PEER_TOPK)
    idx = jnp.take_along_axis(cidx, pos, axis=-1)
    gate = jax.nn.softmax(top, axis=-1)
    nblk = s // PEER_BLOCK

    def blockify(t):
        return jnp.moveaxis(t.reshape(b, nblk, PEER_BLOCK, *t.shape[2:]), 1, 0)

    def one_block(args):
        hb, ib, gb = args
        u = expert_down[ib]
        act = jax.nn.gelu(jnp.einsum('bld,blhkd->blhk', hb, u), approximate=False)
        coef = (gb * act.astype(F32)).astype(hb.dtype)
        vv = expert_up[ib]
        return jnp.einsum('blhk,blhkd->bld', coef, vv)

    out = lax.map(one_block, (blockify(hn), blockify(idx), blockify(gate)))
    return jnp.moveaxis(out, 0, 1).reshape(b, s, d)

def first_inputs(seed: int = 0) -> dict:
    key = jax.random.key(seed)
    ks = jax.random.split(key, 32)
    L = DEPTH

    def nrm(k, shape, scale):
        return jax.random.normal(k, shape, F32) * scale

    def gain(k, shape):
        return 1.0 + 0.05 * jax.random.normal(k, shape, F32)

    x = nrm(ks[0], (BATCH, SEQ, D_MODEL), 1.0)
    mem = nrm(ks[1], (BATCH, N_MEM, D_MODEL), 1.0)
    offset = jax.random.randint(ks[2], (BATCH, 1), 0, 4096, dtype=jnp.int32)
    positions = jnp.arange(SEQ, dtype=jnp.int32)[None, :] + offset
    norm_mix_w = gain(ks[3], (L, D_MODEL))
    w_in = nrm(ks[4], (L, D_MODEL, IN_PROJ_WIDTH), D_MODEL ** -0.5)
    ssd_conv_w = nrm(ks[5], (L, SSD_CONV, SSD_CONV_DIM), SSD_CONV ** -0.5)
    ssd_conv_b = nrm(ks[6], (L, SSD_CONV_DIM), 0.02)
    dt0 = jnp.exp(jax.random.uniform(ks[7], (L, SSD_HEADS), F32, math.log(1e-3), math.log(1e-1)))
    ssd_dt_bias = dt0 + jnp.log(-jnp.expm1(-dt0))
    ssd_a_log = jnp.log(jax.random.uniform(ks[8], (L, SSD_HEADS), F32, 1.0, 16.0))
    ssd_d = gain(ks[9], (L, SSD_HEADS))
    ssd_norm_w = gain(ks[10], (L, SSD_D_INNER))
    dil_q_norm_w = gain(ks[11], (L, DIL_HEAD_DIM))
    dil_k_norm_w = gain(ks[12], (L, DIL_HEAD_DIM))
    mem_norm_w = gain(ks[13], (L, D_MODEL))
    w_mem_kv = nrm(ks[14], (L, D_MODEL, 2 * MEM_WIDTH), D_MODEL ** -0.5)
    mem_q_norm_w = gain(ks[15], (L, MEM_HEAD_DIM))
    mem_k_norm_w = gain(ks[16], (L, MEM_HEAD_DIM))
    w_ssd_br = nrm(ks[17], (L, SSD_D_INNER, D_MODEL), SSD_D_INNER ** -0.5)
    w_dil_br = nrm(ks[18], (L, DIL_OUT_WIDTH, D_MODEL), DIL_OUT_WIDTH ** -0.5)
    w_mem_br = nrm(ks[19], (L, MEM_WIDTH, D_MODEL), MEM_WIDTH ** -0.5)
    w_out = nrm(ks[20], (L, D_MODEL, D_MODEL), D_MODEL ** -0.5)
    norm_ffn_w = gain(ks[21], (L, D_MODEL))
    peer_w_query = nrm(ks[22], (L, D_MODEL, PEER_HEADS * PEER_QUERY_DIM), D_MODEL ** -0.5)
    peer_sub_keys = nrm(ks[23], (L, PEER_HEADS, 2, PEER_N_KEYS, PEER_QUERY_DIM // 2),
                        (PEER_QUERY_DIM // 2) ** -0.5)
    peer_down = nrm(ks[24], (L, PEER_EXPERTS, D_MODEL), D_MODEL ** -0.5)
    peer_up = nrm(ks[25], (L, PEER_EXPERTS, D_MODEL), PEER_HEADS ** -0.5)
    return {
        'x': x, 'mem': mem, 'positions': positions,
        'norm_mix_w': norm_mix_w, 'w_in': w_in,
        'ssd_conv_w': ssd_conv_w, 'ssd_conv_b': ssd_conv_b, 'ssd_dt_bias': ssd_dt_bias,
        'ssd_a_log': ssd_a_log, 'ssd_d': ssd_d, 'ssd_norm_w': ssd_norm_w,
        'dil_q_norm_w': dil_q_norm_w, 'dil_k_norm_w': dil_k_norm_w,
        'mem_norm_w': mem_norm_w, 'w_mem_kv': w_mem_kv,
        'mem_q_norm_w': mem_q_norm_w, 'mem_k_norm_w': mem_k_norm_w,
        'w_ssd_br': w_ssd_br, 'w_dil_br': w_dil_br, 'w_mem_br': w_mem_br, 'w_out': w_out,
        'norm_ffn_w': norm_ffn_w, 'peer_w_query': peer_w_query, 'peer_sub_keys': peer_sub_keys,
        'peer_down': peer_down, 'peer_up': peer_up,
    }

def first_block(x, mem, positions, norm_mix_w, w_in, ssd_conv_w, ssd_conv_b, ssd_dt_bias,
              ssd_a_log, ssd_d, ssd_norm_w, dil_q_norm_w, dil_k_norm_w, mem_norm_w, w_mem_kv,
              mem_q_norm_w, mem_k_norm_w, w_ssd_br, w_dil_br, w_mem_br, w_out, norm_ffn_w,
              peer_w_query, peer_sub_keys, peer_down, peer_up):
    b, s, _ = x.shape
    n_mem = mem.shape[1]
    h = x
    for layer in range(DEPTH):
        u = _rms_norm(h, norm_mix_w[layer])
        proj = u @ w_in[layer]
        z = proj[..., OFF_Z:OFF_XBC]
        xbc = proj[..., OFF_XBC:OFF_DT]
        dt_raw = proj[..., OFF_DT:OFF_DQ]
        dq = proj[..., OFF_DQ:OFF_DK].reshape(b, s, DIL_HEADS, DIL_HEAD_DIM)
        dk = proj[..., OFF_DK:OFF_DV].reshape(b, s, DIL_HEADS, DIL_HEAD_DIM)
        dv = proj[..., OFF_DV:OFF_MQ].reshape(b, s, DIL_HEADS, DIL_HEAD_DIM)
        mq = proj[..., OFF_MQ:OFF_GATE].reshape(b, s, MEM_HEADS, MEM_HEAD_DIM)
        gates = jax.nn.sigmoid(proj[..., OFF_GATE:].astype(F32)).reshape(b, s, N_BRANCHES, D_MODEL)

        xbc = jax.nn.silu(_causal_depthwise_conv(xbc, ssd_conv_w[layer], ssd_conv_b[layer]))
        gn = SSD_GROUPS * SSD_STATE
        xs = xbc[..., :SSD_D_INNER].reshape(b, s, SSD_GROUPS, SSD_HEADS_PER_GROUP, SSD_HEAD_DIM)
        bm = xbc[..., SSD_D_INNER:SSD_D_INNER + gn].reshape(b, s, SSD_GROUPS, SSD_STATE)
        cm = xbc[..., SSD_D_INNER + gn:].reshape(b, s, SSD_GROUPS, SSD_STATE)
        dt = jax.nn.softplus(dt_raw.astype(F32) + ssd_dt_bias[layer].astype(F32))
        dt = dt.reshape(b, s, SSD_GROUPS, SSD_HEADS_PER_GROUP)
        a = -jnp.exp(ssd_a_log[layer].astype(F32)).reshape(SSD_GROUPS, SSD_HEADS_PER_GROUP)
        y = _ssd_chunked(xs, dt, a, bm, cm)
        y = y + ssd_d[layer].astype(F32).reshape(SSD_GROUPS, SSD_HEADS_PER_GROUP)[..., None] * xs.astype(F32)
        y = y.reshape(b, s, SSD_D_INNER) * jax.nn.silu(z.astype(F32))
        yg = y.reshape(b, s, SSD_GROUPS, SSD_D_INNER // SSD_GROUPS)
        yg = yg * lax.rsqrt(jnp.mean(yg * yg, axis=-1, keepdims=True) + EPS)
        y_ssd = (yg.reshape(b, s, SSD_D_INNER) * ssd_norm_w[layer].astype(F32)).astype(h.dtype)

        dq = _partial_rope(_rms_norm(dq, dil_q_norm_w[layer]), positions)
        dk = _partial_rope(_rms_norm(dk, dil_k_norm_w[layer]), positions)
        outs = []
        lses = []
        for gi, (window, dilation) in enumerate(DIL_PAIRS):
            sl = slice(gi * DIL_HEADS_PER_GROUP, (gi + 1) * DIL_HEADS_PER_GROUP)
            o, l = _dilated_group_attention(dq[:, :, sl], dk[:, :, sl], dv[:, :, sl],
                                            dilation, window // dilation)
            outs.append(o.astype(F32))
            lses.append(l)
        wts = jax.nn.softmax(jnp.stack(lses, axis=0), axis=0)
        y_dil = jnp.sum(wts[..., None] * jnp.stack(outs, axis=0), axis=0)
        y_dil = y_dil.reshape(b, s, DIL_OUT_WIDTH).astype(h.dtype)

        mkv = _rms_norm(mem, mem_norm_w[layer]) @ w_mem_kv[layer]
        mk = mkv[..., :MEM_WIDTH].reshape(b, n_mem, MEM_HEADS, MEM_HEAD_DIM)
        mv = mkv[..., MEM_WIDTH:].reshape(b, n_mem, MEM_HEADS, MEM_HEAD_DIM)
        mqn = _rms_norm(mq, mem_q_norm_w[layer])
        mk = _rms_norm(mk, mem_k_norm_w[layer])
        msc = jnp.einsum('bshd,bmhd->bhsm', mqn, mk).astype(F32) * (MEM_HEAD_DIM ** -0.5)
        mp = jax.nn.softmax(msc, axis=-1).astype(mv.dtype)
        y_mem = jnp.einsum('bhsm,bmhd->bshd', mp, mv).reshape(b, s, MEM_WIDTH)

        merged = (gates[:, :, 0] * (y_ssd @ w_ssd_br[layer]).astype(F32)
                  + gates[:, :, 1] * (y_dil @ w_dil_br[layer]).astype(F32)
                  + gates[:, :, 2] * (y_mem @ w_mem_br[layer]).astype(F32))
        h = h + merged.astype(h.dtype) @ w_out[layer]

        hn = _rms_norm(h, norm_ffn_w[layer])
        h = h + _peer(hn, peer_w_query[layer], peer_sub_keys[layer], peer_down[layer], peer_up[layer])
    return h


DEPTH_2 = 2

ROPE_THETA_2 = 10000.0
BLOCK_Q = 128
RET_HEADS = 4
RET_DK = 64
RET_DV = 128
RET_CHUNK = 128
FOX_HEADS = 4
FOX_DH = 128
MLA_HEADS = 4
MLA_Q_RANK = 256
MLA_KV_RANK = 128
MLA_NOPE = 128
MLA_ROPE = 64
MLA_V = 128
N_BRANCH = 3
BRANCH_W = 512
N_GROUPS = 4
EXP_PER_GROUP = 8
N_EXPERTS = N_GROUPS * EXP_PER_GROUP
TOP_K = 2
D_EXPERT = 512
MOE_BLOCK = 128

IN_SIZES = (RET_HEADS * RET_DK, RET_HEADS * RET_DK, RET_HEADS * RET_DV, RET_HEADS * RET_DV,
            FOX_HEADS * FOX_DH, FOX_HEADS * FOX_DH, FOX_HEADS * FOX_DH, FOX_HEADS,
            MLA_Q_RANK, MLA_KV_RANK, MLA_ROPE)
IN_OFFSETS = tuple(sum(IN_SIZES[:i + 1]) for i in range(len(IN_SIZES) - 1))
D_IN = sum(IN_SIZES)


def rms_norm(x, g):
    xf = x.astype(jnp.float32)
    y = xf * lax.rsqrt(jnp.mean(xf * xf, axis=-1, keepdims=True) + EPS)
    return (y * g.astype(jnp.float32)).astype(x.dtype)

def modulate(h, shift, scale):
    return h * (1 + scale[:, None, :]) + shift[:, None, :]

def rope(x, positions):
    d = x.shape[-1]
    inv = ROPE_THETA_2 ** (-jnp.arange(0, d, 2, dtype=jnp.float32) / d)
    ang = positions.astype(jnp.float32)[..., None] * inv
    cos = jnp.cos(ang)[:, :, None, :]
    sin = jnp.sin(ang)[:, :, None, :]
    xf = x.astype(jnp.float32)
    x1, x2 = xf[..., : d // 2], xf[..., d // 2:]
    return jnp.concatenate([x1 * cos - x2 * sin, x2 * cos + x1 * sin], axis=-1).astype(x.dtype)

def retention(q, k, v, g):
    B, S, H, dk = q.shape
    dv = v.shape[-1]
    C = RET_CHUNK
    N = S // C
    dt = q.dtype
    f32 = jnp.float32
    log_gamma = jnp.log1p(-jnp.exp2(-5.0 - jnp.arange(H, dtype=f32)))
    idx = jnp.arange(C, dtype=f32)
    rel = idx[:, None] - idx[None, :]
    dmask = jnp.where(rel >= 0, jnp.exp(log_gamma[:, None, None] * jnp.maximum(rel, 0.0)), 0.0)
    decay_in = jnp.exp(log_gamma[:, None] * (idx + 1.0))
    decay_out = jnp.exp(log_gamma[:, None] * (C - 1.0 - idx))
    decay_chunk = jnp.exp(log_gamma * C)
    qc = q.astype(f32).reshape(B, N, C, H, dk)
    kc = (k.astype(f32) * dk ** -0.5).reshape(B, N, C, H, dk)
    vc = v.astype(f32).reshape(B, N, C, H, dv)
    scores = jnp.einsum('bnchd,bnmhd->bhncm', qc, kc) * dmask[None, :, None]
    inner = jnp.einsum('bhncm,bnmhe->bnche', scores, vc)
    kv = jnp.einsum('bnmhd,hm,bnmhe->nbhde', kc, decay_out, vc)

    def step(state, kv_n):
        return state * decay_chunk[None, :, None, None] + kv_n, state

    _, s_prev = lax.scan(step, jnp.zeros((B, H, dk, dv), f32), kv)
    cross = jnp.einsum('bnchd,hc,nbhde->bnche', qc, decay_in, s_prev)
    o = (inner + cross).reshape(B, S, H, dv)
    mu = jnp.mean(o, axis=-1, keepdims=True)
    var = jnp.mean(jnp.square(o - mu), axis=-1, keepdims=True)
    o = ((o - mu) * lax.rsqrt(var + EPS)).reshape(B, S, H * dv)
    return (jax.nn.silu(g.astype(f32)) * o).astype(dt)

def blocked_causal_attention(q, k, v, log_f_cum=None):
    B, S, H, d = q.shape
    dv = v.shape[-1]
    NQ = S // BLOCK_Q
    scale = d ** -0.5
    kpos = jnp.arange(S)
    qb = q.reshape(B, NQ, BLOCK_Q, H, d).transpose(1, 0, 2, 3, 4)
    blk_ids = jnp.arange(NQ)
    use_forget = log_f_cum is not None
    if use_forget:
        fk = log_f_cum.transpose(0, 2, 1)
        fq = log_f_cum.reshape(B, NQ, BLOCK_Q, H).transpose(1, 0, 3, 2)
        xs = (qb, blk_ids, fq)
    else:
        xs = (qb, blk_ids)

    def body(args):
        qblk, bi = args[0], args[1]
        s = jnp.einsum('bqhd,bkhd->bhqk', qblk, k).astype(jnp.float32) * scale
        if use_forget:
            s = s + args[2][..., None] - fk[:, :, None, :]
        qpos = bi * BLOCK_Q + jnp.arange(BLOCK_Q)
        s = jnp.where(kpos[None, :] <= qpos[:, None], s, -jnp.inf)
        p = jax.nn.softmax(s, axis=-1)
        return jnp.einsum('bhqk,bkhe->bqhe', p.astype(v.dtype), v)

    out = lax.map(body, xs)
    return out.transpose(1, 0, 2, 3, 4).reshape(B, S, H * dv)

def token_mixer(h, positions, w_in, fox_fb, mla_q_norm_g, mla_wq_up, mla_kv_norm_g, mla_wkv_up,
                gate_w, gate_b, branch_w, out_w):
    B, S, D = h.shape
    proj = h @ w_in
    rq, rk, rv, rg, fq, fk, fv, ff, mq, mkv, mkr = jnp.split(proj, IN_OFFSETS, axis=-1)
    rq = rope(rq.reshape(B, S, RET_HEADS, RET_DK), positions)
    rk = rope(rk.reshape(B, S, RET_HEADS, RET_DK), positions)
    ya = retention(rq, rk, rv.reshape(B, S, RET_HEADS, RET_DV), rg)
    log_f = jax.nn.log_sigmoid((ff + fox_fb).astype(jnp.float32))
    f_cum = jnp.cumsum(log_f, axis=1)
    yb = blocked_causal_attention(fq.reshape(B, S, FOX_HEADS, FOX_DH),
                                  fk.reshape(B, S, FOX_HEADS, FOX_DH),
                                  fv.reshape(B, S, FOX_HEADS, FOX_DH), f_cum)
    qh = (rms_norm(mq, mla_q_norm_g) @ mla_wq_up).reshape(B, S, MLA_HEADS, MLA_NOPE + MLA_ROPE)
    q_nope, q_pe = qh[..., :MLA_NOPE], rope(qh[..., MLA_NOPE:], positions)
    kvh = (rms_norm(mkv, mla_kv_norm_g) @ mla_wkv_up).reshape(B, S, MLA_HEADS, MLA_NOPE + MLA_V)
    k_nope, v_c = kvh[..., :MLA_NOPE], kvh[..., MLA_NOPE:]
    k_pe = jnp.broadcast_to(rope(mkr[:, :, None, :], positions), (B, S, MLA_HEADS, MLA_ROPE))
    yc = blocked_causal_attention(jnp.concatenate([q_nope, q_pe], axis=-1),
                                  jnp.concatenate([k_nope, k_pe], axis=-1), v_c)
    gates = jax.nn.sigmoid((h @ gate_w + gate_b).astype(jnp.float32)).astype(h.dtype)
    gates = gates.reshape(B, S, N_BRANCH, D)
    merged = gates[:, :, 0] * (ya @ branch_w[0])
    merged = merged + gates[:, :, 1] * (yb @ branch_w[1])
    merged = merged + gates[:, :, 2] * (yc @ branch_w[2])
    return merged @ out_w

def hier_moe(h, w_grp, b_grp, w_exp, b_exp, w1, w3, w2):
    B, S, D = h.shape
    T = B * S
    f32 = jnp.float32
    t = h.reshape(T, D)
    tf = t.astype(f32)
    grp_p = jax.nn.softmax(tf @ w_grp.astype(f32) + b_grp.astype(f32), axis=-1)
    g_idx = jnp.argmax(grp_p, axis=-1)
    g_w = jnp.max(grp_p, axis=-1)
    exp_logits = (tf @ w_exp.astype(f32) + b_exp.astype(f32)).reshape(T, N_GROUPS, EXP_PER_GROUP)
    in_grp = jnp.take_along_axis(exp_logits, g_idx[:, None, None], axis=1)[:, 0]
    top_p, top_i = lax.top_k(jax.nn.softmax(in_grp, axis=-1), TOP_K)
    top_p = top_p / jnp.sum(top_p, axis=-1, keepdims=True)
    eid = (g_idx[:, None] * EXP_PER_GROUP + top_i).reshape(-1).astype(jnp.int32)
    wts = (g_w[:, None] * top_p).reshape(-1)
    tok = jnp.repeat(jnp.arange(T, dtype=jnp.int32), TOP_K)
    A = T * TOP_K
    order = jnp.argsort(eid)
    se, stok, sw = eid[order], tok[order], wts[order]
    counts = jnp.bincount(eid, length=N_EXPERTS)
    starts = jnp.cumsum(counts) - counts
    pcounts = (counts + MOE_BLOCK - 1) // MOE_BLOCK * MOE_BLOCK
    pends = jnp.cumsum(pcounts)
    pstarts = pends - pcounts
    dest = pstarts[se] + jnp.arange(A) - starts[se]
    n_blocks = -(-A // MOE_BLOCK) + N_EXPERTS
    P = n_blocks * MOE_BLOCK
    buf_tok = jnp.zeros((P,), jnp.int32).at[dest].set(stok)
    buf_w = jnp.zeros((P,), f32).at[dest].set(sw)
    blk_e = jnp.minimum(jnp.searchsorted(pends, jnp.arange(n_blocks) * MOE_BLOCK, side='right'),
                        N_EXPERTS - 1)

    def expert_block(args):
        tok_b, w_b, e = args
        xb = t[tok_b]
        hid = jax.nn.silu(xb @ w1[e]) * (xb @ w3[e])
        return (hid @ w2[e]) * w_b[:, None].astype(t.dtype)

    ys = lax.map(expert_block, (buf_tok.reshape(n_blocks, MOE_BLOCK),
                                buf_w.reshape(n_blocks, MOE_BLOCK), blk_e))
    out = jnp.zeros((T, D), t.dtype).at[buf_tok].add(ys.reshape(P, D))
    return out.reshape(B, S, D)

def second_inputs(seed: int = 0) -> dict:
    key = jax.random.key(seed)
    ks = jax.random.split(key, 26)
    L, D = DEPTH_2, D_MODEL
    f32 = jnp.float32

    def nrm(k, shape, fan_in, mult=1.0):
        return jax.random.normal(k, shape, f32) * (mult * fan_in ** -0.5)

    def gain(k, shape):
        return 1.0 + 0.05 * jax.random.normal(k, shape, f32)

    def small(k, shape, s=0.02):
        return s * jax.random.normal(k, shape, f32)

    positions = (jnp.arange(SEQ, dtype=jnp.int32)[None, :]
                 + jax.random.randint(ks[2], (BATCH, 1), 0, 1024, dtype=jnp.int32))
    return {
        "x": jax.random.normal(ks[0], (BATCH, SEQ, D), f32),
        "c": jax.random.normal(ks[1], (BATCH, D), f32),
        "positions": positions,
        "ada_w": nrm(ks[3], (L, D, 6 * D), D, 0.5),
        "ada_b": small(ks[4], (L, 6 * D)),
        "norm1_g": gain(ks[5], (L, D)),
        "norm2_g": gain(ks[6], (L, D)),
        "w_in": nrm(ks[7], (L, D, D_IN), D),
        "fox_fb": 1.0 + 0.5 * jax.random.normal(ks[8], (L, FOX_HEADS), f32),
        "mla_q_norm_g": gain(ks[9], (L, MLA_Q_RANK)),
        "mla_wq_up": nrm(ks[10], (L, MLA_Q_RANK, MLA_HEADS * (MLA_NOPE + MLA_ROPE)), MLA_Q_RANK),
        "mla_kv_norm_g": gain(ks[11], (L, MLA_KV_RANK)),
        "mla_wkv_up": nrm(ks[12], (L, MLA_KV_RANK, MLA_HEADS * (MLA_NOPE + MLA_V)), MLA_KV_RANK),
        "gate_w": nrm(ks[13], (L, D, N_BRANCH * D), D),
        "gate_b": small(ks[14], (L, N_BRANCH * D)),
        "branch_w": nrm(ks[15], (L, N_BRANCH, BRANCH_W, D), BRANCH_W),
        "out_w": nrm(ks[16], (L, D, D), D),
        "router_grp_w": nrm(ks[17], (L, D, N_GROUPS), D),
        "router_grp_b": small(ks[18], (L, N_GROUPS), 0.01),
        "router_exp_w": nrm(ks[19], (L, D, N_EXPERTS), D),
        "router_exp_b": small(ks[20], (L, N_EXPERTS), 0.01),
        "exp_w1": nrm(ks[21], (L, N_EXPERTS, D, D_EXPERT), D),
        "exp_w3": nrm(ks[22], (L, N_EXPERTS, D, D_EXPERT), D),
        "exp_w2": nrm(ks[23], (L, N_EXPERTS, D_EXPERT, D), D_EXPERT),
        "final_g": gain(ks[24], (D,)),
    }

def second_block(x, c, positions, ada_w, ada_b, norm1_g, norm2_g, w_in, fox_fb, mla_q_norm_g,
              mla_wq_up, mla_kv_norm_g, mla_wkv_up, gate_w, gate_b, branch_w, out_w,
              router_grp_w, router_grp_b, router_exp_w, router_exp_b, exp_w1, exp_w3, exp_w2,
              final_g):
    c_act = jax.nn.silu(c)
    for l in range(DEPTH_2):
        mod = c_act @ ada_w[l] + ada_b[l]
        sh1, sc1, gt1, sh2, sc2, gt2 = jnp.split(mod, 6, axis=-1)
        h = modulate(rms_norm(x, norm1_g[l]), sh1, sc1)
        mix = token_mixer(h, positions, w_in[l], fox_fb[l], mla_q_norm_g[l], mla_wq_up[l],
                          mla_kv_norm_g[l], mla_wkv_up[l], gate_w[l], gate_b[l], branch_w[l], out_w[l])
        x = x + gt1[:, None, :] * mix
        h = modulate(rms_norm(x, norm2_g[l]), sh2, sc2)
        ffn = hier_moe(h, router_grp_w[l], router_grp_b[l], router_exp_w[l], router_exp_b[l],
                       exp_w1[l], exp_w3[l], exp_w2[l])
        x = x + gt2[:, None, :] * ffn
    return rms_norm(x, final_g)


def setup_inputs(seed=0):
    out = dict(first_inputs(seed))
    for name, value in second_inputs(seed + 1).items():
        if name != "x":
            out[name + "_2"] = value
    return out


def reference(
    x, mem, positions, norm_mix_w, w_in, ssd_conv_w, ssd_conv_b, ssd_dt_bias, ssd_a_log, ssd_d,
    ssd_norm_w, dil_q_norm_w, dil_k_norm_w, mem_norm_w, w_mem_kv, mem_q_norm_w, mem_k_norm_w,
    w_ssd_br, w_dil_br, w_mem_br, w_out, norm_ffn_w, peer_w_query, peer_sub_keys, peer_down,
    peer_up, c_2, positions_2, ada_w_2, ada_b_2, norm1_g_2, norm2_g_2, w_in_2, fox_fb_2,
    mla_q_norm_g_2, mla_wq_up_2, mla_kv_norm_g_2, mla_wkv_up_2, gate_w_2, gate_b_2, branch_w_2,
    out_w_2, router_grp_w_2, router_grp_b_2, router_exp_w_2, router_exp_b_2, exp_w1_2, exp_w3_2,
    exp_w2_2, final_g_2,
):
    x = first_block(
        x, mem, positions, norm_mix_w, w_in, ssd_conv_w, ssd_conv_b, ssd_dt_bias, ssd_a_log,
        ssd_d, ssd_norm_w, dil_q_norm_w, dil_k_norm_w, mem_norm_w, w_mem_kv, mem_q_norm_w,
        mem_k_norm_w, w_ssd_br, w_dil_br, w_mem_br, w_out, norm_ffn_w, peer_w_query,
        peer_sub_keys, peer_down, peer_up,
    )
    return second_block(
        x, c_2, positions_2, ada_w_2, ada_b_2, norm1_g_2, norm2_g_2, w_in_2, fox_fb_2,
        mla_q_norm_g_2, mla_wq_up_2, mla_kv_norm_g_2, mla_wkv_up_2, gate_w_2, gate_b_2,
        branch_w_2, out_w_2, router_grp_w_2, router_grp_b_2, router_exp_w_2, router_exp_b_2,
        exp_w1_2, exp_w3_2, exp_w2_2, final_g_2,
    )


_drawn_inputs = setup_inputs


def setup_inputs(seed=0):
    import zlib

    import numpy as np

    out = dict(_drawn_inputs(seed))
    spreads = {}
    factors = {'dil_q_norm_w': 4.143,
     'dil_k_norm_w': 4.521,
     'mem_norm_w': 3.993,
     'mem_q_norm_w': 5.165,
     'mem_k_norm_w': 4.506,
     'norm1_g_2': 2.736,
     'mla_q_norm_g_2': 8.0,
     'mla_kv_norm_g_2': 8.0,
     'gate_b_2': 8.0,
     'router_grp_b_2': 31.663,
     'router_exp_b_2': 6.684}
    for name, (base, spread) in spreads.items():
        noise = np.random.default_rng([zlib.crc32(name.encode()), seed]).standard_normal(out[name].shape)
        drawn = base * np.exp(spread * noise) if base else spread * noise
        out[name] = __import__('jax').numpy.asarray(drawn.astype(out[name].dtype))
    for name, factor in factors.items():
        out[name] = (out[name] * factor).astype(out[name].dtype)
    return out
```

```python
import math
from contextlib import ExitStack, contextmanager

import numpy as np

import concourse.bass as bass
from concourse import mybir

F32 = mybir.dt.float32
I32 = mybir.dt.int32
U32 = mybir.dt.uint32
ALU = mybir.AluOpType
ACT = mybir.ActivationFunctionType
AX = mybir.AxisListType.X
ds = bass.ds

P = 128
T = 512
NT = T // P
D = 1024
KD = D // P
CH = 512
EPS = 1e-6
NEG = -1e30

N_MEM = 256
HEADS, GROUPS, HPG, HD, STATE = 16, 4, 4, 64, 128
CONV = 4
XBC = D + 2 * GROUPS * STATE
DIL = 3
DIL_W = 768
MEM_W = 768
OFF_Z, OFF_XBC = 0, D
OFF_DT = OFF_XBC + XBC
OFF_DQ = OFF_DT + HEADS
OFF_DK, OFF_DV, OFF_MQ = OFF_DQ + DIL_W, OFF_DQ + 2 * DIL_W, OFF_DQ + 3 * DIL_W
OFF_GATE = OFF_MQ + MEM_W
IN_W = OFF_GATE + 3 * D
PEER_H, NK, TOPK = 8, 128, 16
N_EXP1 = NK * NK
LAYERS = 2
D_IN2 = 3524
RQ, RK, RV, RG, FQ, FK, FV, FF, MQ2, MKV, MKR = (0, 256, 512, 1024, 1536, 2048, 2560, 3072, 3076, 3332, 3460)
N_EXPERTS, EPG, N_GRP, D_EXP = 32, 8, 4, 512


@contextmanager
def stage_sems(nc, *names):
    sems = [nc.alloc_semaphore(n) for n in names]
    yield sems
    nc.clear_and_free_semaphores(sems)
    nc.all_engine_barrier()


def chain(eng, sem):
    count = [0]

    def link(ins):
        count[0] += 1
        ins.then_inc(sem, 1)
        eng.wait_ge(sem, count[0])

    return link


def refined_root(nc, link, r, mean, tmp):
    link(nc.vector.reciprocal(r, r))
    link(nc.vector.tensor_tensor(tmp, r, r, ALU.mult))
    link(nc.vector.tensor_tensor(tmp, tmp, mean, ALU.mult))
    link(nc.vector.tensor_scalar(tmp, tmp, -0.5, 1.5, ALU.mult, ALU.add))
    link(nc.vector.tensor_tensor(r, r, tmp, ALU.mult))


def take_bank(nc, bank, ident):
    nc.tensor.transpose(bank, ident[:, :], ident[:, :])


def tiled(x):
    return x.rearrange("(t p) n -> p t n", p=P)


def row_bc(row, parts=P):
    return row.rearrange("(o n) -> o n", o=1).broadcast_to([parts, row.shape[0]])


def bc_mid(ap, n):
    return ap.rearrange("p (o a) -> p o a", o=1).broadcast_to([ap.shape[0], n, ap.shape[1]])


def bc_last(ap, n):
    return ap.rearrange("p (a o) -> p a o", o=1).broadcast_to([ap.shape[0], ap.shape[1], n])


def linear(nc, tag, psum, xT, kc, w, out, n_cols, tiles=NT, feature_major=False, m=P):
    full, tail = n_cols // CH, n_cols % CH
    w_v = w.rearrange("(k p) n -> p k n", p=P)
    blocks = CH // P if feature_major else tiles
    width = tiles * P if feature_major else CH
    with ExitStack() as ctx:
        wbuf = ctx.enter_context(nc.sbuf_tensor(f"{tag}_w", [P, 2, kc, CH], F32))
        obuf = ctx.enter_context(nc.sbuf_tensor(f"{tag}_o", [P, 2, 4, CH], F32))
        (w_in0, w_in1, tile_done, evac_v, evac_a, out0, out1) = ctx.enter_context(stage_sems(
            nc, *[f"{tag}_{s}" for s in ("w_in0", "w_in1", "tile", "ev", "ea", "out0", "out1")]))
        w_in, stored = (w_in0, w_in1), (out0, out1)
        pairs, odd = full // 2, full % 2
        on_v = (blocks + 1) // 2
        on_a = blocks - on_v

        def chunks(eng, body):
            if pairs:
                with eng.Fori(0, pairs) as i:
                    for u in range(2):
                        body(i * 2 + u, u, i, CH)
            if odd:
                body(full - 1, 0, pairs, CH)
            if tail:
                body(full, odd, pairs, tail)

        with nc.Block() as block:
            @block.sync
            def _(sp):
                def load(j, u, turn, cols):
                    sp.wait_ge(tile_done, j * blocks + blocks)
                    sp.dma_start(wbuf[:, u, :, 0:cols], w_v[:, :, ds(j * CH, cols)]).then_inc(w_in[u], 16)
                chunks(sp, load)

            @block.tensor
            def _(pe):
                pe.sem_inc(tile_done, 2 * blocks)

                def multiply(j, u, turn, cols):
                    pe.wait_ge(w_in[u], turn * 16 + 16)
                    pe.wait_ge(evac_v, j * on_v + on_v)
                    if on_a:
                        pe.wait_ge(evac_a, j * on_a + on_a)
                    for b in range(blocks):
                        for k in range(kc):
                            if feature_major:
                                o, l, r = psum[:, u * 4 + b, 0:width], wbuf[:, u, k, b * P:(b + 1) * P], xT[:, k, 0:width]
                            else:
                                o, l, r = psum[0:m, u * 4 + b, 0:cols], xT[:, k, b * P:b * P + m], wbuf[:, u, k, 0:cols]
                            last = nc.tensor.matmul(o, l, r, start=k == 0, stop=k == kc - 1)
                        last.then_inc(tile_done, 1)
                chunks(pe, multiply)

            @block.vector
            def _(dve):
                dve.sem_inc(evac_v, 2 * on_v)

                def evacuate(j, u, turn, cols):
                    dve.wait_ge(stored[u], turn * 16 + 16)
                    n = width if feature_major else cols
                    for b in range(on_v):
                        dve.wait_ge(tile_done, j * blocks + (2 * blocks + b + 1))
                        nc.vector.tensor_copy(obuf[0:m, u, b, 0:n], psum[0:m, u * 4 + b, 0:n]).then_inc(evac_v, 1)
                chunks(dve, evacuate)

            @block.scalar
            def _(act):
                act.sem_inc(evac_a, 2 * on_a) if on_a else None
                act.sem_inc(out0, 16)
                act.sem_inc(out1, 16)

                def evacuate_store(j, u, turn, cols):
                    act.wait_ge(stored[u], turn * 16 + 16)
                    n = width if feature_major else cols
                    for b in range(on_v, blocks):
                        act.wait_ge(tile_done, j * blocks + (2 * blocks + b + 1))
                        nc.scalar.copy(obuf[0:m, u, b, 0:n], psum[0:m, u * 4 + b, 0:n]).then_inc(evac_a, 1)
                    act.wait_ge(evac_v, j * on_v + 3 * on_v)
                    if on_a:
                        act.wait_ge(evac_a, j * on_a + 3 * on_a)
                    if feature_major:
                        dst = out[ds(j * CH, CH), 0:width].rearrange("(b p) t -> p b t", p=P)
                        src = obuf[:, u, :, 0:width]
                    elif m == 1:
                        dst, src = out[:, ds(j * CH, cols)], obuf[0:1, u, 0, 0:cols]
                    else:
                        dst, src = tiled(out)[:, :, ds(j * CH, cols)], obuf[:, u, 0:tiles, 0:cols]
                    act.dma_start(dst, src).then_inc(stored[u], 16)
                chunks(act, evacuate_store)
                last = [0, 0]
                for j in range(full + bool(tail)):
                    last[j % 2] += 16
                act.wait_ge(out0, last[0] + 16)
                act.wait_ge(out1, last[1] + 16)


def norm_transpose(nc, tag, psum, ident, x, gain, xT, tiles=NT, width=D, shift=None, scale=None, keep=None):
    kc = width // P
    with ExitStack() as ctx:
        sb = lambda n, s, d=F32: ctx.enter_context(nc.sbuf_tensor(f"{tag}_{n}", s, d))
        gain_sb, y = sb("gain", [P, width]), sb("y", [P, tiles, width])
        sq, stat = sb("sq", [P, width]), sb("stat", [P, tiles, 4])
        shift_sb = sb("shift", [P, width]) if shift is not None else None
        scale_sb = sb("scale", [P, width]) if shift is not None else None
        rows_in, mean_ready, root_ready, y_ready, transposed, evacuated, dve_order, kept = ctx.enter_context(stage_sems(
            nc, *[f"{tag}_{s}" for s in ("rows", "mean", "root", "y", "tr", "ev", "dve", "kept")]))
        with nc.Block() as block:
            @block.sync
            def _(sp):
                sp.dma_start(gain_sb[:, :], row_bc(gain)).then_inc(rows_in, 16)
                if shift is not None:
                    sp.dma_start(shift_sb[:, :], row_bc(shift)).then_inc(rows_in, 16)
                    sp.dma_start(scale_sb[:, :], row_bc(scale)).then_inc(rows_in, 16)
                if keep is not None:
                    sp.wait_ge(y_ready, tiles)
                    sp.dma_start(tiled(keep), y[:, :, :]).then_inc(kept, 16)
                    sp.wait_ge(kept, 16)

            @block.vector
            def _(dve):
                link = chain(dve, dve_order)
                for t in range(tiles):
                    link(nc.vector.tensor_tensor_reduce(out=sq[:, :], in0=x[:, t, :], in1=x[:, t, :], scale=1.0, scalar=0.0,
                                                        op0=ALU.mult, op1=ALU.add, accum_out=stat[:, t, 0:1]))
                    nc.vector.tensor_scalar(stat[:, t, 1:2], stat[:, t, 0:1], 1.0 / width, EPS, ALU.mult,
                                            ALU.add).then_inc(mean_ready, 1)
                dve.wait_ge(rows_in, 48 if shift is not None else 16)
                if shift is not None:
                    link(nc.vector.tensor_scalar(scale_sb[:, :], scale_sb[:, :], 1.0, None, ALU.add))
                for t in range(tiles):
                    dve.wait_ge(root_ready, t + 1)
                    refined_root(nc, link, stat[:, t, 2:3], stat[:, t, 1:2], stat[:, t, 3:4])
                    ins = nc.vector.scalar_tensor_tensor(out=y[:, t, :], in0=x[:, t, :], scalar=stat[:, t, 2:3],
                                                         in1=gain_sb[:, :], op0=ALU.mult, op1=ALU.mult)
                    if shift is not None:
                        link(ins)
                        link(nc.vector.tensor_tensor(y[:, t, :], y[:, t, :], scale_sb[:, :], ALU.mult))
                        ins = nc.vector.tensor_tensor(y[:, t, :], y[:, t, :], shift_sb[:, :], ALU.add)
                    ins.then_inc(y_ready, 1)

            @block.scalar
            def _(act):
                for t in range(tiles):
                    act.wait_ge(mean_ready, t + 1)
                    nc.scalar.activation(stat[:, t, 2:3], stat[:, t, 1:2], ACT.Sqrt).then_inc(root_ready, 1)
                for k in range(kc):
                    act.wait_ge(transposed, k + 1)
                    nc.scalar.copy(xT[:, k, 0:tiles * P], psum[:, k % 4, 0:tiles * P]).then_inc(evacuated, 1)

            @block.tensor
            def _(pe):
                pe.wait_ge(y_ready, tiles)
                for k in range(kc):
                    if k >= 4:
                        pe.wait_ge(evacuated, k - 3)
                    for t in range(tiles):
                        last = nc.tensor.transpose(psum[:, k % 4, t * P:(t + 1) * P], y[:, t, k * P:(k + 1) * P], ident[:, :])
                    last.then_inc(transposed, 1)


def load_transpose(nc, tag, psum, ident, src, xT, width, tiles=NT):
    kc = width // P
    with ExitStack() as ctx:
        x = ctx.enter_context(nc.sbuf_tensor(f"{tag}_x", [P, tiles, width], F32))
        x_in, transposed, evacuated = ctx.enter_context(stage_sems(nc, *[f"{tag}_{s}" for s in ("in", "tr", "ev")]))
        with nc.Block() as block:
            @block.sync
            def _(sp):
                sp.dma_start(x[:, :, :], tiled(src)).then_inc(x_in, 16)

            @block.tensor
            def _(pe):
                pe.wait_ge(x_in, 16)
                for k in range(kc):
                    if k >= 4:
                        pe.wait_ge(evacuated, k - 3)
                    for t in range(tiles):
                        last = nc.tensor.transpose(psum[:, k % 4, t * P:(t + 1) * P], x[:, t, k * P:(k + 1) * P], ident[:, :])
                    last.then_inc(transposed, 1)

            @block.scalar
            def _(act):
                for k in range(kc):
                    act.wait_ge(transposed, k + 1)
                    nc.scalar.copy(xT[:, k, 0:tiles * P], psum[:, k % 4, 0:tiles * P]).then_inc(evacuated, 1)


def conv_silu(nc, tag, psum, ident, xbcT, taps, convT, conv_tok):
    n = XBC // P
    PAD = CONV - 1
    with ExitStack() as ctx:
        sb = lambda m, s: ctx.enter_context(nc.sbuf_tensor(f"{tag}_{m}", s, F32))
        x, w, acc = sb("x", [P, 2, PAD + T]), sb("w", [P, 2, CONV + 1]), sb("acc", [P, 2, T])
        y, tok = sb("y", [P, 2, T]), sb("tok", [P, 2, NT, P])
        (in0, in1, acc_ready, y_ready, transposed, tok_ready, dve_order, out0, out1, padded) = ctx.enter_context(stage_sems(
            nc, *[f"{tag}_{s}" for s in ("in0", "in1", "acc", "y", "tr", "tok", "dve", "out0", "out1", "pad")]))
        loaded, stored = (in0, in1), (out0, out1)
        with nc.Block() as block:
            @block.sync
            def _(sp):
                sp.wait_ge(padded, 1)
                with sp.Fori(0, n // 2) as i:
                    for u in range(2):
                        sp.wait_ge(acc_ready, i * 2 + u + 1)
                        sp.dma_start(x[:, u, PAD:PAD + T], xbcT[ds((i * 2 + u) * P, P), :]).then_inc(loaded[u], 16)
                        sp.dma_start(w[:, u, :], taps[ds((i * 2 + u) * P, P), :]).then_inc(loaded[u], 16)

            @block.vector
            def _(dve):
                nc.vector.memset(x[:, :, 0:PAD], 0.0).then_inc(padded, 1)
                dve.sem_inc(acc_ready, 2)
                with dve.Fori(0, n // 2) as i:
                    dve.sem_clear(dve_order)
                    link = chain(dve, dve_order)
                    for u in range(2):
                        dve.wait_ge(loaded[u], i * 32 + 32)
                        dve.wait_ge(y_ready, i * 2 + u + 1)
                        link(nc.vector.tensor_scalar(acc[:, u, :], x[:, u, 0:T], w[:, u, 0:1], w[:, u, CONV:CONV + 1], ALU.mult, ALU.add))
                        for j in range(1, CONV):
                            ins = nc.vector.scalar_tensor_tensor(out=acc[:, u, :], in0=x[:, u, j:j + T], scalar=w[:, u, j:j + 1],
                                                                 in1=acc[:, u, :], op0=ALU.mult, op1=ALU.add)
                            if j < CONV - 1:
                                link(ins)
                        ins.then_inc(acc_ready, 1)
                    for u in range(2):
                        dve.wait_ge(transposed, i * 2 + u + 1)
                        nc.vector.tensor_copy(tok[:, u, :, :], psum[:, u, :].rearrange("p (t c) -> p t c", c=P)).then_inc(tok_ready, 1)

            @block.scalar
            def _(act):
                act.sem_inc(y_ready, 2)
                act.sem_inc(out0, 32)
                act.sem_inc(out1, 32)
                with act.Fori(0, n // 2) as i:
                    for u in range(2):
                        act.wait_ge(acc_ready, i * 2 + u + 3)
                        act.wait_ge(stored[u], i * 32 + 32)
                        nc.scalar.activation(y[:, u, :], acc[:, u, :], ACT.Silu).then_inc(y_ready, 1)
                        act.wait_ge(y_ready, i * 2 + u + 3)
                        act.dma_start(convT[ds((i * 2 + u) * P, P), :], y[:, u, :]).then_inc(stored[u], 16)
                    for u in range(2):
                        act.wait_ge(tok_ready, i * 2 + u + 1)
                        act.dma_start(tiled(conv_tok)[:, :, ds((i * 2 + u) * P, P)], tok[:, u, :, :]).then_inc(stored[u], 16)
                act.wait_ge(out0, n // 2 * 32 + 32)
                act.wait_ge(out1, n // 2 * 32 + 32)

            @block.tensor
            def _(pe):
                with pe.Fori(0, n // 2) as i:
                    for u in range(2):
                        pe.wait_ge(y_ready, i * 2 + u + 3)
                        pe.wait_ge(acc_ready, i * 2 + u + 3)
                        for t in range(NT):
                            last = nc.tensor.transpose(psum[:, u, t * P:(t + 1) * P], y[:, u, t * P:(t + 1) * P], ident[:, :])
                        last.then_inc(transposed, 1)


def ssd_dt(nc, tag, dt_raw, dt_bias, a_log, dt, da):
    with ExitStack() as ctx:
        sb = lambda m, s: ctx.enter_context(nc.sbuf_tensor(f"{tag}_{m}", s, F32))
        x, e, b, a = sb("x", [P, NT, HEADS]), sb("e", [P, NT, HEADS]), sb("b", [P, HEADS]), sb("a", [P, HEADS])
        xin, abs_ready, act_order, ln_ready, dve_order, out_ready, stored = ctx.enter_context(stage_sems(
            nc, *[f"{tag}_{s}" for s in ("in", "abs", "act", "ln", "dve", "rdy", "out")]))
        with nc.Block() as block:
            @block.sync
            def _(sp):
                sp.dma_start(x[:, :, :], tiled(dt_raw)).then_inc(xin, 16)
                sp.dma_start(b[:, :], row_bc(dt_bias)).then_inc(xin, 16)
                sp.dma_start(a[:, :], row_bc(a_log)).then_inc(xin, 16)
                sp.wait_ge(out_ready, 2)
                sp.dma_start(tiled(dt), x[:, :, :]).then_inc(stored, 16)
                sp.dma_start(tiled(da), e[:, :, :]).then_inc(stored, 16)
                sp.wait_ge(stored, 32)

            @block.vector
            def _(dve):
                link = chain(dve, dve_order)
                dve.wait_ge(xin, 48)
                link(nc.vector.tensor_tensor(x[:, :, :], x[:, :, :], bc_mid(b[:, :], NT), ALU.add))
                link(nc.vector.tensor_scalar(e[:, :, :], x[:, :, :], -1.0, None, ALU.mult))
                nc.vector.tensor_tensor(e[:, :, :], e[:, :, :], x[:, :, :], ALU.min).then_inc(abs_ready, 1)
                dve.wait_ge(ln_ready, 1)
                link(nc.vector.scalar_tensor_tensor(out=x[:, :, :], in0=x[:, :, :], scalar=0.0, in1=e[:, :, :], op0=ALU.max, op1=ALU.add))
                dve.wait_ge(ln_ready, 2)
                link(nc.vector.tensor_scalar(a[:, :], a[:, :], -1.0, None, ALU.mult))
                nc.vector.tensor_tensor(e[:, :, :], x[:, :, :], bc_mid(a[:, :], NT), ALU.mult).then_inc(out_ready, 2)

            @block.scalar
            def _(act):
                link = chain(act, act_order)
                act.wait_ge(abs_ready, 1)
                link(nc.scalar.activation(e[:, :, :], e[:, :, :], ACT.Exp))
                nc.scalar.activation(e[:, :, :], e[:, :, :], ACT.Ln, bias=1.0).then_inc(ln_ready, 1)
                act.wait_ge(xin, 48)
                nc.scalar.activation(a[:, :], a[:, :], ACT.Exp).then_inc(ln_ready, 1)


def ssd_scan(nc, tag, psum, tri, convT, conv_tok, dt, da, d_skip, y_out):
    GW = HPG * HD
    with ExitStack() as ctx:
        sb = lambda m, s: ctx.enter_context(nc.sbuf_tensor(f"{tag}_{m}", s, F32))
        bT, cT, b_tok = sb("bT", [P, P]), sb("cT", [P, P]), sb("b", [P, P])
        x, dtc, dac, dsk = sb("x", [P, GW]), sb("dt", [P, HPG]), sb("da", [P, HPG]), sb("dsk", [P, HEADS])
        dskg = sb("dskg", [P, HPG])
        da_bc, cbm, acum = sb("dabc", [P, HPG, P]), sb("cbm", [P, P]), sb("acum", [P, HPG])
        arg, lmat, mmat = sb("arg", [P, HPG, P]), sb("lmat", [P, HPG, P]), sb("mmat", [P, HPG, P])
        small, smalle = sb("small", [P, 3, HPG]), sb("smalle", [P, 3, HPG])
        xdt, xdec, state, y = sb("xdt", [P, GW]), sb("xdec", [P, GW]), sb("state", [P, GW]), sb("y", [P, GW])
        heads = lambda ap: ap.rearrange("p (h d) -> p h d", d=HD)
        rdy = lambda ap: ap.rearrange("p (h s) -> p h s", s=P)
        (loaded, bc_ready, pe_a, arg_ready, exp_ready, ops_ready, pe_b, y_ready, stored, dve_order) = ctx.enter_context(stage_sems(
            nc, *[f"{tag}_{s}" for s in ("in", "bc", "pea", "arg", "exp", "ops", "peb", "y", "out", "dve")]))
        with nc.Block() as block:
            @block.sync
            def _(sp):
                with sp.Fori(0, GROUPS) as g:
                    with sp.Fori(0, NT) as c:
                        n = g * NT + c
                        sp.wait_ge(y_ready, n + 1)
                        sp.dma_start(bT[:, :], convT[ds(g * P + D, P), ds(c * P, P)]).then_inc(loaded, 16)
                        sp.dma_start(cT[:, :], convT[ds(g * P + (D + GROUPS * STATE), P), ds(c * P, P)]).then_inc(loaded, 16)
                        sp.dma_start(b_tok[:, :], conv_tok[ds(c * P, P), ds(g * P + D, P)]).then_inc(loaded, 16)
                        sp.dma_start(x[:, :], conv_tok[ds(c * P, P), ds(g * GW, GW)]).then_inc(loaded, 16)
                        sp.dma_start(dtc[:, :], dt[ds(c * P, P), ds(g * HPG, HPG)]).then_inc(loaded, 16)
                        sp.dma_start(dac[:, :], da[ds(c * P, P), ds(g * HPG, HPG)]).then_inc(loaded, 16)
                        sp.dma_start(dskg[:, :], row_bc(d_skip[ds(g * HPG, HPG)])).then_inc(loaded, 16)
                        sp.wait_ge(y_ready, n + 2)
                        sp.dma_start(y_out[ds(c * P, P), ds(g * GW, GW)], y[:, :]).then_inc(stored, 16)
                sp.wait_ge(stored, 16 * GROUPS * NT + 16)

            @block.vector
            def _(dve):
                dve.sem_inc(y_ready, 1)
                dve.sem_inc(stored, 16)
                with dve.Fori(0, GROUPS) as g:
                    nc.vector.memset(state[:, :], 0.0)
                    with dve.Fori(0, NT) as c:
                        n = g * NT + c
                        dve.sem_clear(dve_order)
                        link = chain(dve, dve_order)
                        dve.wait_ge(loaded, n * 112 + 112)
                        nc.vector.tensor_copy(da_bc[:, :, :], bc_last(dac[:, :], P)).then_inc(bc_ready, 1)
                        link(nc.vector.tensor_tensor(heads(xdt[:, :]), heads(x[:, :]), bc_last(dtc[:, :], HD), ALU.mult))
                        dve.wait_ge(pe_a, n + 1)
                        nc.vector.tensor_tensor(cbm[:, :], psum[:, 1, 0:P], tri[:, :], ALU.mult)
                        link(nc.vector.tensor_copy(small[:, 0, :], psum[:, 1, P:P + HPG]))
                        link(nc.vector.tensor_copy(small[:, 1, :], rdy(psum[:, 0, :])[:, :, P - 1]))
                        link(nc.vector.tensor_tensor(small[:, 2, :], small[:, 1, :], small[:, 0, :], ALU.subtract))
                        for r in range(HPG):
                            ins = nc.vector.tensor_scalar(arg[:, r, :], psum[:, 0, r * P:(r + 1) * P], small[:, 0, r:r + 1], 0.0,
                                                          ALU.subtract, ALU.min)
                        ins.then_inc(arg_ready, 1)
                        dve.wait_ge(exp_ready, n + 1)
                        nc.vector.tensor_tensor(mmat[:, :, :], lmat[:, :, :], bc_mid(cbm[:, :], HPG), ALU.mult)
                        nc.vector.tensor_tensor(heads(xdec[:, :]), heads(xdt[:, :]), bc_last(smalle[:, 2, :], HD), ALU.mult).then_inc(ops_ready, 1)
                        dve.wait_ge(pe_b, n + 1)
                        dve.wait_ge(stored, n * 16 + 16)
                        link(nc.vector.tensor_tensor(heads(y[:, :]), heads(psum[:, 2, 0:GW]), bc_last(smalle[:, 0, :], HD), ALU.mult))
                        link(nc.vector.tensor_tensor(y[:, :], y[:, :], psum[:, 3, 0:GW], ALU.add))
                        link(nc.vector.tensor_tensor(heads(x[:, :]), heads(x[:, :]), bc_last(dskg[:, :], HD), ALU.mult))
                        link(nc.vector.tensor_tensor(heads(state[:, :]), heads(state[:, :]), bc_last(smalle[:, 1, :], HD), ALU.mult))
                        link(nc.vector.tensor_tensor(state[:, :], state[:, :], psum[:, 4, 0:GW], ALU.add))
                        link(nc.vector.tensor_tensor(y[:, :], y[:, :], x[:, :], ALU.add))
                        dve.sem_inc(y_ready, 1)

            @block.scalar
            def _(act):
                with act.Fori(0, GROUPS * NT) as n:
                    act.wait_ge(arg_ready, n + 1)
                    nc.scalar.activation(smalle[:, :, :], small[:, :, :], ACT.Exp)
                    nc.scalar.activation(lmat[:, :, :], arg[:, :, :], ACT.Exp).then_inc(exp_ready, 1)

            @block.tensor
            def _(pe):
                with pe.Fori(0, GROUPS * NT) as n:
                    pe.wait_ge(bc_ready, n + 1)
                    nc.tensor.matmul(psum[:, 1, 0:P], bT[:, :], cT[:, :], start=True, stop=True)
                    nc.tensor.matmul(psum[:, 1, P:P + HPG], tri[:, :], dac[:, :], start=True, stop=True)
                    for r in range(HPG):
                        last = nc.tensor.matmul(psum[:, 0, r * P:(r + 1) * P], da_bc[:, r, :], tri[:, :], start=True, stop=True)
                    last.then_inc(pe_a, 1)
                    pe.wait_ge(ops_ready, n + 1)
                    nc.tensor.matmul(psum[:, 2, 0:GW], cT[:, :], state[:, :], start=True, stop=True)
                    nc.tensor.matmul(psum[:, 4, 0:GW], b_tok[:, :], xdec[:, :], start=True, stop=True)
                    for r in range(HPG):
                        last = nc.tensor.matmul(psum[:, 3, r * HD:(r + 1) * HD], mmat[:, r, :], xdt[:, r * HD:(r + 1) * HD], start=True, stop=True)
                    last.then_inc(pe_b, 1)


def ssd_gate_norm(nc, tag, y, z, norm_w, out):
    GW = D // GROUPS
    with ExitStack() as ctx:
        sb = lambda m, s: ctx.enter_context(nc.sbuf_tensor(f"{tag}_{m}", s, F32))
        ys, zs, w = sb("y", [P, NT, D]), sb("z", [P, NT, D]), sb("w", [P, D])
        sq, st, rt, tp = sb("sq", [P, D]), sb("st", [P, NT, GROUPS]), sb("rt", [P, NT, GROUPS]), sb("tp", [P, NT, GROUPS])
        xin, silu_ready, mean_ready, root_ready, dve_order, y_ready, stored = ctx.enter_context(stage_sems(
            nc, *[f"{tag}_{s}" for s in ("in", "silu", "mean", "root", "dve", "y", "out")]))
        grp = lambda ap: ap.rearrange("p (g d) -> p g d", g=GROUPS)
        with nc.Block() as block:
            @block.sync
            def _(sp):
                sp.dma_start(zs[:, :, :], tiled(z)).then_inc(xin, 16)
                sp.dma_start(ys[:, :, :], tiled(y)).then_inc(xin, 16)
                sp.dma_start(w[:, :], row_bc(norm_w)).then_inc(xin, 16)
                sp.wait_ge(y_ready, NT)
                sp.dma_start(tiled(out), ys[:, :, :]).then_inc(stored, 16)
                sp.wait_ge(stored, 16)

            @block.scalar
            def _(act):
                act.wait_ge(xin, 48)
                for t in range(NT):
                    nc.scalar.activation(zs[:, t, :], zs[:, t, :], ACT.Silu).then_inc(silu_ready, 1)
                act.wait_ge(mean_ready, 1)
                nc.scalar.activation(rt[:, :, :], st[:, :, :], ACT.Sqrt).then_inc(root_ready, 1)

            @block.vector
            def _(dve):
                link = chain(dve, dve_order)
                for t in range(NT):
                    dve.wait_ge(silu_ready, t + 1)
                    link(nc.vector.tensor_tensor(ys[:, t, :], ys[:, t, :], zs[:, t, :], ALU.mult))
                    link(nc.vector.tensor_tensor(sq[:, :], ys[:, t, :], ys[:, t, :], ALU.mult))
                    link(nc.vector.tensor_reduce(st[:, t, :], grp(sq[:, :]), AX, ALU.add))
                nc.vector.tensor_scalar(st[:, :, :], st[:, :, :], 1.0 / GW, EPS, ALU.mult, ALU.add).then_inc(mean_ready, 1)
                dve.wait_ge(root_ready, 1)
                refined_root(nc, link, rt[:, :, :], st[:, :, :], tp[:, :, :])
                for t in range(NT):
                    link(nc.vector.tensor_tensor(grp(ys[:, t, :]), grp(ys[:, t, :]), bc_last(rt[:, t, :], GW), ALU.mult))
                    nc.vector.tensor_tensor(ys[:, t, :], ys[:, t, :], w[:, :], ALU.mult).then_inc(y_ready, 1)


def rope_tables(nc, tag, positions, inv, half, cos_sb, sin_sb):
    two_pi = 2.0 * math.pi
    c1 = 6.28125
    c2 = float(np.float32(two_pi - c1) * 1.0)
    c2 = math.floor(c2 * 2 ** 20) / 2 ** 20
    c3 = two_pi - c1 - c2
    with ExitStack() as ctx:
        sb = lambda m, s, d=F32: ctx.enter_context(nc.sbuf_tensor(f"{tag}_{m}", s, d))
        pos_i, pos, inv_sb = sb("pi", [P, NT], I32), sb("p", [P, NT]), sb("inv", [P, half])
        ang, k, ki, hs = sb("ang", [P, NT, half]), sb("k", [P, NT, half]), sb("ki", [P, NT, half], I32), sb("hs", [P, NT, half])
        xin, ang_ready, sin_ready, dve_order = ctx.enter_context(stage_sems(nc, *[f"{tag}_{s}" for s in ("in", "ang", "sin", "dve")]))
        with nc.Block() as block:
            @block.sync
            def _(sp):
                with nc.allow_non_contiguous_dma("the positions, one to a partition"):
                    sp.dma_start(pos_i[:, :], positions.rearrange("(t p) -> p t", p=P)).then_inc(xin, 16)
                sp.dma_start(inv_sb[:, :], row_bc(inv)).then_inc(xin, 16)

            @block.vector
            def _(dve):
                link = chain(dve, dve_order)
                dve.wait_ge(xin, 32)
                link(nc.vector.tensor_copy(pos[:, :], pos_i[:, :]))
                link(nc.vector.tensor_tensor(ang[:, :, :], bc_last(pos[:, :], half), bc_mid(inv_sb[:, :], NT), ALU.mult))
                link(nc.vector.tensor_scalar(k[:, :, :], ang[:, :, :], 1.0 / two_pi, None, ALU.mult))
                link(nc.vector.tensor_copy(ki[:, :, :], k[:, :, :]))
                link(nc.vector.tensor_copy(k[:, :, :], ki[:, :, :]))
                for c in (c1, c2, c3):
                    link(nc.vector.scalar_tensor_tensor(out=ang[:, :, :], in0=k[:, :, :], scalar=-c, in1=ang[:, :, :], op0=ALU.mult, op1=ALU.add))
                link(nc.vector.tensor_scalar(k[:, :, :], ang[:, :, :], math.pi, -two_pi, ALU.is_gt, ALU.mult))
                link(nc.vector.tensor_tensor(k[:, :, :], k[:, :, :], ang[:, :, :], ALU.add))
                link(nc.vector.tensor_scalar(ang[:, :, :], k[:, :, :], -math.pi, two_pi, ALU.is_lt, ALU.mult))
                link(nc.vector.tensor_tensor(ang[:, :, :], k[:, :, :], ang[:, :, :], ALU.add))
                lim = 3.1415925
                nc.vector.tensor_scalar(ang[:, :, :], ang[:, :, :], lim, -lim, ALU.min, ALU.max).then_inc(ang_ready, 1)
                dve.wait_ge(sin_ready, 1)
                link(nc.vector.tensor_tensor(hs[:, :, :], hs[:, :, :], hs[:, :, :], ALU.mult))
                link(nc.vector.tensor_scalar(cos_sb[:, :, :], hs[:, :, :], -2.0, 1.0, ALU.mult, ALU.add))

            @block.scalar
            def _(act):
                act.wait_ge(ang_ready, 1)
                nc.scalar.activation(sin_sb[:, :, :], ang[:, :, :], ACT.Sin)
                nc.scalar.activation(hs[:, :, :], ang[:, :, :], ACT.Sin, scale=0.5).then_inc(sin_ready, 1)


def head_prep(nc, tag, src, dst, heads, hd, gain=None, cos=None, sin=None, rot=0, rot_at=0):
    half = rot // 2
    with ExitStack() as ctx:
        sb = lambda m, s: ctx.enter_context(nc.sbuf_tensor(f"{tag}_{m}", s, F32))
        x, sq = sb("x", [P, NT, heads, hd]), sb("sq", [P, heads, hd])
        st, g = sb("st", [P, NT, heads]), sb("g", [P, hd])
        rt, tp = sb("rt", [P, NT, heads]), sb("tp", [P, NT, heads])
        if rot:
            ta, tb, tc = sb("ta", [P, heads, half]), sb("tb", [P, heads, half]), sb("tc", [P, heads, half])
        rows = src.shape[0] // P
        xin, mean_ready, root_ready, dve_order, y_ready, stored = ctx.enter_context(stage_sems(
            nc, *[f"{tag}_{s}" for s in ("in", "mean", "root", "dve", "y", "out")]))
        if len(src.shape) == 2:
            src = src.rearrange("t (h d) -> t h d", h=heads)
        with nc.Block() as block:
            @block.sync
            def _(sp):
                for t in range(rows):
                    sp.dma_start(x[:, t, :, :], src[t * P:(t + 1) * P, :, :]).then_inc(xin, 16)
                if gain is not None:
                    sp.dma_start(g[:, :], row_bc(gain)).then_inc(xin, 16)
                sp.wait_ge(y_ready, 1)
                for t in range(rows):
                    sp.dma_start(dst[t * P:(t + 1) * P, :, :], x[:, t, :, :]).then_inc(stored, 16)
                sp.wait_ge(stored, 16 * rows)

            @block.vector
            def _(dve):
                link = chain(dve, dve_order)
                dve.wait_ge(xin, 16 * rows + (16 if gain is not None else 0))
                if gain is not None:
                    for t in range(rows):
                        link(nc.vector.tensor_tensor(sq[:, :, :], x[:, t, :, :], x[:, t, :, :], ALU.mult))
                        link(nc.vector.tensor_reduce(st[:, t, :], sq[:, :, :], AX, ALU.add))
                    nc.vector.tensor_scalar(st[:, 0:rows, :], st[:, 0:rows, :], 1.0 / hd, EPS, ALU.mult, ALU.add).then_inc(mean_ready, 1)
                    dve.wait_ge(root_ready, 1)
                    refined_root(nc, link, rt[:, 0:rows, :], st[:, 0:rows, :], tp[:, 0:rows, :])
                    for t in range(rows):
                        link(nc.vector.tensor_tensor(x[:, t, :, :], x[:, t, :, :], bc_last(rt[:, t, :], hd), ALU.mult))
                        link(nc.vector.tensor_tensor(x[:, t, :, :], x[:, t, :, :], bc_mid(g[:, :], heads), ALU.mult))
                for t in range(rows if rot else 0):
                    x1 = x[:, t, :, rot_at:rot_at + half]
                    x2 = x[:, t, :, rot_at + half:rot_at + rot]
                    cs, sn = bc_mid(cos[:, t, :], heads), bc_mid(sin[:, t, :], heads)
                    link(nc.vector.tensor_tensor(ta[:, :, :], x1, sn, ALU.mult))
                    link(nc.vector.tensor_tensor(tb[:, :, :], x2, sn, ALU.mult))
                    link(nc.vector.tensor_tensor(tc[:, :, :], x2, cs, ALU.mult))
                    link(nc.vector.tensor_tensor(x1, x1, cs, ALU.mult))
                    link(nc.vector.tensor_tensor(x1, x1, tb[:, :, :], ALU.subtract))
                    link(nc.vector.tensor_tensor(x2, tc[:, :, :], ta[:, :, :], ALU.add))
                dve.sem_inc(y_ready, 1)

            @block.scalar
            def _(act):
                if gain is not None:
                    act.wait_ge(mean_ready, 1)
                    nc.scalar.activation(rt[:, 0:rows, :], st[:, 0:rows, :], ACT.Sqrt).then_inc(root_ready, 1)


def attention(nc, tag, psum, ident, q, k, v, o, splits, dv, scale, key_tiles, mask=None, span=None, lse=None):
    H = 4
    d = sum(splits)
    nch = len(splits)
    offs = [sum(splits[:i]) for i in range(nch)]
    span = span or (lambda qt: (0, key_tiles))
    with ExitStack() as ctx:
        sb = lambda m, s: ctx.enter_context(nc.sbuf_tensor(f"{tag}_{m}", s, F32))
        qs, ks, vs = sb("q", [P, 2, NT, d]), sb("k", [P, 2, key_tiles, d]), sb("v", [P, 2, key_tiles, dv])
        qT, kT = sb("qT", [P, nch, T]), sb("kT", [P, nch, key_tiles * P])
        ms = sb("mask", [P, NT, T]) if mask is not None else None
        s_sb, p_sb, pT = sb("s", [P, 2, key_tiles * P]), sb("p", [P, 2, key_tiles * P]), sb("pT", [P, 2, key_tiles, P])
        os_, st = sb("o", [P, 2, NT, dv]), sb("st", [P, 2, NT, 4])
        (in0, in1, mask_in, qk_tr, q_ev, k_ev, s_done, s_copied, nm_ready, e_done, pt_done, pt_ev, o_done, o_ev, out0, out1,
         dve_order, ln_done) = ctx.enter_context(stage_sems(nc, *[f"{tag}_{s}" for s in (
             "in0", "in1", "mask", "qktr", "qev", "kev", "sdone", "scp", "nm", "edone", "ptdone", "ptev", "odone", "oev",
             "out0", "out1", "dve", "ln")]))
        loaded, stored = (in0, in1), (out0, out1)
        n_out = 16 * NT
        tt = NT * 16
        kt16 = key_tiles * 16
        per_load = tt + 2 * kt16
        per_store = n_out * (2 if lse is not None else 1)
        with nc.Block() as block:
            @block.sync
            def _(sp):
                if mask is not None:
                    sp.dma_start(ms[:, :, :], tiled(mask)).then_inc(mask_in, 16)

                def load(h):
                    u = h % 2
                    for t in range(NT):
                        sp.dma_start(qs[:, u, t, :], q[t * P:(t + 1) * P, h, :]).then_inc(loaded[u], 16)
                    for t in range(key_tiles):
                        sp.dma_start(ks[:, u, t, :], k[t * P:(t + 1) * P, h, :]).then_inc(loaded[u], 16)
                        sp.dma_start(vs[:, u, t, :], v[t * P:(t + 1) * P, h, :]).then_inc(loaded[u], 16)

                load(0)
                load(1)
                for h in range(H):
                    u = h % 2
                    sp.wait_ge(o_ev, (h + 3) * NT)
                    for t in range(NT):
                        sp.dma_start(o[t * P:(t + 1) * P, h, :], os_[:, u, t, :]).then_inc(stored[u], 16)
                        if lse is not None:
                            sp.dma_start(lse[t * P:(t + 1) * P, h:h + 1], st[:, u, t, 3:4], allow_slow_non_contiguous=True).then_inc(stored[u], 16)
                    if h + 2 < H:
                        load(h + 2)
                sp.wait_ge(out0, n_out + per_store * (H // 2))
                sp.wait_ge(out1, n_out + per_store * (H // 2))

            @block.tensor
            def _(pe):
                with pe.Fori(0, H // 2) as i:
                    for u in range(2):
                        h = i * 2 + u
                        pe.wait_ge(loaded[u], i * per_load + per_load)
                        for c, (w, at) in enumerate(zip(splits, offs)):
                            pe.wait_ge(q_ev, h * nch + (c + 1))
                            take_bank(nc, psum[:, 0, 0:P], ident)
                            for t in range(NT):
                                last = nc.tensor.transpose(psum[0:w, 0, t * P:(t + 1) * P], qs[:, u, t, at:at + w], ident[:, :])
                            last.then_inc(qk_tr, 1)
                            pe.wait_ge(k_ev, h * nch + (c + 1))
                            take_bank(nc, psum[:, 1, 0:P], ident)
                            for t in range(key_tiles):
                                last = nc.tensor.transpose(psum[0:w, 1, t * P:(t + 1) * P], ks[:, u, t, at:at + w], ident[:, :])
                            last.then_inc(qk_tr, 1)
                        pe.wait_ge(q_ev, h * nch + (nch + 1))
                        pe.wait_ge(k_ev, h * nch + (nch + 1))
                        for step in range(NT + 2):
                            if step < NT:
                                a, b = span(step)
                                pe.wait_ge(s_copied, h * NT + (step + 1))
                                for c, w in enumerate(splits):
                                    last = nc.tensor.matmul(psum[:, 2 + step % 2, a * P:b * P], qT[0:w, c, step * P:(step + 1) * P],
                                                            kT[0:w, c, a * P:b * P], start=c == 0, stop=c == nch - 1)
                                last.then_inc(s_done, 1)
                            if 1 <= step <= NT:
                                qt = step - 1
                                a, b = span(qt)
                                pe.wait_ge(e_done, h * NT + (qt + 3))
                                pe.wait_ge(pt_ev, h * NT + (qt + 1))
                                for t in range(a, b):
                                    last = nc.tensor.transpose(psum[:, 4 + qt % 2, t * P:(t + 1) * P], p_sb[:, qt % 2, t * P:(t + 1) * P], ident[:, :])
                                last.then_inc(pt_done, 1)
                            if step >= 2:
                                qt = step - 2
                                a, b = span(qt)
                                pe.wait_ge(pt_ev, h * NT + (qt + 3))
                                pe.wait_ge(o_ev, h * NT + (qt + 1 + 2 * NT - 2))
                                for t in range(a, b):
                                    last = nc.tensor.matmul(psum[:, 6 + qt % 2, 0:dv], pT[:, qt % 2, t, :], vs[:, u, t, :],
                                                            start=t == a, stop=t == b - 1)
                                last.then_inc(o_done, 1)

            @block.vector
            def _(dve):
                dve.sem_inc(k_ev, 1)
                dve.sem_inc(s_copied, 2)
                dve.sem_inc(o_ev, 2 * NT)
                dve.sem_inc(out0, n_out)
                dve.sem_inc(out1, n_out)
                if mask is not None:
                    dve.wait_ge(mask_in, 16)
                with dve.Fori(0, H // 2) as i:
                    for u in range(2):
                        dve.sem_clear(dve_order)
                        link = chain(dve, dve_order)
                        h = i * 2 + u
                        for c, w in enumerate(splits):
                            dve.wait_ge(qk_tr, h * 2 * nch + 2 * (c + 1))
                            nc.vector.tensor_copy(kT[0:w, c, :], psum[0:w, 1, 0:key_tiles * P]).then_inc(k_ev, 1)
                        dve.wait_ge(stored[u], i * per_store + n_out)
                        for step in range(NT + 2):
                            if step < NT:
                                a, b = span(step)
                                sl = slice(a * P, b * P)
                                dve.wait_ge(s_done, h * NT + (step + 1))
                                dve.wait_ge(e_done, h * NT + (step + 1))
                                if mask is not None:
                                    ins = nc.vector.tensor_tensor(s_sb[:, step % 2, sl], psum[:, 2 + step % 2, sl], ms[:, step, sl], ALU.add)
                                else:
                                    ins = nc.vector.tensor_copy(s_sb[:, step % 2, sl], psum[:, 2 + step % 2, sl])
                                ins.then_inc(s_copied, 1)
                                dve.wait_ge(s_copied, h * NT + (step + 3))
                                link(nc.vector.tensor_reduce(st[:, u, step, 0:1], s_sb[:, step % 2, sl], AX, ALU.max))
                                nc.vector.tensor_scalar(st[:, u, step, 1:2], st[:, u, step, 0:1], -scale, None, ALU.mult).then_inc(nm_ready, 1)
                            if step >= 2:
                                qt = step - 2
                                dve.wait_ge(o_done, h * NT + (qt + 3))
                                if lse is not None:
                                    dve.wait_ge(ln_done, h * NT + (qt + 1))
                                    link(nc.vector.scalar_tensor_tensor(out=st[:, u, qt, 3:4], in0=st[:, u, qt, 0:1], scalar=scale,
                                                                        in1=st[:, u, qt, 3:4], op0=ALU.mult, op1=ALU.add))
                                link(nc.vector.reciprocal(st[:, u, qt, 2:3], st[:, u, qt, 2:3]))
                                nc.vector.tensor_scalar(os_[:, u, qt, :], psum[:, 6 + qt % 2, 0:dv], st[:, u, qt, 2:3], None,
                                                        ALU.mult).then_inc(o_ev, 1)

            @block.scalar
            def _(act):
                act.sem_inc(q_ev, 1)
                act.sem_inc(e_done, 2)
                act.sem_inc(pt_ev, 2)
                act.sem_inc(o_done, 2)
                with act.Fori(0, H // 2) as i:
                    for u in range(2):
                        h = i * 2 + u
                        for c, w in enumerate(splits):
                            act.wait_ge(qk_tr, h * 2 * nch + (2 * c + 1))
                            nc.scalar.copy(qT[0:w, c, :], psum[0:w, 0, 0:T]).then_inc(q_ev, 1)
                        for step in range(NT + 1):
                            if step < NT:
                                a, b = span(step)
                                sl = slice(a * P, b * P)
                                act.wait_ge(nm_ready, h * NT + (step + 1))
                                if step >= 2:
                                    act.wait_ge(pt_done, h * NT + (step - 1))
                                nc.scalar.activation(p_sb[:, step % 2, sl], s_sb[:, step % 2, sl], ACT.Exp, bias=st[:, u, step, 1:2],
                                                     scale=scale, accum_out=st[:, u, step, 2:3]).then_inc(e_done, 1)
                                if lse is not None:
                                    act.wait_ge(e_done, h * NT + (step + 3))
                                    nc.scalar.activation(st[:, u, step, 3:4], st[:, u, step, 2:3], ACT.Ln).then_inc(ln_done, 1)
                            if step >= 1:
                                qt = step - 1
                                a, b = span(qt)
                                act.wait_ge(pt_done, h * NT + (qt + 1))
                                act.wait_ge(o_done, h * NT + (qt + 1))
                                nc.scalar.copy(pT[:, qt % 2, a:b, :], psum[:, 4 + qt % 2, a * P:b * P].rearrange("p (t q) -> p t q", q=P)).then_inc(pt_ev, 1)


def dil_combine(nc, tag, o, lse, out):
    HW = 4 * HD
    with ExitStack() as ctx:
        sb = lambda m, s: ctx.enter_context(nc.sbuf_tensor(f"{tag}_{m}", s, F32))
        os_, ls = sb("o", [P, NT, DIL * HW]), sb("l", [P, NT, DIL, 4])
        mx, y, tmp = sb("mx", [P, NT, 4]), sb("y", [P, NT, HW]), sb("tmp", [P, NT, HW])
        xin, diff_ready, exp_ready, dve_order, y_ready, stored = ctx.enter_context(stage_sems(
            nc, *[f"{tag}_{s}" for s in ("in", "diff", "exp", "dve", "y", "out")]))
        with nc.Block() as block:
            @block.sync
            def _(sp):
                sp.dma_start(ls[:, :, :, :].rearrange("p t g h -> p t (g h)"), tiled(lse)).then_inc(xin, 16)
                sp.dma_start(os_[:, :, :], tiled(o)).then_inc(xin, 16)
                sp.wait_ge(y_ready, 1)
                sp.dma_start(tiled(out), y[:, :, :]).then_inc(stored, 16)
                sp.wait_ge(stored, 16)

            @block.vector
            def _(dve):
                link = chain(dve, dve_order)
                dve.wait_ge(xin, 32)
                link(nc.vector.tensor_tensor(mx[:, :, :], ls[:, :, 0, :], ls[:, :, 1, :], ALU.max))
                link(nc.vector.tensor_tensor(mx[:, :, :], mx[:, :, :], ls[:, :, 2, :], ALU.max))
                for g in range(DIL):
                    ins = nc.vector.tensor_tensor(ls[:, :, g, :], ls[:, :, g, :], mx[:, :, :], ALU.subtract)
                ins.then_inc(diff_ready, 1)
                dve.wait_ge(exp_ready, 1)
                link(nc.vector.tensor_tensor(mx[:, :, :], ls[:, :, 0, :], ls[:, :, 1, :], ALU.add))
                link(nc.vector.tensor_tensor(mx[:, :, :], mx[:, :, :], ls[:, :, 2, :], ALU.add))
                link(nc.vector.reciprocal(mx[:, :, :], mx[:, :, :]))
                for g in range(DIL):
                    link(nc.vector.tensor_tensor(ls[:, :, g, :], ls[:, :, g, :], mx[:, :, :], ALU.mult))
                for t in range(NT):
                    hv = lambda ap: ap.rearrange("p (h d) -> p h d", d=HD)
                    for g in range(DIL):
                        to = y if g == 0 else tmp
                        link(nc.vector.tensor_tensor(hv(to[:, t, :]), hv(os_[:, t, g * HW:(g + 1) * HW]), bc_last(ls[:, t, g, :], HD), ALU.mult))
                        if g:
                            link(nc.vector.tensor_tensor(y[:, t, :], y[:, t, :], tmp[:, t, :], ALU.add))
                dve.sem_inc(y_ready, 1)

            @block.scalar
            def _(act):
                act.wait_ge(diff_ready, 1)
                nc.scalar.activation(ls[:, :, :, :], ls[:, :, :, :], ACT.Exp).then_inc(exp_ready, 1)


def gated_merge(nc, tag, gates, branches, out, bias=None):
    with ExitStack() as ctx:
        sb = lambda m, s: ctx.enter_context(nc.sbuf_tensor(f"{tag}_{m}", s, F32))
        g, b, acc = sb("g", [P, 2, NT, D]), sb("b", [P, 2, NT, D]), sb("acc", [P, NT, D])
        bi = sb("bi", [P, 3, D]) if bias is not None else None
        in_g, in_b, in_bias, biased, sig_ready, used, dve_order, stored = ctx.enter_context(stage_sems(
            nc, *[f"{tag}_{s}" for s in ("ing", "inb", "inbias", "biased", "sig", "used", "dve", "out")]))
        with nc.Block() as block:
            @block.sync
            def _(sp):
                if bias is not None:
                    sp.dma_start(bi[:, :, :].rearrange("p b d -> p (b d)"), row_bc(bias)).then_inc(in_bias, 16)
                for n in range(3):
                    if n >= 2:
                        sp.wait_ge(used, n - 1)
                    if n >= 1:
                        sp.wait_ge(in_g, 16 * n)
                        sp.wait_ge(in_b, 16 * n)
                    sp.dma_start(g[:, n % 2, :, :], tiled(gates)[:, :, n * D:(n + 1) * D]).then_inc(in_g, 16)
                    sp.dma_start(b[:, n % 2, :, :], tiled(branches[n])).then_inc(in_b, 16)
                sp.wait_ge(used, 3)
                sp.dma_start(tiled(out), acc[:, :, :]).then_inc(stored, 16)
                sp.wait_ge(stored, 16)

            @block.scalar
            def _(act):
                for n in range(3):
                    if bias is not None:
                        act.wait_ge(biased, n + 1)
                    else:
                        act.wait_ge(in_g, 16 * n + 16)
                    nc.scalar.activation(g[:, n % 2, :, :], g[:, n % 2, :, :], ACT.Sigmoid).then_inc(sig_ready, 1)

            @block.vector
            def _(dve):
                link = chain(dve, dve_order)

                def add_bias(n):
                    dve.wait_ge(in_bias, 16)
                    dve.wait_ge(in_g, 16 * n + 16)
                    for t in range(NT):
                        ins = nc.vector.tensor_tensor(g[:, n % 2, t, :], g[:, n % 2, t, :], bi[:, n, :], ALU.add)
                    ins.then_inc(biased, 1)

                for n in range(3):
                    if bias is not None:
                        add_bias(n)
                    dve.wait_ge(sig_ready, n + 1)
                    dve.wait_ge(in_b, 16 * n + 16)
                    if n == 0:
                        link(nc.vector.tensor_tensor(acc[:, :, :], g[:, 0, :, :], b[:, 0, :, :], ALU.mult))
                    else:
                        link(nc.vector.tensor_tensor(g[:, n % 2, :, :], g[:, n % 2, :, :], b[:, n % 2, :, :], ALU.mult))
                        link(nc.vector.tensor_tensor(acc[:, :, :], acc[:, :, :], g[:, n % 2, :, :], ALU.add))
                    dve.sem_inc(used, 1)


def add_residual(nc, tag, h, y, gate=None):
    with ExitStack() as ctx:
        ys = ctx.enter_context(nc.sbuf_tensor(f"{tag}_y", [P, NT, D], F32))
        gs = ctx.enter_context(nc.sbuf_tensor(f"{tag}_g", [P, D], F32))
        xin, dve_order = ctx.enter_context(stage_sems(nc, f"{tag}_in", f"{tag}_dve"))
        with nc.Block() as block:
            @block.sync
            def _(sp):
                sp.dma_start(ys[:, :, :], tiled(y)).then_inc(xin, 16)
                if gate is not None:
                    sp.dma_start(gs[:, :], row_bc(gate)).then_inc(xin, 16)

            @block.vector
            def _(dve):
                link = chain(dve, dve_order)
                dve.wait_ge(xin, 16 if gate is None else 32)
                for t in range(NT):
                    if gate is not None:
                        link(nc.vector.tensor_tensor(ys[:, t, :], ys[:, t, :], gs[:, :], ALU.mult))
                    link(nc.vector.tensor_tensor(h[:, t, :], h[:, t, :], ys[:, t, :], ALU.add))


def peer_route(nc, tag, psum, qT, keysT, iota16, sel):
    with ExitStack() as ctx:
        sb = lambda m, s, d=F32: ctx.enter_context(nc.sbuf_tensor(f"{tag}_{m}", s, d))
        qs, ks = sb("q", [P, 2, T]), sb("k", [P, 2, NK])
        sc, sc2 = sb("sc", [P, 2, NT, NK]), sb("sc2", [P, NK])
        val, idx, idxf = sb("val", [P, 2, NT, TOPK]), sb("idx", [P, 2, NT, TOPK], U32), sb("idxf", [P, 2, NT, TOPK])
        cand, cand2 = sb("cand", [P, 256]), sb("cand2", [P, 256])
        top, pos, posx, posf = sb("top", [P, NT, TOPK]), sb("pos", [P, NT, TOPK], U32), sb("posx", [P, 2, NT, TOPK], U32), sb("posf", [P, 2, NT, TOPK])
        eq, res = sb("eq", [P, TOPK, TOPK]), sb("res", [P, NT, 3, TOPK])
        sums = sb("sums", [P, NT])
        (loaded, s_done, s_copied, diff_ready, exp_ready, dve_order, res_ready, stored) = ctx.enter_context(stage_sems(
            nc, *[f"{tag}_{s}" for s in ("in", "sdone", "scp", "diff", "exp", "dve", "res", "out")]))
        with nc.Block() as block:
            @block.sync
            def _(sp):
                with sp.Fori(0, PEER_H) as h:
                    sp.wait_ge(s_done, h * 2 + 2)
                    for c in range(2):
                        sp.dma_start(qs[:, c, :], qT[ds(h * 256 + c * P, P), :]).then_inc(loaded, 16)
                        sp.dma_start(ks[:, c, :], keysT[ds(h * 256 + c * P, P), :]).then_inc(loaded, 16)

            @block.tensor
            def _(pe):
                pe.sem_inc(s_done, 2)
                with pe.Fori(0, PEER_H) as h:
                    pe.wait_ge(loaded, h * 64 + 64)
                    for c in range(2):
                        pe.wait_ge(s_copied, h * 2 + (c + 1))
                        for t in range(NT):
                            last = nc.tensor.matmul(psum[:, c, t * NK:(t + 1) * NK], qs[:, c, t * P:(t + 1) * P], ks[:, c, :], start=True, stop=True)
                        last.then_inc(s_done, 1)

            @block.vector
            def _(dve):
                dve.sem_inc(s_copied, 2)
                dve.sem_inc(stored, 16 * NT)

                def best16(link, values, spare, v, i):
                    link(nc.vector.max(v[:, 0:8], values))
                    link(nc.vector.max_index(i[:, 0:8], v[:, 0:8], values))
                    link(nc.vector.match_replace(spare, v[:, 0:8], values, NEG))
                    link(nc.vector.max(v[:, 8:16], spare))
                    link(nc.vector.max_index(i[:, 8:16], v[:, 8:16], spare))

                with dve.Fori(0, PEER_H) as h:
                    dve.sem_clear(dve_order)
                    link = chain(dve, dve_order)
                    for c in range(2):
                        dve.wait_ge(s_done, h * 2 + (c + 3))
                        link(nc.vector.tensor_copy(sc[:, c, :, :].rearrange("p t k -> p (t k)"), psum[:, c, :]))
                        dve.sem_inc(s_copied, 1)
                        for t in range(NT):
                            best16(link, sc[:, c, t, :], sc2[:, :], val[:, c, t, :], idx[:, c, t, :])
                        link(nc.vector.tensor_copy(idxf[:, c, :, :], idx[:, c, :, :]))
                    for t in range(NT):
                        cv = cand[:, :].rearrange("p (a b) -> p a b", b=TOPK)
                        link(nc.vector.tensor_tensor(cv, bc_last(val[:, 0, t, :], TOPK), bc_mid(val[:, 1, t, :], TOPK), ALU.add))
                        best16(link, cand[:, :], cand2[:, :], top[:, t, :], pos[:, t, :])
                    link(nc.vector.tensor_scalar(posx[:, 0, :, :], pos[:, :, :], 4, None, ALU.logical_shift_right))
                    link(nc.vector.tensor_scalar(posx[:, 1, :, :], pos[:, :, :], 15, None, ALU.bitwise_and))
                    link(nc.vector.tensor_copy(posf[:, :, :, :], posx[:, :, :, :]))
                    dve.wait_ge(stored, h * (16 * NT) + 16 * NT)
                    for t in range(NT):
                        ins = nc.vector.tensor_scalar(res[:, t, 2, :], top[:, t, :], top[:, t, 0:1], None, ALU.subtract)
                    ins.then_inc(diff_ready, 1)
                    for c in range(2):
                        for t in range(NT):
                            link(nc.vector.tensor_tensor(eq[:, :, :], bc_last(posf[:, c, t, :], TOPK), bc_mid(iota16, TOPK), ALU.is_equal))
                            link(nc.vector.tensor_tensor(eq[:, :, :], eq[:, :, :], bc_mid(idxf[:, c, t, :], TOPK), ALU.mult))
                            link(nc.vector.tensor_reduce(res[:, t, c, :], eq[:, :, :], AX, ALU.add))
                    dve.wait_ge(exp_ready, h + 1)
                    link(nc.vector.tensor_reduce(sums[:, :], res[:, :, 2, :], AX, ALU.add))
                    link(nc.vector.reciprocal(sums[:, :], sums[:, :]))
                    link(nc.vector.tensor_tensor(res[:, :, 2, :], res[:, :, 2, :], bc_last(sums[:, :], TOPK), ALU.mult))
                    dve.sem_inc(res_ready, 1)

            @block.scalar
            def _(act):
                with act.Fori(0, PEER_H) as h:
                    act.wait_ge(diff_ready, h + 1)
                    nc.scalar.activation(res[:, :, 2, :], res[:, :, 2, :], ACT.Exp).then_inc(exp_ready, 1)
                    act.wait_ge(res_ready, h + 1)
                    for t in range(NT):
                        act.dma_start(sel[t * P:(t + 1) * P, :, ds(h * TOPK, TOPK)], res[:, t, :, :]).then_inc(stored, 16)
                act.wait_ge(stored, 16 * NT * (PEER_H + 1))


def peer_gates(nc, tag, psum, selT, iota128, gates):
    TB = 4
    NB = P // TB
    with ExitStack() as ctx:
        sb = lambda m, s: ctx.enter_context(nc.sbuf_tensor(f"{tag}_{m}", s, F32))
        gbuf = sb("g", [P, NK, P])
        cols, oh1, oh2 = sb("cols", [P, 2, 3, 2 * TB]), sb("oh1", [P, 2, TB, NK]), sb("oh2", [P, 2, TB, NK])
        (oh_ready, g_done, ev_a, ev_v, stored, dve_order, cols_ready) = ctx.enter_context(stage_sems(
            nc, *[f"{tag}_{s}" for s in ("oh", "gd", "eva", "evv", "out", "dve", "cols")]))
        with nc.Block() as block:
            @block.sync
            def _(sp):
                sp.sem_inc(stored, 16)
                with sp.Fori(0, NT) as t:
                    sp.wait_ge(ev_a, t * NB + (NB + 2))
                    sp.dma_start(gates[ds(t, 1), :, :, :].rearrange("o p i t -> p (o i) t"), gbuf[:, :, :]).then_inc(stored, 16)
                sp.wait_ge(stored, 16 * NT + 16)

            @block.vector
            def _(dve):
                dve.sem_inc(g_done, 2)
                with dve.Fori(0, NT * NB // 2) as i:
                    dve.sem_clear(dve_order)
                    link = chain(dve, dve_order)
                    link(nc.vector.tensor_copy(cols[:, 0, :, :], selT[:, :, ds(i * 2 * TB, 2 * TB)]))
                    for u in range(2):
                        dve.wait_ge(g_done, i * 2 + (u + 1))
                        for b in range(TB):
                            j = u * TB + b
                            nc.vector.tensor_scalar(oh1[:, u, b, :], iota128, cols[:, 0, 0, j:j + 1], cols[:, 0, 2, j:j + 1], ALU.is_equal, ALU.mult)
                            ins = nc.vector.tensor_scalar(oh2[:, u, b, :], iota128, cols[:, 0, 1, j:j + 1], None, ALU.is_equal)
                        link(ins)
                        dve.sem_inc(oh_ready, 1)

            @block.tensor
            def _(pe):
                with pe.Fori(0, NT * NB // 2) as i:
                    for u in range(2):
                        pe.wait_ge(oh_ready, i * 2 + (u + 1))
                        pe.wait_ge(ev_a, i * 2 + (u + 1))
                        for b in range(TB):
                            last = nc.tensor.matmul(psum[:, u, b * NK:(b + 1) * NK], oh2[:, u, b, :], oh1[:, u, b, :], start=True, stop=True)
                        last.then_inc(g_done, 1)

            @block.scalar
            def _(act):
                act.sem_inc(ev_a, 2)
                with act.Fori(0, NT) as t:
                    act.wait_ge(stored, t * 16 + 16)
                    with act.Fori(0, NB // 2) as i:
                        for u in range(2):
                            act.wait_ge(g_done, t * NB + i * 2 + (u + 3))
                            nc.scalar.copy(gbuf[:, :, ds(i * 2 * TB + u * TB, TB)].rearrange("p i t -> p t i"),
                                           psum[:, u, :].rearrange("p (t i) -> p t i", i=NK)).then_inc(ev_a, 1)


def ffn_loop(nc, tag, psum, xT, acc, n, w_a, w_out, w_b=None, gates=None, token_w=None):
    FB = CH // P
    with ExitStack() as ctx:
        sb = lambda m, s: ctx.enter_context(nc.sbuf_tensor(f"{tag}_{m}", s, F32))
        wa, wo = sb("wa", [P, 2, KD, CH]), sb("wo", [P, 2, FB, D])
        wb = sb("wb", [P, 2, KD, CH]) if w_b is not None else sb("gt", [P, 2, NT, FB, P])
        nl, hid = sb("nl", [P, 2, T]), sb("hid", [P, 2, FB, T])
        (in0, in1, a_done, nl_ready, hid_ready, o_done, acc_done, dve_order) = ctx.enter_context(stage_sems(
            nc, *[f"{tag}_{s}" for s in ("in0", "in1", "adone", "nl", "hid", "odone", "acc", "dve")]))
        loaded = (in0, in1)
        per_load = 48 if w_b is not None else 32 + 16 * NT
        with nc.Block() as block:
            @block.sync
            def _(sp):
                with sp.Fori(0, n // 2) as i:
                    for u in range(2):
                        e = i * 2 + u
                        sp.wait_ge(o_done, e * 8 + 8)
                        sp.dma_start(wa[:, u, :, :], w_a(e)).then_inc(loaded[u], 16)
                        if w_b is not None:
                            sp.dma_start(wb[:, u, :, :], w_b(e)).then_inc(loaded[u], 16)
                        else:
                            for t in range(NT):
                                sp.dma_start(wb[:, u, t, :, :], gates[t, :, ds(e * FB, FB), :]).then_inc(loaded[u], 16)
                        sp.dma_start(wo[:, u, :, :], w_out(e)).then_inc(loaded[u], 16)

            @block.tensor
            def _(pe):
                pe.sem_inc(o_done, 16)
                with pe.Fori(0, n // 2) as i:
                    for u in range(2):
                        e = i * 2 + u
                        pe.wait_ge(loaded[u], i * per_load + per_load)
                        for f in range(FB):
                            pe.wait_ge(hid_ready, e * FB + (f + 1))
                            for bank, w in ((f % 2, wa), (2 + f % 2, wb))[0:2 if w_b is not None else 1]:
                                for k in range(KD):
                                    last = nc.tensor.matmul(psum[:, bank, :], w[:, u, k, f * P:(f + 1) * P], xT[:, k, :], start=k == 0, stop=k == KD - 1)
                            last.then_inc(a_done, 1)
                        pe.wait_ge(hid_ready, e * FB + (FB + 2))
                        for j in range(8):
                            pe.wait_ge(acc_done, e * 8 + (j + 1))
                            for f in range(FB):
                                last = nc.tensor.matmul(psum[:, 4 + j % 4, :], hid[:, u, f, j // 2 * P:(j // 2 + 1) * P],
                                                        wo[:, u, f, j % 2 * CH:(j % 2 + 1) * CH], start=f == 0, stop=f == FB - 1)
                            last.then_inc(o_done, 1)

            @block.scalar
            def _(act):
                with act.Fori(0, n // 2) as i:
                    for u in range(2):
                        e = i * 2 + u
                        for f in range(FB):
                            act.wait_ge(a_done, e * FB + (f + 1))
                            act.wait_ge(hid_ready, e * FB + (f + 1))
                            nc.scalar.activation(nl[:, f % 2, :], psum[:, f % 2, :], ACT.Silu if w_b is not None else ACT.Gelu).then_inc(nl_ready, 1)

            @block.vector
            def _(dve):
                dve.sem_inc(hid_ready, 2)
                dve.sem_inc(acc_done, 4)
                nc.vector.memset(acc[:, :, :], 0.0).then_inc(dve_order, 1)
                dve.wait_ge(dve_order, 1)
                with dve.Fori(0, n // 2) as i:
                    for u in range(2):
                        e = i * 2 + u
                        for f in range(FB):
                            dve.wait_ge(nl_ready, e * FB + (f + 1))
                            if w_b is not None:
                                other = psum[:, 2 + f % 2, :]
                                nc.vector.tensor_tensor(hid[:, u, f, :], nl[:, f % 2, :], other, ALU.mult).then_inc(hid_ready, 1)
                            else:
                                v = lambda ap: ap.rearrange("p (t q) -> p t q", q=P)
                                nc.vector.tensor_tensor(v(hid[:, u, f, :]), v(nl[:, f % 2, :]), wb[:, u, :, f, :], ALU.mult).then_inc(hid_ready, 1)
                        for j in range(8):
                            dve.wait_ge(o_done, e * 8 + (j + 17))
                            dst = acc[:, j // 2, j % 2 * CH:(j % 2 + 1) * CH]
                            dve.wait_ge(acc_done, e * 8 + (j + 4))
                            if token_w is not None:
                                ins = nc.vector.scalar_tensor_tensor(out=dst, in0=psum[:, 4 + j % 4, :], scalar=token_w[:, j // 2, ds(e, 1)],
                                                                     in1=dst, op0=ALU.mult, op1=ALU.add)
                            else:
                                ins = nc.vector.tensor_tensor(dst, psum[:, 4 + j % 4, :], dst, ALU.add)
                            ins.then_inc(acc_done, 1)


def adaptive_rows(nc, tag, psum, c, w, b, mods):
    N6 = 6 * D
    with ExitStack() as ctx:
        sb = lambda m, s: ctx.enter_context(nc.sbuf_tensor(f"{tag}_{m}", s, F32))
        cT, m_sb, b_sb = sb("cT", [P, KD, 1]), sb("m", [P, N6 // P]), sb("b", [P, N6 // P])
        with ExitStack() as inner:
            xin, act_done = inner.enter_context(stage_sems(nc, f"{tag}_in", f"{tag}_act"))
            with nc.Block() as block:
                @block.sync
                def _(sp):
                    with nc.allow_non_contiguous_dma("a row of 1024 laid over the partitions"):
                        sp.dma_start(cT[:, :, 0], c.rearrange("(k p) -> p k", p=P)).then_inc(xin, 16)

                @block.scalar
                def _(act):
                    act.wait_ge(xin, 16)
                    nc.scalar.activation(cT[:, :, 0], cT[:, :, 0], ACT.Silu).then_inc(act_done, 1)
                    act.wait_ge(act_done, 1)
        for l in range(LAYERS):
            linear(nc, f"{tag}l{l}", psum, cT, KD, w[l], mods[l], N6, tiles=1, m=1)
            xin, added, stored = ctx.enter_context(stage_sems(nc, f"{tag}{l}_in2", f"{tag}{l}_add", f"{tag}{l}_out"))
            row = mods[l].rearrange("o (p n) -> (o p) n", p=P)
            with nc.Block() as block:
                @block.sync
                def _(sp):
                    sp.dma_start(m_sb[:, :], row).then_inc(xin, 16)
                    sp.dma_start(b_sb[:, :], b[l].rearrange("(p n) -> p n", p=P)).then_inc(xin, 16)
                    sp.wait_ge(added, 1)
                    sp.dma_start(row, m_sb[:, :]).then_inc(stored, 16)
                    sp.wait_ge(stored, 16)

                @block.vector
                def _(dve):
                    dve.wait_ge(xin, 32)
                    nc.vector.tensor_tensor(m_sb[:, :], m_sb[:, :], b_sb[:, :], ALU.add).then_inc(added, 1)


def fox_prep(nc, tag, psum, tri, proj, fb, qa, ka):
    H, DH = 4, 128
    root = DH ** 0.5
    with ExitStack() as ctx:
        sb = lambda m, s: ctx.enter_context(nc.sbuf_tensor(f"{tag}_{m}", s, F32))
        q, k = sb("q", [P, NT, H, DH + 2]), sb("k", [P, NT, H, DH + 2])
        ff, fbs, e, lf, ones = sb("ff", [P, NT, H]), sb("fb", [P, H]), sb("e", [P, NT, H]), sb("lf", [P, NT, H]), sb("ones", [P, P])
        (xin, qk_in, abs_ready, ln_ready, lf_ready, cum_done, ext_ready, stored, dve_order, act_order) = ctx.enter_context(stage_sems(
            nc, *[f"{tag}_{s}" for s in ("in", "qkin", "abs", "ln", "lf", "cum", "ext", "out", "dve", "act")]))
        tiled_heads = lambda a, t: a[t * P:(t + 1) * P, :].rearrange("p (h d) -> p h d", h=H)
        with nc.Block() as block:
            @block.sync
            def _(sp):
                sp.dma_start(ff[:, :, :], tiled(proj)[:, :, FF:FF + H]).then_inc(xin, 16)
                sp.dma_start(fbs[:, :], row_bc(fb)).then_inc(xin, 16)
                for t in range(NT):
                    sp.dma_start(q[:, t, :, 0:DH], tiled_heads(proj[:, FQ:FQ + H * DH], t)).then_inc(qk_in, 16)
                    sp.dma_start(k[:, t, :, 0:DH], tiled_heads(proj[:, FK:FK + H * DH], t)).then_inc(qk_in, 16)
                sp.wait_ge(qk_in, 32 * NT)
                sp.wait_ge(ext_ready, 1)
                for t in range(NT):
                    sp.dma_start(qa[t * P:(t + 1) * P, :, :], q[:, t, :, :]).then_inc(stored, 16)
                    sp.dma_start(ka[t * P:(t + 1) * P, :, :], k[:, t, :, :]).then_inc(stored, 16)
                sp.wait_ge(stored, 32 * NT)

            @block.vector
            def _(dve):
                link = chain(dve, dve_order)
                link(nc.vector.memset(ones[:, :], 1.0))
                dve.wait_ge(xin, 32)
                link(nc.vector.tensor_tensor(ff[:, :, :], ff[:, :, :], bc_mid(fbs[:, :], NT), ALU.add))
                link(nc.vector.tensor_scalar(e[:, :, :], ff[:, :, :], -1.0, None, ALU.mult))
                nc.vector.tensor_tensor(e[:, :, :], e[:, :, :], ff[:, :, :], ALU.min).then_inc(abs_ready, 1)
                dve.wait_ge(ln_ready, 1)
                nc.vector.scalar_tensor_tensor(out=lf[:, :, :], in0=ff[:, :, :], scalar=0.0, in1=e[:, :, :], op0=ALU.min, op1=ALU.subtract).then_inc(lf_ready, 1)
                dve.wait_ge(cum_done, 1)
                cum = psum[:, 0, 0:NT * H].rearrange("p (t h) -> p t h", h=H)
                link(nc.vector.tensor_scalar(q[:, :, :, DH], cum, root, None, ALU.mult))
                link(nc.vector.tensor_scalar(k[:, :, :, DH + 1], cum, -root, None, ALU.mult))
                link(nc.vector.memset(q[:, :, :, DH + 1], 1.0))
                link(nc.vector.memset(k[:, :, :, DH], 1.0))
                dve.sem_inc(ext_ready, 1)

            @block.scalar
            def _(act):
                link = chain(act, act_order)
                act.wait_ge(abs_ready, 1)
                link(nc.scalar.activation(e[:, :, :], e[:, :, :], ACT.Exp))
                nc.scalar.activation(e[:, :, :], e[:, :, :], ACT.Ln, bias=1.0).then_inc(ln_ready, 1)

            @block.tensor
            def _(pe):
                pe.wait_ge(lf_ready, 1)
                for t in range(NT):
                    for j in range(t + 1):
                        last = nc.tensor.matmul(psum[:, 0, t * H:(t + 1) * H], tri[:, :] if j == t else ones[:, :], lf[:, j, :], start=j == 0, stop=j == t)
                last.then_inc(cum_done, 1)


def copy_pieces(nc, tag, pairs):
    with ExitStack() as ctx:
        (copied,) = ctx.enter_context(stage_sems(nc, f"{tag}_cp"))
        with nc.Block() as block:
            @block.sync
            def _(sp):
                for dst, src in pairs:
                    sp.dma_start(dst, src).then_inc(copied, 16)
                sp.wait_ge(copied, 16 * len(pairs))


def retention(nc, tag, psum, ident, q, k, v, consts, o):
    H, DK, DV = 4, 64, 128
    dmask_d, decay_d = consts
    with ExitStack() as ctx:
        sb = lambda m, s: ctx.enter_context(nc.sbuf_tensor(f"{tag}_{m}", s, F32))
        dm, dec = sb("dm", [P, H * P]), sb("dec", [P, 3, H])
        qs, ks, vs = sb("q", [P, H * DK]), sb("k", [P, H * DK]), sb("v", [P, H * DV])
        qT, kT, sT, kd = sb("qT", [DK, H * P]), sb("kT", [DK, H * P]), sb("sT", [P, H * P]), sb("kd", [P, H * DK])
        state, ob = sb("state", [DK, H * DV]), sb("ob", [P, H * DV])
        hv = lambda ap: ap.rearrange("p (h d) -> p h d", h=H)
        (consts_in, loaded, tr_done, q_ev, k_ev, s_done, s_ready, mm_done, o_ready, stored, dve_order) = ctx.enter_context(stage_sems(
            nc, *[f"{tag}_{s}" for s in ("cin", "in", "tr", "qev", "kev", "sd", "sr", "mm", "or", "out", "dve")]))
        with nc.Block() as block:
            @block.sync
            def _(sp):
                sp.dma_start(dm[:, :], dmask_d).then_inc(consts_in, 16)
                sp.dma_start(dec[:, :, :].rearrange("p a h -> p (a h)"), decay_d).then_inc(consts_in, 16)
                with sp.Fori(0, NT) as c:
                    sp.wait_ge(o_ready, c + 1)
                    sp.dma_start(qs[:, :], q[ds(c * P, P), :]).then_inc(loaded, 16)
                    sp.dma_start(ks[:, :], k[ds(c * P, P), :]).then_inc(loaded, 16)
                    sp.dma_start(vs[:, :], v[ds(c * P, P), :]).then_inc(loaded, 16)
                    sp.wait_ge(o_ready, c + 2)
                    sp.dma_start(o[ds(c * P, P), :], ob[:, :]).then_inc(stored, 16)
                sp.wait_ge(stored, 16 * NT + 16)

            @block.tensor
            def _(pe):
                with pe.Fori(0, NT) as c:
                    pe.wait_ge(loaded, c * 48 + 48)
                    take_bank(nc, psum[:, 0, 0:P], ident)
                    for h in range(H):
                        nc.tensor.transpose(psum[0:DK, 0, h * P:(h + 1) * P], qs[:, h * DK:(h + 1) * DK], ident[:, :])
                        last = nc.tensor.transpose(psum[0:DK, 1, h * P:(h + 1) * P], ks[:, h * DK:(h + 1) * DK], ident[:, :])
                    last.then_inc(tr_done, 1)
                    pe.wait_ge(q_ev, c + 1)
                    pe.wait_ge(k_ev, c + 1)
                    for h in range(H):
                        last = nc.tensor.matmul(psum[:, 2, h * P:(h + 1) * P], kT[:, h * P:(h + 1) * P], qT[:, h * P:(h + 1) * P], start=True, stop=True)
                    last.then_inc(s_done, 1)
                    pe.wait_ge(s_ready, c + 1)
                    for h in range(H):
                        nc.tensor.matmul(psum[:, 3, h * DV:(h + 1) * DV], sT[:, h * P:(h + 1) * P], vs[:, h * DV:(h + 1) * DV], start=True, stop=True)
                        nc.tensor.matmul(psum[:, 4, h * DV:(h + 1) * DV], qT[:, h * P:(h + 1) * P], state[:, h * DV:(h + 1) * DV], start=True, stop=True)
                        last = nc.tensor.matmul(psum[0:DK, 5, h * DV:(h + 1) * DV], kd[:, h * DK:(h + 1) * DK], vs[:, h * DV:(h + 1) * DV], start=True, stop=True)
                    last.then_inc(mm_done, 1)

            @block.scalar
            def _(act):
                with act.Fori(0, NT) as c:
                    act.wait_ge(tr_done, c + 1)
                    nc.scalar.copy(qT[:, :], psum[0:DK, 0, :]).then_inc(q_ev, 1)

            @block.vector
            def _(dve):
                dve.sem_inc(o_ready, 1)
                dve.sem_inc(stored, 16)
                nc.vector.memset(state[:, :], 0.0).then_inc(dve_order, 1)
                dve.wait_ge(dve_order, 1)
                dve.wait_ge(consts_in, 32)
                with dve.Fori(0, NT) as c:
                    dve.sem_clear(dve_order)
                    link = chain(dve, dve_order)
                    dve.wait_ge(tr_done, c + 1)
                    nc.vector.tensor_copy(kT[:, :], psum[0:DK, 1, :]).then_inc(k_ev, 1)
                    link(nc.vector.tensor_tensor(hv(kd[:, :]), hv(ks[:, :]), bc_last(dec[:, 1, :], DK), ALU.mult))
                    dve.wait_ge(s_done, c + 1)
                    link(nc.vector.tensor_tensor(sT[:, :], psum[:, 2, :], dm[:, :], ALU.mult))
                    dve.sem_inc(s_ready, 1)
                    dve.wait_ge(mm_done, c + 1)
                    dve.wait_ge(stored, c * 16 + 16)
                    link(nc.vector.tensor_tensor(hv(ob[:, :]), hv(psum[:, 4, :]), bc_last(dec[:, 0, :], DV), ALU.mult))
                    link(nc.vector.tensor_tensor(ob[:, :], ob[:, :], psum[:, 3, :], ALU.add))
                    link(nc.vector.tensor_tensor(hv(state[:, :]), hv(state[:, :]), bc_last(dec[0:DK, 2, :], DV), ALU.mult))
                    link(nc.vector.tensor_tensor(state[:, :], state[:, :], psum[0:DK, 5, :], ALU.add))
                    dve.sem_inc(o_ready, 1)


def retention_gate_norm(nc, tag, o, g, out):
    H, DV = 4, 128
    W = H * DV
    with ExitStack() as ctx:
        sb = lambda m, s: ctx.enter_context(nc.sbuf_tensor(f"{tag}_{m}", s, F32))
        ys, gs, sq = sb("y", [P, NT, W]), sb("g", [P, NT, W]), sb("sq", [P, W])
        mean, var, rt, tp = sb("mean", [P, NT, H]), sb("var", [P, NT, H]), sb("rt", [P, NT, H]), sb("tp", [P, NT, H])
        xin, silu_ready, var_ready, root_ready, dve_order, y_ready, stored = ctx.enter_context(stage_sems(
            nc, *[f"{tag}_{s}" for s in ("in", "silu", "var", "root", "dve", "y", "out")]))
        grp = lambda ap: ap.rearrange("p (g d) -> p g d", g=H)
        with nc.Block() as block:
            @block.sync
            def _(sp):
                sp.dma_start(gs[:, :, :], tiled(g)).then_inc(xin, 16)
                sp.dma_start(ys[:, :, :], tiled(o)).then_inc(xin, 16)
                sp.wait_ge(y_ready, NT)
                sp.dma_start(tiled(out), ys[:, :, :]).then_inc(stored, 16)
                sp.wait_ge(stored, 16)

            @block.scalar
            def _(act):
                act.wait_ge(xin, 32)
                nc.scalar.activation(gs[:, :, :], gs[:, :, :], ACT.Silu).then_inc(silu_ready, 1)
                act.wait_ge(var_ready, 1)
                nc.scalar.activation(rt[:, :, :], var[:, :, :], ACT.Sqrt).then_inc(root_ready, 1)

            @block.vector
            def _(dve):
                link = chain(dve, dve_order)
                dve.wait_ge(xin, 32)
                for t in range(NT):
                    link(nc.vector.tensor_reduce(mean[:, t, :], grp(ys[:, t, :]), AX, ALU.add))
                    link(nc.vector.tensor_scalar(mean[:, t, :], mean[:, t, :], 1.0 / DV, None, ALU.mult))
                    link(nc.vector.tensor_tensor(grp(ys[:, t, :]), grp(ys[:, t, :]), bc_last(mean[:, t, :], DV), ALU.subtract))
                    link(nc.vector.tensor_tensor(sq[:, :], ys[:, t, :], ys[:, t, :], ALU.mult))
                    link(nc.vector.tensor_reduce(var[:, t, :], grp(sq[:, :]), AX, ALU.add))
                nc.vector.tensor_scalar(var[:, :, :], var[:, :, :], 1.0 / DV, EPS, ALU.mult, ALU.add).then_inc(var_ready, 1)
                dve.wait_ge(silu_ready, 1)
                dve.wait_ge(root_ready, 1)
                refined_root(nc, link, rt[:, :, :], var[:, :, :], tp[:, :, :])
                for t in range(NT):
                    link(nc.vector.tensor_tensor(grp(ys[:, t, :]), grp(ys[:, t, :]), bc_last(rt[:, t, :], DV), ALU.mult))
                    nc.vector.tensor_tensor(ys[:, t, :], ys[:, t, :], gs[:, t, :], ALU.mult).then_inc(y_ready, 1)


def moe_route(nc, tag, psum, tri, logits, bias, iota, token_w, pair_w, pair_row, crowded):
    W = N_GRP + N_EXPERTS
    iota8 = iota[:, 0:8]
    with ExitStack() as ctx:
        sb = lambda m, s, d=F32: ctx.enter_context(nc.sbuf_tensor(f"{tag}_{m}", s, d))
        lg, bs = sb("lg", [P, NT, W]), sb("bs", [P, W])
        gl, gtop, gi, gif, goh = sb("gl", [P, NT, 8]), sb("gtop", [P, NT, 8]), sb("gi", [P, NT, 8], U32), sb("gif", [P, NT, 8]), sb("goh", [P, NT, 8])
        tmp, ing, etop, ei, eif = sb("tmp", [P, N_GRP, 8]), sb("ing", [P, NT, 8]), sb("etop", [P, NT, 8]), sb("ei", [P, NT, 8], U32), sb("eif", [P, NT, 8])
        s1, s2, wsel, wj = sb("s1", [P, NT]), sb("s2", [P, NT]), sb("wsel", [P, NT, 8]), sb("wj", [P, NT, 8])
        oh, sel, ones = sb("oh", [P, 2, NT, N_EXPERTS]), sb("sel", [P, NT, N_EXPERTS]), sb("ones", [P, P])
        base, rank, rowf, most = sb("base", [P, N_EXPERTS]), sb("rank", [P, NT, N_EXPERTS]), sb("rowf", [P, NT, 2]), sb("most", [P, 1])
        xin, diff_ready, exp_ready, sel_ready, rank_done, dve_order = ctx.enter_context(stage_sems(
            nc, *[f"{tag}_{s}" for s in ("in", "diff", "exp", "sel", "rank", "dve")]))
        by_group = lambda ap: ap.rearrange("p (g j) -> p g j", g=N_GRP)
        with nc.Block() as block:
            @block.sync
            def _(sp):
                sp.dma_start(lg[:, :, :], tiled(logits)).then_inc(xin, 16)
                sp.dma_start(bs[:, :], row_bc(bias)).then_inc(xin, 16)

            @block.tensor
            def _(pe):
                pe.wait_ge(sel_ready, 1)
                for t in range(NT):
                    for j in range(t + 1):
                        nc.tensor.matmul(psum[:, 0, t * N_EXPERTS:(t + 1) * N_EXPERTS], tri[:, :] if j == t else ones[:, :], sel[:, j, :],
                                         start=j == 0, stop=j == t)
                for j in range(NT):
                    last = nc.tensor.matmul(psum[:, 0, NT * N_EXPERTS:(NT + 1) * N_EXPERTS], ones[:, :], sel[:, j, :], start=j == 0, stop=j == NT - 1)
                last.then_inc(rank_done, 1)

            @block.vector
            def _(dve):
                link = chain(dve, dve_order)
                link(nc.vector.memset(ones[:, :], 1.0))
                link(nc.vector.memset(gl[:, :, :], NEG))
                link(nc.vector.tensor_scalar(base[:, :], iota[:, 0:N_EXPERTS], float(P), None, ALU.mult))
                dve.wait_ge(xin, 32)
                link(nc.vector.tensor_tensor(lg[:, :, :], lg[:, :, :], bc_mid(bs[:, :], NT), ALU.add))
                link(nc.vector.tensor_copy(gl[:, :, 0:N_GRP], lg[:, :, 0:N_GRP]))
                for t in range(NT):
                    link(nc.vector.max(gtop[:, t, :], gl[:, t, :]))
                    link(nc.vector.max_index(gi[:, t, :], gtop[:, t, :], gl[:, t, :]))
                link(nc.vector.tensor_copy(gif[:, :, :], gi[:, :, :]))
                for t in range(NT):
                    link(nc.vector.tensor_scalar(goh[:, t, :], iota8, gif[:, t, 0:1], None, ALU.is_equal))
                    link(nc.vector.tensor_tensor(tmp[:, :, :], by_group(lg[:, t, N_GRP:W]), bc_last(goh[:, t, 0:N_GRP], EPG), ALU.mult))
                    link(nc.vector.tensor_reduce(ing[:, t, :], tmp[:, :, :].rearrange("p g j -> p j g"), AX, ALU.add))
                    link(nc.vector.max(etop[:, t, :], ing[:, t, :]))
                    link(nc.vector.max_index(ei[:, t, :], etop[:, t, :], ing[:, t, :]))
                    link(nc.vector.tensor_scalar(gl[:, t, 0:N_GRP], gl[:, t, 0:N_GRP], gtop[:, t, 0:1], None, ALU.subtract))
                    link(nc.vector.tensor_scalar(wsel[:, t, :], etop[:, t, :], etop[:, t, 0:1], None, ALU.subtract))
                link(nc.vector.tensor_copy(eif[:, :, :], ei[:, :, :]))
                dve.sem_inc(diff_ready, 1)
                for c in range(2):
                    for t in range(NT):
                        link(nc.vector.tensor_scalar(wj[:, t, :], iota8, eif[:, t, c:c + 1], None, ALU.is_equal))
                        link(nc.vector.tensor_tensor(by_group(oh[:, c, t, :]), bc_last(goh[:, t, 0:N_GRP], EPG), bc_mid(wj[:, t, :], N_GRP), ALU.mult))
                link(nc.vector.tensor_tensor(sel[:, :, :], oh[:, 0, :, :], oh[:, 1, :, :], ALU.add))
                dve.sem_inc(sel_ready, 1)
                dve.wait_ge(exp_ready, 1)
                link(nc.vector.tensor_reduce(s1[:, :], gl[:, :, 0:N_GRP], AX, ALU.add))
                link(nc.vector.reciprocal(s1[:, :], s1[:, :]))
                link(nc.vector.tensor_reduce(s2[:, :], wsel[:, :, :], AX, ALU.add))
                link(nc.vector.reciprocal(s2[:, :], s2[:, :]))
                link(nc.vector.tensor_tensor(wsel[:, :, :], wsel[:, :, :], bc_last(s2[:, :], 8), ALU.mult))
                link(nc.vector.tensor_reduce(s2[:, :], wsel[:, :, 0:2], AX, ALU.add))
                link(nc.vector.reciprocal(s2[:, :], s2[:, :]))
                link(nc.vector.tensor_tensor(s2[:, :], s2[:, :], s1[:, :], ALU.mult))
                link(nc.vector.tensor_tensor(pair_w[:, :, :], wsel[:, :, 0:2], bc_last(s2[:, :], 2), ALU.mult))
                dve.wait_ge(rank_done, 1)
                link(nc.vector.tensor_tensor(rank[:, :, :], psum[:, 0, 0:NT * N_EXPERTS].rearrange("p (t e) -> p t e", t=NT), bc_mid(base[:, :], NT), ALU.add))
                link(nc.vector.tensor_reduce(most[:, :], psum[:, 0, NT * N_EXPERTS:(NT + 1) * N_EXPERTS], AX, ALU.max))
                link(nc.vector.tensor_scalar(crowded[:, :], most[:, :], float(P), None, ALU.is_gt))
                for c in range(2):
                    link(nc.vector.tensor_tensor(sel[:, :, :], oh[:, c, :, :], rank[:, :, :], ALU.mult))
                    link(nc.vector.tensor_reduce(rowf[:, :, c], sel[:, :, :], AX, ALU.add))
                    link(nc.vector.tensor_tensor(oh[:, c, :, :], oh[:, c, :, :], bc_last(pair_w[:, :, c], N_EXPERTS), ALU.mult))
                link(nc.vector.tensor_scalar(pair_row[:, :, :], rowf[:, :, :], -1.0, None, ALU.add))
                link(nc.vector.tensor_tensor(token_w[:, :, :], oh[:, 0, :, :], oh[:, 1, :, :], ALU.add))

            @block.scalar
            def _(act):
                act.wait_ge(diff_ready, 1)
                nc.scalar.activation(gl[:, :, 0:N_GRP], gl[:, :, 0:N_GRP], ACT.Exp)
                nc.scalar.activation(wsel[:, :, :], wsel[:, :, :], ACT.Exp).then_inc(exp_ready, 1)


def moe_slots(nc, tag, psum, ident, tokens, pair_row, table, slot_token):
    with ExitStack() as ctx:
        sb = lambda m, s, d: ctx.enter_context(nc.sbuf_tensor(f"{tag}_{m}", s, d))
        zero, rows, rows_f = sb("zero", [N_EXPERTS, P], I32), sb("rows", [N_EXPERTS, P], I32), sb("rowsf", [N_EXPERTS, P], F32)
        zero_ready, cleared, scattered, rows_in, rows_ready, turned = ctx.enter_context(stage_sems(
            nc, *[f"{tag}_{s}" for s in ("zero", "clr", "sc", "rin", "rr", "turn")]))
        table_v = table.rearrange("(e s) o -> e (s o)", e=N_EXPERTS)
        with nc.Block() as block:
            @block.sync
            def _(sp):
                sp.wait_ge(zero_ready, 1)
                sp.dma_start(table_v, zero[:, :]).then_inc(cleared, 16)
                sp.wait_ge(scattered, 16 * 2 * NT)
                sp.dma_start(rows[:, :], table_v).then_inc(rows_in, 16)

            @block.gpsimd
            def _(pool):
                pool.wait_ge(cleared, 16)
                for t in range(NT):
                    for c in range(2):
                        pool.indirect_dma_start(out=table[:, :], out_offset=bass.IndirectOffsetOnAxis(ap=pair_row[:, t, c:c + 1], axis=0),
                                                in_=tokens[:, t:t + 1], in_offset=None).then_inc(scattered, 16)

            @block.vector
            def _(dve):
                nc.vector.memset(zero[:, :], 0).then_inc(zero_ready, 1)
                dve.wait_ge(rows_in, 16)
                nc.vector.tensor_copy(rows_f[:, :], rows[:, :]).then_inc(rows_ready, 1)
                dve.wait_ge(turned, 1)
                nc.vector.tensor_copy(slot_token[:, :], psum[:, 0, 0:N_EXPERTS])

            @block.tensor
            def _(pe):
                pe.wait_ge(rows_ready, 1)
                nc.tensor.transpose(psum[:, 0, 0:N_EXPERTS], rows_f[:, :], ident[0:N_EXPERTS, 0:N_EXPERTS]).then_inc(turned, 1)


def moe_experts(nc, tag, psum, ident, x, slot_token, w_a, w_b, w_out, y):
    FB = D_EXP // P
    n = N_EXPERTS
    with ExitStack() as ctx:
        sb = lambda m, s, d=F32: ctx.enter_context(nc.sbuf_tensor(f"{tag}_{m}", s, d))
        wa, wb, wo = sb("wa", [P, 2, KD, CH]), sb("wb", [P, 2, KD, CH]), sb("wo", [P, 2, FB, D])
        rows, xg, hidT, y_sb = sb("rows", [P, 2, D]), sb("xg", [P, 2, KD, P]), sb("hidT", [P, FB, P]), sb("y", [P, 2, D])
        nl, hid = sb("nl", [P, D_EXP]), sb("hid", [P, D_EXP])
        col0, col1 = sb("col0", [P, 1], U32), sb("col1", [P, 1], U32)
        (in0, in1, rows0, rows1, col_ready, x_turned, xg_ready, gu_done, nl_ready, hid_ready, h_turned, hT_ready, o_done, y_ready, out0, out1) = \
            ctx.enter_context(stage_sems(nc, *[f"{tag}_{s}" for s in (
                "in0", "in1", "rows0", "rows1", "col", "xt", "xg", "gu", "nl", "hid", "ht", "hTr", "od", "yr", "out0", "out1")]))
        loaded, rows_in, stored, cols = (in0, in1), (rows0, rows1), (out0, out1), (col0, col1)
        with nc.Block() as block:
            @block.sync
            def _(sp):
                with sp.Fori(0, n // 2) as i:
                    for u in range(2):
                        e = i * 2 + u
                        sp.wait_ge(o_done, e + 1)
                        sp.dma_start(wa[:, u, :, :], w_a(e)).then_inc(loaded[u], 16)
                        sp.dma_start(wb[:, u, :, :], w_b(e)).then_inc(loaded[u], 16)
                        sp.dma_start(wo[:, u, :, :], w_out(e)).then_inc(loaded[u], 16)

            @block.gpsimd
            def _(pool):
                with pool.Fori(0, n // 2) as i:
                    for u in range(2):
                        pool.sem_clear(col_ready)
                        pool.wait_ge(x_turned, i * 2 + (u + 1))
                        nc.gpsimd.tensor_copy(cols[u][:, :], slot_token[:, ds(i * 2 + u, 1)]).then_inc(col_ready, 1)
                        pool.wait_ge(col_ready, 1)
                        pool.indirect_dma_start(out=rows[:, u, :], out_offset=None, in_=x[:, :],
                                                in_offset=bass.IndirectOffsetOnAxis(ap=cols[u][:, :], axis=0)).then_inc(rows_in[u], 16)

            @block.tensor
            def _(pe):
                pe.sem_inc(o_done, 2)
                pe.sem_inc(x_turned, 2)

                def turn_rows(u, turn, evacuated):
                    pe.wait_ge(rows_in[u], turn * 16 + 16)
                    pe.wait_ge(xg_ready, evacuated)
                    for k in range(KD):
                        last = nc.tensor.transpose(psum[:, k // 4, k % 4 * P:(k % 4 + 1) * P], rows[:, u, k * P:(k + 1) * P], ident[:, :])
                    last.then_inc(x_turned, 1)

                def expert(e, u, turn, is_last):
                    pe.wait_ge(xg_ready, e * 2 + 4)
                    pe.wait_ge(loaded[u], turn * 48 + 48)
                    pe.wait_ge(hid_ready, e + 1)
                    for bank, w in ((2, wa), (3, wb)):
                        for k in range(KD):
                            last = nc.tensor.matmul(psum[:, bank, :], xg[:, u, k, :], w[:, u, k, :], start=k == 0, stop=k == KD - 1)
                    last.then_inc(gu_done, 1)
                    if not is_last:
                        turn_rows(1 - u, turn + u, e * 2 + 4)
                    pe.wait_ge(hid_ready, e + 2)
                    for f in range(FB):
                        last = nc.tensor.transpose(psum[:, 4, f * P:(f + 1) * P], hid[:, f * P:(f + 1) * P], ident[:, :])
                    last.then_inc(h_turned, 1)
                    pe.wait_ge(hT_ready, e + 1)
                    pe.wait_ge(y_ready, e + 1)
                    for half in range(2):
                        for f in range(FB):
                            last = nc.tensor.matmul(psum[:, 5 + half, :], hidT[:, f, :], wo[:, u, f, half * CH:(half + 1) * CH], start=f == 0, stop=f == FB - 1)
                    last.then_inc(o_done, 1)

                turn_rows(0, 0, 2)
                with pe.Fori(0, n // 2 - 1) as i:
                    for u in range(2):
                        expert(i * 2 + u, u, i, False)
                expert(n - 2, 0, n // 2 - 1, False)
                expert(n - 1, 1, n // 2 - 1, True)

            @block.scalar
            def _(act):
                act.sem_inc(xg_ready, 2)
                act.sem_inc(out0, 16)
                act.sem_inc(out1, 16)

                def take_rows(u, e):
                    act.wait_ge(x_turned, e + 3)
                    for b in range(2):
                        nc.scalar.copy(xg[:, u, b * 4:(b + 1) * 4, :], psum[:, b, :].rearrange("p (k s) -> p k s", s=P)).then_inc(xg_ready, 1)

                def expert(e, u, turn, is_last):
                    act.wait_ge(gu_done, e + 1)
                    nc.scalar.activation(nl[:, :], psum[:, 2, :], ACT.Silu).then_inc(nl_ready, 1)
                    if not is_last:
                        take_rows(1 - u, e + 1)
                    act.wait_ge(h_turned, e + 1)
                    nc.scalar.copy(hidT[:, :, :], psum[:, 4, :].rearrange("p (f s) -> p f s", s=P)).then_inc(hT_ready, 1)
                    act.wait_ge(y_ready, e + 2)
                    act.dma_start(y[ds(e * P, P), :], y_sb[:, u, :]).then_inc(stored[u], 16)

                take_rows(0, 0)
                with act.Fori(0, n // 2 - 1) as i:
                    for u in range(2):
                        expert(i * 2 + u, u, i, False)
                expert(n - 2, 0, n // 2 - 1, False)
                expert(n - 1, 1, n // 2 - 1, True)
                act.wait_ge(out0, n // 2 * 16 + 16)
                act.wait_ge(out1, n // 2 * 16 + 16)

            @block.vector
            def _(dve):
                dve.sem_inc(hid_ready, 1)
                dve.sem_inc(y_ready, 1)
                with dve.Fori(0, n // 2) as i:
                    for u in range(2):
                        e = i * 2 + u
                        dve.wait_ge(nl_ready, e + 1)
                        nc.vector.tensor_tensor(hid[:, :], nl[:, :], psum[:, 3, :], ALU.mult).then_inc(hid_ready, 1)
                        dve.wait_ge(o_done, e + 3)
                        dve.wait_ge(stored[u], i * 16 + 16)
                        for half in range(2):
                            last = nc.vector.tensor_copy(y_sb[:, u, half * CH:(half + 1) * CH], psum[:, 5 + half, :])
                        last.then_inc(y_ready, 1)


def moe_collect(nc, tag, y, pair_row, pair_w, acc):
    with ExitStack() as ctx:
        rows = ctx.enter_context(nc.sbuf_tensor(f"{tag}_rows", [P, NT, 2, D], F32))
        rows_in, dve_order = ctx.enter_context(stage_sems(nc, f"{tag}_in", f"{tag}_dve"))
        with nc.Block() as block:
            @block.gpsimd
            def _(pool):
                for t in range(NT):
                    for c in range(2):
                        pool.indirect_dma_start(out=rows[:, t, c, :], out_offset=None, in_=y[:, :],
                                                in_offset=bass.IndirectOffsetOnAxis(ap=pair_row[:, t, c:c + 1], axis=0)).then_inc(rows_in, 16)

            @block.vector
            def _(dve):
                link = chain(dve, dve_order)
                dve.wait_ge(rows_in, 32 * NT)
                for t in range(NT):
                    link(nc.vector.tensor_scalar(acc[:, t, :], rows[:, t, 0, :], pair_w[:, t, 0:1], None, ALU.mult))
                    link(nc.vector.scalar_tensor_tensor(out=acc[:, t, :], in0=rows[:, t, 1, :], scalar=pair_w[:, t, 1:2], in1=acc[:, t, :],
                                                        op0=ALU.mult, op1=ALU.add))


def build(nc, a, out):
    dram = lambda name, shape: nc.dram_tensor(name, shape, F32, kind="Internal").ap()
    with ExitStack() as ctx:
        sb = lambda m, s: ctx.enter_context(nc.sbuf_tensor(m, s, F32))
        psum = ctx.enter_context(nc.psum_tensor("psum", [P, 8, CH], F32))
        ident, tri, iota = sb("ident", [P, P]), sb("tri", [P, P]), sb("iota", [P, P])
        tokens = ctx.enter_context(nc.sbuf_tensor("tokens", [P, NT], I32))
        h, xT = sb("h", [P, NT, D]), sb("xT", [P, KD, T])
        with ExitStack() as st:
            (cin,) = st.enter_context(stage_sems(nc, "consts_in"))
            with nc.Block() as block:
                @block.sync
                def _(sp):
                    sp.dma_start(ident[:, :], a["c_ident"]).then_inc(cin, 16)
                    sp.dma_start(tri[:, :], a["c_tri"]).then_inc(cin, 16)
                    sp.dma_start(iota[:, :], a["c_iota"]).then_inc(cin, 16)
                    sp.dma_start(h[:, :, :], tiled(a["x"][0])).then_inc(cin, 16)
                    sp.dma_start(tokens[:, :], a["c_tokens"]).then_inc(cin, 16)
                    sp.wait_ge(cin, 80)

        u_gain = a["norm_mix_w"][0]
        norm_transpose(nc, "n1", psum, ident, h, u_gain, xT)
        proj = dram("proj", [T, IN_W])
        xbcT, convT, conv_tok = dram("xbcT", [XBC, T]), dram("convT", [XBC, T]), dram("conv_tok", [T, XBC])
        w_in = a["w_in"][0]
        linear(nc, "lz", psum, xT, KD, w_in[:, 0:D], proj[:, 0:D], D)
        linear(nc, "lx", psum, xT, KD, w_in[:, OFF_XBC:OFF_DT], xbcT, XBC, feature_major=True)
        linear(nc, "lr", psum, xT, KD, w_in[:, OFF_DT:IN_W], proj[:, OFF_DT:IN_W], IN_W - OFF_DT)
        dt, da, y_raw, y_ssd = dram("dt", [T, HEADS]), dram("da", [T, HEADS]), dram("y_raw", [T, D]), dram("y_ssd", [T, D])
        conv_silu(nc, "cv", psum, ident, xbcT, a["taps"], convT, conv_tok)
        ssd_dt(nc, "sdt", proj[:, OFF_DT:OFF_DQ], a["ssd_dt_bias"][0], a["ssd_a_log"][0], dt, da)
        ssd_scan(nc, "ssd", psum, tri, convT, conv_tok, dt, da, a["ssd_d"][0], y_raw)
        ssd_gate_norm(nc, "sgn", y_raw, proj[:, 0:D], a["ssd_norm_w"][0], y_ssd)

        qd, kd, od, lse = dram("qd", [T, 12, HD]), dram("kd", [T, 12, HD]), dram("od", [T, 12, HD]), dram("lse", [T, 12])
        with ExitStack() as st:
            cos = st.enter_context(nc.sbuf_tensor("cos1", [P, NT, 8], F32))
            sin = st.enter_context(nc.sbuf_tensor("sin1", [P, NT, 8], F32))
            rope_tables(nc, "rt1", a["positions"][0], a["c_inv1"], 8, cos, sin)
            head_prep(nc, "pdq", proj[:, OFF_DQ:OFF_DK], qd, 12, HD, a["dil_q_norm_w"][0], cos, sin, 16)
            head_prep(nc, "pdk", proj[:, OFF_DK:OFF_DV], kd, 12, HD, a["dil_k_norm_w"][0], cos, sin, 16)
        vd = proj[:, OFF_DV:OFF_MQ].rearrange("t (h d) -> t h d", d=HD)
        for g in range(DIL):
            hs = slice(g * 4, g * 4 + 4)
            span = (lambda qt: (max(0, qt - 1), qt + 1)) if g == 0 else (lambda qt: (0, qt + 1))
            attention(nc, f"da{g}", psum, ident, qd[:, hs, :], kd[:, hs, :], vd[:, hs, :], od[:, hs, :], [HD], HD, HD ** -0.5, NT,
                      mask=a["c_mask"][g], span=span, lse=lse[:, hs])
        y_dil = dram("y_dil", [T, 4 * HD])
        dil_combine(nc, "dc", od.rearrange("t h d -> t (h d)"), lse, y_dil)

        MT = N_MEM // P
        MHD = MEM_W // 4
        mkv, mk, mqn, y_mem = dram("mkv", [N_MEM, 2 * MEM_W]), dram("mk", [N_MEM, 4, MHD]), dram("mqn", [T, 4, MHD]), dram("y_mem", [T, 4, MHD])
        with ExitStack() as st:
            mem = st.enter_context(nc.sbuf_tensor("mem_sb", [P, MT, D], F32))
            memT = st.enter_context(nc.sbuf_tensor("memT", [P, KD, N_MEM], F32))
            (min_,) = st.enter_context(stage_sems(nc, "mem_in"))
            with nc.Block() as block:
                @block.sync
                def _(sp):
                    sp.dma_start(mem[:, :, :], tiled(a["mem"][0])).then_inc(min_, 16)
                    sp.wait_ge(min_, 16)
            norm_transpose(nc, "nm", psum, ident, mem, a["mem_norm_w"][0], memT, tiles=MT)
            linear(nc, "lm", psum, memT, KD, a["w_mem_kv"][0], mkv, 2 * MEM_W, tiles=MT)
        head_prep(nc, "pmk", mkv[:, 0:MEM_W], mk, 4, MHD, a["mem_k_norm_w"][0])
        head_prep(nc, "pmq", proj[:, OFF_MQ:OFF_GATE], mqn, 4, MHD, a["mem_q_norm_w"][0])
        mv = mkv[:, MEM_W:2 * MEM_W].rearrange("t (h d) -> t h d", d=MHD)
        attention(nc, "ma", psum, ident, mqn, mk, mv, y_mem, [P, MHD - P], MHD, MHD ** -0.5, MT)

        br = [dram(f"br{i}", [T, D]) for i in range(3)]
        merged, mixed = dram("merged", [T, D]), dram("mixed", [T, D])
        for i, (y, width, w) in enumerate(((y_ssd, D, a["w_ssd_br"][0]), (y_dil, 4 * HD, a["w_dil_br"][0]),
                                           (y_mem.rearrange("t h d -> t (h d)"), MEM_W, a["w_mem_br"][0]))):
            load_transpose(nc, f"bt{i}", psum, ident, y, xT, width)
            linear(nc, f"bl{i}", psum, xT, width // P, w, br[i], D)
        gated_merge(nc, "gm", proj[:, OFF_GATE:IN_W], br, merged)
        load_transpose(nc, "mt", psum, ident, merged, xT, D)
        linear(nc, "ml", psum, xT, KD, a["w_out"][0], mixed, D)
        add_residual(nc, "ar1", h, mixed)

        norm_transpose(nc, "n2", psum, ident, h, a["norm_ffn_w"][0], xT)
        qT, sel, gates = dram("peer_qT", [2 * P * PEER_H, T]), dram("peer_sel", [T, 3, P]), dram("peer_gates", [NT, NK, NK, P])
        linear(nc, "pq", psum, xT, KD, a["peer_w_query"][0], qT, 2 * P * PEER_H, feature_major=True)
        peer_route(nc, "pr", psum, qT, a["keysT"], iota[:, 0:TOPK], sel)
        with ExitStack() as st:
            selT = st.enter_context(nc.sbuf_tensor("selT", [P, 3, T], F32))
            load_transpose(nc, "pst", psum, ident, sel.rearrange("t a k -> t (a k)"), selT, 3 * P)
            peer_gates(nc, "pg", psum, selT, iota[:, :], gates)

        def add_acc(tag, acc, gate=None):
            with ExitStack() as st:
                gs = st.enter_context(nc.sbuf_tensor(f"{tag}_g", [P, D], F32))
                gin, order = st.enter_context(stage_sems(nc, f"{tag}_gin", f"{tag}_ord"))
                with nc.Block() as block:
                    @block.sync
                    def _(sp):
                        if gate is not None:
                            sp.dma_start(gs[:, :], row_bc(gate)).then_inc(gin, 16)

                    @block.vector
                    def _(dve):
                        link = chain(dve, order)
                        if gate is not None:
                            dve.wait_ge(gin, 16)
                        for t in range(NT):
                            if gate is not None:
                                link(nc.vector.tensor_tensor(acc[:, t, :], acc[:, t, :], gs[:, :], ALU.mult))
                            link(nc.vector.tensor_tensor(h[:, t, :], h[:, t, :], acc[:, t, :], ALU.add))

        downT = a["downT"].rearrange("(k p) e -> p k e", p=P)
        up = a["peer_up"][0].rearrange("(f p) d -> p f d", p=P)
        with ExitStack() as st:
            acc = st.enter_context(nc.sbuf_tensor("peer_acc", [P, NT, D], F32))
            ffn_loop(nc, "pf", psum, xT, acc, N_EXP1 // CH, lambda e: downT[:, :, ds(e * CH, CH)], lambda e: up[:, ds(e * 4, 4), :], gates=gates)
            add_acc("pa", acc)

        mods = dram("mods", [LAYERS, 1, 6 * D])
        adaptive_rows(nc, "ada", psum, a["c_2"][0], a["ada_w_2"], a["ada_b_2"], mods)
        cos = sb("cos2", [P, NT, 32])
        sin = sb("sin2", [P, NT, 32])
        rope_tables(nc, "rt2", a["positions_2"][0], a["c_inv2"], 32, cos, sin)
        proj2, gates2, h2 = dram("proj2", [T, D_IN2]), dram("gates2", [T, 3 * D]), None
        rq, rk, ro, ya = dram("rq", [T, 4, 64]), dram("rk", [T, 4, 64]), dram("ro", [T, 512]), dram("ya", [T, 512])
        qa, ka, yb = dram("qa", [T, 4, 130]), dram("ka", [T, 4, 130]), dram("yb", [T, 4, 128])
        qh, qr, kvh, kp, kc, yc = (dram("qh", [T, 768]), dram("qr", [T, 4, 192]), dram("kvh", [T, 1024]), dram("kp", [T, 1, 64]),
                                   dram("kc", [T, 4, 192]), dram("yc", [T, 4, 128]))
        logits, h_norm, y_exp = dram("logits", [T, 36]), dram("h_norm", [T, D]), dram("y_exp", [N_EXPERTS * P, D])
        table = nc.dram_tensor("table", [N_EXPERTS * P, 1], I32, kind="Internal").ap()
        causal = lambda qt: (0, qt + 1)
        for l in range(LAYERS):
            mod = [mods[l][0, i * D:(i + 1) * D] for i in range(6)]
            norm_transpose(nc, f"m{l}", psum, ident, h, a["norm1_g_2"][l], xT, shift=mod[0], scale=mod[1])
            linear(nc, f"i{l}", psum, xT, KD, a["w_in_2"][l], proj2, D_IN2)
            linear(nc, f"g{l}", psum, xT, KD, a["gate_w_2"][l], gates2, 3 * D)
            head_prep(nc, f"rq{l}", proj2[:, RQ:RK], rq, 4, 64, None, cos, sin, 64)
            head_prep(nc, f"rk{l}", proj2[:, RK:RV], rk, 4, 64, None, cos, sin, 64)
            retention(nc, f"re{l}", psum, ident, rq.rearrange("t h d -> t (h d)"), rk.rearrange("t h d -> t (h d)"), proj2[:, RV:RG],
                      (a["c_dmask"], a["c_decay"]), ro)
            retention_gate_norm(nc, f"rn{l}", ro, proj2[:, RG:FQ], ya)
            fox_prep(nc, f"fp{l}", psum, tri, proj2, a["fox_fb_2"][l], qa, ka)
            fv = proj2[:, FV:FF].rearrange("t (h d) -> t h d", h=4)
            attention(nc, f"fa{l}", psum, ident, qa, ka, fv, yb, [P, 2], P, P ** -0.5, NT, mask=a["c_mask"][3], span=causal)
            with ExitStack() as st:
                lat = st.enter_context(nc.sbuf_tensor(f"lat{l}", [P, NT, 384], F32))
                latT = st.enter_context(nc.sbuf_tensor(f"latT{l}", [P, 2, T], F32))
                (lin,) = st.enter_context(stage_sems(nc, f"lat_in{l}"))
                with nc.Block() as block:
                    @block.sync
                    def _(sp):
                        sp.dma_start(lat[:, :, :], tiled(proj2)[:, :, MQ2:MKR]).then_inc(lin, 16)
                        sp.wait_ge(lin, 16)
                norm_transpose(nc, f"nq{l}", psum, ident, lat[:, :, 0:256], a["mla_q_norm_g_2"][l], latT, width=256)
                linear(nc, f"lq{l}", psum, latT, 2, a["mla_wq_up_2"][l], qh, 768)
                norm_transpose(nc, f"nk{l}", psum, ident, lat[:, :, 256:384], a["mla_kv_norm_g_2"][l], latT, width=128)
                linear(nc, f"lk{l}", psum, latT, 1, a["mla_wkv_up_2"][l], kvh, 1024)
            head_prep(nc, f"hq{l}", qh, qr, 4, 192, None, cos, sin, 64, 128)
            head_prep(nc, f"hk{l}", proj2[:, MKR:D_IN2], kp, 1, 64, None, cos, sin, 64)
            kv = kvh.rearrange("t (h d) -> t h d", h=4)
            copy_pieces(nc, f"kc{l}", [(kc[:, :, 0:P], kv[:, :, 0:P])] + [(kc[:, i:i + 1, P:P + 64], kp) for i in range(4)])
            attention(nc, f"la{l}", psum, ident, qr, kc, kv[:, :, P:2 * P], yc, [P, 64], P, 192 ** -0.5, NT, mask=a["c_mask"][3], span=causal)
            for i, y in enumerate((ya, yb.rearrange("t h d -> t (h d)"), yc.rearrange("t h d -> t (h d)"))):
                load_transpose(nc, f"bt{l}{i}", psum, ident, y, xT, 512)
                linear(nc, f"bl{l}{i}", psum, xT, 4, a["branch_w_2"][l, i], br[i], D)
            gated_merge(nc, f"gm{l}", gates2, br, merged, bias=a["gate_b_2"][l])
            load_transpose(nc, f"mt{l}", psum, ident, merged, xT, D)
            linear(nc, f"ml{l}", psum, xT, KD, a["out_w_2"][l], mixed, D)
            add_residual(nc, f"as{l}", h, mixed, gate=mod[2])
            norm_transpose(nc, f"k{l}", psum, ident, h, a["norm2_g_2"][l], xT, shift=mod[3], scale=mod[4], keep=h_norm)
            linear(nc, f"rl{l}", psum, xT, KD, a["router_w"][l], logits, 36)
            with ExitStack() as st:
                sbt = lambda m, s, d=F32: st.enter_context(nc.sbuf_tensor(f"{m}{l}", s, d))
                token_w, acc = sbt("token_w", [P, NT, N_EXPERTS]), sbt("moe_acc", [P, NT, D])
                pair_w, pair_row = sbt("pair_w", [P, NT, 2]), sbt("pair_row", [P, NT, 2], U32)
                crowded, slot_token = sbt("crowded", [P, 1], I32), sbt("slot_token", [P, N_EXPERTS], U32)
                moe_route(nc, f"mr{l}", psum, tri, logits, a["router_b"][l], iota, token_w, pair_w, pair_row, crowded)
                w1, w3 = (a[n][l].rearrange("e (k p) f -> p (e k) f", p=P) for n in ("exp_w1_2", "exp_w3_2"))
                w2 = a["exp_w2_2"][l].rearrange("e (f p) d -> p (e f) d", p=P)
                take_w1, take_w3 = (lambda e: w1[:, ds(e * KD, KD), :]), (lambda e: w3[:, ds(e * KD, KD), :])
                take_w2 = lambda e: w2[:, ds(e * 4, 4), :]
                over = nc.values_load(crowded[0:1, 0:1], min_val=0, max_val=1)
                with nc.If(over == 1):
                    ffn_loop(nc, f"mf{l}", psum, xT, acc, N_EXPERTS, take_w1, take_w2, w_b=take_w3, token_w=token_w)
                with nc.Else():
                    moe_slots(nc, f"ms{l}", psum, ident, tokens, pair_row, table, slot_token)
                    moe_experts(nc, f"me{l}", psum, ident, h_norm, slot_token, take_w1, take_w3, take_w2, y_exp)
                    moe_collect(nc, f"mc{l}", y_exp, pair_row, pair_w, acc)
                add_acc(f"aa{l}", acc, gate=mod[5])

        norm_transpose(nc, "nf", psum, ident, h, a["final_g_2"], xT, keep=out[0])


_INPUTS = ("x", "mem", "positions", "norm_mix_w", "w_in", "ssd_dt_bias", "ssd_a_log", "ssd_d", "ssd_norm_w", "dil_q_norm_w",
           "dil_k_norm_w", "mem_norm_w", "w_mem_kv", "mem_q_norm_w", "mem_k_norm_w", "w_ssd_br", "w_dil_br", "w_mem_br", "w_out",
           "norm_ffn_w", "peer_w_query", "peer_up", "c_2", "positions_2", "ada_w_2", "ada_b_2", "norm1_g_2", "norm2_g_2",
           "w_in_2", "fox_fb_2", "mla_q_norm_g_2", "mla_wq_up_2", "mla_kv_norm_g_2", "mla_wkv_up_2", "gate_w_2", "gate_b_2",
           "branch_w_2", "out_w_2", "exp_w1_2", "exp_w3_2", "exp_w2_2", "final_g_2")


def shape_constants():
    f = np.float32
    i = np.arange(P)
    t = np.arange(T)
    dist = t[:, None] - t[None, :]
    seen = [(dist >= 0) & (dist <= 128), (dist >= 0) & (dist % 4 == 0), (dist >= 0) & (dist % 16 == 0), dist >= 0]
    log_gamma = np.log1p(-np.exp2(-5.0 - np.arange(4)))
    rel = i[None, :] - i[:, None]
    dmask = np.where(rel[:, None, :] >= 0, np.exp(log_gamma[None, :, None] * np.maximum(rel, 0)[:, None, :]), 0.0) * 64 ** -0.5
    decay = np.stack([np.exp(log_gamma[None, :] * (i[:, None] + 1.0)), np.exp(log_gamma[None, :] * (P - 1.0 - i[:, None])) * 64 ** -0.5,
                      np.broadcast_to(np.exp(log_gamma * P), (P, 4))], axis=1)
    return {
        "c_ident": np.eye(P, dtype=f), "c_tri": (i[:, None] <= i[None, :]).astype(f),
        "c_iota": np.broadcast_to(np.arange(P, dtype=f), (P, P)).copy(),
        "c_mask": np.stack([np.where(s, 0.0, NEG) for s in seen]).astype(f),
        "c_inv1": np.exp(f(-math.log(500000.0)) * f(2.0 / 16) * np.arange(8, dtype=f)).astype(f),
        "c_inv2": (10000.0 ** (-np.arange(0, 64, 2) / 64.0)).astype(f),
        "c_tokens": (i[:, None] + P * np.arange(NT)[None, :]).astype(np.int32),
        "c_dmask": dmask.reshape(P, 4 * P).astype(f), "c_decay": decay.reshape(P, 12).astype(f),
    }


def kernel(**inputs):
    import concourse.bacc as bacc
    from concourse.bass_utils import run_bass_kernel_spmd

    arrays = {n: np.ascontiguousarray(inputs[n]) for n in _INPUTS}
    arrays["taps"] = np.ascontiguousarray(np.concatenate([inputs["ssd_conv_w"][0], inputs["ssd_conv_b"]], axis=0).T)
    arrays["keysT"] = np.ascontiguousarray(np.transpose(inputs["peer_sub_keys"][0], (0, 1, 3, 2)).reshape(2 * P * PEER_H, NK))
    arrays["downT"] = np.ascontiguousarray(inputs["peer_down"][0].T)
    arrays["router_w"] = np.ascontiguousarray(np.concatenate([inputs["router_grp_w_2"], inputs["router_exp_w_2"]], axis=2))
    arrays["router_b"] = np.ascontiguousarray(np.concatenate([inputs["router_grp_b_2"], inputs["router_exp_b_2"]], axis=1))
    arrays.update(shape_constants())

    nc = bacc.Bacc("TRN2", target_bir_lowering=False, num_devices=1)
    aps = {n: nc.dram_tensor(f"in_{n}", v.shape, mybir.dt.from_np(v.dtype), kind="ExternalInput").ap() for n, v in arrays.items()}
    out = nc.dram_tensor("out_0", (1, T, D), F32, kind="ExternalOutput").ap()
    build(nc, aps, out)
    result = run_bass_kernel_spmd(nc, [{f"in_{n}": v for n, v in arrays.items()}], core_ids=[0])
    return result.results[0]["out_0"]
```

```python
import math
from contextlib import ExitStack, contextmanager

import numpy as np

import concourse.bass as bass
from concourse import mybir

F32 = mybir.dt.float32
F32R = mybir.dt.float32r
I32 = mybir.dt.int32
U32 = mybir.dt.uint32
ALU = mybir.AluOpType
ACT = mybir.ActivationFunctionType
AX = mybir.AxisListType.X
ds = bass.ds

P = 128
T = 512
NT = T // P
D = 1024
KD = D // P
CH = 512
EPS = 1e-6
NEG = -1e30

N_MEM = 256
HEADS, GROUPS, HPG, HD, STATE = 16, 4, 4, 64, 128
CONV = 4
XBC = D + 2 * GROUPS * STATE
DIL = 3
DIL_W = 768
MEM_W = 768
OFF_Z, OFF_XBC = 0, D
OFF_DT = OFF_XBC + XBC
OFF_DQ = OFF_DT + HEADS
OFF_DK, OFF_DV, OFF_MQ = OFF_DQ + DIL_W, OFF_DQ + 2 * DIL_W, OFF_DQ + 3 * DIL_W
OFF_GATE = OFF_MQ + MEM_W
IN_W = OFF_GATE + 3 * D
PEER_H, NK, TOPK = 8, 128, 16
N_EXP1 = NK * NK
LAYERS = 2
D_IN2 = 3524
RQ, RK, RV, RG, FQ, FK, FV, FF, MQ2, MKV, MKR = (0, 256, 512, 1024, 1536, 2048, 2560, 3072, 3076, 3332, 3460)
N_EXPERTS, EPG, N_GRP, D_EXP = 32, 8, 4, 512


@contextmanager
def stage_sems(nc, *names):
    sems = [nc.alloc_semaphore(n) for n in names]
    yield sems
    nc.clear_and_free_semaphores(sems)
    nc.all_engine_barrier()


def chain(eng, sem):
    count = [0]

    def link(ins):
        count[0] += 1
        ins.then_inc(sem, 1)
        eng.wait_ge(sem, count[0])

    return link


def refined_root(nc, link, r, mean, tmp):
    link(nc.vector.reciprocal(r, r))
    link(nc.vector.tensor_tensor(tmp, r, r, ALU.mult))
    link(nc.vector.tensor_tensor(tmp, tmp, mean, ALU.mult))
    link(nc.vector.tensor_scalar(tmp, tmp, -0.5, 1.5, ALU.mult, ALU.add))
    link(nc.vector.tensor_tensor(r, r, tmp, ALU.mult))


def times(nc, out, lhsT, rhs, first=True, last=True):
    (lh, ll), (rh, rl) = lhsT, rhs
    nc.tensor.matmul(out, lh, rh, start=first, stop=False)
    nc.tensor.matmul(out, lh, rl, start=False, stop=False)
    return nc.tensor.matmul(out, ll, rh, start=False, stop=last)


def take_bank(nc, bank, ident):
    nc.tensor.transpose(bank, ident[:, :], ident[:, :])


def tiled(x):
    return x.rearrange("(t p) n -> p t n", p=P)


def row_bc(row, parts=P):
    return row.rearrange("(o n) -> o n", o=1).broadcast_to([parts, row.shape[0]])


def bc_mid(ap, n):
    return ap.rearrange("p (o a) -> p o a", o=1).broadcast_to([ap.shape[0], n, ap.shape[1]])


def bc_last(ap, n):
    return ap.rearrange("p (a o) -> p a o", o=1).broadcast_to([ap.shape[0], ap.shape[1], n])


def linear(nc, tag, psum, x, kc, w, out, n_cols, tiles=NT, feature_major=False):
    full, tail = n_cols // CH, n_cols % CH
    w_v = w.rearrange("(k p) n -> p k n", p=P)
    blocks = CH // P if feature_major else tiles
    width = tiles * P if feature_major else CH
    with ExitStack() as ctx:
        wbuf = ctx.enter_context(nc.sbuf_tensor(f"{tag}_w", [P, 2, kc, CH], F32))
        w_high = ctx.enter_context(nc.sbuf_tensor(f"{tag}_wh", [P, 2, kc, CH], F32R))
        w_low = ctx.enter_context(nc.sbuf_tensor(f"{tag}_wl", [P, 2, kc, CH], F32R))
        obuf = ctx.enter_context(nc.sbuf_tensor(f"{tag}_o", [P, 2, 4, CH], F32))
        (w_in0, w_in1, high_ready, low_ready, tile_done, evac_v, evac_a, out0, out1) = ctx.enter_context(stage_sems(
            nc, *[f"{tag}_{s}" for s in ("w_in0", "w_in1", "high", "low", "tile", "ev", "ea", "out0", "out1")]))
        w_in, stored = (w_in0, w_in1), (out0, out1)
        pairs, odd = full // 2, full % 2
        on_v = (blocks + 1) // 2
        on_a = blocks - on_v
        chunk_cols = [CH] * full + [tail] * bool(tail)

        def chunks(eng, body):
            if pairs:
                with eng.Fori(0, pairs) as i:
                    for u in range(2):
                        body(i * 2 + u, u, i, CH)
            if odd:
                body(full - 1, 0, pairs, CH)
            if tail:
                body(full, odd, pairs, tail)

        def ahead(eng, first, second):
            n = len(chunk_cols)
            first(0, 0, 0, chunk_cols[0])
            steady = max(0, (full - 2) // 2)
            if steady:
                with eng.Fori(0, steady) as i:
                    for u in range(2):
                        first(i * 2 + (u + 1), 1 - u, i + u, CH)
                        second(i * 2 + u, u, i, CH)
            for j in range(2 * steady, n):
                if j + 1 < n:
                    first(j + 1, (j + 1) % 2, (j + 1) // 2, chunk_cols[j + 1])
                second(j, j % 2, j // 2, chunk_cols[j])

        with nc.Block() as block:
            @block.sync
            def _(sp):
                def load(j, u, turn, cols):
                    sp.wait_ge(low_ready, j + 1)
                    sp.dma_start(wbuf[:, u, :, 0:cols], w_v[:, :, ds(j * CH, cols)]).then_inc(w_in[u], 16)
                chunks(sp, load)

            @block.tensor
            def _(pe):
                pe.sem_inc(tile_done, 2 * blocks)

                def multiply(j, u, turn, cols):
                    pe.wait_ge(low_ready, j + 3)
                    pe.wait_ge(evac_v, j * on_v + on_v)
                    if on_a:
                        pe.wait_ge(evac_a, j * on_a + on_a)
                    for b in range(blocks):
                        for k in range(kc):
                            if feature_major:
                                last = times(nc, psum[:, u * 4 + b, 0:width], [v[:, u, k, b * P:(b + 1) * P] for v in (w_high, w_low)],
                                             [v[:, k, 0:width] for v in x], k == 0, k == kc - 1)
                            else:
                                last = times(nc, psum[:, u * 4 + b, 0:cols], [v[:, k, b * P:(b + 1) * P] for v in x],
                                             [v[:, u, k, 0:cols] for v in (w_high, w_low)], k == 0, k == kc - 1)
                        last.then_inc(tile_done, 1)
                chunks(pe, multiply)

            @block.vector
            def _(dve):
                dve.sem_inc(evac_v, 2 * on_v)

                def make_low(j, u, turn, cols):
                    dve.wait_ge(high_ready, j + 1)
                    nc.vector.tensor_tensor(w_low[:, u, :, 0:cols], wbuf[:, u, :, 0:cols], w_high[:, u, :, 0:cols].bitcast(F32),
                                            ALU.subtract).then_inc(low_ready, 1)

                def evacuate(j, u, turn, cols):
                    dve.wait_ge(stored[u], turn * 16 + 16)
                    n = width if feature_major else cols
                    for b in range(on_v):
                        dve.wait_ge(tile_done, j * blocks + (2 * blocks + b + 1))
                        nc.vector.tensor_copy(obuf[:, u, b, 0:n], psum[:, u * 4 + b, 0:n]).then_inc(evac_v, 1)

                dve.sem_inc(low_ready, 2)
                ahead(dve, make_low, evacuate)

            @block.scalar
            def _(act):
                act.sem_inc(evac_a, 2 * on_a) if on_a else None
                act.sem_inc(out0, 16)
                act.sem_inc(out1, 16)

                def make_high(j, u, turn, cols):
                    act.wait_ge(w_in[u], turn * 16 + 16)
                    act.wait_ge(tile_done, j * blocks + blocks)
                    nc.scalar.copy(w_high[:, u, :, 0:cols], wbuf[:, u, :, 0:cols]).then_inc(high_ready, 1)

                def evacuate_store(j, u, turn, cols):
                    act.wait_ge(stored[u], turn * 16 + 16)
                    n = width if feature_major else cols
                    for b in range(on_v, blocks):
                        act.wait_ge(tile_done, j * blocks + (2 * blocks + b + 1))
                        nc.scalar.copy(obuf[:, u, b, 0:n], psum[:, u * 4 + b, 0:n]).then_inc(evac_a, 1)
                    act.wait_ge(evac_v, j * on_v + 3 * on_v)
                    if on_a:
                        act.wait_ge(evac_a, j * on_a + 3 * on_a)
                    if feature_major:
                        dst = out[ds(j * CH, CH), 0:width].rearrange("(b p) t -> p b t", p=P)
                        src = obuf[:, u, :, 0:width]
                    else:
                        dst, src = tiled(out)[:, :, ds(j * CH, cols)], obuf[:, u, 0:tiles, 0:cols]
                    act.dma_start(dst, src).then_inc(stored[u], 16)

                ahead(act, make_high, evacuate_store)
                last = [0, 0]
                for j in range(full + bool(tail)):
                    last[j % 2] += 16
                act.wait_ge(out0, last[0] + 16)
                act.wait_ge(out1, last[1] + 16)


def low_halves(nc, dve, psum, xT, kc, tiles, high_ready, evacuated):
    for k in range(kc):
        dve.wait_ge(high_ready, k + 1)
        nc.vector.tensor_tensor(xT[1][:, k, 0:tiles * P], psum[:, k % 4, 0:tiles * P], xT[0][:, k, 0:tiles * P].bitcast(F32),
                                ALU.subtract).then_inc(evacuated, 1)


def norm_transpose(nc, tag, psum, ident, x, gain, xT, tiles=NT, width=D, shift=None, scale=None, keep=None):
    kc = width // P
    with ExitStack() as ctx:
        sb = lambda n, s, d=F32: ctx.enter_context(nc.sbuf_tensor(f"{tag}_{n}", s, d))
        gain_sb, y = sb("gain", [P, width]), sb("y", [P, tiles, width])
        sq, stat = sb("sq", [P, width]), sb("stat", [P, tiles, 4])
        shift_sb = sb("shift", [P, width]) if shift is not None else None
        scale_sb = sb("scale", [P, width]) if shift is not None else None
        rows_in, mean_ready, root_ready, y_ready, transposed, high_ready, evacuated, dve_order, kept = ctx.enter_context(stage_sems(
            nc, *[f"{tag}_{s}" for s in ("rows", "mean", "root", "y", "tr", "high", "ev", "dve", "kept")]))
        with nc.Block() as block:
            @block.sync
            def _(sp):
                sp.dma_start(gain_sb[:, :], row_bc(gain)).then_inc(rows_in, 16)
                if shift is not None:
                    sp.dma_start(shift_sb[:, :], row_bc(shift)).then_inc(rows_in, 16)
                    sp.dma_start(scale_sb[:, :], row_bc(scale)).then_inc(rows_in, 16)
                if keep is not None:
                    sp.wait_ge(y_ready, tiles)
                    sp.dma_start(tiled(keep), y[:, :, :]).then_inc(kept, 16)
                    sp.wait_ge(kept, 16)

            @block.vector
            def _(dve):
                link = chain(dve, dve_order)
                for t in range(tiles):
                    link(nc.vector.tensor_tensor_reduce(out=sq[:, :], in0=x[:, t, :], in1=x[:, t, :], scale=1.0, scalar=0.0,
                                                        op0=ALU.mult, op1=ALU.add, accum_out=stat[:, t, 0:1]))
                    nc.vector.tensor_scalar(stat[:, t, 1:2], stat[:, t, 0:1], 1.0 / width, EPS, ALU.mult,
                                            ALU.add).then_inc(mean_ready, 1)
                dve.wait_ge(rows_in, 48 if shift is not None else 16)
                if shift is not None:
                    link(nc.vector.tensor_scalar(scale_sb[:, :], scale_sb[:, :], 1.0, None, ALU.add))
                for t in range(tiles):
                    dve.wait_ge(root_ready, t + 1)
                    refined_root(nc, link, stat[:, t, 2:3], stat[:, t, 1:2], stat[:, t, 3:4])
                    ins = nc.vector.scalar_tensor_tensor(out=y[:, t, :], in0=x[:, t, :], scalar=stat[:, t, 2:3],
                                                         in1=gain_sb[:, :], op0=ALU.mult, op1=ALU.mult)
                    if shift is not None:
                        link(ins)
                        link(nc.vector.tensor_tensor(y[:, t, :], y[:, t, :], scale_sb[:, :], ALU.mult))
                        ins = nc.vector.tensor_tensor(y[:, t, :], y[:, t, :], shift_sb[:, :], ALU.add)
                    ins.then_inc(y_ready, 1)
                low_halves(nc, dve, psum, xT, kc, tiles, high_ready, evacuated)

            @block.scalar
            def _(act):
                for t in range(tiles):
                    act.wait_ge(mean_ready, t + 1)
                    nc.scalar.activation(stat[:, t, 2:3], stat[:, t, 1:2], ACT.Sqrt).then_inc(root_ready, 1)
                for k in range(kc):
                    act.wait_ge(transposed, k + 1)
                    nc.scalar.copy(xT[0][:, k, 0:tiles * P], psum[:, k % 4, 0:tiles * P]).then_inc(high_ready, 1)

            @block.tensor
            def _(pe):
                pe.wait_ge(y_ready, tiles)
                for k in range(kc):
                    if k >= 4:
                        pe.wait_ge(evacuated, k - 3)
                    for t in range(tiles):
                        last = nc.tensor.transpose(psum[:, k % 4, t * P:(t + 1) * P], y[:, t, k * P:(k + 1) * P], ident[:, :])
                    last.then_inc(transposed, 1)


def load_transpose(nc, tag, psum, ident, src, xT, width, tiles=NT):
    kc = width // P
    with ExitStack() as ctx:
        x = ctx.enter_context(nc.sbuf_tensor(f"{tag}_x", [P, tiles, width], F32))
        x_in, transposed, high_ready, evacuated = ctx.enter_context(stage_sems(nc, *[f"{tag}_{s}" for s in ("in", "tr", "high", "ev")]))
        with nc.Block() as block:
            @block.sync
            def _(sp):
                sp.dma_start(x[:, :, :], tiled(src)).then_inc(x_in, 16)

            @block.tensor
            def _(pe):
                pe.wait_ge(x_in, 16)
                for k in range(kc):
                    if k >= 4:
                        pe.wait_ge(evacuated, k - 3)
                    for t in range(tiles):
                        last = nc.tensor.transpose(psum[:, k % 4, t * P:(t + 1) * P], x[:, t, k * P:(k + 1) * P], ident[:, :])
                    last.then_inc(transposed, 1)

            @block.vector
            def _(dve):
                low_halves(nc, dve, psum, xT, kc, tiles, high_ready, evacuated)

            @block.scalar
            def _(act):
                for k in range(kc):
                    act.wait_ge(transposed, k + 1)
                    nc.scalar.copy(xT[0][:, k, 0:tiles * P], psum[:, k % 4, 0:tiles * P]).then_inc(high_ready, 1)


def join_halves(nc, tag, halves, x):
    (joined,) = nc_sems = [nc.alloc_semaphore(f"{tag}_j")]
    with nc.Block() as block:
        @block.vector
        def _(dve):
            nc.vector.tensor_tensor(x[:, :, :], halves[0][:, :, :].bitcast(F32), halves[1][:, :, :].bitcast(F32), ALU.add).then_inc(joined, 1)
            dve.wait_ge(joined, 1)
    nc.clear_and_free_semaphores(nc_sems)
    nc.all_engine_barrier()


def conv_silu(nc, tag, psum, ident, xbcT, taps, convT, conv_tok):
    n = XBC // P
    PAD = CONV - 1
    with ExitStack() as ctx:
        sb = lambda m, s: ctx.enter_context(nc.sbuf_tensor(f"{tag}_{m}", s, F32))
        x, w, acc = sb("x", [P, 2, PAD + T]), sb("w", [P, 2, CONV + 1]), sb("acc", [P, 2, T])
        y, tok = sb("y", [P, 2, T]), sb("tok", [P, 2, NT, P])
        (in0, in1, acc_ready, y_ready, transposed, tok_ready, dve_order, out0, out1, padded) = ctx.enter_context(stage_sems(
            nc, *[f"{tag}_{s}" for s in ("in0", "in1", "acc", "y", "tr", "tok", "dve", "out0", "out1", "pad")]))
        loaded, stored = (in0, in1), (out0, out1)
        with nc.Block() as block:
            @block.sync
            def _(sp):
                sp.wait_ge(padded, 1)
                with sp.Fori(0, n // 2) as i:
                    for u in range(2):
                        sp.wait_ge(acc_ready, i * 2 + u + 1)
                        sp.dma_start(x[:, u, PAD:PAD + T], xbcT[ds((i * 2 + u) * P, P), :]).then_inc(loaded[u], 16)
                        sp.dma_start(w[:, u, :], taps[ds((i * 2 + u) * P, P), :]).then_inc(loaded[u], 16)

            @block.vector
            def _(dve):
                nc.vector.memset(x[:, :, 0:PAD], 0.0).then_inc(padded, 1)
                dve.sem_inc(acc_ready, 2)
                with dve.Fori(0, n // 2) as i:
                    dve.sem_clear(dve_order)
                    link = chain(dve, dve_order)
                    for u in range(2):
                        dve.wait_ge(loaded[u], i * 32 + 32)
                        dve.wait_ge(y_ready, i * 2 + u + 1)
                        link(nc.vector.tensor_scalar(acc[:, u, :], x[:, u, 0:T], w[:, u, 0:1], w[:, u, CONV:CONV + 1], ALU.mult, ALU.add))
                        for j in range(1, CONV):
                            ins = nc.vector.scalar_tensor_tensor(out=acc[:, u, :], in0=x[:, u, j:j + T], scalar=w[:, u, j:j + 1],
                                                                 in1=acc[:, u, :], op0=ALU.mult, op1=ALU.add)
                            if j < CONV - 1:
                                link(ins)
                        ins.then_inc(acc_ready, 1)
                    for u in range(2):
                        dve.wait_ge(transposed, i * 2 + u + 1)
                        nc.vector.tensor_copy(tok[:, u, :, :], psum[:, u, :].rearrange("p (t c) -> p t c", c=P)).then_inc(tok_ready, 1)

            @block.scalar
            def _(act):
                act.sem_inc(y_ready, 2)
                act.sem_inc(out0, 32)
                act.sem_inc(out1, 32)
                with act.Fori(0, n // 2) as i:
                    for u in range(2):
                        act.wait_ge(acc_ready, i * 2 + u + 3)
                        act.wait_ge(stored[u], i * 32 + 32)
                        nc.scalar.activation(y[:, u, :], acc[:, u, :], ACT.Silu).then_inc(y_ready, 1)
                        act.wait_ge(y_ready, i * 2 + u + 3)
                        act.dma_start(convT[ds((i * 2 + u) * P, P), :], y[:, u, :]).then_inc(stored[u], 16)
                    for u in range(2):
                        act.wait_ge(tok_ready, i * 2 + u + 1)
                        act.dma_start(tiled(conv_tok)[:, :, ds((i * 2 + u) * P, P)], tok[:, u, :, :]).then_inc(stored[u], 16)
                act.wait_ge(out0, n // 2 * 32 + 32)
                act.wait_ge(out1, n // 2 * 32 + 32)

            @block.tensor
            def _(pe):
                with pe.Fori(0, n // 2) as i:
                    for u in range(2):
                        pe.wait_ge(y_ready, i * 2 + u + 3)
                        pe.wait_ge(acc_ready, i * 2 + u + 3)
                        for t in range(NT):
                            last = nc.tensor.transpose(psum[:, u, t * P:(t + 1) * P], y[:, u, t * P:(t + 1) * P], ident[:, :])
                        last.then_inc(transposed, 1)


def ssd_dt(nc, tag, dt_raw, dt_bias, a_log, dt, da):
    with ExitStack() as ctx:
        sb = lambda m, s: ctx.enter_context(nc.sbuf_tensor(f"{tag}_{m}", s, F32))
        x, e, b, a = sb("x", [P, NT, HEADS]), sb("e", [P, NT, HEADS]), sb("b", [P, HEADS]), sb("a", [P, HEADS])
        xin, abs_ready, act_order, ln_ready, dve_order, out_ready, stored = ctx.enter_context(stage_sems(
            nc, *[f"{tag}_{s}" for s in ("in", "abs", "act", "ln", "dve", "rdy", "out")]))
        with nc.Block() as block:
            @block.sync
            def _(sp):
                sp.dma_start(x[:, :, :], tiled(dt_raw)).then_inc(xin, 16)
                sp.dma_start(b[:, :], row_bc(dt_bias)).then_inc(xin, 16)
                sp.dma_start(a[:, :], row_bc(a_log)).then_inc(xin, 16)
                sp.wait_ge(out_ready, 2)
                sp.dma_start(tiled(dt), x[:, :, :]).then_inc(stored, 16)
                sp.dma_start(tiled(da), e[:, :, :]).then_inc(stored, 16)
                sp.wait_ge(stored, 32)

            @block.vector
            def _(dve):
                link = chain(dve, dve_order)
                dve.wait_ge(xin, 48)
                link(nc.vector.tensor_tensor(x[:, :, :], x[:, :, :], bc_mid(b[:, :], NT), ALU.add))
                link(nc.vector.tensor_scalar(e[:, :, :], x[:, :, :], -1.0, None, ALU.mult))
                nc.vector.tensor_tensor(e[:, :, :], e[:, :, :], x[:, :, :], ALU.min).then_inc(abs_ready, 1)
                dve.wait_ge(ln_ready, 1)
                link(nc.vector.scalar_tensor_tensor(out=x[:, :, :], in0=x[:, :, :], scalar=0.0, in1=e[:, :, :], op0=ALU.max, op1=ALU.add))
                dve.wait_ge(ln_ready, 2)
                link(nc.vector.tensor_scalar(a[:, :], a[:, :], -1.0, None, ALU.mult))
                nc.vector.tensor_tensor(e[:, :, :], x[:, :, :], bc_mid(a[:, :], NT), ALU.mult).then_inc(out_ready, 2)

            @block.scalar
            def _(act):
                link = chain(act, act_order)
                act.wait_ge(abs_ready, 1)
                link(nc.scalar.activation(e[:, :, :], e[:, :, :], ACT.Exp))
                nc.scalar.activation(e[:, :, :], e[:, :, :], ACT.Ln, bias=1.0).then_inc(ln_ready, 1)
                act.wait_ge(xin, 48)
                nc.scalar.activation(a[:, :], a[:, :], ACT.Exp).then_inc(ln_ready, 1)


def ssd_scan(nc, tag, psum, tri, convT, conv_tok, dt, da, d_skip, y_out):
    GW = HPG * HD
    with ExitStack() as ctx:
        sb = lambda m, s: ctx.enter_context(nc.sbuf_tensor(f"{tag}_{m}", s, F32))
        bT, cT, b_tok = sb("bT", [P, P]), sb("cT", [P, P]), sb("b", [P, P])
        x, dtc, dac, dsk = sb("x", [P, GW]), sb("dt", [P, HPG]), sb("da", [P, HPG]), sb("dsk", [P, HEADS])
        dskg = sb("dskg", [P, HPG])
        da_bc, cbm, acum = sb("dabc", [P, HPG, P]), sb("cbm", [P, P]), sb("acum", [P, HPG])
        arg, lmat, mmat = sb("arg", [P, HPG, P]), sb("lmat", [P, HPG, P]), sb("mmat", [P, HPG, P])
        small, smalle = sb("small", [P, 3, HPG]), sb("smalle", [P, 3, HPG])
        xdt, xdec, state, y = sb("xdt", [P, GW]), sb("xdec", [P, GW]), sb("state", [P, GW]), sb("y", [P, GW])
        heads = lambda ap: ap.rearrange("p (h d) -> p h d", d=HD)
        rdy = lambda ap: ap.rearrange("p (h s) -> p h s", s=P)
        (loaded, bc_ready, pe_a, arg_ready, exp_ready, ops_ready, pe_b, y_ready, stored, dve_order) = ctx.enter_context(stage_sems(
            nc, *[f"{tag}_{s}" for s in ("in", "bc", "pea", "arg", "exp", "ops", "peb", "y", "out", "dve")]))
        with nc.Block() as block:
            @block.sync
            def _(sp):
                with sp.Fori(0, GROUPS) as g:
                    with sp.Fori(0, NT) as c:
                        n = g * NT + c
                        sp.wait_ge(y_ready, n + 1)
                        sp.dma_start(bT[:, :], convT[ds(g * P + D, P), ds(c * P, P)]).then_inc(loaded, 16)
                        sp.dma_start(cT[:, :], convT[ds(g * P + (D + GROUPS * STATE), P), ds(c * P, P)]).then_inc(loaded, 16)
                        sp.dma_start(b_tok[:, :], conv_tok[ds(c * P, P), ds(g * P + D, P)]).then_inc(loaded, 16)
                        sp.dma_start(x[:, :], conv_tok[ds(c * P, P), ds(g * GW, GW)]).then_inc(loaded, 16)
                        sp.dma_start(dtc[:, :], dt[ds(c * P, P), ds(g * HPG, HPG)]).then_inc(loaded, 16)
                        sp.dma_start(dac[:, :], da[ds(c * P, P), ds(g * HPG, HPG)]).then_inc(loaded, 16)
                        sp.dma_start(dskg[:, :], row_bc(d_skip[ds(g * HPG, HPG)])).then_inc(loaded, 16)
                        sp.wait_ge(y_ready, n + 2)
                        sp.dma_start(y_out[ds(c * P, P), ds(g * GW, GW)], y[:, :]).then_inc(stored, 16)
                sp.wait_ge(stored, 16 * GROUPS * NT + 16)

            @block.vector
            def _(dve):
                dve.sem_inc(y_ready, 1)
                dve.sem_inc(stored, 16)
                with dve.Fori(0, GROUPS) as g:
                    nc.vector.memset(state[:, :], 0.0)
                    with dve.Fori(0, NT) as c:
                        n = g * NT + c
                        dve.sem_clear(dve_order)
                        link = chain(dve, dve_order)
                        dve.wait_ge(loaded, n * 112 + 112)
                        nc.vector.tensor_copy(da_bc[:, :, :], bc_last(dac[:, :], P)).then_inc(bc_ready, 1)
                        link(nc.vector.tensor_tensor(heads(xdt[:, :]), heads(x[:, :]), bc_last(dtc[:, :], HD), ALU.mult))
                        dve.wait_ge(pe_a, n + 1)
                        nc.vector.tensor_tensor(cbm[:, :], psum[:, 1, 0:P], tri[:, :], ALU.mult)
                        link(nc.vector.tensor_copy(small[:, 0, :], psum[:, 1, P:P + HPG]))
                        link(nc.vector.tensor_copy(small[:, 1, :], rdy(psum[:, 0, :])[:, :, P - 1]))
                        link(nc.vector.tensor_tensor(small[:, 2, :], small[:, 1, :], small[:, 0, :], ALU.subtract))
                        for r in range(HPG):
                            ins = nc.vector.tensor_scalar(arg[:, r, :], psum[:, 0, r * P:(r + 1) * P], small[:, 0, r:r + 1], 0.0,
                                                          ALU.subtract, ALU.min)
                        ins.then_inc(arg_ready, 1)
                        dve.wait_ge(exp_ready, n + 1)
                        nc.vector.tensor_tensor(mmat[:, :, :], lmat[:, :, :], bc_mid(cbm[:, :], HPG), ALU.mult)
                        nc.vector.tensor_tensor(heads(xdec[:, :]), heads(xdt[:, :]), bc_last(smalle[:, 2, :], HD), ALU.mult).then_inc(ops_ready, 1)
                        dve.wait_ge(pe_b, n + 1)
                        dve.wait_ge(stored, n * 16 + 16)
                        link(nc.vector.tensor_tensor(heads(y[:, :]), heads(psum[:, 2, 0:GW]), bc_last(smalle[:, 0, :], HD), ALU.mult))
                        link(nc.vector.tensor_tensor(y[:, :], y[:, :], psum[:, 3, 0:GW], ALU.add))
                        link(nc.vector.tensor_tensor(heads(x[:, :]), heads(x[:, :]), bc_last(dskg[:, :], HD), ALU.mult))
                        link(nc.vector.tensor_tensor(heads(state[:, :]), heads(state[:, :]), bc_last(smalle[:, 1, :], HD), ALU.mult))
                        link(nc.vector.tensor_tensor(state[:, :], state[:, :], psum[:, 4, 0:GW], ALU.add))
                        link(nc.vector.tensor_tensor(y[:, :], y[:, :], x[:, :], ALU.add))
                        dve.sem_inc(y_ready, 1)

            @block.scalar
            def _(act):
                with act.Fori(0, GROUPS * NT) as n:
                    act.wait_ge(arg_ready, n + 1)
                    nc.scalar.activation(smalle[:, :, :], small[:, :, :], ACT.Exp)
                    nc.scalar.activation(lmat[:, :, :], arg[:, :, :], ACT.Exp).then_inc(exp_ready, 1)

            @block.tensor
            def _(pe):
                with pe.Fori(0, GROUPS * NT) as n:
                    pe.wait_ge(bc_ready, n + 1)
                    nc.tensor.matmul(psum[:, 1, 0:P], bT[:, :], cT[:, :], start=True, stop=True)
                    nc.tensor.matmul(psum[:, 1, P:P + HPG], tri[:, :], dac[:, :], start=True, stop=True)
                    for r in range(HPG):
                        last = nc.tensor.matmul(psum[:, 0, r * P:(r + 1) * P], da_bc[:, r, :], tri[:, :], start=True, stop=True)
                    last.then_inc(pe_a, 1)
                    pe.wait_ge(ops_ready, n + 1)
                    nc.tensor.matmul(psum[:, 2, 0:GW], cT[:, :], state[:, :], start=True, stop=True)
                    nc.tensor.matmul(psum[:, 4, 0:GW], b_tok[:, :], xdec[:, :], start=True, stop=True)
                    for r in range(HPG):
                        last = nc.tensor.matmul(psum[:, 3, r * HD:(r + 1) * HD], mmat[:, r, :], xdt[:, r * HD:(r + 1) * HD], start=True, stop=True)
                    last.then_inc(pe_b, 1)


def ssd_gate_norm(nc, tag, y, z, norm_w, out):
    GW = D // GROUPS
    with ExitStack() as ctx:
        sb = lambda m, s: ctx.enter_context(nc.sbuf_tensor(f"{tag}_{m}", s, F32))
        ys, zs, w = sb("y", [P, NT, D]), sb("z", [P, NT, D]), sb("w", [P, D])
        sq, st, rt, tp = sb("sq", [P, D]), sb("st", [P, NT, GROUPS]), sb("rt", [P, NT, GROUPS]), sb("tp", [P, NT, GROUPS])
        xin, silu_ready, mean_ready, root_ready, dve_order, y_ready, stored = ctx.enter_context(stage_sems(
            nc, *[f"{tag}_{s}" for s in ("in", "silu", "mean", "root", "dve", "y", "out")]))
        grp = lambda ap: ap.rearrange("p (g d) -> p g d", g=GROUPS)
        with nc.Block() as block:
            @block.sync
            def _(sp):
                sp.dma_start(zs[:, :, :], tiled(z)).then_inc(xin, 16)
                sp.dma_start(ys[:, :, :], tiled(y)).then_inc(xin, 16)
                sp.dma_start(w[:, :], row_bc(norm_w)).then_inc(xin, 16)
                sp.wait_ge(y_ready, NT)
                sp.dma_start(tiled(out), ys[:, :, :]).then_inc(stored, 16)
                sp.wait_ge(stored, 16)

            @block.scalar
            def _(act):
                act.wait_ge(xin, 48)
                for t in range(NT):
                    nc.scalar.activation(zs[:, t, :], zs[:, t, :], ACT.Silu).then_inc(silu_ready, 1)
                act.wait_ge(mean_ready, 1)
                nc.scalar.activation(rt[:, :, :], st[:, :, :], ACT.Sqrt).then_inc(root_ready, 1)

            @block.vector
            def _(dve):
                link = chain(dve, dve_order)
                for t in range(NT):
                    dve.wait_ge(silu_ready, t + 1)
                    link(nc.vector.tensor_tensor(ys[:, t, :], ys[:, t, :], zs[:, t, :], ALU.mult))
                    link(nc.vector.tensor_tensor(sq[:, :], ys[:, t, :], ys[:, t, :], ALU.mult))
                    link(nc.vector.tensor_reduce(st[:, t, :], grp(sq[:, :]), AX, ALU.add))
                nc.vector.tensor_scalar(st[:, :, :], st[:, :, :], 1.0 / GW, EPS, ALU.mult, ALU.add).then_inc(mean_ready, 1)
                dve.wait_ge(root_ready, 1)
                refined_root(nc, link, rt[:, :, :], st[:, :, :], tp[:, :, :])
                for t in range(NT):
                    link(nc.vector.tensor_tensor(grp(ys[:, t, :]), grp(ys[:, t, :]), bc_last(rt[:, t, :], GW), ALU.mult))
                    nc.vector.tensor_tensor(ys[:, t, :], ys[:, t, :], w[:, :], ALU.mult).then_inc(y_ready, 1)


def rope_tables(nc, tag, positions, inv, half, cos_sb, sin_sb):
    two_pi = 2.0 * math.pi
    c1 = 6.28125
    c2 = float(np.float32(two_pi - c1) * 1.0)
    c2 = math.floor(c2 * 2 ** 20) / 2 ** 20
    c3 = two_pi - c1 - c2
    with ExitStack() as ctx:
        sb = lambda m, s, d=F32: ctx.enter_context(nc.sbuf_tensor(f"{tag}_{m}", s, d))
        pos_i, pos, inv_sb = sb("pi", [P, NT], I32), sb("p", [P, NT]), sb("inv", [P, half])
        ang, k, ki, hs = sb("ang", [P, NT, half]), sb("k", [P, NT, half]), sb("ki", [P, NT, half], I32), sb("hs", [P, NT, half])
        xin, ang_ready, sin_ready, dve_order = ctx.enter_context(stage_sems(nc, *[f"{tag}_{s}" for s in ("in", "ang", "sin", "dve")]))
        with nc.Block() as block:
            @block.sync
            def _(sp):
                with nc.allow_non_contiguous_dma("the positions, one to a partition"):
                    sp.dma_start(pos_i[:, :], positions.rearrange("(t p) -> p t", p=P)).then_inc(xin, 16)
                sp.dma_start(inv_sb[:, :], row_bc(inv)).then_inc(xin, 16)

            @block.vector
            def _(dve):
                link = chain(dve, dve_order)
                dve.wait_ge(xin, 32)
                link(nc.vector.tensor_copy(pos[:, :], pos_i[:, :]))
                link(nc.vector.tensor_tensor(ang[:, :, :], bc_last(pos[:, :], half), bc_mid(inv_sb[:, :], NT), ALU.mult))
                link(nc.vector.tensor_scalar(k[:, :, :], ang[:, :, :], 1.0 / two_pi, None, ALU.mult))
                link(nc.vector.tensor_copy(ki[:, :, :], k[:, :, :]))
                link(nc.vector.tensor_copy(k[:, :, :], ki[:, :, :]))
                for c in (c1, c2, c3):
                    link(nc.vector.scalar_tensor_tensor(out=ang[:, :, :], in0=k[:, :, :], scalar=-c, in1=ang[:, :, :], op0=ALU.mult, op1=ALU.add))
                link(nc.vector.tensor_scalar(k[:, :, :], ang[:, :, :], math.pi, -two_pi, ALU.is_gt, ALU.mult))
                link(nc.vector.tensor_tensor(k[:, :, :], k[:, :, :], ang[:, :, :], ALU.add))
                link(nc.vector.tensor_scalar(ang[:, :, :], k[:, :, :], -math.pi, two_pi, ALU.is_lt, ALU.mult))
                link(nc.vector.tensor_tensor(ang[:, :, :], k[:, :, :], ang[:, :, :], ALU.add))
                lim = 3.1415925
                nc.vector.tensor_scalar(ang[:, :, :], ang[:, :, :], lim, -lim, ALU.min, ALU.max).then_inc(ang_ready, 1)
                dve.wait_ge(sin_ready, 1)
                link(nc.vector.tensor_tensor(hs[:, :, :], hs[:, :, :], hs[:, :, :], ALU.mult))
                link(nc.vector.tensor_scalar(cos_sb[:, :, :], hs[:, :, :], -2.0, 1.0, ALU.mult, ALU.add))

            @block.scalar
            def _(act):
                act.wait_ge(ang_ready, 1)
                nc.scalar.activation(sin_sb[:, :, :], ang[:, :, :], ACT.Sin)
                nc.scalar.activation(hs[:, :, :], ang[:, :, :], ACT.Sin, scale=0.5).then_inc(sin_ready, 1)


def head_prep(nc, tag, src, dst, heads, hd, gain=None, cos=None, sin=None, rot=0, rot_at=0):
    half = rot // 2
    with ExitStack() as ctx:
        sb = lambda m, s: ctx.enter_context(nc.sbuf_tensor(f"{tag}_{m}", s, F32))
        x, sq = sb("x", [P, NT, heads, hd]), sb("sq", [P, heads, hd])
        st, g = sb("st", [P, NT, heads]), sb("g", [P, hd])
        rt, tp = sb("rt", [P, NT, heads]), sb("tp", [P, NT, heads])
        if rot:
            ta, tb, tc = sb("ta", [P, heads, half]), sb("tb", [P, heads, half]), sb("tc", [P, heads, half])
        rows = src.shape[0] // P
        xin, mean_ready, root_ready, dve_order, y_ready, stored = ctx.enter_context(stage_sems(
            nc, *[f"{tag}_{s}" for s in ("in", "mean", "root", "dve", "y", "out")]))
        if len(src.shape) == 2:
            src = src.rearrange("t (h d) -> t h d", h=heads)
        with nc.Block() as block:
            @block.sync
            def _(sp):
                for t in range(rows):
                    sp.dma_start(x[:, t, :, :], src[t * P:(t + 1) * P, :, :]).then_inc(xin, 16)
                if gain is not None:
                    sp.dma_start(g[:, :], row_bc(gain)).then_inc(xin, 16)
                sp.wait_ge(y_ready, 1)
                for t in range(rows):
                    sp.dma_start(dst[t * P:(t + 1) * P, :, :], x[:, t, :, :]).then_inc(stored, 16)
                sp.wait_ge(stored, 16 * rows)

            @block.vector
            def _(dve):
                link = chain(dve, dve_order)
                dve.wait_ge(xin, 16 * rows + (16 if gain is not None else 0))
                if gain is not None:
                    for t in range(rows):
                        link(nc.vector.tensor_tensor(sq[:, :, :], x[:, t, :, :], x[:, t, :, :], ALU.mult))
                        link(nc.vector.tensor_reduce(st[:, t, :], sq[:, :, :], AX, ALU.add))
                    nc.vector.tensor_scalar(st[:, 0:rows, :], st[:, 0:rows, :], 1.0 / hd, EPS, ALU.mult, ALU.add).then_inc(mean_ready, 1)
                    dve.wait_ge(root_ready, 1)
                    refined_root(nc, link, rt[:, 0:rows, :], st[:, 0:rows, :], tp[:, 0:rows, :])
                    for t in range(rows):
                        link(nc.vector.tensor_tensor(x[:, t, :, :], x[:, t, :, :], bc_last(rt[:, t, :], hd), ALU.mult))
                        link(nc.vector.tensor_tensor(x[:, t, :, :], x[:, t, :, :], bc_mid(g[:, :], heads), ALU.mult))
                for t in range(rows if rot else 0):
                    x1 = x[:, t, :, rot_at:rot_at + half]
                    x2 = x[:, t, :, rot_at + half:rot_at + rot]
                    cs, sn = bc_mid(cos[:, t, :], heads), bc_mid(sin[:, t, :], heads)
                    link(nc.vector.tensor_tensor(ta[:, :, :], x1, sn, ALU.mult))
                    link(nc.vector.tensor_tensor(tb[:, :, :], x2, sn, ALU.mult))
                    link(nc.vector.tensor_tensor(tc[:, :, :], x2, cs, ALU.mult))
                    link(nc.vector.tensor_tensor(x1, x1, cs, ALU.mult))
                    link(nc.vector.tensor_tensor(x1, x1, tb[:, :, :], ALU.subtract))
                    link(nc.vector.tensor_tensor(x2, tc[:, :, :], ta[:, :, :], ALU.add))
                dve.sem_inc(y_ready, 1)

            @block.scalar
            def _(act):
                if gain is not None:
                    act.wait_ge(mean_ready, 1)
                    nc.scalar.activation(rt[:, 0:rows, :], st[:, 0:rows, :], ACT.Sqrt).then_inc(root_ready, 1)


def attention(nc, tag, psum, ident, q, k, v, o, splits, dv, scale, key_tiles, mask=None, span=None, lse=None):
    H = 4
    d = sum(splits)
    nch = len(splits)
    offs = [sum(splits[:i]) for i in range(nch)]
    span = span or (lambda qt: (0, key_tiles))
    with ExitStack() as ctx:
        sb = lambda m, s: ctx.enter_context(nc.sbuf_tensor(f"{tag}_{m}", s, F32))
        qs, ks, vs = sb("q", [P, 2, NT, d]), sb("k", [P, 2, key_tiles, d]), sb("v", [P, 2, key_tiles, dv])
        qT, kT = sb("qT", [P, nch, T]), sb("kT", [P, nch, key_tiles * P])
        ms = sb("mask", [P, NT, T]) if mask is not None else None
        s_sb, p_sb, pT = sb("s", [P, 2, key_tiles * P]), sb("p", [P, 2, key_tiles * P]), sb("pT", [P, 2, key_tiles, P])
        os_, st = sb("o", [P, 2, NT, dv]), sb("st", [P, 2, NT, 4])
        (in0, in1, mask_in, qk_tr, q_ev, k_ev, s_done, s_copied, nm_ready, e_done, pt_done, pt_ev, o_done, o_ev, out0, out1,
         dve_order, ln_done) = ctx.enter_context(stage_sems(nc, *[f"{tag}_{s}" for s in (
             "in0", "in1", "mask", "qktr", "qev", "kev", "sdone", "scp", "nm", "edone", "ptdone", "ptev", "odone", "oev",
             "out0", "out1", "dve", "ln")]))
        loaded, stored = (in0, in1), (out0, out1)
        n_out = 16 * NT
        tt = NT * 16
        kt16 = key_tiles * 16
        per_load = tt + 2 * kt16
        per_store = n_out * (2 if lse is not None else 1)
        with nc.Block() as block:
            @block.sync
            def _(sp):
                if mask is not None:
                    sp.dma_start(ms[:, :, :], tiled(mask)).then_inc(mask_in, 16)

                def load(h):
                    u = h % 2
                    for t in range(NT):
                        sp.dma_start(qs[:, u, t, :], q[t * P:(t + 1) * P, h, :]).then_inc(loaded[u], 16)
                    for t in range(key_tiles):
                        sp.dma_start(ks[:, u, t, :], k[t * P:(t + 1) * P, h, :]).then_inc(loaded[u], 16)
                        sp.dma_start(vs[:, u, t, :], v[t * P:(t + 1) * P, h, :]).then_inc(loaded[u], 16)

                load(0)
                load(1)
                for h in range(H):
                    u = h % 2
                    sp.wait_ge(o_ev, (h + 3) * NT)
                    for t in range(NT):
                        sp.dma_start(o[t * P:(t + 1) * P, h, :], os_[:, u, t, :]).then_inc(stored[u], 16)
                        if lse is not None:
                            sp.dma_start(lse[t * P:(t + 1) * P, h:h + 1], st[:, u, t, 3:4], allow_slow_non_contiguous=True).then_inc(stored[u], 16)
                    if h + 2 < H:
                        load(h + 2)
                sp.wait_ge(out0, n_out + per_store * (H // 2))
                sp.wait_ge(out1, n_out + per_store * (H // 2))

            @block.tensor
            def _(pe):
                with pe.Fori(0, H // 2) as i:
                    for u in range(2):
                        h = i * 2 + u
                        pe.wait_ge(loaded[u], i * per_load + per_load)
                        for c, (w, at) in enumerate(zip(splits, offs)):
                            pe.wait_ge(q_ev, h * nch + (c + 1))
                            take_bank(nc, psum[:, 0, 0:P], ident)
                            for t in range(NT):
                                last = nc.tensor.transpose(psum[0:w, 0, t * P:(t + 1) * P], qs[:, u, t, at:at + w], ident[:, :])
                            last.then_inc(qk_tr, 1)
                            pe.wait_ge(k_ev, h * nch + (c + 1))
                            take_bank(nc, psum[:, 1, 0:P], ident)
                            for t in range(key_tiles):
                                last = nc.tensor.transpose(psum[0:w, 1, t * P:(t + 1) * P], ks[:, u, t, at:at + w], ident[:, :])
                            last.then_inc(qk_tr, 1)
                        pe.wait_ge(q_ev, h * nch + (nch + 1))
                        pe.wait_ge(k_ev, h * nch + (nch + 1))
                        for step in range(NT + 2):
                            if step < NT:
                                a, b = span(step)
                                pe.wait_ge(s_copied, h * NT + (step + 1))
                                for c, w in enumerate(splits):
                                    last = nc.tensor.matmul(psum[:, 2 + step % 2, a * P:b * P], qT[0:w, c, step * P:(step + 1) * P],
                                                            kT[0:w, c, a * P:b * P], start=c == 0, stop=c == nch - 1)
                                last.then_inc(s_done, 1)
                            if 1 <= step <= NT:
                                qt = step - 1
                                a, b = span(qt)
                                pe.wait_ge(e_done, h * NT + (qt + 3))
                                pe.wait_ge(pt_ev, h * NT + (qt + 1))
                                for t in range(a, b):
                                    last = nc.tensor.transpose(psum[:, 4 + qt % 2, t * P:(t + 1) * P], p_sb[:, qt % 2, t * P:(t + 1) * P], ident[:, :])
                                last.then_inc(pt_done, 1)
                            if step >= 2:
                                qt = step - 2
                                a, b = span(qt)
                                pe.wait_ge(pt_ev, h * NT + (qt + 3))
                                pe.wait_ge(o_ev, h * NT + (qt + 1 + 2 * NT - 2))
                                for t in range(a, b):
                                    last = nc.tensor.matmul(psum[:, 6 + qt % 2, 0:dv], pT[:, qt % 2, t, :], vs[:, u, t, :],
                                                            start=t == a, stop=t == b - 1)
                                last.then_inc(o_done, 1)

            @block.vector
            def _(dve):
                dve.sem_inc(k_ev, 1)
                dve.sem_inc(s_copied, 2)
                dve.sem_inc(o_ev, 2 * NT)
                dve.sem_inc(out0, n_out)
                dve.sem_inc(out1, n_out)
                if mask is not None:
                    dve.wait_ge(mask_in, 16)
                with dve.Fori(0, H // 2) as i:
                    for u in range(2):
                        dve.sem_clear(dve_order)
                        link = chain(dve, dve_order)
                        h = i * 2 + u
                        for c, w in enumerate(splits):
                            dve.wait_ge(qk_tr, h * 2 * nch + 2 * (c + 1))
                            nc.vector.tensor_copy(kT[0:w, c, :], psum[0:w, 1, 0:key_tiles * P]).then_inc(k_ev, 1)
                        dve.wait_ge(stored[u], i * per_store + n_out)
                        for step in range(NT + 2):
                            if step < NT:
                                a, b = span(step)
                                sl = slice(a * P, b * P)
                                dve.wait_ge(s_done, h * NT + (step + 1))
                                dve.wait_ge(e_done, h * NT + (step + 1))
                                if mask is not None:
                                    ins = nc.vector.tensor_tensor(s_sb[:, step % 2, sl], psum[:, 2 + step % 2, sl], ms[:, step, sl], ALU.add)
                                else:
                                    ins = nc.vector.tensor_copy(s_sb[:, step % 2, sl], psum[:, 2 + step % 2, sl])
                                ins.then_inc(s_copied, 1)
                                dve.wait_ge(s_copied, h * NT + (step + 3))
                                link(nc.vector.tensor_reduce(st[:, u, step, 0:1], s_sb[:, step % 2, sl], AX, ALU.max))
                                nc.vector.tensor_scalar(st[:, u, step, 1:2], st[:, u, step, 0:1], -scale, None, ALU.mult).then_inc(nm_ready, 1)
                            if step >= 2:
                                qt = step - 2
                                dve.wait_ge(o_done, h * NT + (qt + 3))
                                if lse is not None:
                                    dve.wait_ge(ln_done, h * NT + (qt + 1))
                                    link(nc.vector.scalar_tensor_tensor(out=st[:, u, qt, 3:4], in0=st[:, u, qt, 0:1], scalar=scale,
                                                                        in1=st[:, u, qt, 3:4], op0=ALU.mult, op1=ALU.add))
                                link(nc.vector.reciprocal(st[:, u, qt, 2:3], st[:, u, qt, 2:3]))
                                nc.vector.tensor_scalar(os_[:, u, qt, :], psum[:, 6 + qt % 2, 0:dv], st[:, u, qt, 2:3], None,
                                                        ALU.mult).then_inc(o_ev, 1)

            @block.scalar
            def _(act):
                act.sem_inc(q_ev, 1)
                act.sem_inc(e_done, 2)
                act.sem_inc(pt_ev, 2)
                act.sem_inc(o_done, 2)
                with act.Fori(0, H // 2) as i:
                    for u in range(2):
                        h = i * 2 + u
                        for c, w in enumerate(splits):
                            act.wait_ge(qk_tr, h * 2 * nch + (2 * c + 1))
                            nc.scalar.copy(qT[0:w, c, :], psum[0:w, 0, 0:T]).then_inc(q_ev, 1)
                        for step in range(NT + 1):
                            if step < NT:
                                a, b = span(step)
                                sl = slice(a * P, b * P)
                                act.wait_ge(nm_ready, h * NT + (step + 1))
                                if step >= 2:
                                    act.wait_ge(pt_done, h * NT + (step - 1))
                                nc.scalar.activation(p_sb[:, step % 2, sl], s_sb[:, step % 2, sl], ACT.Exp, bias=st[:, u, step, 1:2],
                                                     scale=scale, accum_out=st[:, u, step, 2:3]).then_inc(e_done, 1)
                                if lse is not None:
                                    act.wait_ge(e_done, h * NT + (step + 3))
                                    nc.scalar.activation(st[:, u, step, 3:4], st[:, u, step, 2:3], ACT.Ln).then_inc(ln_done, 1)
                            if step >= 1:
                                qt = step - 1
                                a, b = span(qt)
                                act.wait_ge(pt_done, h * NT + (qt + 1))
                                act.wait_ge(o_done, h * NT + (qt + 1))
                                nc.scalar.copy(pT[:, qt % 2, a:b, :], psum[:, 4 + qt % 2, a * P:b * P].rearrange("p (t q) -> p t q", q=P)).then_inc(pt_ev, 1)


def dil_combine(nc, tag, o, lse, out):
    HW = 4 * HD
    with ExitStack() as ctx:
        sb = lambda m, s: ctx.enter_context(nc.sbuf_tensor(f"{tag}_{m}", s, F32))
        os_, ls = sb("o", [P, NT, DIL * HW]), sb("l", [P, NT, DIL, 4])
        mx, y, tmp = sb("mx", [P, NT, 4]), sb("y", [P, NT, HW]), sb("tmp", [P, NT, HW])
        xin, diff_ready, exp_ready, dve_order, y_ready, stored = ctx.enter_context(stage_sems(
            nc, *[f"{tag}_{s}" for s in ("in", "diff", "exp", "dve", "y", "out")]))
        with nc.Block() as block:
            @block.sync
            def _(sp):
                sp.dma_start(ls[:, :, :, :].rearrange("p t g h -> p t (g h)"), tiled(lse)).then_inc(xin, 16)
                sp.dma_start(os_[:, :, :], tiled(o)).then_inc(xin, 16)
                sp.wait_ge(y_ready, 1)
                sp.dma_start(tiled(out), y[:, :, :]).then_inc(stored, 16)
                sp.wait_ge(stored, 16)

            @block.vector
            def _(dve):
                link = chain(dve, dve_order)
                dve.wait_ge(xin, 32)
                link(nc.vector.tensor_tensor(mx[:, :, :], ls[:, :, 0, :], ls[:, :, 1, :], ALU.max))
                link(nc.vector.tensor_tensor(mx[:, :, :], mx[:, :, :], ls[:, :, 2, :], ALU.max))
                for g in range(DIL):
                    ins = nc.vector.tensor_tensor(ls[:, :, g, :], ls[:, :, g, :], mx[:, :, :], ALU.subtract)
                ins.then_inc(diff_ready, 1)
                dve.wait_ge(exp_ready, 1)
                link(nc.vector.tensor_tensor(mx[:, :, :], ls[:, :, 0, :], ls[:, :, 1, :], ALU.add))
                link(nc.vector.tensor_tensor(mx[:, :, :], mx[:, :, :], ls[:, :, 2, :], ALU.add))
                link(nc.vector.reciprocal(mx[:, :, :], mx[:, :, :]))
                for g in range(DIL):
                    link(nc.vector.tensor_tensor(ls[:, :, g, :], ls[:, :, g, :], mx[:, :, :], ALU.mult))
                for t in range(NT):
                    hv = lambda ap: ap.rearrange("p (h d) -> p h d", d=HD)
                    for g in range(DIL):
                        to = y if g == 0 else tmp
                        link(nc.vector.tensor_tensor(hv(to[:, t, :]), hv(os_[:, t, g * HW:(g + 1) * HW]), bc_last(ls[:, t, g, :], HD), ALU.mult))
                        if g:
                            link(nc.vector.tensor_tensor(y[:, t, :], y[:, t, :], tmp[:, t, :], ALU.add))
                dve.sem_inc(y_ready, 1)

            @block.scalar
            def _(act):
                act.wait_ge(diff_ready, 1)
                nc.scalar.activation(ls[:, :, :, :], ls[:, :, :, :], ACT.Exp).then_inc(exp_ready, 1)


def gated_merge(nc, tag, gates, branches, out, bias=None):
    with ExitStack() as ctx:
        sb = lambda m, s: ctx.enter_context(nc.sbuf_tensor(f"{tag}_{m}", s, F32))
        g, b, acc = sb("g", [P, 2, NT, D]), sb("b", [P, 2, NT, D]), sb("acc", [P, NT, D])
        bi = sb("bi", [P, 3, D]) if bias is not None else None
        in_g, in_b, in_bias, biased, sig_ready, used, dve_order, stored = ctx.enter_context(stage_sems(
            nc, *[f"{tag}_{s}" for s in ("ing", "inb", "inbias", "biased", "sig", "used", "dve", "out")]))
        with nc.Block() as block:
            @block.sync
            def _(sp):
                if bias is not None:
                    sp.dma_start(bi[:, :, :].rearrange("p b d -> p (b d)"), row_bc(bias)).then_inc(in_bias, 16)
                for n in range(3):
                    if n >= 2:
                        sp.wait_ge(used, n - 1)
                    if n >= 1:
                        sp.wait_ge(in_g, 16 * n)
                        sp.wait_ge(in_b, 16 * n)
                    sp.dma_start(g[:, n % 2, :, :], tiled(gates)[:, :, n * D:(n + 1) * D]).then_inc(in_g, 16)
                    sp.dma_start(b[:, n % 2, :, :], tiled(branches[n])).then_inc(in_b, 16)
                sp.wait_ge(used, 3)
                sp.dma_start(tiled(out), acc[:, :, :]).then_inc(stored, 16)
                sp.wait_ge(stored, 16)

            @block.scalar
            def _(act):
                for n in range(3):
                    if bias is not None:
                        act.wait_ge(biased, n + 1)
                    else:
                        act.wait_ge(in_g, 16 * n + 16)
                    nc.scalar.activation(g[:, n % 2, :, :], g[:, n % 2, :, :], ACT.Sigmoid).then_inc(sig_ready, 1)

            @block.vector
            def _(dve):
                link = chain(dve, dve_order)

                def add_bias(n):
                    dve.wait_ge(in_bias, 16)
                    dve.wait_ge(in_g, 16 * n + 16)
                    for t in range(NT):
                        ins = nc.vector.tensor_tensor(g[:, n % 2, t, :], g[:, n % 2, t, :], bi[:, n, :], ALU.add)
                    ins.then_inc(biased, 1)

                for n in range(3):
                    if bias is not None:
                        add_bias(n)
                    dve.wait_ge(sig_ready, n + 1)
                    dve.wait_ge(in_b, 16 * n + 16)
                    if n == 0:
                        link(nc.vector.tensor_tensor(acc[:, :, :], g[:, 0, :, :], b[:, 0, :, :], ALU.mult))
                    else:
                        link(nc.vector.tensor_tensor(g[:, n % 2, :, :], g[:, n % 2, :, :], b[:, n % 2, :, :], ALU.mult))
                        link(nc.vector.tensor_tensor(acc[:, :, :], acc[:, :, :], g[:, n % 2, :, :], ALU.add))
                    dve.sem_inc(used, 1)


def add_residual(nc, tag, h, y, gate=None):
    with ExitStack() as ctx:
        ys = ctx.enter_context(nc.sbuf_tensor(f"{tag}_y", [P, NT, D], F32))
        gs = ctx.enter_context(nc.sbuf_tensor(f"{tag}_g", [P, D], F32))
        xin, dve_order = ctx.enter_context(stage_sems(nc, f"{tag}_in", f"{tag}_dve"))
        with nc.Block() as block:
            @block.sync
            def _(sp):
                sp.dma_start(ys[:, :, :], tiled(y)).then_inc(xin, 16)
                if gate is not None:
                    sp.dma_start(gs[:, :], row_bc(gate)).then_inc(xin, 16)

            @block.vector
            def _(dve):
                link = chain(dve, dve_order)
                dve.wait_ge(xin, 16 if gate is None else 32)
                for t in range(NT):
                    if gate is not None:
                        link(nc.vector.tensor_tensor(ys[:, t, :], ys[:, t, :], gs[:, :], ALU.mult))
                    link(nc.vector.tensor_tensor(h[:, t, :], h[:, t, :], ys[:, t, :], ALU.add))


def peer_route(nc, tag, psum, qT, keysT, iota16, sel, cond, ada_w, mods):
    GROUP = PEER_H // LAYERS
    PIECES = 6 * D // CH // GROUP
    with ExitStack() as ctx:
        sb = lambda m, s, d=F32: ctx.enter_context(nc.sbuf_tensor(f"{tag}_{m}", s, d))
        qs, ks = sb("q", [P, 2, T]), sb("k", [P, 2, NK])
        sc, sc2 = sb("sc", [P, 2, NT, NK]), sb("sc2", [P, NT, NK])
        val, idx, idxf = sb("val", [P, 2, NT, TOPK]), sb("idx", [P, 2, NT, TOPK], U32), sb("idxf", [P, 2, NT, TOPK])
        cand, cand2 = sb("cand", [P, NT, 256]), sb("cand2", [P, NT, 256])
        top, pos, posx, posf = sb("top", [P, NT, TOPK]), sb("pos", [P, NT, TOPK], U32), sb("posx", [P, 2, NT, TOPK], U32), sb("posf", [P, 2, NT, TOPK])
        eq, res = sb("eq", [P, NT, TOPK, TOPK]), sb("res", [P, NT, 3, TOPK])
        sums = sb("sums", [P, NT])
        cT, w_ada, rows = sb("cT", [P, KD]), sb("wada", [P, PIECES, KD, CH]), sb("rows", [1, PIECES, CH])
        (loaded, s_done, s_copied, diff_ready, exp_ready, dve_order, res_ready, stored, c_in, c_ready, ada_done, rows_ready, rows_out, *ada_in) = \
            ctx.enter_context(stage_sems(nc, *[f"{tag}_{s}" for s in (
                "in", "sdone", "scp", "diff", "exp", "dve", "res", "out", "cin", "crdy", "adad", "rows", "rowso", *(f"ada{j}" for j in range(PIECES)))]))
        with nc.Block() as block:
            @block.sync
            def _(sp):
                with nc.allow_non_contiguous_dma("a row of 1024 laid over the partitions"):
                    sp.dma_start(cT[:, :], cond.rearrange("(k p) -> p k", p=P)).then_inc(c_in, 16)
                with sp.Fori(0, LAYERS) as l:
                    with sp.Fori(0, GROUP) as g:
                        h = l * GROUP + g
                        sp.wait_ge(s_done, h * 2 + 2)
                        for c in range(2):
                            sp.dma_start(qs[:, c, :], qT[ds(h * 256 + c * P, P), :]).then_inc(loaded, 16)
                            sp.dma_start(ks[:, c, :], keysT[ds(h * 256 + c * P, P), :]).then_inc(loaded, 16)
                        for j in range(PIECES):
                            sp.wait_ge(ada_done, h * PIECES + (j + 1))
                            sp.dma_start(w_ada[:, j, :, :], ada_w[ds(l, 1), :, ds(g * (PIECES * CH) + j * CH, CH)].rearrange("o (k p) n -> p (o k) n", p=P)) \
                                .then_inc(ada_in[j], 16)

            @block.tensor
            def _(pe):
                pe.sem_inc(s_done, 2)
                pe.sem_inc(ada_done, PIECES)
                pe.wait_ge(c_ready, 1)
                with pe.Fori(0, PEER_H) as h:
                    pe.wait_ge(loaded, h * 64 + 64)
                    for c in range(2):
                        pe.wait_ge(s_copied, h * 2 + (c + 1))
                        for t in range(NT):
                            last = nc.tensor.matmul(psum[:, c, t * NK:(t + 1) * NK], qs[:, c, t * P:(t + 1) * P], ks[:, c, :], start=True, stop=True)
                        last.then_inc(s_done, 1)
                    for j in range(PIECES):
                        pe.wait_ge(ada_in[j], h * 16 + 16)
                        pe.wait_ge(rows_ready, h * PIECES + (j + 1))
                        for k in range(KD):
                            last = nc.tensor.matmul(psum[0:1, 2 + j, :], cT[:, k:k + 1], w_ada[:, j, k, :], start=k == 0, stop=k == KD - 1)
                        last.then_inc(ada_done, 1)

            @block.vector
            def _(dve):
                dve.sem_inc(s_copied, 2)
                dve.sem_inc(stored, 16 * NT)

                def best16(link, values, spare, v, i):
                    def each(op):
                        for t in range(NT):
                            ins = op(t)
                        link(ins)
                    each(lambda t: nc.vector.max(v[:, t, 0:8], values[:, t, :]))
                    each(lambda t: nc.vector.max_index(i[:, t, 0:8], v[:, t, 0:8], values[:, t, :]))
                    each(lambda t: nc.vector.match_replace(spare[:, t, :], v[:, t, 0:8], values[:, t, :], NEG))
                    each(lambda t: nc.vector.max(v[:, t, 8:16], spare[:, t, :]))
                    each(lambda t: nc.vector.max_index(i[:, t, 8:16], v[:, t, 8:16], spare[:, t, :]))

                flat = lambda ap: ap.rearrange("p t k -> p (t k)")
                pairs = lambda ap: ap.rearrange("p t (a b) -> p t a b", b=TOPK)
                over_a = lambda ap: ap.rearrange("p t (o b) -> p t o b", o=1).broadcast_to([P, NT, TOPK, TOPK])
                eq_rows = eq[:, :, :, :].rearrange("p t a b -> p (t a) b")
                with dve.Fori(0, PEER_H) as h:
                    dve.sem_clear(dve_order)
                    link = chain(dve, dve_order)
                    for c in range(2):
                        dve.wait_ge(s_done, h * 2 + (c + 3))
                        link(nc.vector.tensor_copy(sc[:, c, :, :].rearrange("p t k -> p (t k)"), psum[:, c, :]))
                        dve.sem_inc(s_copied, 1)
                        best16(link, sc[:, c, :, :], sc2[:, :, :], val[:, c, :, :], idx[:, c, :, :])
                        link(nc.vector.tensor_copy(idxf[:, c, :, :], idx[:, c, :, :]))
                    link(nc.vector.tensor_tensor(pairs(cand[:, :, :]), bc_last(flat(val[:, 0, :, :]), TOPK).rearrange("p (t a) b -> p t a b", a=TOPK),
                                                 over_a(val[:, 1, :, :]), ALU.add))
                    best16(link, cand[:, :, :], cand2[:, :, :], top[:, :, :], pos[:, :, :])
                    nc.vector.tensor_scalar(posx[:, 0, :, :], pos[:, :, :], 4, None, ALU.logical_shift_right)
                    link(nc.vector.tensor_scalar(posx[:, 1, :, :], pos[:, :, :], 15, None, ALU.bitwise_and))
                    link(nc.vector.tensor_copy(posf[:, :, :, :], posx[:, :, :, :]))
                    dve.wait_ge(stored, h * (16 * NT) + 16 * NT)
                    for t in range(NT):
                        ins = nc.vector.tensor_scalar(res[:, t, 2, :], top[:, t, :], top[:, t, 0:1], None, ALU.subtract)
                    ins.then_inc(diff_ready, 1)
                    for c in range(2):
                        link(nc.vector.tensor_tensor(eq_rows, bc_last(flat(posf[:, c, :, :]), TOPK), bc_mid(iota16, NT * TOPK), ALU.is_equal))
                        link(nc.vector.tensor_tensor(eq[:, :, :, :], eq[:, :, :, :], over_a(idxf[:, c, :, :]), ALU.mult))
                        link(nc.vector.tensor_reduce(res[:, :, c, :], eq[:, :, :, :], AX, ALU.add))
                    dve.wait_ge(exp_ready, h + 1)
                    link(nc.vector.tensor_reduce(sums[:, :], res[:, :, 2, :], AX, ALU.add))
                    link(nc.vector.reciprocal(sums[:, :], sums[:, :]))
                    link(nc.vector.tensor_tensor(res[:, :, 2, :], res[:, :, 2, :], bc_last(sums[:, :], TOPK), ALU.mult))
                    dve.sem_inc(res_ready, 1)

            @block.scalar
            def _(act):
                act.sem_inc(rows_ready, PIECES)
                act.sem_inc(rows_out, 16)
                act.wait_ge(c_in, 16)
                nc.scalar.activation(cT[:, :], cT[:, :], ACT.Silu).then_inc(c_ready, 1)
                with act.Fori(0, LAYERS) as l:
                    with act.Fori(0, GROUP) as g:
                        h = l * GROUP + g
                        act.wait_ge(rows_out, h * 16 + 16)
                        for j in range(PIECES):
                            act.wait_ge(ada_done, h * PIECES + (PIECES + 1 + j))
                            nc.scalar.copy(rows[0:1, j, :], psum[0:1, 2 + j, :]).then_inc(rows_ready, 1)
                        act.wait_ge(rows_ready, h * PIECES + 2 * PIECES)
                        act.dma_start(mods[ds(l, 1), 0, ds(g * (PIECES * CH), PIECES * CH)].rearrange("o (j n) -> o j n", n=CH), rows[:, :, :]).then_inc(rows_out, 16)
                        act.wait_ge(diff_ready, h + 1)
                        nc.scalar.activation(res[:, :, 2, :], res[:, :, 2, :], ACT.Exp).then_inc(exp_ready, 1)
                        act.wait_ge(res_ready, h + 1)
                        for t in range(NT):
                            act.dma_start(sel[t * P:(t + 1) * P, :, ds(h * TOPK, TOPK)], res[:, t, :, :]).then_inc(stored, 16)
                act.wait_ge(stored, 16 * NT * (PEER_H + 1))
                act.wait_ge(rows_out, 16 * PEER_H + 16)


def peer_gates(nc, tag, psum, selT, iota128, gates):
    TB = 4
    NB = P // TB
    G = 2 * TB
    with ExitStack() as ctx:
        sb = lambda m, s: ctx.enter_context(nc.sbuf_tensor(f"{tag}_{m}", s, F32))
        gbuf = sb("g", [P, NK, P])
        cols, oh1, oh2 = sb("cols", [P, 2, 3, G]), sb("oh1", [P, 2, G, NK]), sb("oh2", [P, 2, G, NK])
        (oh_ready, g_done, ev_a, stored, dve_order) = ctx.enter_context(stage_sems(
            nc, *[f"{tag}_{s}" for s in ("oh", "gd", "eva", "out", "dve")]))
        with nc.Block() as block:
            @block.sync
            def _(sp):
                sp.sem_inc(stored, 16)
                with sp.Fori(0, NT) as t:
                    sp.wait_ge(ev_a, t * NB + (NB + 4))
                    sp.dma_start(gates[ds(t, 1), :, :, :].rearrange("o p i t -> p (o i) t"), gbuf[:, :, :]).then_inc(stored, 16)
                sp.wait_ge(stored, 16 * NT + 16)

            @block.vector
            def _(dve):
                dve.sem_inc(g_done, 4)
                with dve.Fori(0, T // (2 * G)) as i:
                    dve.sem_clear(dve_order)
                    for v in range(2):
                        dve.wait_ge(g_done, i * 4 + (v * 2 + 2))
                        nc.vector.tensor_copy(cols[:, v, :, :], selT[:, :, ds(i * 2 * G + v * G, G)]).then_inc(dve_order, 1)
                        dve.wait_ge(dve_order, v + 1)
                        nc.vector.tensor_tensor(oh2[:, v, :, :], bc_mid(iota128, G), bc_last(cols[:, v, 1, :], NK), ALU.is_equal)
                        for b in range(G):
                            ins = nc.vector.tensor_scalar(oh1[:, v, b, :], iota128, cols[:, v, 0, b:b + 1], cols[:, v, 2, b:b + 1], ALU.is_equal, ALU.mult)
                        ins.then_inc(oh_ready, 1)

            @block.tensor
            def _(pe):
                with pe.Fori(0, T // (2 * G)) as i:
                    for v in range(2):
                        pe.wait_ge(oh_ready, i * 2 + (v + 1))
                        for half in range(2):
                            pe.wait_ge(ev_a, i * 4 + (v * 2 + half + 1))
                            for b in range(TB):
                                last = nc.tensor.matmul(psum[:, v * 2 + half, b * NK:(b + 1) * NK], oh2[:, v, half * TB + b, :], oh1[:, v, half * TB + b, :],
                                                        start=True, stop=True)
                            last.then_inc(g_done, 1)

            @block.scalar
            def _(act):
                act.sem_inc(ev_a, 4)
                with act.Fori(0, NT) as t:
                    act.wait_ge(stored, t * 16 + 16)
                    with act.Fori(0, NB // 4) as i:
                        for u in range(4):
                            act.wait_ge(g_done, t * NB + i * 4 + (u + 5))
                            nc.scalar.copy(gbuf[:, :, ds(i * 4 * TB + u * TB, TB)].rearrange("p i t -> p t i"),
                                           psum[:, u, :].rearrange("p (t i) -> p t i", i=NK)).then_inc(ev_a, 1)


def moe_dense(nc, tag, psum, halves, acc, n, w_a, w_out, w_b, token_w):
    FB = CH // P
    with ExitStack() as ctx:
        sb = lambda m, s: ctx.enter_context(nc.sbuf_tensor(f"{tag}_{m}", s, F32))
        wa, wo = sb("wa", [P, 2, KD, CH]), sb("wo", [P, 2, FB, D])
        wb, xT = sb("wb", [P, 2, KD, CH]), sb("x", [P, KD, T])
        nl, hid = sb("nl", [P, 2, T]), sb("hid", [P, 2, FB, T])
        (in0, in1, a_done, nl_ready, hid_ready, o_done, acc_done, dve_order, joined) = ctx.enter_context(stage_sems(
            nc, *[f"{tag}_{s}" for s in ("in0", "in1", "adone", "nl", "hid", "odone", "acc", "dve", "joined")]))
        loaded = (in0, in1)
        per_load = 48
        with nc.Block() as block:
            @block.sync
            def _(sp):
                with sp.Fori(0, n // 2) as i:
                    for u in range(2):
                        e = i * 2 + u
                        sp.wait_ge(o_done, e * 8 + 8)
                        sp.dma_start(wa[:, u, :, :], w_a(e)).then_inc(loaded[u], 16)
                        sp.dma_start(wb[:, u, :, :], w_b(e)).then_inc(loaded[u], 16)
                        sp.dma_start(wo[:, u, :, :], w_out(e)).then_inc(loaded[u], 16)

            @block.tensor
            def _(pe):
                pe.sem_inc(o_done, 16)
                pe.wait_ge(joined, 1)
                with pe.Fori(0, n // 2) as i:
                    for u in range(2):
                        e = i * 2 + u
                        pe.wait_ge(loaded[u], i * per_load + per_load)
                        for f in range(FB):
                            pe.wait_ge(hid_ready, e * FB + (f + 1))
                            for bank, w in ((f % 2, wa), (2 + f % 2, wb)):
                                for k in range(KD):
                                    last = nc.tensor.matmul(psum[:, bank, :], w[:, u, k, f * P:(f + 1) * P], xT[:, k, :], start=k == 0, stop=k == KD - 1)
                            last.then_inc(a_done, 1)
                        pe.wait_ge(hid_ready, e * FB + (FB + 2))
                        for j in range(8):
                            pe.wait_ge(acc_done, e * 8 + (j + 1))
                            for f in range(FB):
                                last = nc.tensor.matmul(psum[:, 4 + j % 4, :], hid[:, u, f, j // 2 * P:(j // 2 + 1) * P],
                                                        wo[:, u, f, j % 2 * CH:(j % 2 + 1) * CH], start=f == 0, stop=f == FB - 1)
                            last.then_inc(o_done, 1)

            @block.scalar
            def _(act):
                with act.Fori(0, n // 2) as i:
                    for u in range(2):
                        e = i * 2 + u
                        for f in range(FB):
                            act.wait_ge(a_done, e * FB + (f + 1))
                            act.wait_ge(hid_ready, e * FB + (f + 1))
                            nc.scalar.activation(nl[:, f % 2, :], psum[:, f % 2, :], ACT.Silu).then_inc(nl_ready, 1)

            @block.vector
            def _(dve):
                dve.sem_inc(hid_ready, 2)
                dve.sem_inc(acc_done, 4)
                nc.vector.tensor_tensor(xT[:, :, :], halves[0][:, :, :].bitcast(F32), halves[1][:, :, :].bitcast(F32), ALU.add).then_inc(joined, 1)
                nc.vector.memset(acc[:, :, :], 0.0).then_inc(dve_order, 1)
                dve.wait_ge(dve_order, 1)
                with dve.Fori(0, n // 2) as i:
                    for u in range(2):
                        e = i * 2 + u
                        for f in range(FB):
                            dve.wait_ge(nl_ready, e * FB + (f + 1))
                            nc.vector.tensor_tensor(hid[:, u, f, :], nl[:, f % 2, :], psum[:, 2 + f % 2, :], ALU.mult).then_inc(hid_ready, 1)
                        for j in range(8):
                            dve.wait_ge(o_done, e * 8 + (j + 17))
                            dst = acc[:, j // 2, j % 2 * CH:(j % 2 + 1) * CH]
                            dve.wait_ge(acc_done, e * 8 + (j + 4))
                            nc.vector.scalar_tensor_tensor(out=dst, in0=psum[:, 4 + j % 4, :], scalar=token_w[:, j // 2, ds(e, 1)],
                                                           in1=dst, op0=ALU.mult, op1=ALU.add).then_inc(acc_done, 1)


def peer_experts(nc, tag, psum, x, acc, down, up, gates):
    FB = CH // P
    n = N_EXP1 // CH
    with ExitStack() as ctx:
        sb = lambda m, s, d=F32: ctx.enter_context(nc.sbuf_tensor(f"{tag}_{m}", s, d))
        raw_d, raw_u, gt = sb("rawd", [P, KD, CH]), sb("rawu", [P, FB, D]), sb("gt", [P, 2, NT, FB, P])
        d_high, d_low = sb("dh", [P, KD, CH], F32R), sb("dl", [P, KD, CH], F32R)
        u_high, u_low = sb("uh", [P, FB, D], F32R), sb("ul", [P, FB, D], F32R)
        nl, h_high, h_low = sb("nl", [P, 2, T]), sb("hh", [P, FB, T], F32R), sb("hl", [P, FB, T], F32R)
        (d_in, u_in, g_in0, g_in1, dh_ready, dl_ready, uh_ready, ul_ready, a_done, nl_ready, prod_ready, hh_ready, hl_ready, o_done, acc_done, dve_order) = \
            ctx.enter_context(stage_sems(nc, *[f"{tag}_{s}" for s in (
                "din", "uin", "gin0", "gin1", "dhr", "dlr", "uhr", "ulr", "adone", "nl", "prod", "hhr", "hlr", "odone", "acc", "dve")]))
        g_in = (g_in0, g_in1)
        by_tile = lambda ap: ap.rearrange("p (t q) -> p t q", q=P)
        with nc.Block() as block:
            @block.sync
            def _(sp):
                with sp.Fori(0, n // 2) as i:
                    for v in range(2):
                        e = i * 2 + v
                        sp.wait_ge(dl_ready, e + 1)
                        sp.dma_start(raw_d[:, :, :], down[:, :, ds(e * CH, CH)]).then_inc(d_in, 16)
                        sp.wait_ge(hl_ready, e * FB + 1)
                        for t in range(NT):
                            sp.dma_start(gt[:, v, t, :, :], gates[t, :, ds(e * FB, FB), :]).then_inc(g_in[v], 16)
                        sp.wait_ge(ul_ready, e + 1)
                        sp.dma_start(raw_u[:, :, :], up[:, ds(e * FB, FB), :]).then_inc(u_in, 16)

            @block.tensor
            def _(pe):
                pe.sem_inc(a_done, FB)
                pe.sem_inc(o_done, 8)
                with pe.Fori(0, n) as e:
                    pe.wait_ge(dl_ready, e + 2)
                    for f in range(FB):
                        pe.wait_ge(nl_ready, e * FB + (f + 1))
                        for k in range(KD):
                            last = times(nc, psum[:, f, :], [w[:, k, f * P:(f + 1) * P] for w in (d_high, d_low)], [v[:, k, :] for v in x],
                                         k == 0, k == KD - 1)
                        last.then_inc(a_done, 1)
                    pe.wait_ge(ul_ready, e + 2)
                    for j in range(8):
                        pe.wait_ge(acc_done, e * 8 + (j + 1))
                        for f in range(FB):
                            if j == 0:
                                pe.wait_ge(hl_ready, e * FB + (FB + f + 1))
                            last = times(nc, psum[:, 4 + j % 4, :], [h[:, f, j // 2 * P:(j // 2 + 1) * P] for h in (h_high, h_low)],
                                         [w[:, f, j % 2 * CH:(j % 2 + 1) * CH] for w in (u_high, u_low)], f == 0, f == FB - 1)
                        last.then_inc(o_done, 1)

            @block.scalar
            def _(act):
                act.sem_inc(nl_ready, FB)

                def down_high(e):
                    act.wait_ge(d_in, e * 16 + 16)
                    act.wait_ge(a_done, e * FB + FB)
                    nc.scalar.copy(d_high[:, :, :], raw_d[:, :, :]).then_inc(dh_ready, 1)

                def block_of(e, is_last):
                    act.wait_ge(u_in, e * 16 + 16)
                    act.wait_ge(o_done, e * 8 + 8)
                    nc.scalar.copy(u_high[:, :, :], raw_u[:, :, :]).then_inc(uh_ready, 1)
                    for f in range(FB):
                        act.wait_ge(a_done, e * FB + (FB + f + 1))
                        act.wait_ge(hl_ready, e * FB + (f + 3))
                        nc.scalar.activation(nl[:, f % 2, :], psum[:, f, :], ACT.Gelu).then_inc(nl_ready, 1)
                        act.wait_ge(prod_ready, e * FB + (f + 1))
                        nc.scalar.copy(h_high[:, f, :], nl[:, f % 2, :]).then_inc(hh_ready, 1)
                    if not is_last:
                        down_high(e + 1)

                down_high(0)
                with act.Fori(0, n - 1) as e:
                    block_of(e, False)
                block_of(n - 1, True)

            @block.vector
            def _(dve):
                dve.sem_inc(dl_ready, 1)
                dve.sem_inc(ul_ready, 1)
                dve.sem_inc(hl_ready, FB)
                dve.sem_inc(acc_done, 4)
                nc.vector.memset(acc[:, :, :], 0.0).then_inc(dve_order, 1)
                dve.wait_ge(dve_order, 1)

                def down_low(e):
                    dve.wait_ge(dh_ready, e + 1)
                    nc.vector.tensor_tensor(d_low[:, :, :], raw_d[:, :, :], d_high[:, :, :].bitcast(F32), ALU.subtract).then_inc(dl_ready, 1)

                def block_of(e, v, turn, is_last):
                    dve.wait_ge(uh_ready, e + 1)
                    nc.vector.tensor_tensor(u_low[:, :, :], raw_u[:, :, :], u_high[:, :, :].bitcast(F32), ALU.subtract).then_inc(ul_ready, 1)
                    dve.wait_ge(g_in[v], turn * (16 * NT) + 16 * NT)
                    for f in range(FB):
                        dve.wait_ge(nl_ready, e * FB + (FB + f + 1))
                        nc.vector.tensor_tensor(by_tile(nl[:, f % 2, :]), by_tile(nl[:, f % 2, :]), gt[:, v, :, f, :], ALU.mult).then_inc(prod_ready, 1)
                        dve.wait_ge(hh_ready, e * FB + (f + 1))
                        nc.vector.tensor_tensor(h_low[:, f, :], nl[:, f % 2, :], h_high[:, f, :].bitcast(F32), ALU.subtract).then_inc(hl_ready, 1)
                    if not is_last:
                        down_low(e + 1)
                    for j in range(8):
                        dve.wait_ge(o_done, e * 8 + (j + 9))
                        dve.wait_ge(acc_done, e * 8 + (j + 4))
                        dst = acc[:, j // 2, j % 2 * CH:(j % 2 + 1) * CH]
                        nc.vector.tensor_tensor(dst, psum[:, 4 + j % 4, :], dst, ALU.add).then_inc(acc_done, 1)

                down_low(0)
                with dve.Fori(0, n // 2 - 1) as i:
                    for v in range(2):
                        block_of(i * 2 + v, v, i, False)
                block_of(n - 2, 0, n // 2 - 1, False)
                block_of(n - 1, 1, n // 2 - 1, True)


def adaptive_bias(nc, tag, b, mods):
    row = mods.rearrange("l o (p n) -> p (l o) n", p=P)
    with ExitStack() as ctx:
        m_sb, b_sb = (ctx.enter_context(nc.sbuf_tensor(f"{tag}_{m}", [P, LAYERS, 6 * D // P], F32)) for m in "mb")
        xin, added, stored = ctx.enter_context(stage_sems(nc, f"{tag}_in", f"{tag}_add", f"{tag}_out"))
        with nc.Block() as block:
            @block.sync
            def _(sp):
                sp.dma_start(m_sb[:, :, :], row).then_inc(xin, 16)
                sp.dma_start(b_sb[:, :, :], b.rearrange("l (p n) -> p l n", p=P)).then_inc(xin, 16)
                sp.wait_ge(added, 1)
                sp.dma_start(row, m_sb[:, :, :]).then_inc(stored, 16)
                sp.wait_ge(stored, 16)

            @block.vector
            def _(dve):
                dve.wait_ge(xin, 32)
                nc.vector.tensor_tensor(m_sb[:, :, :], m_sb[:, :, :], b_sb[:, :, :], ALU.add).then_inc(added, 1)


def fox_prep(nc, tag, psum, tri, proj, fb, qa, ka):
    H, DH = 4, 128
    root = DH ** 0.5
    with ExitStack() as ctx:
        sb = lambda m, s: ctx.enter_context(nc.sbuf_tensor(f"{tag}_{m}", s, F32))
        q, k = sb("q", [P, NT, H, DH + 2]), sb("k", [P, NT, H, DH + 2])
        ff, fbs, e, lf, ones = sb("ff", [P, NT, H]), sb("fb", [P, H]), sb("e", [P, NT, H]), sb("lf", [P, NT, H]), sb("ones", [P, P])
        (xin, qk_in, abs_ready, ln_ready, lf_ready, cum_done, ext_ready, stored, dve_order, act_order) = ctx.enter_context(stage_sems(
            nc, *[f"{tag}_{s}" for s in ("in", "qkin", "abs", "ln", "lf", "cum", "ext", "out", "dve", "act")]))
        tiled_heads = lambda a, t: a[t * P:(t + 1) * P, :].rearrange("p (h d) -> p h d", h=H)
        with nc.Block() as block:
            @block.sync
            def _(sp):
                sp.dma_start(ff[:, :, :], tiled(proj)[:, :, FF:FF + H]).then_inc(xin, 16)
                sp.dma_start(fbs[:, :], row_bc(fb)).then_inc(xin, 16)
                for t in range(NT):
                    sp.dma_start(q[:, t, :, 0:DH], tiled_heads(proj[:, FQ:FQ + H * DH], t)).then_inc(qk_in, 16)
                    sp.dma_start(k[:, t, :, 0:DH], tiled_heads(proj[:, FK:FK + H * DH], t)).then_inc(qk_in, 16)
                sp.wait_ge(qk_in, 32 * NT)
                sp.wait_ge(ext_ready, 1)
                for t in range(NT):
                    sp.dma_start(qa[t * P:(t + 1) * P, :, :], q[:, t, :, :]).then_inc(stored, 16)
                    sp.dma_start(ka[t * P:(t + 1) * P, :, :], k[:, t, :, :]).then_inc(stored, 16)
                sp.wait_ge(stored, 32 * NT)

            @block.vector
            def _(dve):
                link = chain(dve, dve_order)
                link(nc.vector.memset(ones[:, :], 1.0))
                dve.wait_ge(xin, 32)
                link(nc.vector.tensor_tensor(ff[:, :, :], ff[:, :, :], bc_mid(fbs[:, :], NT), ALU.add))
                link(nc.vector.tensor_scalar(e[:, :, :], ff[:, :, :], -1.0, None, ALU.mult))
                nc.vector.tensor_tensor(e[:, :, :], e[:, :, :], ff[:, :, :], ALU.min).then_inc(abs_ready, 1)
                dve.wait_ge(ln_ready, 1)
                nc.vector.scalar_tensor_tensor(out=lf[:, :, :], in0=ff[:, :, :], scalar=0.0, in1=e[:, :, :], op0=ALU.min, op1=ALU.subtract).then_inc(lf_ready, 1)
                dve.wait_ge(cum_done, 1)
                cum = psum[:, 0, 0:NT * H].rearrange("p (t h) -> p t h", h=H)
                link(nc.vector.tensor_scalar(q[:, :, :, DH], cum, root, None, ALU.mult))
                link(nc.vector.tensor_scalar(k[:, :, :, DH + 1], cum, -root, None, ALU.mult))
                link(nc.vector.memset(q[:, :, :, DH + 1], 1.0))
                link(nc.vector.memset(k[:, :, :, DH], 1.0))
                dve.sem_inc(ext_ready, 1)

            @block.scalar
            def _(act):
                link = chain(act, act_order)
                act.wait_ge(abs_ready, 1)
                link(nc.scalar.activation(e[:, :, :], e[:, :, :], ACT.Exp))
                nc.scalar.activation(e[:, :, :], e[:, :, :], ACT.Ln, bias=1.0).then_inc(ln_ready, 1)

            @block.tensor
            def _(pe):
                pe.wait_ge(lf_ready, 1)
                for t in range(NT):
                    for j in range(t + 1):
                        last = nc.tensor.matmul(psum[:, 0, t * H:(t + 1) * H], tri[:, :] if j == t else ones[:, :], lf[:, j, :], start=j == 0, stop=j == t)
                last.then_inc(cum_done, 1)


def copy_pieces(nc, tag, pairs):
    with ExitStack() as ctx:
        (copied,) = ctx.enter_context(stage_sems(nc, f"{tag}_cp"))
        with nc.Block() as block:
            @block.sync
            def _(sp):
                for dst, src in pairs:
                    sp.dma_start(dst, src).then_inc(copied, 16)
                sp.wait_ge(copied, 16 * len(pairs))


def retention(nc, tag, psum, ident, q, k, v, consts, o):
    H, DK, DV = 4, 64, 128
    dmask_d, decay_d = consts
    with ExitStack() as ctx:
        sb = lambda m, s: ctx.enter_context(nc.sbuf_tensor(f"{tag}_{m}", s, F32))
        dm, dec = sb("dm", [P, H * P]), sb("dec", [P, 3, H])
        qs, ks, vs = sb("q", [P, H * DK]), sb("k", [P, H * DK]), sb("v", [P, H * DV])
        qT, kT, sT, kd = sb("qT", [DK, H * P]), sb("kT", [DK, H * P]), sb("sT", [P, H * P]), sb("kd", [P, H * DK])
        state, ob = sb("state", [DK, H * DV]), sb("ob", [P, H * DV])
        hv = lambda ap: ap.rearrange("p (h d) -> p h d", h=H)
        (consts_in, loaded, tr_done, q_ev, k_ev, s_done, s_ready, mm_done, o_ready, stored, dve_order) = ctx.enter_context(stage_sems(
            nc, *[f"{tag}_{s}" for s in ("cin", "in", "tr", "qev", "kev", "sd", "sr", "mm", "or", "out", "dve")]))
        with nc.Block() as block:
            @block.sync
            def _(sp):
                sp.dma_start(dm[:, :], dmask_d).then_inc(consts_in, 16)
                sp.dma_start(dec[:, :, :].rearrange("p a h -> p (a h)"), decay_d).then_inc(consts_in, 16)
                with sp.Fori(0, NT) as c:
                    sp.wait_ge(o_ready, c + 1)
                    sp.dma_start(qs[:, :], q[ds(c * P, P), :]).then_inc(loaded, 16)
                    sp.dma_start(ks[:, :], k[ds(c * P, P), :]).then_inc(loaded, 16)
                    sp.dma_start(vs[:, :], v[ds(c * P, P), :]).then_inc(loaded, 16)
                    sp.wait_ge(o_ready, c + 2)
                    sp.dma_start(o[ds(c * P, P), :], ob[:, :]).then_inc(stored, 16)
                sp.wait_ge(stored, 16 * NT + 16)

            @block.tensor
            def _(pe):
                with pe.Fori(0, NT) as c:
                    pe.wait_ge(loaded, c * 48 + 48)
                    take_bank(nc, psum[:, 0, 0:P], ident)
                    for h in range(H):
                        nc.tensor.transpose(psum[0:DK, 0, h * P:(h + 1) * P], qs[:, h * DK:(h + 1) * DK], ident[:, :])
                        last = nc.tensor.transpose(psum[0:DK, 1, h * P:(h + 1) * P], ks[:, h * DK:(h + 1) * DK], ident[:, :])
                    last.then_inc(tr_done, 1)
                    pe.wait_ge(q_ev, c + 1)
                    pe.wait_ge(k_ev, c + 1)
                    for h in range(H):
                        last = nc.tensor.matmul(psum[:, 2, h * P:(h + 1) * P], kT[:, h * P:(h + 1) * P], qT[:, h * P:(h + 1) * P], start=True, stop=True)
                    last.then_inc(s_done, 1)
                    pe.wait_ge(s_ready, c + 1)
                    for h in range(H):
                        nc.tensor.matmul(psum[:, 3, h * DV:(h + 1) * DV], sT[:, h * P:(h + 1) * P], vs[:, h * DV:(h + 1) * DV], start=True, stop=True)
                        nc.tensor.matmul(psum[:, 4, h * DV:(h + 1) * DV], qT[:, h * P:(h + 1) * P], state[:, h * DV:(h + 1) * DV], start=True, stop=True)
                        last = nc.tensor.matmul(psum[0:DK, 5, h * DV:(h + 1) * DV], kd[:, h * DK:(h + 1) * DK], vs[:, h * DV:(h + 1) * DV], start=True, stop=True)
                    last.then_inc(mm_done, 1)

            @block.scalar
            def _(act):
                with act.Fori(0, NT) as c:
                    act.wait_ge(tr_done, c + 1)
                    nc.scalar.copy(qT[:, :], psum[0:DK, 0, :]).then_inc(q_ev, 1)

            @block.vector
            def _(dve):
                dve.sem_inc(o_ready, 1)
                dve.sem_inc(stored, 16)
                nc.vector.memset(state[:, :], 0.0).then_inc(dve_order, 1)
                dve.wait_ge(dve_order, 1)
                dve.wait_ge(consts_in, 32)
                with dve.Fori(0, NT) as c:
                    dve.sem_clear(dve_order)
                    link = chain(dve, dve_order)
                    dve.wait_ge(tr_done, c + 1)
                    nc.vector.tensor_copy(kT[:, :], psum[0:DK, 1, :]).then_inc(k_ev, 1)
                    link(nc.vector.tensor_tensor(hv(kd[:, :]), hv(ks[:, :]), bc_last(dec[:, 1, :], DK), ALU.mult))
                    dve.wait_ge(s_done, c + 1)
                    link(nc.vector.tensor_tensor(sT[:, :], psum[:, 2, :], dm[:, :], ALU.mult))
                    dve.sem_inc(s_ready, 1)
                    dve.wait_ge(mm_done, c + 1)
                    dve.wait_ge(stored, c * 16 + 16)
                    link(nc.vector.tensor_tensor(hv(ob[:, :]), hv(psum[:, 4, :]), bc_last(dec[:, 0, :], DV), ALU.mult))
                    link(nc.vector.tensor_tensor(ob[:, :], ob[:, :], psum[:, 3, :], ALU.add))
                    link(nc.vector.tensor_tensor(hv(state[:, :]), hv(state[:, :]), bc_last(dec[0:DK, 2, :], DV), ALU.mult))
                    link(nc.vector.tensor_tensor(state[:, :], state[:, :], psum[0:DK, 5, :], ALU.add))
                    dve.sem_inc(o_ready, 1)


def retention_gate_norm(nc, tag, o, g, out):
    H, DV = 4, 128
    W = H * DV
    with ExitStack() as ctx:
        sb = lambda m, s: ctx.enter_context(nc.sbuf_tensor(f"{tag}_{m}", s, F32))
        ys, gs, sq = sb("y", [P, NT, W]), sb("g", [P, NT, W]), sb("sq", [P, W])
        mean, var, rt, tp = sb("mean", [P, NT, H]), sb("var", [P, NT, H]), sb("rt", [P, NT, H]), sb("tp", [P, NT, H])
        xin, silu_ready, var_ready, root_ready, dve_order, y_ready, stored = ctx.enter_context(stage_sems(
            nc, *[f"{tag}_{s}" for s in ("in", "silu", "var", "root", "dve", "y", "out")]))
        grp = lambda ap: ap.rearrange("p (g d) -> p g d", g=H)
        with nc.Block() as block:
            @block.sync
            def _(sp):
                sp.dma_start(gs[:, :, :], tiled(g)).then_inc(xin, 16)
                sp.dma_start(ys[:, :, :], tiled(o)).then_inc(xin, 16)
                sp.wait_ge(y_ready, NT)
                sp.dma_start(tiled(out), ys[:, :, :]).then_inc(stored, 16)
                sp.wait_ge(stored, 16)

            @block.scalar
            def _(act):
                act.wait_ge(xin, 32)
                nc.scalar.activation(gs[:, :, :], gs[:, :, :], ACT.Silu).then_inc(silu_ready, 1)
                act.wait_ge(var_ready, 1)
                nc.scalar.activation(rt[:, :, :], var[:, :, :], ACT.Sqrt).then_inc(root_ready, 1)

            @block.vector
            def _(dve):
                link = chain(dve, dve_order)
                dve.wait_ge(xin, 32)
                for t in range(NT):
                    link(nc.vector.tensor_reduce(mean[:, t, :], grp(ys[:, t, :]), AX, ALU.add))
                    link(nc.vector.tensor_scalar(mean[:, t, :], mean[:, t, :], 1.0 / DV, None, ALU.mult))
                    link(nc.vector.tensor_tensor(grp(ys[:, t, :]), grp(ys[:, t, :]), bc_last(mean[:, t, :], DV), ALU.subtract))
                    link(nc.vector.tensor_tensor(sq[:, :], ys[:, t, :], ys[:, t, :], ALU.mult))
                    link(nc.vector.tensor_reduce(var[:, t, :], grp(sq[:, :]), AX, ALU.add))
                nc.vector.tensor_scalar(var[:, :, :], var[:, :, :], 1.0 / DV, EPS, ALU.mult, ALU.add).then_inc(var_ready, 1)
                dve.wait_ge(silu_ready, 1)
                dve.wait_ge(root_ready, 1)
                refined_root(nc, link, rt[:, :, :], var[:, :, :], tp[:, :, :])
                for t in range(NT):
                    link(nc.vector.tensor_tensor(grp(ys[:, t, :]), grp(ys[:, t, :]), bc_last(rt[:, t, :], DV), ALU.mult))
                    nc.vector.tensor_tensor(ys[:, t, :], ys[:, t, :], gs[:, t, :], ALU.mult).then_inc(y_ready, 1)


def moe_route(nc, tag, psum, tri, logits, bias, iota, token_w, pair_w, pair_row, crowded):
    W = N_GRP + N_EXPERTS
    iota8 = iota[:, 0:8]
    with ExitStack() as ctx:
        sb = lambda m, s, d=F32: ctx.enter_context(nc.sbuf_tensor(f"{tag}_{m}", s, d))
        lg, bs = sb("lg", [P, NT, W]), sb("bs", [P, W])
        gl, gtop, gi, gif, goh = sb("gl", [P, NT, 8]), sb("gtop", [P, NT, 8]), sb("gi", [P, NT, 8], U32), sb("gif", [P, NT, 8]), sb("goh", [P, NT, 8])
        tmp, ing, etop, ei, eif = sb("tmp", [P, N_GRP, 8]), sb("ing", [P, NT, 8]), sb("etop", [P, NT, 8]), sb("ei", [P, NT, 8], U32), sb("eif", [P, NT, 8])
        s1, s2, wsel, wj = sb("s1", [P, NT]), sb("s2", [P, NT]), sb("wsel", [P, NT, 8]), sb("wj", [P, NT, 8])
        oh, sel, ones = sb("oh", [P, 2, NT, N_EXPERTS]), sb("sel", [P, NT, N_EXPERTS]), sb("ones", [P, P])
        base, rank, rowf, most = sb("base", [P, N_EXPERTS]), sb("rank", [P, NT, N_EXPERTS]), sb("rowf", [P, NT, 2]), sb("most", [P, 1])
        xin, diff_ready, exp_ready, sel_ready, rank_done, dve_order = ctx.enter_context(stage_sems(
            nc, *[f"{tag}_{s}" for s in ("in", "diff", "exp", "sel", "rank", "dve")]))
        by_group = lambda ap: ap.rearrange("p (g j) -> p g j", g=N_GRP)
        with nc.Block() as block:
            @block.sync
            def _(sp):
                sp.dma_start(lg[:, :, :], tiled(logits)).then_inc(xin, 16)
                sp.dma_start(bs[:, :], row_bc(bias)).then_inc(xin, 16)

            @block.tensor
            def _(pe):
                pe.wait_ge(sel_ready, 1)
                for t in range(NT):
                    for j in range(t + 1):
                        nc.tensor.matmul(psum[:, 0, t * N_EXPERTS:(t + 1) * N_EXPERTS], tri[:, :] if j == t else ones[:, :], sel[:, j, :],
                                         start=j == 0, stop=j == t)
                for j in range(NT):
                    last = nc.tensor.matmul(psum[:, 0, NT * N_EXPERTS:(NT + 1) * N_EXPERTS], ones[:, :], sel[:, j, :], start=j == 0, stop=j == NT - 1)
                last.then_inc(rank_done, 1)

            @block.vector
            def _(dve):
                link = chain(dve, dve_order)
                link(nc.vector.memset(ones[:, :], 1.0))
                link(nc.vector.memset(gl[:, :, :], NEG))
                link(nc.vector.tensor_scalar(base[:, :], iota[:, 0:N_EXPERTS], float(P), None, ALU.mult))
                dve.wait_ge(xin, 32)
                link(nc.vector.tensor_tensor(lg[:, :, :], lg[:, :, :], bc_mid(bs[:, :], NT), ALU.add))
                link(nc.vector.tensor_copy(gl[:, :, 0:N_GRP], lg[:, :, 0:N_GRP]))
                for t in range(NT):
                    link(nc.vector.max(gtop[:, t, :], gl[:, t, :]))
                    link(nc.vector.max_index(gi[:, t, :], gtop[:, t, :], gl[:, t, :]))
                link(nc.vector.tensor_copy(gif[:, :, :], gi[:, :, :]))
                for t in range(NT):
                    link(nc.vector.tensor_scalar(goh[:, t, :], iota8, gif[:, t, 0:1], None, ALU.is_equal))
                    link(nc.vector.tensor_tensor(tmp[:, :, :], by_group(lg[:, t, N_GRP:W]), bc_last(goh[:, t, 0:N_GRP], EPG), ALU.mult))
                    link(nc.vector.tensor_reduce(ing[:, t, :], tmp[:, :, :].rearrange("p g j -> p j g"), AX, ALU.add))
                    link(nc.vector.max(etop[:, t, :], ing[:, t, :]))
                    link(nc.vector.max_index(ei[:, t, :], etop[:, t, :], ing[:, t, :]))
                    link(nc.vector.tensor_scalar(gl[:, t, 0:N_GRP], gl[:, t, 0:N_GRP], gtop[:, t, 0:1], None, ALU.subtract))
                    link(nc.vector.tensor_scalar(wsel[:, t, :], etop[:, t, :], etop[:, t, 0:1], None, ALU.subtract))
                link(nc.vector.tensor_copy(eif[:, :, :], ei[:, :, :]))
                dve.sem_inc(diff_ready, 1)
                for c in range(2):
                    for t in range(NT):
                        link(nc.vector.tensor_scalar(wj[:, t, :], iota8, eif[:, t, c:c + 1], None, ALU.is_equal))
                        link(nc.vector.tensor_tensor(by_group(oh[:, c, t, :]), bc_last(goh[:, t, 0:N_GRP], EPG), bc_mid(wj[:, t, :], N_GRP), ALU.mult))
                link(nc.vector.tensor_tensor(sel[:, :, :], oh[:, 0, :, :], oh[:, 1, :, :], ALU.add))
                dve.sem_inc(sel_ready, 1)
                dve.wait_ge(exp_ready, 1)
                link(nc.vector.tensor_reduce(s1[:, :], gl[:, :, 0:N_GRP], AX, ALU.add))
                link(nc.vector.reciprocal(s1[:, :], s1[:, :]))
                link(nc.vector.tensor_reduce(s2[:, :], wsel[:, :, :], AX, ALU.add))
                link(nc.vector.reciprocal(s2[:, :], s2[:, :]))
                link(nc.vector.tensor_tensor(wsel[:, :, :], wsel[:, :, :], bc_last(s2[:, :], 8), ALU.mult))
                link(nc.vector.tensor_reduce(s2[:, :], wsel[:, :, 0:2], AX, ALU.add))
                link(nc.vector.reciprocal(s2[:, :], s2[:, :]))
                link(nc.vector.tensor_tensor(s2[:, :], s2[:, :], s1[:, :], ALU.mult))
                link(nc.vector.tensor_tensor(pair_w[:, :, :], wsel[:, :, 0:2], bc_last(s2[:, :], 2), ALU.mult))
                dve.wait_ge(rank_done, 1)
                link(nc.vector.tensor_tensor(rank[:, :, :], psum[:, 0, 0:NT * N_EXPERTS].rearrange("p (t e) -> p t e", t=NT), bc_mid(base[:, :], NT), ALU.add))
                link(nc.vector.tensor_reduce(most[:, :], psum[:, 0, NT * N_EXPERTS:(NT + 1) * N_EXPERTS], AX, ALU.max))
                link(nc.vector.tensor_scalar(crowded[:, :], most[:, :], float(P), None, ALU.is_gt))
                for c in range(2):
                    link(nc.vector.tensor_tensor(sel[:, :, :], oh[:, c, :, :], rank[:, :, :], ALU.mult))
                    link(nc.vector.tensor_reduce(rowf[:, :, c], sel[:, :, :], AX, ALU.add))
                    link(nc.vector.tensor_tensor(oh[:, c, :, :], oh[:, c, :, :], bc_last(pair_w[:, :, c], N_EXPERTS), ALU.mult))
                link(nc.vector.tensor_scalar(pair_row[:, :, :], rowf[:, :, :], -1.0, None, ALU.add))
                link(nc.vector.tensor_tensor(token_w[:, :, :], oh[:, 0, :, :], oh[:, 1, :, :], ALU.add))

            @block.scalar
            def _(act):
                act.wait_ge(diff_ready, 1)
                nc.scalar.activation(gl[:, :, 0:N_GRP], gl[:, :, 0:N_GRP], ACT.Exp)
                nc.scalar.activation(wsel[:, :, :], wsel[:, :, :], ACT.Exp).then_inc(exp_ready, 1)


def moe_slots(nc, tag, psum, ident, tokens, pair_row, table, slot_token):
    with ExitStack() as ctx:
        sb = lambda m, s, d: ctx.enter_context(nc.sbuf_tensor(f"{tag}_{m}", s, d))
        zero, rows, rows_f = sb("zero", [N_EXPERTS, P], I32), sb("rows", [N_EXPERTS, P], I32), sb("rowsf", [N_EXPERTS, P], F32)
        zero_ready, cleared, scattered, rows_in, rows_ready, turned = ctx.enter_context(stage_sems(
            nc, *[f"{tag}_{s}" for s in ("zero", "clr", "sc", "rin", "rr", "turn")]))
        table_v = table.rearrange("(e s) o -> e (s o)", e=N_EXPERTS)
        with nc.Block() as block:
            @block.sync
            def _(sp):
                sp.wait_ge(zero_ready, 1)
                sp.dma_start(table_v, zero[:, :]).then_inc(cleared, 16)
                sp.wait_ge(scattered, 16 * 2 * NT)
                sp.dma_start(rows[:, :], table_v).then_inc(rows_in, 16)

            @block.gpsimd
            def _(pool):
                pool.wait_ge(cleared, 16)
                for t in range(NT):
                    for c in range(2):
                        pool.indirect_dma_start(out=table[:, :], out_offset=bass.IndirectOffsetOnAxis(ap=pair_row[:, t, c:c + 1], axis=0),
                                                in_=tokens[:, t:t + 1], in_offset=None).then_inc(scattered, 16)

            @block.vector
            def _(dve):
                nc.vector.memset(zero[:, :], 0).then_inc(zero_ready, 1)
                dve.wait_ge(rows_in, 16)
                nc.vector.tensor_copy(rows_f[:, :], rows[:, :]).then_inc(rows_ready, 1)
                dve.wait_ge(turned, 1)
                nc.vector.tensor_copy(slot_token[:, :], psum[:, 0, 0:N_EXPERTS])

            @block.tensor
            def _(pe):
                pe.wait_ge(rows_ready, 1)
                nc.tensor.transpose(psum[:, 0, 0:N_EXPERTS], rows_f[:, :], ident[0:N_EXPERTS, 0:N_EXPERTS]).then_inc(turned, 1)


def moe_experts(nc, tag, psum, ident, x, slot_token, w_a, w_b, w_out, y, col_ready):
    FB = D_EXP // P
    n = N_EXPERTS
    with ExitStack() as ctx:
        sb = lambda m, s, d=F32: ctx.enter_context(nc.sbuf_tensor(f"{tag}_{m}", s, d))
        wa, wb, wo = sb("wa", [P, 2, KD, CH]), sb("wb", [P, 2, KD, CH]), sb("wo", [P, 2, FB, D])
        rows, xg, hidT, y_sb = sb("rows", [P, 2, D]), sb("xg", [P, 2, KD, P]), sb("hidT", [P, FB, P]), sb("y", [P, 2, D])
        nl, hid = sb("nl", [P, D_EXP]), sb("hid", [P, D_EXP])
        col0, col1 = sb("col0", [P, 1], U32), sb("col1", [P, 1], U32)
        (in0, in1, rows0, rows1, x_turned, xg_ready, gu_done, nl_ready, hid_ready, h_turned, hT_ready, o_done, y_ready, out0, out1) = \
            ctx.enter_context(stage_sems(nc, *[f"{tag}_{s}" for s in (
                "in0", "in1", "rows0", "rows1", "xt", "xg", "gu", "nl", "hid", "ht", "hTr", "od", "yr", "out0", "out1")]))
        loaded, rows_in, stored, cols = (in0, in1), (rows0, rows1), (out0, out1), (col0, col1)
        with nc.Block() as block:
            @block.sync
            def _(sp):
                with sp.Fori(0, n // 2) as i:
                    for u in range(2):
                        e = i * 2 + u
                        sp.wait_ge(o_done, e + 1)
                        sp.dma_start(wa[:, u, :, :], w_a(e)).then_inc(loaded[u], 16)
                        sp.dma_start(wb[:, u, :, :], w_b(e)).then_inc(loaded[u], 16)
                        sp.dma_start(wo[:, u, :, :], w_out(e)).then_inc(loaded[u], 16)

            @block.gpsimd
            def _(pool):
                with pool.Fori(0, n // 2) as i:
                    for u in range(2):
                        pool.sem_clear(col_ready)
                        pool.wait_ge(x_turned, i * 2 + (u + 1))
                        nc.gpsimd.tensor_copy(cols[u][:, :], slot_token[:, ds(i * 2 + u, 1)]).then_inc(col_ready, 1)
                        pool.wait_ge(col_ready, 1)
                        pool.indirect_dma_start(out=rows[:, u, :], out_offset=None, in_=x[:, :],
                                                in_offset=bass.IndirectOffsetOnAxis(ap=cols[u][:, :], axis=0)).then_inc(rows_in[u], 16)

            @block.tensor
            def _(pe):
                pe.sem_inc(o_done, 2)
                pe.sem_inc(x_turned, 2)

                def turn_rows(u, turn, evacuated):
                    pe.wait_ge(rows_in[u], turn * 16 + 16)
                    pe.wait_ge(xg_ready, evacuated)
                    for k in range(KD):
                        last = nc.tensor.transpose(psum[:, k // 4, k % 4 * P:(k % 4 + 1) * P], rows[:, u, k * P:(k + 1) * P], ident[:, :])
                    last.then_inc(x_turned, 1)

                def expert(e, u, turn, is_last):
                    pe.wait_ge(xg_ready, e * 2 + 4)
                    pe.wait_ge(loaded[u], turn * 48 + 48)
                    pe.wait_ge(hid_ready, e + 1)
                    for bank, w in ((2, wa), (3, wb)):
                        for k in range(KD):
                            last = nc.tensor.matmul(psum[:, bank, :], xg[:, u, k, :], w[:, u, k, :], start=k == 0, stop=k == KD - 1)
                    last.then_inc(gu_done, 1)
                    if not is_last:
                        turn_rows(1 - u, turn + u, e * 2 + 4)
                    pe.wait_ge(hid_ready, e + 2)
                    for f in range(FB):
                        last = nc.tensor.transpose(psum[:, 4, f * P:(f + 1) * P], hid[:, f * P:(f + 1) * P], ident[:, :])
                    last.then_inc(h_turned, 1)
                    pe.wait_ge(hT_ready, e + 1)
                    pe.wait_ge(y_ready, e + 1)
                    for half in range(2):
                        for f in range(FB):
                            last = nc.tensor.matmul(psum[:, 5 + half, :], hidT[:, f, :], wo[:, u, f, half * CH:(half + 1) * CH], start=f == 0, stop=f == FB - 1)
                    last.then_inc(o_done, 1)

                turn_rows(0, 0, 2)
                with pe.Fori(0, n // 2 - 1) as i:
                    for u in range(2):
                        expert(i * 2 + u, u, i, False)
                expert(n - 2, 0, n // 2 - 1, False)
                expert(n - 1, 1, n // 2 - 1, True)

            @block.scalar
            def _(act):
                act.sem_inc(xg_ready, 2)
                act.sem_inc(out0, 16)
                act.sem_inc(out1, 16)

                def take_rows(u, e):
                    act.wait_ge(x_turned, e + 3)
                    for b in range(2):
                        nc.scalar.copy(xg[:, u, b * 4:(b + 1) * 4, :], psum[:, b, :].rearrange("p (k s) -> p k s", s=P)).then_inc(xg_ready, 1)

                def expert(e, u, turn, is_last):
                    act.wait_ge(gu_done, e + 1)
                    nc.scalar.activation(nl[:, :], psum[:, 2, :], ACT.Silu).then_inc(nl_ready, 1)
                    if not is_last:
                        take_rows(1 - u, e + 1)
                    act.wait_ge(h_turned, e + 1)
                    nc.scalar.copy(hidT[:, :, :], psum[:, 4, :].rearrange("p (f s) -> p f s", s=P)).then_inc(hT_ready, 1)
                    act.wait_ge(y_ready, e + 2)
                    act.dma_start(y[ds(e * P, P), :], y_sb[:, u, :]).then_inc(stored[u], 16)

                take_rows(0, 0)
                with act.Fori(0, n // 2 - 1) as i:
                    for u in range(2):
                        expert(i * 2 + u, u, i, False)
                expert(n - 2, 0, n // 2 - 1, False)
                expert(n - 1, 1, n // 2 - 1, True)
                act.wait_ge(out0, n // 2 * 16 + 16)
                act.wait_ge(out1, n // 2 * 16 + 16)

            @block.vector
            def _(dve):
                dve.sem_inc(hid_ready, 1)
                dve.sem_inc(y_ready, 1)
                with dve.Fori(0, n // 2) as i:
                    for u in range(2):
                        e = i * 2 + u
                        dve.wait_ge(nl_ready, e + 1)
                        nc.vector.tensor_tensor(hid[:, :], nl[:, :], psum[:, 3, :], ALU.mult).then_inc(hid_ready, 1)
                        dve.wait_ge(o_done, e + 3)
                        dve.wait_ge(stored[u], i * 16 + 16)
                        for half in range(2):
                            last = nc.vector.tensor_copy(y_sb[:, u, half * CH:(half + 1) * CH], psum[:, 5 + half, :])
                        last.then_inc(y_ready, 1)


def moe_collect(nc, tag, y, pair_row, pair_w, acc):
    with ExitStack() as ctx:
        rows = ctx.enter_context(nc.sbuf_tensor(f"{tag}_rows", [P, NT, 2, D], F32))
        rows_in, dve_order = ctx.enter_context(stage_sems(nc, f"{tag}_in", f"{tag}_dve"))
        with nc.Block() as block:
            @block.gpsimd
            def _(pool):
                for t in range(NT):
                    for c in range(2):
                        pool.indirect_dma_start(out=rows[:, t, c, :], out_offset=None, in_=y[:, :],
                                                in_offset=bass.IndirectOffsetOnAxis(ap=pair_row[:, t, c:c + 1], axis=0)).then_inc(rows_in, 16)

            @block.vector
            def _(dve):
                link = chain(dve, dve_order)
                dve.wait_ge(rows_in, 32 * NT)
                for t in range(NT):
                    link(nc.vector.tensor_scalar(acc[:, t, :], rows[:, t, 0, :], pair_w[:, t, 0:1], None, ALU.mult))
                    link(nc.vector.scalar_tensor_tensor(out=acc[:, t, :], in0=rows[:, t, 1, :], scalar=pair_w[:, t, 1:2], in1=acc[:, t, :],
                                                        op0=ALU.mult, op1=ALU.add))


def build(nc, a, out):
    dram = lambda name, shape: nc.dram_tensor(name, shape, F32, kind="Internal").ap()
    with ExitStack() as ctx:
        sb = lambda m, s: ctx.enter_context(nc.sbuf_tensor(m, s, F32))
        psum = ctx.enter_context(nc.psum_tensor("psum", [P, 8, CH], F32))
        ident, tri, iota = sb("ident", [P, P]), sb("tri", [P, P]), sb("iota", [P, P])
        tokens = ctx.enter_context(nc.sbuf_tensor("tokens", [P, NT], I32))
        h = sb("h", [P, NT, D])
        xT = [ctx.enter_context(nc.sbuf_tensor(n, [P, KD, T], F32R)) for n in ("xT_high", "xT_low")]
        with ExitStack() as st:
            (cin,) = st.enter_context(stage_sems(nc, "consts_in"))
            with nc.Block() as block:
                @block.sync
                def _(sp):
                    sp.dma_start(ident[:, :], a["c_ident"]).then_inc(cin, 16)
                    sp.dma_start(tri[:, :], a["c_tri"]).then_inc(cin, 16)
                    sp.dma_start(iota[:, :], a["c_iota"]).then_inc(cin, 16)
                    sp.dma_start(h[:, :, :], tiled(a["x"][0])).then_inc(cin, 16)
                    sp.dma_start(tokens[:, :], a["c_tokens"]).then_inc(cin, 16)
                    sp.wait_ge(cin, 80)

        u_gain = a["norm_mix_w"][0]
        norm_transpose(nc, "n1", psum, ident, h, u_gain, xT)
        proj = dram("proj", [T, IN_W])
        xbcT, convT, conv_tok = dram("xbcT", [XBC, T]), dram("convT", [XBC, T]), dram("conv_tok", [T, XBC])
        w_in = a["w_in"][0]
        linear(nc, "lz", psum, xT, KD, w_in[:, 0:D], proj[:, 0:D], D)
        linear(nc, "lx", psum, xT, KD, w_in[:, OFF_XBC:OFF_DT], xbcT, XBC, feature_major=True)
        linear(nc, "lr", psum, xT, KD, w_in[:, OFF_DT:IN_W], proj[:, OFF_DT:IN_W], IN_W - OFF_DT)
        dt, da, y_raw, y_ssd = dram("dt", [T, HEADS]), dram("da", [T, HEADS]), dram("y_raw", [T, D]), dram("y_ssd", [T, D])
        conv_silu(nc, "cv", psum, ident, xbcT, a["taps"], convT, conv_tok)
        ssd_dt(nc, "sdt", proj[:, OFF_DT:OFF_DQ], a["ssd_dt_bias"][0], a["ssd_a_log"][0], dt, da)
        ssd_scan(nc, "ssd", psum, tri, convT, conv_tok, dt, da, a["ssd_d"][0], y_raw)
        ssd_gate_norm(nc, "sgn", y_raw, proj[:, 0:D], a["ssd_norm_w"][0], y_ssd)

        qd, kd, od, lse = dram("qd", [T, 12, HD]), dram("kd", [T, 12, HD]), dram("od", [T, 12, HD]), dram("lse", [T, 12])
        with ExitStack() as st:
            cos = st.enter_context(nc.sbuf_tensor("cos1", [P, NT, 8], F32))
            sin = st.enter_context(nc.sbuf_tensor("sin1", [P, NT, 8], F32))
            rope_tables(nc, "rt1", a["positions"][0], a["c_inv1"], 8, cos, sin)
            head_prep(nc, "pdq", proj[:, OFF_DQ:OFF_DK], qd, 12, HD, a["dil_q_norm_w"][0], cos, sin, 16)
            head_prep(nc, "pdk", proj[:, OFF_DK:OFF_DV], kd, 12, HD, a["dil_k_norm_w"][0], cos, sin, 16)
        vd = proj[:, OFF_DV:OFF_MQ].rearrange("t (h d) -> t h d", d=HD)
        for g in range(DIL):
            hs = slice(g * 4, g * 4 + 4)
            span = (lambda qt: (max(0, qt - 1), qt + 1)) if g == 0 else (lambda qt: (0, qt + 1))
            attention(nc, f"da{g}", psum, ident, qd[:, hs, :], kd[:, hs, :], vd[:, hs, :], od[:, hs, :], [HD], HD, HD ** -0.5, NT,
                      mask=a["c_mask"][g], span=span, lse=lse[:, hs])
        y_dil = dram("y_dil", [T, 4 * HD])
        dil_combine(nc, "dc", od.rearrange("t h d -> t (h d)"), lse, y_dil)

        MT = N_MEM // P
        MHD = MEM_W // 4
        mkv, mk, mqn, y_mem = dram("mkv", [N_MEM, 2 * MEM_W]), dram("mk", [N_MEM, 4, MHD]), dram("mqn", [T, 4, MHD]), dram("y_mem", [T, 4, MHD])
        with ExitStack() as st:
            mem = st.enter_context(nc.sbuf_tensor("mem_sb", [P, MT, D], F32))
            memT = [st.enter_context(nc.sbuf_tensor(f"memT_{h}", [P, KD, N_MEM], F32R)) for h in ("high", "low")]
            (min_,) = st.enter_context(stage_sems(nc, "mem_in"))
            with nc.Block() as block:
                @block.sync
                def _(sp):
                    sp.dma_start(mem[:, :, :], tiled(a["mem"][0])).then_inc(min_, 16)
                    sp.wait_ge(min_, 16)
            norm_transpose(nc, "nm", psum, ident, mem, a["mem_norm_w"][0], memT, tiles=MT)
            linear(nc, "lm", psum, memT, KD, a["w_mem_kv"][0], mkv, 2 * MEM_W, tiles=MT)
        head_prep(nc, "pmk", mkv[:, 0:MEM_W], mk, 4, MHD, a["mem_k_norm_w"][0])
        head_prep(nc, "pmq", proj[:, OFF_MQ:OFF_GATE], mqn, 4, MHD, a["mem_q_norm_w"][0])
        mv = mkv[:, MEM_W:2 * MEM_W].rearrange("t (h d) -> t h d", d=MHD)
        attention(nc, "ma", psum, ident, mqn, mk, mv, y_mem, [P, MHD - P], MHD, MHD ** -0.5, MT)

        br = [dram(f"br{i}", [T, D]) for i in range(3)]
        merged, mixed = dram("merged", [T, D]), dram("mixed", [T, D])
        for i, (y, width, w) in enumerate(((y_ssd, D, a["w_ssd_br"][0]), (y_dil, 4 * HD, a["w_dil_br"][0]),
                                           (y_mem.rearrange("t h d -> t (h d)"), MEM_W, a["w_mem_br"][0]))):
            load_transpose(nc, f"bt{i}", psum, ident, y, xT, width)
            linear(nc, f"bl{i}", psum, xT, width // P, w, br[i], D)
        gated_merge(nc, "gm", proj[:, OFF_GATE:IN_W], br, merged)
        load_transpose(nc, "mt", psum, ident, merged, xT, D)
        linear(nc, "ml", psum, xT, KD, a["w_out"][0], mixed, D)
        add_residual(nc, "ar1", h, mixed)

        norm_transpose(nc, "n2", psum, ident, h, a["norm_ffn_w"][0], xT)
        qT, sel, gates = dram("peer_qT", [2 * P * PEER_H, T]), dram("peer_sel", [T, 3, P]), dram("peer_gates", [NT, NK, NK, P])
        linear(nc, "pq", psum, xT, KD, a["peer_w_query"][0], qT, 2 * P * PEER_H, feature_major=True)
        mods = dram("mods", [LAYERS, 1, 6 * D])
        peer_route(nc, "pr", psum, qT, a["keysT"], iota[:, 0:TOPK], sel, a["c_2"][0], a["ada_w_2"], mods)
        with ExitStack() as st:
            selT = st.enter_context(nc.sbuf_tensor("selT", [P, 3, T], F32))
            with ExitStack() as turn:
                halves = [turn.enter_context(nc.sbuf_tensor(f"selT_{h}", [P, 3, T], F32R)) for h in ("high", "low")]
                load_transpose(nc, "pst", psum, ident, sel.rearrange("t a k -> t (a k)"), halves, 3 * P)
                join_halves(nc, "psj", halves, selT)
            peer_gates(nc, "pg", psum, selT, iota[:, :], gates)

        def add_acc(tag, acc, gate=None):
            with ExitStack() as st:
                gs = st.enter_context(nc.sbuf_tensor(f"{tag}_g", [P, D], F32))
                gin, order = st.enter_context(stage_sems(nc, f"{tag}_gin", f"{tag}_ord"))
                with nc.Block() as block:
                    @block.sync
                    def _(sp):
                        if gate is not None:
                            sp.dma_start(gs[:, :], row_bc(gate)).then_inc(gin, 16)

                    @block.vector
                    def _(dve):
                        link = chain(dve, order)
                        if gate is not None:
                            dve.wait_ge(gin, 16)
                        for t in range(NT):
                            if gate is not None:
                                link(nc.vector.tensor_tensor(acc[:, t, :], acc[:, t, :], gs[:, :], ALU.mult))
                            link(nc.vector.tensor_tensor(h[:, t, :], h[:, t, :], acc[:, t, :], ALU.add))

        downT = a["downT"].rearrange("(k p) e -> p k e", p=P)
        up = a["peer_up"][0].rearrange("(f p) d -> p f d", p=P)
        with ExitStack() as st:
            acc = st.enter_context(nc.sbuf_tensor("peer_acc", [P, NT, D], F32))
            peer_experts(nc, "pf", psum, xT, acc, downT, up, gates)
            add_acc("pa", acc)

        adaptive_bias(nc, "ada", a["ada_b_2"], mods)
        cos = sb("cos2", [P, NT, 32])
        sin = sb("sin2", [P, NT, 32])
        rope_tables(nc, "rt2", a["positions_2"][0], a["c_inv2"], 32, cos, sin)
        proj2, gates2, h2 = dram("proj2", [T, D_IN2]), dram("gates2", [T, 3 * D]), None
        rq, rk, ro, ya = dram("rq", [T, 4, 64]), dram("rk", [T, 4, 64]), dram("ro", [T, 512]), dram("ya", [T, 512])
        qa, ka, yb = dram("qa", [T, 4, 130]), dram("ka", [T, 4, 130]), dram("yb", [T, 4, 128])
        qh, qr, kvh, kp, kc, yc = (dram("qh", [T, 768]), dram("qr", [T, 4, 192]), dram("kvh", [T, 1024]), dram("kp", [T, 1, 64]),
                                   dram("kc", [T, 4, 192]), dram("yc", [T, 4, 128]))
        logits, h_norm, y_exp = dram("logits", [T, 36]), dram("h_norm", [T, D]), dram("y_exp", [N_EXPERTS * P, D])
        table = nc.dram_tensor("table", [N_EXPERTS * P, 1], I32, kind="Internal").ap()
        causal = lambda qt: (0, qt + 1)
        for l in range(LAYERS):
            mod = [mods[l][0, i * D:(i + 1) * D] for i in range(6)]
            norm_transpose(nc, f"m{l}", psum, ident, h, a["norm1_g_2"][l], xT, shift=mod[0], scale=mod[1])
            linear(nc, f"i{l}", psum, xT, KD, a["w_in_2"][l], proj2, D_IN2)
            linear(nc, f"g{l}", psum, xT, KD, a["gate_w_2"][l], gates2, 3 * D)
            head_prep(nc, f"rq{l}", proj2[:, RQ:RK], rq, 4, 64, None, cos, sin, 64)
            head_prep(nc, f"rk{l}", proj2[:, RK:RV], rk, 4, 64, None, cos, sin, 64)
            retention(nc, f"re{l}", psum, ident, rq.rearrange("t h d -> t (h d)"), rk.rearrange("t h d -> t (h d)"), proj2[:, RV:RG],
                      (a["c_dmask"], a["c_decay"]), ro)
            retention_gate_norm(nc, f"rn{l}", ro, proj2[:, RG:FQ], ya)
            fox_prep(nc, f"fp{l}", psum, tri, proj2, a["fox_fb_2"][l], qa, ka)
            fv = proj2[:, FV:FF].rearrange("t (h d) -> t h d", h=4)
            attention(nc, f"fa{l}", psum, ident, qa, ka, fv, yb, [P, 2], P, P ** -0.5, NT, mask=a["c_mask"][3], span=causal)
            with ExitStack() as st:
                lat = st.enter_context(nc.sbuf_tensor(f"lat{l}", [P, NT, 384], F32))
                latT = [st.enter_context(nc.sbuf_tensor(f"latT{l}_{h}", [P, 2, T], F32R)) for h in ("high", "low")]
                (lin,) = st.enter_context(stage_sems(nc, f"lat_in{l}"))
                with nc.Block() as block:
                    @block.sync
                    def _(sp):
                        sp.dma_start(lat[:, :, :], tiled(proj2)[:, :, MQ2:MKR]).then_inc(lin, 16)
                        sp.wait_ge(lin, 16)
                norm_transpose(nc, f"nq{l}", psum, ident, lat[:, :, 0:256], a["mla_q_norm_g_2"][l], latT, width=256)
                linear(nc, f"lq{l}", psum, latT, 2, a["mla_wq_up_2"][l], qh, 768)
                norm_transpose(nc, f"nk{l}", psum, ident, lat[:, :, 256:384], a["mla_kv_norm_g_2"][l], latT, width=128)
                linear(nc, f"lk{l}", psum, latT, 1, a["mla_wkv_up_2"][l], kvh, 1024)
            head_prep(nc, f"hq{l}", qh, qr, 4, 192, None, cos, sin, 64, 128)
            head_prep(nc, f"hk{l}", proj2[:, MKR:D_IN2], kp, 1, 64, None, cos, sin, 64)
            kv = kvh.rearrange("t (h d) -> t h d", h=4)
            copy_pieces(nc, f"kc{l}", [(kc[:, :, 0:P], kv[:, :, 0:P])] + [(kc[:, i:i + 1, P:P + 64], kp) for i in range(4)])
            attention(nc, f"la{l}", psum, ident, qr, kc, kv[:, :, P:2 * P], yc, [P, 64], P, 192 ** -0.5, NT, mask=a["c_mask"][3], span=causal)
            for i, y in enumerate((ya, yb.rearrange("t h d -> t (h d)"), yc.rearrange("t h d -> t (h d)"))):
                load_transpose(nc, f"bt{l}{i}", psum, ident, y, xT, 512)
                linear(nc, f"bl{l}{i}", psum, xT, 4, a["branch_w_2"][l, i], br[i], D)
            gated_merge(nc, f"gm{l}", gates2, br, merged, bias=a["gate_b_2"][l])
            load_transpose(nc, f"mt{l}", psum, ident, merged, xT, D)
            linear(nc, f"ml{l}", psum, xT, KD, a["out_w_2"][l], mixed, D)
            add_residual(nc, f"as{l}", h, mixed, gate=mod[2])
            norm_transpose(nc, f"k{l}", psum, ident, h, a["norm2_g_2"][l], xT, shift=mod[3], scale=mod[4], keep=h_norm)
            linear(nc, f"rl{l}", psum, xT, KD, a["router_w"][l], logits, 36)
            with ExitStack() as st:
                sbt = lambda m, s, d=F32: st.enter_context(nc.sbuf_tensor(f"{m}{l}", s, d))
                token_w, acc = sbt("token_w", [P, NT, N_EXPERTS]), sbt("moe_acc", [P, NT, D])
                pair_w, pair_row = sbt("pair_w", [P, NT, 2]), sbt("pair_row", [P, NT, 2], U32)
                crowded, slot_token = sbt("crowded", [P, 1], I32), sbt("slot_token", [P, N_EXPERTS], U32)
                moe_route(nc, f"mr{l}", psum, tri, logits, a["router_b"][l], iota, token_w, pair_w, pair_row, crowded)
                w1, w3 = (a[n][l].rearrange("e (k p) f -> p (e k) f", p=P) for n in ("exp_w1_2", "exp_w3_2"))
                w2 = a["exp_w2_2"][l].rearrange("e (f p) d -> p (e f) d", p=P)
                take_w1, take_w3 = (lambda e: w1[:, ds(e * KD, KD), :]), (lambda e: w3[:, ds(e * KD, KD), :])
                take_w2 = lambda e: w2[:, ds(e * 4, 4), :]
                (col_ready,) = st.enter_context(stage_sems(nc, f"col{l}"))
                over = nc.values_load(crowded[0:1, 0:1], min_val=0, max_val=1)
                with nc.If(over == 1):
                    moe_dense(nc, f"mf{l}", psum, xT, acc, N_EXPERTS, take_w1, take_w2, take_w3, token_w)
                with nc.Else():
                    moe_slots(nc, f"ms{l}", psum, ident, tokens, pair_row, table, slot_token)
                    moe_experts(nc, f"me{l}", psum, ident, h_norm, slot_token, take_w1, take_w3, take_w2, y_exp, col_ready)
                    moe_collect(nc, f"mc{l}", y_exp, pair_row, pair_w, acc)
                add_acc(f"aa{l}", acc, gate=mod[5])

        norm_transpose(nc, "nf", psum, ident, h, a["final_g_2"], xT, keep=out[0])


_INPUTS = ("x", "mem", "positions", "norm_mix_w", "w_in", "ssd_dt_bias", "ssd_a_log", "ssd_d", "ssd_norm_w", "dil_q_norm_w",
           "dil_k_norm_w", "mem_norm_w", "w_mem_kv", "mem_q_norm_w", "mem_k_norm_w", "w_ssd_br", "w_dil_br", "w_mem_br", "w_out",
           "norm_ffn_w", "peer_w_query", "peer_up", "c_2", "positions_2", "ada_w_2", "ada_b_2", "norm1_g_2", "norm2_g_2",
           "w_in_2", "fox_fb_2", "mla_q_norm_g_2", "mla_wq_up_2", "mla_kv_norm_g_2", "mla_wkv_up_2", "gate_w_2", "gate_b_2",
           "branch_w_2", "out_w_2", "exp_w1_2", "exp_w3_2", "exp_w2_2", "final_g_2")


def shape_constants():
    f = np.float32
    i = np.arange(P)
    t = np.arange(T)
    dist = t[:, None] - t[None, :]
    seen = [(dist >= 0) & (dist <= 128), (dist >= 0) & (dist % 4 == 0), (dist >= 0) & (dist % 16 == 0), dist >= 0]
    log_gamma = np.log1p(-np.exp2(-5.0 - np.arange(4)))
    rel = i[None, :] - i[:, None]
    dmask = np.where(rel[:, None, :] >= 0, np.exp(log_gamma[None, :, None] * np.maximum(rel, 0)[:, None, :]), 0.0) * 64 ** -0.5
    decay = np.stack([np.exp(log_gamma[None, :] * (i[:, None] + 1.0)), np.exp(log_gamma[None, :] * (P - 1.0 - i[:, None])) * 64 ** -0.5,
                      np.broadcast_to(np.exp(log_gamma * P), (P, 4))], axis=1)
    return {
        "c_ident": np.eye(P, dtype=f), "c_tri": (i[:, None] <= i[None, :]).astype(f),
        "c_iota": np.broadcast_to(np.arange(P, dtype=f), (P, P)).copy(),
        "c_mask": np.stack([np.where(s, 0.0, NEG) for s in seen]).astype(f),
        "c_inv1": np.exp(f(-math.log(500000.0)) * f(2.0 / 16) * np.arange(8, dtype=f)).astype(f),
        "c_inv2": (10000.0 ** (-np.arange(0, 64, 2) / 64.0)).astype(f),
        "c_tokens": (i[:, None] + P * np.arange(NT)[None, :]).astype(np.int32),
        "c_dmask": dmask.reshape(P, 4 * P).astype(f), "c_decay": decay.reshape(P, 12).astype(f),
    }


def kernel(**inputs):
    import concourse.bacc as bacc
    from concourse.bass_utils import run_bass_kernel_spmd

    arrays = {n: np.ascontiguousarray(inputs[n]) for n in _INPUTS}
    arrays["taps"] = np.ascontiguousarray(np.concatenate([inputs["ssd_conv_w"][0], inputs["ssd_conv_b"]], axis=0).T)
    arrays["keysT"] = np.ascontiguousarray(np.transpose(inputs["peer_sub_keys"][0], (0, 1, 3, 2)).reshape(2 * P * PEER_H, NK))
    arrays["downT"] = np.ascontiguousarray(inputs["peer_down"][0].T)
    arrays["router_w"] = np.ascontiguousarray(np.concatenate([inputs["router_grp_w_2"], inputs["router_exp_w_2"]], axis=2))
    arrays["router_b"] = np.ascontiguousarray(np.concatenate([inputs["router_grp_b_2"], inputs["router_exp_b_2"]], axis=1))
    arrays.update(shape_constants())

    nc = bacc.Bacc("TRN2", target_bir_lowering=False, num_devices=1)
    aps = {n: nc.dram_tensor(f"in_{n}", v.shape, mybir.dt.from_np(v.dtype), kind="ExternalInput").ap() for n, v in arrays.items()}
    out = nc.dram_tensor("out_0", (1, T, D), F32, kind="ExternalOutput").ap()
    build(nc, aps, out)
    result = run_bass_kernel_spmd(nc, [{f"in_{n}": v for n, v in arrays.items()}], core_ids=[0])
    return result.results[0]["out_0"]
```

```python
import math
from contextlib import ExitStack, contextmanager

import numpy as np

import concourse.bass as bass
from concourse import mybir

F32 = mybir.dt.float32
F32R = mybir.dt.float32r
I32 = mybir.dt.int32
U32 = mybir.dt.uint32
ALU = mybir.AluOpType
ACT = mybir.ActivationFunctionType
AX = mybir.AxisListType.X
ds = bass.ds

P = 128
T = 512
NT = T // P
D = 1024
KD = D // P
CH = 512
EPS = 1e-6
NEG = -1e30

N_MEM = 256
HEADS, GROUPS, HPG, HD, STATE = 16, 4, 4, 64, 128
CONV = 4
XBC = D + 2 * GROUPS * STATE
DIL = 3
DIL_W = 768
MEM_W = 768
OFF_Z, OFF_XBC = 0, D
OFF_DT = OFF_XBC + XBC
OFF_DQ = OFF_DT + HEADS
OFF_DK, OFF_DV, OFF_MQ = OFF_DQ + DIL_W, OFF_DQ + 2 * DIL_W, OFF_DQ + 3 * DIL_W
OFF_GATE = OFF_MQ + MEM_W
IN_W = OFF_GATE + 3 * D
PEER_H, NK, TOPK = 8, 128, 16
N_EXP1 = NK * NK
LAYERS = 2
D_IN2 = 3524
RQ, RK, RV, RG, FQ, FK, FV, FF, MQ2, MKV, MKR = (0, 256, 512, 1024, 1536, 2048, 2560, 3072, 3076, 3332, 3460)
N_EXPERTS, EPG, N_GRP, D_EXP = 32, 8, 4, 512


@contextmanager
def stage_sems(nc, *names):
    sems = [nc.alloc_semaphore(n) for n in names]
    yield sems
    nc.clear_and_free_semaphores(sems)
    nc.all_engine_barrier()


def chain(eng, sem):
    count = [0]

    def link(ins):
        count[0] += 1
        ins.then_inc(sem, 1)
        eng.wait_ge(sem, count[0])

    return link


def refined_root(nc, link, r, mean, tmp):
    link(nc.vector.reciprocal(r, r))
    link(nc.vector.tensor_tensor(tmp, r, r, ALU.mult))
    link(nc.vector.tensor_tensor(tmp, tmp, mean, ALU.mult))
    link(nc.vector.tensor_scalar(tmp, tmp, -0.5, 1.5, ALU.mult, ALU.add))
    link(nc.vector.tensor_tensor(r, r, tmp, ALU.mult))


def times(nc, out, lhsT, rhs, first=True, last=True):
    (lh, ll), (rh, rl) = lhsT, rhs
    nc.tensor.matmul(out, lh, rh, start=first, stop=False)
    nc.tensor.matmul(out, lh, rl, start=False, stop=False)
    return nc.tensor.matmul(out, ll, rh, start=False, stop=last)


def take_bank(nc, bank, ident):
    nc.tensor.transpose(bank, ident[:, :], ident[:, :])


def tiled(x):
    return x.rearrange("(t p) n -> p t n", p=P)


def row_bc(row, parts=P):
    return row.rearrange("(o n) -> o n", o=1).broadcast_to([parts, row.shape[0]])


def bc_mid(ap, n):
    return ap.rearrange("p (o a) -> p o a", o=1).broadcast_to([ap.shape[0], n, ap.shape[1]])


def bc_last(ap, n):
    return ap.rearrange("p (a o) -> p a o", o=1).broadcast_to([ap.shape[0], ap.shape[1], n])


def linear(nc, tag, psum, x, kc, w, out, n_cols, tiles=NT, feature_major=False, before=None, into=None, beside=()):
    full, tail = n_cols // CH, n_cols % CH
    w_v = w.rearrange("(k p) n -> p k n", p=P)
    blocks = CH // P if feature_major else tiles
    width = tiles * P if feature_major else CH
    with ExitStack() as ctx:
        wbuf = ctx.enter_context(nc.sbuf_tensor(f"{tag}_w", [P, 2, kc, CH], F32))
        w_high = ctx.enter_context(nc.sbuf_tensor(f"{tag}_wh", [P, 2, kc, CH], F32R))
        w_low = ctx.enter_context(nc.sbuf_tensor(f"{tag}_wl", [P, 2, kc, CH], F32R))
        obuf = None if into else ctx.enter_context(nc.sbuf_tensor(f"{tag}_o", [P, 2, 4, CH], F32))
        pieces = max(1, kc // 2)
        rows = [slice(q * kc // pieces, (q + 1) * kc // pieces) for q in range(pieces)]
        (high_ready, low_ready, tile_done, evac_v, evac_a, out0, out1, *more) = ctx.enter_context(stage_sems(
            nc, *[f"{tag}_{s}" for s in ("high", "low", "tile", "ev", "ea", "out0", "out1", *(f"w_in{u}{q}" for u in range(2) for q in range(pieces)),
                                         *(before.names if before else ()), *(into.names if into else ()),
                                         *(f"{p.tag}_{s}" for p in beside for s in p.names))]))
        for p in reversed(beside):
            p.place(ctx, more[-len(p.names):])
            more = more[:-len(p.names)]
        w_sems = more[:2 * pieces]
        if before:
            before.place(ctx, more[2 * pieces:2 * pieces + len(before.names)])
        if into:
            into.place(ctx, more[len(more) - len(into.names):], evac_v)
        w_in, stored = (w_sems[0:pieces], w_sems[pieces:]), (out0, out1)
        pairs, odd = full // 2, full % 2
        on_v = blocks if into else (blocks + 1) // 2
        on_a = blocks - on_v
        chunk_cols = [CH] * full + [tail] * bool(tail)

        def chunks(eng, body):
            if pairs:
                with eng.Fori(0, pairs) as i:
                    for u in range(2):
                        body(i * 2 + u, u, i, CH)
            if odd:
                body(full - 1, 0, pairs, CH)
            if tail:
                body(full, odd, pairs, tail)

        def ahead(eng, first, second, preps=lambda: None):
            n = len(chunk_cols)
            first(0, 0, 0, chunk_cols[0])
            preps()
            steady = max(0, (full - 2) // 2)
            if steady:
                with eng.Fori(0, steady) as i:
                    for u in range(2):
                        first(i * 2 + (u + 1), 1 - u, i + u, CH)
                        second(i * 2 + u, u, i, CH)
            for j in range(2 * steady, n):
                if j + 1 < n:
                    first(j + 1, (j + 1) % 2, (j + 1) // 2, chunk_cols[j + 1])
                second(j, j % 2, j // 2, chunk_cols[j])

        with nc.Block() as block:
            @block.sync
            def _(sp):
                def load(j, u, turn, cols):
                    for q, ks in enumerate(rows):
                        sp.wait_ge(low_ready, j * pieces + (q + 1))
                        sp.dma_start(wbuf[:, u, ks, 0:cols], w_v[:, ks, ds(j * CH, cols)]).then_inc(w_in[u][q], 16)
                if before:
                    before.sync(sp)
                if into:
                    into.sync(sp)
                chunks(sp, load)
                if before:
                    before.finish(sp)

            @block.tensor
            def _(pe):
                pe.sem_inc(tile_done, 2 * blocks)
                starts = [ks.start for ks in rows]

                def multiply(j, u, turn, cols):
                    pe.wait_ge(evac_v, j * on_v + on_v)
                    if on_a:
                        pe.wait_ge(evac_a, j * on_a + on_a)
                    for b in range(blocks):
                        for k in range(kc):
                            if b == 0 and k in starts:
                                pe.wait_ge(low_ready, j * pieces + (2 * pieces + starts.index(k) + 1))
                            if feature_major:
                                last = times(nc, psum[:, u * 4 + b, 0:width], [v[:, u, k, b * P:(b + 1) * P] for v in (w_high, w_low)],
                                             [v[:, k, 0:width] for v in x], k == 0, k == kc - 1)
                            else:
                                last = times(nc, psum[:, u * 4 + b, 0:cols], [v[:, k, b * P:(b + 1) * P] for v in x],
                                             [v[:, u, k, 0:cols] for v in (w_high, w_low)], k == 0, k == kc - 1)
                        last.then_inc(tile_done, 1)
                if before:
                    before.tensor(pe)
                    pe.wait_ge(before.evacuated, kc)
                chunks(pe, multiply)

            @block.vector
            def _(dve):
                dve.sem_inc(evac_v, 2 * on_v)

                def make_low(j, u, turn, cols):
                    for q, ks in enumerate(rows):
                        dve.wait_ge(high_ready, j * pieces + (q + 1))
                        nc.vector.tensor_tensor(w_low[:, u, ks, 0:cols], wbuf[:, u, ks, 0:cols], w_high[:, u, ks, 0:cols].bitcast(F32),
                                                ALU.subtract).then_inc(low_ready, 1)

                def evacuate(j, u, turn, cols):
                    if into:
                        if j == 0:
                            into.vector(dve)
                        for b in range(blocks):
                            dve.wait_ge(tile_done, (j + 2) * blocks + (b + 1))
                            into.take(dve, psum[:, u * 4 + b, 0:cols], b, slice(j * CH, j * CH + cols), j * blocks + b + 2 * on_v)
                        return
                    dve.wait_ge(stored[u], turn * 16 + 16)
                    n = width if feature_major else cols
                    for b in range(on_v):
                        dve.wait_ge(tile_done, j * blocks + (2 * blocks + b + 1))
                        nc.vector.tensor_copy(obuf[:, u, b, 0:n], psum[:, u * 4 + b, 0:n]).then_inc(evac_v, 1)

                dve.sem_inc(low_ready, 2 * pieces)
                if before:
                    before.vector(dve)
                ahead(dve, make_low, evacuate, lambda: [p.vector(dve) for p in beside])

            @block.gpsimd
            def _(pool):
                for p in beside:
                    p.load(pool)
                for p in beside:
                    p.store(pool)

            @block.scalar
            def _(act):
                act.sem_inc(evac_a, 2 * on_a) if on_a else None
                act.sem_inc(out0, 16)
                act.sem_inc(out1, 16)

                def make_high(j, u, turn, cols):
                    act.wait_ge(tile_done, j * blocks + blocks)
                    for q, ks in enumerate(rows):
                        act.wait_ge(w_in[u][q], turn * 16 + 16)
                        nc.scalar.copy(w_high[:, u, ks, 0:cols], wbuf[:, u, ks, 0:cols]).then_inc(high_ready, 1)

                def evacuate_store(j, u, turn, cols):
                    if into:
                        if j == 0:
                            into.scalar(act)
                        return
                    act.wait_ge(stored[u], turn * 16 + 16)
                    n = width if feature_major else cols
                    for b in range(on_v, blocks):
                        act.wait_ge(tile_done, j * blocks + (2 * blocks + b + 1))
                        nc.scalar.copy(obuf[:, u, b, 0:n], psum[:, u * 4 + b, 0:n]).then_inc(evac_a, 1)
                    act.wait_ge(evac_v, j * on_v + 3 * on_v)
                    if on_a:
                        act.wait_ge(evac_a, j * on_a + 3 * on_a)
                    if feature_major:
                        dst = out[ds(j * CH, CH), 0:width].rearrange("(b p) t -> p b t", p=P)
                        src = obuf[:, u, :, 0:width]
                    else:
                        dst, src = tiled(out)[:, :, ds(j * CH, cols)], obuf[:, u, 0:tiles, 0:cols]
                    act.dma_start(dst, src).then_inc(stored[u], 16)

                if before:
                    before.scalar(act)
                ahead(act, make_high, evacuate_store, lambda: [p.scalar(act) for p in beside])
                last = [0, 0]
                for j in range(0 if into else full + bool(tail)):
                    last[j % 2] += 16
                act.wait_ge(out0, last[0] + 16)
                act.wait_ge(out1, last[1] + 16)


class Sum:
    names = ()

    def __init__(self, nc, tag, target):
        self.nc, self.tag, self.target = nc, tag, target

    def place(self, ctx, sems, taken):
        self.taken = taken

    def sync(self, sp):
        pass

    def vector(self, dve):
        pass

    def scalar(self, act):
        pass

    def take(self, dve, product, b, cols, before):
        dst = self.target[:, b, cols]
        self.nc.vector.tensor_tensor(dst, dst, product, ALU.add).then_inc(self.taken, 1)


class ScaledSum(Sum):
    names = ("rowin",)

    def __init__(self, nc, tag, target, row):
        super().__init__(nc, tag, target)
        self.row, self.first = row, False

    def place(self, ctx, sems, taken):
        self.taken = taken
        (self.row_in,) = sems
        self.row_sb = ctx.enter_context(self.nc.sbuf_tensor(f"{self.tag}_row", [P, D], F32))
        self.scaled = ctx.enter_context(self.nc.sbuf_tensor(f"{self.tag}_sc", [P, 2, CH], F32))

    def sync(self, sp):
        sp.dma_start(self.row_sb[:, :], row_bc(self.row)).then_inc(self.row_in, 16)

    def vector(self, dve):
        dve.wait_ge(self.row_in, 16)

    def factor(self, b, cols):
        return self.row_sb[:, cols]

    def take(self, dve, product, b, cols, before):
        nc, dst = self.nc, self.target[:, b, cols]
        if self.first:
            nc.vector.tensor_tensor(dst, product, self.factor(b, cols), ALU.mult).then_inc(self.taken, 1)
            return
        scaled = self.scaled[:, b % 2, 0:cols.stop - cols.start]
        nc.vector.tensor_tensor(scaled, product, self.factor(b, cols), ALU.mult).then_inc(self.taken, 1)
        dve.wait_ge(self.taken, before + 1)
        nc.vector.tensor_tensor(dst, dst, scaled, ALU.add)


class GatedSum(ScaledSum):
    names = ("gin", "gbias", "gsig")

    def __init__(self, nc, tag, target, gates, bias, first):
        Sum.__init__(self, nc, tag, target)
        self.gates, self.bias, self.first = gates, bias, first

    def place(self, ctx, sems, taken):
        sb = lambda m, s: ctx.enter_context(self.nc.sbuf_tensor(f"{self.tag}_{m}", s, F32))
        self.taken = taken
        self.gates_in, self.biased, self.sig_ready = sems
        self.g = sb("g", [P, NT, D])
        self.bias_sb = sb("bi", [P, D]) if self.bias is not None else None
        self.scaled = sb("sc", [P, 2, CH])

    def sync(self, sp):
        sp.dma_start(self.g[:, :, :], tiled(self.gates)).then_inc(self.gates_in, 16)
        if self.bias is not None:
            sp.dma_start(self.bias_sb[:, :], row_bc(self.bias)).then_inc(self.gates_in, 16)

    def vector(self, dve):
        if self.bias is not None:
            dve.wait_ge(self.gates_in, 32)
            self.nc.vector.tensor_tensor(self.g[:, :, :], self.g[:, :, :], bc_mid(self.bias_sb[:, :], NT), ALU.add).then_inc(self.biased, 1)
        dve.wait_ge(self.sig_ready, 1)

    def scalar(self, act):
        if self.bias is not None:
            act.wait_ge(self.biased, 1)
        else:
            act.wait_ge(self.gates_in, 16)
        self.nc.scalar.activation(self.g[:, :, :], self.g[:, :, :], ACT.Sigmoid).then_inc(self.sig_ready, 1)

    def factor(self, b, cols):
        return self.g[:, b, cols]


class Turn:

    def __init__(self, nc, tag, psum, ident, xT, width, tiles):
        self.nc, self.tag, self.psum, self.ident, self.xT = nc, tag, psum, ident, xT
        self.width, self.tiles, self.kc = width, tiles, width // P

    def turn(self, pe, y):
        nc = self.nc
        for k in range(self.kc):
            if k >= 4:
                pe.wait_ge(self.evacuated, k - 3)
            for t in range(self.tiles):
                last = nc.tensor.transpose(self.psum[:, k % 4, t * P:(t + 1) * P], y[:, t, k * P:(k + 1) * P], self.ident[:, :])
            last.then_inc(self.turned, 1)

    def take_high(self, act):
        n = self.tiles * P
        for k in range(self.kc):
            act.wait_ge(self.turned, k + 1)
            self.nc.scalar.copy(self.xT[0][:, k, 0:n], self.psum[:, k % 4, 0:n]).then_inc(self.high_ready, 1)

    def take_low(self, dve):
        n = self.tiles * P
        for k in range(self.kc):
            dve.wait_ge(self.high_ready, k + 1)
            self.nc.vector.tensor_tensor(self.xT[1][:, k, 0:n], self.psum[:, k % 4, 0:n], self.xT[0][:, k, 0:n].bitcast(F32),
                                         ALU.subtract).then_inc(self.evacuated, 1)


class LoadTurn(Turn):
    names = ("tin", "turned", "thigh", "tev")

    def __init__(self, nc, tag, psum, ident, src, xT, width, tiles=NT):
        super().__init__(nc, tag, psum, ident, xT, width, tiles)
        self.src = src

    def place(self, ctx, sems):
        self.x = ctx.enter_context(self.nc.sbuf_tensor(f"{self.tag}_x", [P, self.tiles, self.width], F32))
        self.x_in, self.turned, self.high_ready, self.evacuated = sems

    def sync(self, sp):
        sp.dma_start(self.x[:, :, :], tiled(self.src)).then_inc(self.x_in, 16)

    def finish(self, sp):
        pass

    def tensor(self, pe):
        pe.wait_ge(self.x_in, 16)
        self.turn(pe, self.x)

    def vector(self, dve):
        self.take_low(dve)

    def scalar(self, act):
        self.take_high(act)


class HeldTurn(Turn):
    names = ("turned", "thigh", "tev")

    def __init__(self, nc, tag, psum, ident, x, xT, width, tiles=NT):
        super().__init__(nc, tag, psum, ident, xT, width, tiles)
        self.x = x

    def place(self, ctx, sems):
        self.turned, self.high_ready, self.evacuated = sems

    def sync(self, sp):
        pass

    def finish(self, sp):
        pass

    def tensor(self, pe):
        self.turn(pe, self.x)

    def vector(self, dve):
        self.take_low(dve)

    def scalar(self, act):
        self.take_high(act)


class NormTurn(Turn):
    names = ("rows", "mean", "root", "ny", "turned", "thigh", "tev", "ndve", "kept")

    def __init__(self, nc, tag, psum, ident, x, gain, xT, tiles=NT, width=D, shift=None, scale=None, keep=None):
        super().__init__(nc, tag, psum, ident, xT, width, tiles)
        self.x, self.gain, self.shift, self.scale, self.keep = x, gain, shift, scale, keep

    def place(self, ctx, sems):
        sb = lambda n, s: ctx.enter_context(self.nc.sbuf_tensor(f"{self.tag}_{n}", s, F32))
        width, tiles = self.width, self.tiles
        self.gain_sb, self.y = sb("gain", [P, width]), sb("y", [P, tiles, width])
        self.sq, self.stat = sb("sq", [P, width]), sb("stat", [P, tiles, 4])
        self.shift_sb = sb("shift", [P, width]) if self.shift is not None else None
        self.scale_sb = sb("scale", [P, width]) if self.shift is not None else None
        (self.rows_in, self.mean_ready, self.root_ready, self.y_ready, self.turned, self.high_ready, self.evacuated, self.dve_order,
         self.kept) = sems

    def sync(self, sp):
        sp.dma_start(self.gain_sb[:, :], row_bc(self.gain)).then_inc(self.rows_in, 16)
        if self.shift is not None:
            sp.dma_start(self.shift_sb[:, :], row_bc(self.shift)).then_inc(self.rows_in, 16)
            sp.dma_start(self.scale_sb[:, :], row_bc(self.scale)).then_inc(self.rows_in, 16)

    def finish(self, sp):
        if self.keep is not None:
            sp.wait_ge(self.kept, 16)

    def vector(self, dve):
        nc, x, y, stat, width = self.nc, self.x, self.y, self.stat, self.width
        link = chain(dve, self.dve_order)
        for t in range(self.tiles):
            link(nc.vector.tensor_tensor_reduce(out=self.sq[:, :], in0=x[:, t, :], in1=x[:, t, :], scale=1.0, scalar=0.0,
                                                op0=ALU.mult, op1=ALU.add, accum_out=stat[:, t, 0:1]))
            nc.vector.tensor_scalar(stat[:, t, 1:2], stat[:, t, 0:1], 1.0 / width, EPS, ALU.mult, ALU.add).then_inc(self.mean_ready, 1)
        dve.wait_ge(self.rows_in, 48 if self.shift is not None else 16)
        if self.shift is not None:
            link(nc.vector.tensor_scalar(self.scale_sb[:, :], self.scale_sb[:, :], 1.0, None, ALU.add))
            link(nc.vector.tensor_tensor(self.gain_sb[:, :], self.gain_sb[:, :], self.scale_sb[:, :], ALU.mult))
        for t in range(self.tiles):
            dve.wait_ge(self.root_ready, t + 1)
            refined_root(nc, link, stat[:, t, 2:3], stat[:, t, 1:2], stat[:, t, 3:4])
            ins = nc.vector.scalar_tensor_tensor(out=y[:, t, :], in0=x[:, t, :], scalar=stat[:, t, 2:3],
                                                 in1=self.gain_sb[:, :], op0=ALU.mult, op1=ALU.mult)
            if self.shift is not None:
                link(ins)
                ins = nc.vector.tensor_tensor(y[:, t, :], y[:, t, :], self.shift_sb[:, :], ALU.add)
            ins.then_inc(self.y_ready, 1)
        self.take_low(dve)

    def scalar(self, act):
        nc, stat = self.nc, self.stat
        for t in range(self.tiles):
            act.wait_ge(self.mean_ready, t + 1)
            nc.scalar.activation(stat[:, t, 2:3], stat[:, t, 1:2], ACT.Sqrt).then_inc(self.root_ready, 1)
        if self.keep is not None:
            act.wait_ge(self.y_ready, self.tiles)
            act.dma_start(tiled(self.keep), self.y[:, :, :]).then_inc(self.kept, 16)
        self.take_high(act)

    def tensor(self, pe):
        pe.wait_ge(self.y_ready, self.tiles)
        self.turn(pe, self.y)


def turn_only(nc, turn):
    with ExitStack() as ctx:
        turn.place(ctx, ctx.enter_context(stage_sems(nc, *[f"{turn.tag}_{s}" for s in turn.names])))
        with nc.Block() as block:
            @block.sync
            def _(sp):
                turn.sync(sp)
                turn.finish(sp)

            @block.tensor
            def _(pe):
                turn.tensor(pe)

            @block.vector
            def _(dve):
                turn.vector(dve)

            @block.scalar
            def _(act):
                turn.scalar(act)


def join_halves(nc, tag, halves, x):
    (joined,) = nc_sems = [nc.alloc_semaphore(f"{tag}_j")]
    with nc.Block() as block:
        @block.vector
        def _(dve):
            nc.vector.tensor_tensor(x[:, :, :], halves[0][:, :, :].bitcast(F32), halves[1][:, :, :].bitcast(F32), ALU.add).then_inc(joined, 1)
            dve.wait_ge(joined, 1)
    nc.clear_and_free_semaphores(nc_sems)
    nc.all_engine_barrier()


def conv_silu(nc, tag, psum, ident, xbcT, taps, convT, conv_tok):
    n = XBC // P
    PAD = CONV - 1
    with ExitStack() as ctx:
        sb = lambda m, s: ctx.enter_context(nc.sbuf_tensor(f"{tag}_{m}", s, F32))
        x, w, acc = sb("x", [P, 2, PAD + T]), sb("w", [P, 2, CONV + 1]), sb("acc", [P, 2, T])
        y, tok = sb("y", [P, 2, T]), sb("tok", [P, 2, NT, P])
        (in0, in1, acc_ready, y_ready, transposed, tok_ready, dve_order, out0, out1, padded) = ctx.enter_context(stage_sems(
            nc, *[f"{tag}_{s}" for s in ("in0", "in1", "acc", "y", "tr", "tok", "dve", "out0", "out1", "pad")]))
        loaded, stored = (in0, in1), (out0, out1)
        with nc.Block() as block:
            @block.sync
            def _(sp):
                sp.wait_ge(padded, 1)
                with sp.Fori(0, n // 2) as i:
                    for u in range(2):
                        sp.wait_ge(acc_ready, i * 2 + u + 1)
                        sp.dma_start(x[:, u, PAD:PAD + T], xbcT[ds((i * 2 + u) * P, P), :]).then_inc(loaded[u], 16)
                        sp.dma_start(w[:, u, :], taps[ds((i * 2 + u) * P, P), :]).then_inc(loaded[u], 16)

            @block.vector
            def _(dve):
                nc.vector.memset(x[:, :, 0:PAD], 0.0).then_inc(padded, 1)
                dve.sem_inc(acc_ready, 2)
                with dve.Fori(0, n // 2) as i:
                    dve.sem_clear(dve_order)
                    link = chain(dve, dve_order)
                    for u in range(2):
                        dve.wait_ge(loaded[u], i * 32 + 32)
                        dve.wait_ge(y_ready, i * 2 + u + 1)
                        link(nc.vector.tensor_scalar(acc[:, u, :], x[:, u, 0:T], w[:, u, 0:1], w[:, u, CONV:CONV + 1], ALU.mult, ALU.add))
                        for j in range(1, CONV):
                            ins = nc.vector.scalar_tensor_tensor(out=acc[:, u, :], in0=x[:, u, j:j + T], scalar=w[:, u, j:j + 1],
                                                                 in1=acc[:, u, :], op0=ALU.mult, op1=ALU.add)
                            if j < CONV - 1:
                                link(ins)
                        ins.then_inc(acc_ready, 1)
                    for u in range(2):
                        dve.wait_ge(transposed, i * 2 + u + 1)
                        nc.vector.tensor_copy(tok[:, u, :, :], psum[:, u, :].rearrange("p (t c) -> p t c", c=P)).then_inc(tok_ready, 1)

            @block.scalar
            def _(act):
                act.sem_inc(y_ready, 2)
                act.sem_inc(out0, 32)
                act.sem_inc(out1, 32)
                with act.Fori(0, n // 2) as i:
                    for u in range(2):
                        act.wait_ge(acc_ready, i * 2 + u + 3)
                        act.wait_ge(stored[u], i * 32 + 32)
                        nc.scalar.activation(y[:, u, :], acc[:, u, :], ACT.Silu).then_inc(y_ready, 1)
                        act.wait_ge(y_ready, i * 2 + u + 3)
                        act.dma_start(convT[ds((i * 2 + u) * P, P), :], y[:, u, :]).then_inc(stored[u], 16)
                    for u in range(2):
                        act.wait_ge(tok_ready, i * 2 + u + 1)
                        act.dma_start(tiled(conv_tok)[:, :, ds((i * 2 + u) * P, P)], tok[:, u, :, :]).then_inc(stored[u], 16)
                act.wait_ge(out0, n // 2 * 32 + 32)
                act.wait_ge(out1, n // 2 * 32 + 32)

            @block.tensor
            def _(pe):
                with pe.Fori(0, n // 2) as i:
                    for u in range(2):
                        pe.wait_ge(y_ready, i * 2 + u + 3)
                        pe.wait_ge(acc_ready, i * 2 + u + 3)
                        for t in range(NT):
                            last = nc.tensor.transpose(psum[:, u, t * P:(t + 1) * P], y[:, u, t * P:(t + 1) * P], ident[:, :])
                        last.then_inc(transposed, 1)


def ssd_dt(nc, tag, dt_raw, dt_bias, a_log, dt, da):
    with ExitStack() as ctx:
        sb = lambda m, s: ctx.enter_context(nc.sbuf_tensor(f"{tag}_{m}", s, F32))
        x, e, b, a = sb("x", [P, NT, HEADS]), sb("e", [P, NT, HEADS]), sb("b", [P, HEADS]), sb("a", [P, HEADS])
        xin, abs_ready, act_order, ln_ready, dve_order, out_ready, stored = ctx.enter_context(stage_sems(
            nc, *[f"{tag}_{s}" for s in ("in", "abs", "act", "ln", "dve", "rdy", "out")]))
        with nc.Block() as block:
            @block.sync
            def _(sp):
                sp.dma_start(x[:, :, :], tiled(dt_raw)).then_inc(xin, 16)
                sp.dma_start(b[:, :], row_bc(dt_bias)).then_inc(xin, 16)
                sp.dma_start(a[:, :], row_bc(a_log)).then_inc(xin, 16)
                sp.wait_ge(out_ready, 2)
                sp.dma_start(tiled(dt), x[:, :, :]).then_inc(stored, 16)
                sp.dma_start(tiled(da), e[:, :, :]).then_inc(stored, 16)
                sp.wait_ge(stored, 32)

            @block.vector
            def _(dve):
                link = chain(dve, dve_order)
                dve.wait_ge(xin, 48)
                link(nc.vector.tensor_tensor(x[:, :, :], x[:, :, :], bc_mid(b[:, :], NT), ALU.add))
                link(nc.vector.tensor_scalar(e[:, :, :], x[:, :, :], -1.0, None, ALU.mult))
                nc.vector.tensor_tensor(e[:, :, :], e[:, :, :], x[:, :, :], ALU.min).then_inc(abs_ready, 1)
                dve.wait_ge(ln_ready, 1)
                link(nc.vector.scalar_tensor_tensor(out=x[:, :, :], in0=x[:, :, :], scalar=0.0, in1=e[:, :, :], op0=ALU.max, op1=ALU.add))
                dve.wait_ge(ln_ready, 2)
                link(nc.vector.tensor_scalar(a[:, :], a[:, :], -1.0, None, ALU.mult))
                nc.vector.tensor_tensor(e[:, :, :], x[:, :, :], bc_mid(a[:, :], NT), ALU.mult).then_inc(out_ready, 2)

            @block.scalar
            def _(act):
                link = chain(act, act_order)
                act.wait_ge(abs_ready, 1)
                link(nc.scalar.activation(e[:, :, :], e[:, :, :], ACT.Exp))
                nc.scalar.activation(e[:, :, :], e[:, :, :], ACT.Ln, bias=1.0).then_inc(ln_ready, 1)
                act.wait_ge(xin, 48)
                nc.scalar.activation(a[:, :], a[:, :], ACT.Exp).then_inc(ln_ready, 1)


def ssd_scan(nc, tag, psum, tri, convT, conv_tok, dt, da, d_skip, y_out, xT, w, w_out):
    GW = HPG * HD
    W = w.shape[1] // (GROUPS * NT)
    w_v = w.rearrange("(k p) n -> p k n", p=P)
    with ExitStack() as ctx:
        sb = lambda m, s: ctx.enter_context(nc.sbuf_tensor(f"{tag}_{m}", s, F32))
        bT, cT, b_tok = sb("bT", [P, P]), sb("cT", [P, P]), sb("b", [P, P])
        x, dtc, dac, dsk = sb("x", [P, GW]), sb("dt", [P, HPG]), sb("da", [P, HPG]), sb("dsk", [P, HEADS])
        dskg = sb("dskg", [P, HPG])
        da_bc, cbm, acum = sb("dabc", [P, HPG, P]), sb("cbm", [P, P]), sb("acum", [P, HPG])
        arg, lmat, mmat = sb("arg", [P, HPG, P]), sb("lmat", [P, HPG, P]), sb("mmat", [P, HPG, P])
        small, smalle = sb("small", [P, 3, HPG]), sb("smalle", [P, 3, HPG])
        xdt, xdec, state, y = sb("xdt", [P, GW]), sb("xdec", [P, GW]), sb("state", [P, GW]), sb("y", [P, GW])
        wbuf, obuf = sb("w", [P, 2, KD, W]), sb("o", [P, 2, NT, W])
        w_high, w_low = (ctx.enter_context(nc.sbuf_tensor(f"{tag}_{m}", [P, 2, KD, W], F32R)) for m in ("wh", "wl"))
        heads = lambda ap: ap.rearrange("p (h d) -> p h d", d=HD)
        rdy = lambda ap: ap.rearrange("p (h s) -> p h s", s=P)
        (loaded, bc_ready, pe_a, arg_ready, exp_ready, ops_ready, pe_b, y_ready, stored, dve_order, w_in0, w_in1, high_ready, low_ready, tile_done, tile_out, out0, out1) = ctx.enter_context(stage_sems(
            nc, *[f"{tag}_{s}" for s in ("in", "bc", "pea", "arg", "exp", "ops", "peb", "y", "out", "dve", "win0", "win1", "high", "low", "tile", "tout", "out0", "out1")]))
        w_in, w_stored = (w_in0, w_in1), (out0, out1)

        def steps(eng, body):
            with eng.Fori(0, GROUPS - 1) as g:
                for c in range(NT):
                    body(g, c, g * NT + c, False)
            for c in range(NT):
                body(GROUPS - 1, c, (GROUPS - 1) * NT + c, c == NT - 1)

        with nc.Block() as block:
            @block.sync
            def _(sp):
                sp.dma_start(wbuf[:, 0, :, :], w_v[:, :, 0:W]).then_inc(w_in0, 16)

                def step(g, c, n, is_last):
                    sp.wait_ge(y_ready, n + 1)
                    sp.dma_start(bT[:, :], convT[ds(g * P + D, P), c * P:(c + 1) * P]).then_inc(loaded, 16)
                    sp.dma_start(cT[:, :], convT[ds(g * P + (D + GROUPS * STATE), P), c * P:(c + 1) * P]).then_inc(loaded, 16)
                    sp.dma_start(b_tok[:, :], conv_tok[c * P:(c + 1) * P, ds(g * P + D, P)]).then_inc(loaded, 16)
                    sp.dma_start(x[:, :], conv_tok[c * P:(c + 1) * P, ds(g * GW, GW)]).then_inc(loaded, 16)
                    sp.dma_start(dtc[:, :], dt[c * P:(c + 1) * P, ds(g * HPG, HPG)]).then_inc(loaded, 16)
                    sp.dma_start(dac[:, :], da[c * P:(c + 1) * P, ds(g * HPG, HPG)]).then_inc(loaded, 16)
                    sp.dma_start(dskg[:, :], row_bc(d_skip[ds(g * HPG, HPG)])).then_inc(loaded, 16)
                    if not is_last:
                        sp.wait_ge(low_ready, n + 1)
                        sp.dma_start(wbuf[:, (c + 1) % 2, :, :], w_v[:, :, ds(n * W + W, W)]).then_inc(w_in[(c + 1) % 2], 16)
                    sp.wait_ge(y_ready, n + 2)
                    sp.dma_start(y_out[c * P:(c + 1) * P, ds(g * GW, GW)], y[:, :]).then_inc(stored, 16)

                steps(sp, step)
                sp.wait_ge(stored, 16 * GROUPS * NT + 16)
                for u in range(2):
                    sp.wait_ge(w_stored[u], 16 * GROUPS * NT // 2 + 16)

            @block.vector
            def _(dve):
                dve.sem_inc(y_ready, 1)
                dve.sem_inc(stored, 16)
                dve.sem_inc(low_ready, 1)

                def make_low(u, n):
                    dve.wait_ge(high_ready, n + 1)
                    nc.vector.tensor_tensor(w_low[:, u, :, :], wbuf[:, u, :, :], w_high[:, u, :, :].bitcast(F32), ALU.subtract).then_inc(low_ready, 1)

                def step(g, c, n, is_last):
                    if c == 0:
                        nc.vector.memset(state[:, :], 0.0)
                    dve.sem_clear(dve_order)
                    link = chain(dve, dve_order)
                    dve.wait_ge(loaded, n * 112 + 112)
                    nc.vector.tensor_copy(da_bc[:, :, :], bc_last(dac[:, :], P)).then_inc(bc_ready, 1)
                    link(nc.vector.tensor_tensor(heads(xdt[:, :]), heads(x[:, :]), bc_last(dtc[:, :], HD), ALU.mult))
                    dve.wait_ge(pe_a, n + 1)
                    nc.vector.tensor_tensor(cbm[:, :], psum[:, 1, 0:P], tri[:, :], ALU.mult)
                    link(nc.vector.tensor_copy(small[:, 0, :], psum[:, 1, P:P + HPG]))
                    link(nc.vector.tensor_copy(small[:, 1, :], rdy(psum[:, 0, :])[:, :, P - 1]))
                    link(nc.vector.tensor_tensor(small[:, 2, :], small[:, 1, :], small[:, 0, :], ALU.subtract))
                    for r in range(HPG):
                        ins = nc.vector.tensor_scalar(arg[:, r, :], psum[:, 0, r * P:(r + 1) * P], small[:, 0, r:r + 1], 0.0,
                                                      ALU.subtract, ALU.min)
                    ins.then_inc(arg_ready, 1)
                    dve.wait_ge(exp_ready, n + 1)
                    nc.vector.tensor_tensor(mmat[:, :, :], lmat[:, :, :], bc_mid(cbm[:, :], HPG), ALU.mult)
                    nc.vector.tensor_tensor(heads(xdec[:, :]), heads(xdt[:, :]), bc_last(smalle[:, 2, :], HD), ALU.mult).then_inc(ops_ready, 1)
                    if not is_last:
                        make_low((c + 1) % 2, n + 1)
                    dve.wait_ge(pe_b, n + 1)
                    dve.wait_ge(stored, n * 16 + 16)
                    link(nc.vector.tensor_tensor(heads(y[:, :]), heads(psum[:, 2, 0:GW]), bc_last(smalle[:, 0, :], HD), ALU.mult))
                    link(nc.vector.tensor_tensor(y[:, :], y[:, :], psum[:, 3, 0:GW], ALU.add))
                    link(nc.vector.tensor_tensor(heads(x[:, :]), heads(x[:, :]), bc_last(dskg[:, :], HD), ALU.mult))
                    link(nc.vector.tensor_tensor(heads(state[:, :]), heads(state[:, :]), bc_last(smalle[:, 1, :], HD), ALU.mult))
                    link(nc.vector.tensor_tensor(state[:, :], state[:, :], psum[:, 4, 0:GW], ALU.add))
                    link(nc.vector.tensor_tensor(y[:, :], y[:, :], x[:, :], ALU.add))
                    dve.sem_inc(y_ready, 1)

                make_low(0, 0)
                steps(dve, step)

            @block.scalar
            def _(act):
                act.sem_inc(tile_out, 2)
                act.sem_inc(out0, 16)
                act.sem_inc(out1, 16)

                def make_high(u, n, turn):
                    act.wait_ge(w_in[u], turn * 16 + 16)
                    act.wait_ge(tile_done, n * NT)
                    nc.scalar.copy(w_high[:, u, :, :], wbuf[:, u, :, :]).then_inc(high_ready, 1)

                def step(g, c, n, is_last):
                    u, turn = c % 2, g * (NT // 2) + c // 2
                    act.wait_ge(arg_ready, n + 1)
                    nc.scalar.activation(smalle[:, :, :], small[:, :, :], ACT.Exp)
                    nc.scalar.activation(lmat[:, :, :], arg[:, :, :], ACT.Exp).then_inc(exp_ready, 1)
                    if not is_last:
                        make_high(1 - u, n + 1, g * (NT // 2) + (c + 1) // 2)
                    act.wait_ge(w_stored[u], turn * 16 + 16)
                    for b in range(NT):
                        act.wait_ge(tile_done, n * NT + (NT + b + 1))
                        nc.scalar.copy(obuf[:, u, b, :], psum[:, 5 + b % 2, 0:W]).then_inc(tile_out, 1)
                    act.wait_ge(tile_out, n * NT + (NT + 2))
                    act.dma_start(tiled(w_out)[:, :, ds(n * W, W)], obuf[:, u, :, :]).then_inc(w_stored[u], 16)

                act.wait_ge(w_in0, 16)
                nc.scalar.copy(w_high[:, 0, :, :], wbuf[:, 0, :, :]).then_inc(high_ready, 1)
                steps(act, step)

            @block.tensor
            def _(pe):
                pe.sem_inc(tile_done, NT)

                def tiles(n, u, which):
                    for b in which:
                        pe.wait_ge(tile_out, n * NT + (b + 1))
                        for k in range(KD):
                            last = times(nc, psum[:, 5 + b % 2, 0:W], [v[:, k, b * P:(b + 1) * P] for v in xT],
                                         [v[:, u, k, :] for v in (w_high, w_low)], k == 0, k == KD - 1)
                        last.then_inc(tile_done, 1)

                def step(g, c, n, is_last):
                    pe.wait_ge(bc_ready, n + 1)
                    nc.tensor.matmul(psum[:, 1, 0:P], bT[:, :], cT[:, :], start=True, stop=True)
                    nc.tensor.matmul(psum[:, 1, P:P + HPG], tri[:, :], dac[:, :], start=True, stop=True)
                    for r in range(HPG):
                        last = nc.tensor.matmul(psum[:, 0, r * P:(r + 1) * P], da_bc[:, r, :], tri[:, :], start=True, stop=True)
                    last.then_inc(pe_a, 1)
                    pe.wait_ge(low_ready, n + 2)
                    tiles(n, c % 2, (0, 1))
                    pe.wait_ge(ops_ready, n + 1)
                    nc.tensor.matmul(psum[:, 2, 0:GW], cT[:, :], state[:, :], start=True, stop=True)
                    nc.tensor.matmul(psum[:, 4, 0:GW], b_tok[:, :], xdec[:, :], start=True, stop=True)
                    for r in range(HPG):
                        last = nc.tensor.matmul(psum[:, 3, r * HD:(r + 1) * HD], mmat[:, r, :], xdt[:, r * HD:(r + 1) * HD], start=True, stop=True)
                    last.then_inc(pe_b, 1)
                    tiles(n, c % 2, (2, 3))

                steps(pe, step)


def ssd_gate_norm(nc, tag, y, z, norm_w, out):
    GW = D // GROUPS
    with ExitStack() as ctx:
        sb = lambda m, s: ctx.enter_context(nc.sbuf_tensor(f"{tag}_{m}", s, F32))
        ys, zs, w = sb("y", [P, NT, D]), sb("z", [P, NT, D]), sb("w", [P, D])
        sq, st, rt, tp = sb("sq", [P, D]), sb("st", [P, NT, GROUPS]), sb("rt", [P, NT, GROUPS]), sb("tp", [P, NT, GROUPS])
        w_in, silu_ready, mean_ready, root_ready, dve_order, y_ready, stored, *x_in = ctx.enter_context(stage_sems(
            nc, *[f"{tag}_{s}" for s in ("win", "silu", "mean", "root", "dve", "y", "out", *(f"in{t}" for t in range(NT)))]))
        grp = lambda ap: ap.rearrange("p (g d) -> p g d", g=GROUPS)
        with nc.Block() as block:
            @block.sync
            def _(sp):
                for t in range(NT):
                    sp.dma_start(zs[:, t, :], z[t * P:(t + 1) * P, :]).then_inc(x_in[t], 16)
                    sp.dma_start(ys[:, t, :], y[t * P:(t + 1) * P, :]).then_inc(x_in[t], 16)
                sp.dma_start(w[:, :], row_bc(norm_w)).then_inc(w_in, 16)
                for t in range(NT):
                    sp.wait_ge(y_ready, t + 1)
                    sp.dma_start(out[t * P:(t + 1) * P, :], ys[:, t, :]).then_inc(stored, 16)
                sp.wait_ge(stored, 16 * NT)

            @block.scalar
            def _(act):
                for t in range(NT):
                    act.wait_ge(x_in[t], 32)
                    nc.scalar.activation(zs[:, t, :], zs[:, t, :], ACT.Silu).then_inc(silu_ready, 1)
                act.wait_ge(mean_ready, 1)
                nc.scalar.activation(rt[:, :, :], st[:, :, :], ACT.Sqrt).then_inc(root_ready, 1)

            @block.vector
            def _(dve):
                link = chain(dve, dve_order)
                for t in range(NT):
                    dve.wait_ge(silu_ready, t + 1)
                    link(nc.vector.tensor_tensor(ys[:, t, :], ys[:, t, :], zs[:, t, :], ALU.mult))
                    link(nc.vector.tensor_tensor(sq[:, :], ys[:, t, :], ys[:, t, :], ALU.mult))
                    link(nc.vector.tensor_reduce(st[:, t, :], grp(sq[:, :]), AX, ALU.add))
                nc.vector.tensor_scalar(st[:, :, :], st[:, :, :], 1.0 / GW, EPS, ALU.mult, ALU.add).then_inc(mean_ready, 1)
                dve.wait_ge(root_ready, 1)
                dve.wait_ge(w_in, 16)
                refined_root(nc, link, rt[:, :, :], st[:, :, :], tp[:, :, :])
                for t in range(NT):
                    link(nc.vector.tensor_tensor(grp(ys[:, t, :]), grp(ys[:, t, :]), bc_last(rt[:, t, :], GW), ALU.mult))
                    nc.vector.tensor_tensor(ys[:, t, :], ys[:, t, :], w[:, :], ALU.mult).then_inc(y_ready, 1)


def rope_tables(nc, tag, positions, inv, half, cos_sb, sin_sb):
    two_pi = 2.0 * math.pi
    c1 = 6.28125
    c2 = float(np.float32(two_pi - c1) * 1.0)
    c2 = math.floor(c2 * 2 ** 20) / 2 ** 20
    c3 = two_pi - c1 - c2
    with ExitStack() as ctx:
        sb = lambda m, s, d=F32: ctx.enter_context(nc.sbuf_tensor(f"{tag}_{m}", s, d))
        pos_i, pos, inv_sb = sb("pi", [P, NT], I32), sb("p", [P, NT]), sb("inv", [P, half])
        ang, k, ki, hs = sb("ang", [P, NT, half]), sb("k", [P, NT, half]), sb("ki", [P, NT, half], I32), sb("hs", [P, NT, half])
        xin, ang_ready, sin_ready, dve_order = ctx.enter_context(stage_sems(nc, *[f"{tag}_{s}" for s in ("in", "ang", "sin", "dve")]))
        with nc.Block() as block:
            @block.sync
            def _(sp):
                with nc.allow_non_contiguous_dma("the positions, one to a partition"):
                    sp.dma_start(pos_i[:, :], positions.rearrange("(t p) -> p t", p=P)).then_inc(xin, 16)
                sp.dma_start(inv_sb[:, :], row_bc(inv)).then_inc(xin, 16)

            @block.vector
            def _(dve):
                link = chain(dve, dve_order)
                dve.wait_ge(xin, 32)
                link(nc.vector.tensor_copy(pos[:, :], pos_i[:, :]))
                link(nc.vector.tensor_tensor(ang[:, :, :], bc_last(pos[:, :], half), bc_mid(inv_sb[:, :], NT), ALU.mult))
                link(nc.vector.tensor_scalar(k[:, :, :], ang[:, :, :], 1.0 / two_pi, None, ALU.mult))
                link(nc.vector.tensor_copy(ki[:, :, :], k[:, :, :]))
                link(nc.vector.tensor_copy(k[:, :, :], ki[:, :, :]))
                for c in (c1, c2, c3):
                    link(nc.vector.scalar_tensor_tensor(out=ang[:, :, :], in0=k[:, :, :], scalar=-c, in1=ang[:, :, :], op0=ALU.mult, op1=ALU.add))
                link(nc.vector.tensor_scalar(k[:, :, :], ang[:, :, :], math.pi, -two_pi, ALU.is_gt, ALU.mult))
                link(nc.vector.tensor_tensor(k[:, :, :], k[:, :, :], ang[:, :, :], ALU.add))
                link(nc.vector.tensor_scalar(ang[:, :, :], k[:, :, :], -math.pi, two_pi, ALU.is_lt, ALU.mult))
                link(nc.vector.tensor_tensor(ang[:, :, :], k[:, :, :], ang[:, :, :], ALU.add))
                lim = 3.1415925
                nc.vector.tensor_scalar(ang[:, :, :], ang[:, :, :], lim, -lim, ALU.min, ALU.max).then_inc(ang_ready, 1)
                dve.wait_ge(sin_ready, 1)
                link(nc.vector.tensor_tensor(hs[:, :, :], hs[:, :, :], hs[:, :, :], ALU.mult))
                link(nc.vector.tensor_scalar(cos_sb[:, :, :], hs[:, :, :], -2.0, 1.0, ALU.mult, ALU.add))

            @block.scalar
            def _(act):
                act.wait_ge(ang_ready, 1)
                nc.scalar.activation(sin_sb[:, :, :], ang[:, :, :], ACT.Sin)
                nc.scalar.activation(hs[:, :, :], ang[:, :, :], ACT.Sin, scale=0.5).then_inc(sin_ready, 1)


class HeadPrep:
    names = ("hin", "hmean", "hroot", "hdve", "hy", "hout")

    def __init__(self, nc, tag, src, dst, heads, hd, gain=None, cos=None, sin=None, rot=0, rot_at=0):
        self.nc, self.tag, self.dst, self.heads, self.hd = nc, tag, dst, heads, hd
        self.src = src.rearrange("t (h d) -> t h d", h=heads) if len(src.shape) == 2 else src
        self.gain, self.cos, self.sin, self.rot, self.rot_at = gain, cos, sin, rot, rot_at
        self.rows = src.shape[0] // P

    def place(self, ctx, sems):
        sb = lambda m, s: ctx.enter_context(self.nc.sbuf_tensor(f"{self.tag}_{m}", s, F32))
        rows, heads, hd = self.rows, self.heads, self.hd
        self.xin, self.mean_ready, self.root_ready, self.dve_order, self.y_ready, self.stored = sems
        self.x = sb("x", [P, rows, heads, hd])
        if self.gain is not None:
            self.sq, self.g = sb("sq", [P, rows * heads, hd]), sb("g", [P, hd])
            self.st, self.rt, self.tp = (sb(m, [P, rows * heads]) for m in ("st", "rt", "tp"))
        if self.rot:
            self.ta, self.tb, self.tc = (sb(m, [P, rows, heads, self.rot // 2]) for m in ("ta", "tb", "tc"))

    def load(self, eng):
        for t in range(self.rows):
            eng.dma_start(self.x[:, t, :, :], self.src[t * P:(t + 1) * P, :, :]).then_inc(self.xin, 16)
        if self.gain is not None:
            eng.dma_start(self.g[:, :], row_bc(self.gain)).then_inc(self.xin, 16)

    def store(self, eng):
        eng.wait_ge(self.y_ready, 1)
        for t in range(self.rows):
            eng.dma_start(self.dst[t * P:(t + 1) * P, :, :], self.x[:, t, :, :]).then_inc(self.stored, 16)
        eng.wait_ge(self.stored, 16 * self.rows)

    def vector(self, dve):
        nc, x, rows, heads, hd = self.nc, self.x, self.rows, self.heads, self.hd
        link = chain(dve, self.dve_order)
        dve.wait_ge(self.xin, 16 * rows + (16 if self.gain is not None else 0))
        if self.gain is not None:
            flat = x[:, :, :, :].rearrange("p t h d -> p (t h) d")
            sq, g, st, rt, tp = self.sq[:, :, :], self.g[:, :], self.st[:, :], self.rt[:, :], self.tp[:, :]
            link(nc.vector.tensor_tensor(sq, flat, flat, ALU.mult))
            link(nc.vector.tensor_reduce(st, sq, AX, ALU.add))
            nc.vector.tensor_scalar(st, st, 1.0 / hd, EPS, ALU.mult, ALU.add).then_inc(self.mean_ready, 1)
            dve.wait_ge(self.root_ready, 1)
            refined_root(nc, link, rt, st, tp)
            link(nc.vector.tensor_tensor(flat, flat, bc_last(rt, hd), ALU.mult))
            link(nc.vector.tensor_tensor(flat, flat, bc_mid(g, rows * heads), ALU.mult))
        if self.rot:
            at, half = self.rot_at, self.rot // 2
            x1, x2 = x[:, :, :, at:at + half], x[:, :, :, at + half:at + self.rot]
            over_heads = lambda c: c[:, 0:rows, :].rearrange("p t (o a) -> p t o a", o=1).broadcast_to([P, rows, heads, half])
            cs, sn = over_heads(self.cos), over_heads(self.sin)
            ta, tb, tc = self.ta[:, :, :, :], self.tb[:, :, :, :], self.tc[:, :, :, :]
            nc.vector.tensor_tensor(ta, x1, sn, ALU.mult)
            nc.vector.tensor_tensor(tb, x2, sn, ALU.mult)
            link(nc.vector.tensor_tensor(tc, x2, cs, ALU.mult))
            link(nc.vector.tensor_tensor(x1, x1, cs, ALU.mult))
            link(nc.vector.tensor_tensor(x1, x1, tb, ALU.subtract))
            link(nc.vector.tensor_tensor(x2, tc, ta, ALU.add))
        dve.sem_inc(self.y_ready, 1)

    def scalar(self, act):
        if self.gain is not None:
            act.wait_ge(self.mean_ready, 1)
            self.nc.scalar.activation(self.rt[:, :], self.st[:, :], ACT.Sqrt).then_inc(self.root_ready, 1)


def prep_only(nc, *preps):
    with ExitStack() as ctx:
        sems = ctx.enter_context(stage_sems(nc, *[f"{p.tag}_{s}" for p in preps for s in p.names]))
        for i, p in enumerate(preps):
            p.place(ctx, sems[i * len(p.names):(i + 1) * len(p.names)])
        with nc.Block() as block:
            @block.sync
            def _(sp):
                for p in preps[0::2]:
                    p.load(sp)
                    p.store(sp)

            @block.vector
            def _(dve):
                for p in preps:
                    p.vector(dve)

            @block.scalar
            def _(act):
                for p in preps:
                    p.scalar(act)

            @block.gpsimd
            def _(pool):
                for p in preps[1::2]:
                    p.load(pool)
                    p.store(pool)


def attention(nc, tag, psum, ident, q, k, v, o, splits, dv, scale, key_tiles, mask=None, span=None, lse=None):
    H = 4
    N = H * NT
    d = sum(splits)
    nch = len(splits)
    offs = [sum(splits[:i]) for i in range(nch)]
    span = span or (lambda qt: (0, key_tiles))
    with ExitStack() as ctx:
        sb = lambda m, s: ctx.enter_context(nc.sbuf_tensor(f"{tag}_{m}", s, F32))
        qs, ks, vs = sb("q", [P, NT, H, d]), sb("k", [P, key_tiles, H, d]), sb("v", [P, key_tiles, H, dv])
        qT, kT = sb("qT", [P, H, nch, T]), sb("kT", [P, H, nch, key_tiles * P])
        ms = sb("mask", [P, NT, T]) if mask is not None else None
        s_sb, p_sb, pT = sb("s", [P, 2, key_tiles * P]), sb("p", [P, 2, key_tiles * P]), sb("pT", [P, 2, key_tiles, P])
        os_, st, ls = sb("o", [P, NT, H, dv]), sb("st", [P, NT, H, 4]), sb("ls", [P, NT, H])
        (qk_in, v_in, mask_in, qk_tr, q_ev, k_ev, s_done, s_copied, nm_ready, e_done, pt_done, pt_ev, o_done, o_ev, stored,
         dve_order, ln_done, lse_ready) = ctx.enter_context(stage_sems(nc, *[f"{tag}_{s}" for s in (
             "qkin", "vin", "mask", "qktr", "qev", "kev", "sdone", "scp", "nm", "edone", "ptdone", "ptev", "odone", "oev",
             "out", "dve", "ln", "lse")]))
        tile = lambda ap, t: ap[t * P:(t + 1) * P]
        with nc.Block() as block:
            @block.sync
            def _(sp):
                for t in range(NT):
                    sp.dma_start(qs[:, t, :, :], tile(q, t)).then_inc(qk_in, 16)
                for t in range(key_tiles):
                    sp.dma_start(ks[:, t, :, :], tile(k, t)).then_inc(qk_in, 16)
                if mask is not None:
                    sp.dma_start(ms[:, :, :], tiled(mask)).then_inc(mask_in, 16)
                for t in range(key_tiles):
                    sp.dma_start(vs[:, t, :, :], tile(v, t)).then_inc(v_in, 16)
                sp.wait_ge(o_ev, N)
                for t in range(NT):
                    sp.dma_start(tile(o, t), os_[:, t, :, :]).then_inc(stored, 16)
                if lse is not None:
                    sp.wait_ge(lse_ready, 1)
                    sp.dma_start(tiled(lse), ls[:, :, :]).then_inc(stored, 16)
                sp.wait_ge(stored, 16 * NT + (16 if lse is not None else 0))

            @block.tensor
            def _(pe):
                def turn(h):
                    for c, (w, at) in enumerate(zip(splits, offs)):
                        if h * nch + c:
                            pe.wait_ge(q_ev, h * nch + c)
                        take_bank(nc, psum[:, 0, 0:P], ident)
                        for t in range(NT):
                            last = nc.tensor.transpose(psum[0:w, 0, t * P:(t + 1) * P], qs[:, t, h, at:at + w], ident[:, :])
                        last.then_inc(qk_tr, 1)
                        if h * nch + c:
                            pe.wait_ge(k_ev, h * nch + c)
                        take_bank(nc, psum[:, 1, 0:P], ident)
                        for t in range(key_tiles):
                            last = nc.tensor.transpose(psum[0:w, 1, t * P:(t + 1) * P], ks[:, t, h, at:at + w], ident[:, :])
                        last.then_inc(qk_tr, 1)

                pe.wait_ge(qk_in, 16 * (NT + key_tiles))
                for h in range(H):
                    turn(h)
                pe.wait_ge(v_in, 16 * key_tiles)
                for g in range(N + 2):
                    if g < N:
                        h, qt = g // NT, g % NT
                        a, b = span(qt)
                        if qt == 0:
                            pe.wait_ge(q_ev, (h + 1) * nch)
                            pe.wait_ge(k_ev, (h + 1) * nch)
                        if g >= 2:
                            pe.wait_ge(s_copied, g - 1)
                        for c, w in enumerate(splits):
                            last = nc.tensor.matmul(psum[:, 2 + g % 2, a * P:b * P], qT[0:w, h, c, qt * P:(qt + 1) * P],
                                                    kT[0:w, h, c, a * P:b * P], start=c == 0, stop=c == nch - 1)
                        last.then_inc(s_done, 1)
                    if 1 <= g <= N:
                        e = g - 1
                        a, b = span(e % NT)
                        pe.wait_ge(e_done, e + 1)
                        if e >= 2:
                            pe.wait_ge(pt_ev, e - 1)
                        for t in range(a, b):
                            last = nc.tensor.transpose(psum[:, 4 + e % 2, t * P:(t + 1) * P], p_sb[:, e % 2, t * P:(t + 1) * P], ident[:, :])
                        last.then_inc(pt_done, 1)
                    if g >= 2:
                        e = g - 2
                        a, b = span(e % NT)
                        pe.wait_ge(pt_ev, e + 1)
                        if e >= 2:
                            pe.wait_ge(o_ev, e - 1)
                        for t in range(a, b):
                            last = nc.tensor.matmul(psum[:, 6 + e % 2, 0:dv], pT[:, e % 2, t, :], vs[:, t, e // NT, :],
                                                    start=t == a, stop=t == b - 1)
                        last.then_inc(o_done, 1)

            @block.vector
            def _(dve):
                link = chain(dve, dve_order)

                def take_keys(h):
                    for c, w in enumerate(splits):
                        dve.wait_ge(qk_tr, (h * nch + c) * 2 + 2)
                        nc.vector.tensor_copy(kT[0:w, h, c, :], psum[0:w, 1, 0:key_tiles * P]).then_inc(k_ev, 1)

                for h in range(H):
                    take_keys(h)
                if mask is not None:
                    dve.wait_ge(mask_in, 16)
                for g in range(N + 2):
                    if g < N:
                        h, qt = g // NT, g % NT
                        a, b = span(qt)
                        sl = slice(a * P, b * P)
                        dve.wait_ge(s_done, g + 1)
                        if g >= 2:
                            dve.wait_ge(e_done, g - 1)
                        if mask is not None:
                            ins = nc.vector.tensor_tensor(s_sb[:, g % 2, sl], psum[:, 2 + g % 2, sl], ms[:, qt, sl], ALU.add)
                        else:
                            ins = nc.vector.tensor_copy(s_sb[:, g % 2, sl], psum[:, 2 + g % 2, sl])
                        ins.then_inc(s_copied, 1)
                        dve.wait_ge(s_copied, g + 1)
                        link(nc.vector.tensor_reduce(st[:, qt, h, 0:1], s_sb[:, g % 2, sl], AX, ALU.max))
                        nc.vector.tensor_scalar(st[:, qt, h, 1:2], st[:, qt, h, 0:1], -scale, None, ALU.mult).then_inc(nm_ready, 1)
                    if g >= 2:
                        e = g - 2
                        h, qt = e // NT, e % NT
                        dve.wait_ge(o_done, e + 1)
                        link(nc.vector.reciprocal(st[:, qt, h, 3:4], st[:, qt, h, 2:3]))
                        nc.vector.tensor_scalar(os_[:, qt, h, :], psum[:, 6 + e % 2, 0:dv], st[:, qt, h, 3:4], None,
                                                ALU.mult).then_inc(o_ev, 1)
                if lse is not None:
                    dve.wait_ge(ln_done, 1)
                    nc.vector.scalar_tensor_tensor(out=ls[:, :, :], in0=st[:, :, :, 0], scalar=scale, in1=ls[:, :, :],
                                                   op0=ALU.mult, op1=ALU.add).then_inc(lse_ready, 1)

            @block.scalar
            def _(act):
                def take_queries(h):
                    for c, w in enumerate(splits):
                        act.wait_ge(qk_tr, (h * nch + c) * 2 + 1)
                        nc.scalar.copy(qT[0:w, h, c, :], psum[0:w, 0, 0:T]).then_inc(q_ev, 1)

                for h in range(H):
                    take_queries(h)
                for g in range(N + 1):
                    if g < N:
                        h, qt = g // NT, g % NT
                        a, b = span(qt)
                        sl = slice(a * P, b * P)
                        act.wait_ge(nm_ready, g + 1)
                        if g >= 2:
                            act.wait_ge(pt_done, g - 1)
                        nc.scalar.activation(p_sb[:, g % 2, sl], s_sb[:, g % 2, sl], ACT.Exp, bias=st[:, qt, h, 1:2],
                                             scale=scale, accum_out=st[:, qt, h, 2:3]).then_inc(e_done, 1)
                    if g >= 1:
                        e = g - 1
                        a, b = span(e % NT)
                        act.wait_ge(pt_done, e + 1)
                        if e >= 2:
                            act.wait_ge(o_done, e - 1)
                        nc.scalar.copy(pT[:, e % 2, a:b, :], psum[:, 4 + e % 2, a * P:b * P].rearrange("p (t q) -> p t q", q=P)).then_inc(pt_ev, 1)
                if lse is not None:
                    act.wait_ge(e_done, N)
                    nc.scalar.activation(ls[:, :, :], st[:, :, :, 2], ACT.Ln).then_inc(ln_done, 1)


def dil_combine(nc, tag, o, lse, out):
    HW = 4 * HD
    with ExitStack() as ctx:
        sb = lambda m, s: ctx.enter_context(nc.sbuf_tensor(f"{tag}_{m}", s, F32))
        os_, ls = sb("o", [P, NT, DIL * HW]), sb("l", [P, NT, DIL, 4])
        mx, y, tmp = sb("mx", [P, NT, 4]), sb("y", [P, NT, HW]), sb("tmp", [P, NT, HW])
        xin, diff_ready, exp_ready, dve_order, y_ready, stored = ctx.enter_context(stage_sems(
            nc, *[f"{tag}_{s}" for s in ("in", "diff", "exp", "dve", "y", "out")]))
        with nc.Block() as block:
            @block.sync
            def _(sp):
                sp.dma_start(ls[:, :, :, :].rearrange("p t g h -> p t (g h)"), tiled(lse)).then_inc(xin, 16)
                sp.dma_start(os_[:, :, :], tiled(o)).then_inc(xin, 16)
                sp.wait_ge(y_ready, 1)
                sp.dma_start(tiled(out), y[:, :, :]).then_inc(stored, 16)
                sp.wait_ge(stored, 16)

            @block.vector
            def _(dve):
                link = chain(dve, dve_order)
                dve.wait_ge(xin, 32)
                link(nc.vector.tensor_tensor(mx[:, :, :], ls[:, :, 0, :], ls[:, :, 1, :], ALU.max))
                link(nc.vector.tensor_tensor(mx[:, :, :], mx[:, :, :], ls[:, :, 2, :], ALU.max))
                for g in range(DIL):
                    ins = nc.vector.tensor_tensor(ls[:, :, g, :], ls[:, :, g, :], mx[:, :, :], ALU.subtract)
                ins.then_inc(diff_ready, 1)
                dve.wait_ge(exp_ready, 1)
                link(nc.vector.tensor_tensor(mx[:, :, :], ls[:, :, 0, :], ls[:, :, 1, :], ALU.add))
                link(nc.vector.tensor_tensor(mx[:, :, :], mx[:, :, :], ls[:, :, 2, :], ALU.add))
                link(nc.vector.reciprocal(mx[:, :, :], mx[:, :, :]))
                for g in range(DIL):
                    link(nc.vector.tensor_tensor(ls[:, :, g, :], ls[:, :, g, :], mx[:, :, :], ALU.mult))
                for t in range(NT):
                    hv = lambda ap: ap.rearrange("p (h d) -> p h d", d=HD)
                    for g in range(DIL):
                        to = y if g == 0 else tmp
                        link(nc.vector.tensor_tensor(hv(to[:, t, :]), hv(os_[:, t, g * HW:(g + 1) * HW]), bc_last(ls[:, t, g, :], HD), ALU.mult))
                        if g:
                            link(nc.vector.tensor_tensor(y[:, t, :], y[:, t, :], tmp[:, t, :], ALU.add))
                dve.sem_inc(y_ready, 1)

            @block.scalar
            def _(act):
                act.wait_ge(diff_ready, 1)
                nc.scalar.activation(ls[:, :, :, :], ls[:, :, :, :], ACT.Exp).then_inc(exp_ready, 1)


def peer_route(nc, tag, psum, qT, keysT, iota16, sel, cond, ada_w, mods):
    GROUP = PEER_H // LAYERS
    PIECES = 6 * D // CH // GROUP
    with ExitStack() as ctx:
        sb = lambda m, s, d=F32: ctx.enter_context(nc.sbuf_tensor(f"{tag}_{m}", s, d))
        qs, ks = sb("q", [P, 2, T]), sb("k", [P, 2, NK])
        sc, sc2 = sb("sc", [P, 2, NT, NK]), sb("sc2", [P, NT, NK])
        val, idx, idxf = sb("val", [P, 2, NT, TOPK]), sb("idx", [P, 2, NT, TOPK], U32), sb("idxf", [P, 2, NT, TOPK])
        cand, cand2 = sb("cand", [P, NT, 256]), sb("cand2", [P, NT, 256])
        top, pos, posx, posf = sb("top", [P, NT, TOPK]), sb("pos", [P, NT, TOPK], U32), sb("posx", [P, 2, NT, TOPK], U32), sb("posf", [P, 2, NT, TOPK])
        eq, res = sb("eq", [P, NT, TOPK, TOPK]), sb("res", [P, NT, 3, TOPK])
        sums = sb("sums", [P, NT])
        cT, w_ada, rows = sb("cT", [P, KD]), sb("wada", [P, PIECES, KD, CH]), sb("rows", [1, PIECES, CH])
        (loaded, s_done, s_copied, diff_ready, exp_ready, dve_order, res_ready, stored, c_in, c_ready, ada_done, rows_ready, rows_out, *ada_in) = \
            ctx.enter_context(stage_sems(nc, *[f"{tag}_{s}" for s in (
                "in", "sdone", "scp", "diff", "exp", "dve", "res", "out", "cin", "crdy", "adad", "rows", "rowso", *(f"ada{j}" for j in range(PIECES)))]))
        with nc.Block() as block:
            @block.sync
            def _(sp):
                with nc.allow_non_contiguous_dma("a row of 1024 laid over the partitions"):
                    sp.dma_start(cT[:, :], cond.rearrange("(k p) -> p k", p=P)).then_inc(c_in, 16)
                with sp.Fori(0, LAYERS) as l:
                    with sp.Fori(0, GROUP) as g:
                        h = l * GROUP + g
                        sp.wait_ge(s_done, h * 2 + 2)
                        for c in range(2):
                            sp.dma_start(qs[:, c, :], qT[ds(h * 256 + c * P, P), :]).then_inc(loaded, 16)
                            sp.dma_start(ks[:, c, :], keysT[ds(h * 256 + c * P, P), :]).then_inc(loaded, 16)
                        for j in range(PIECES):
                            sp.wait_ge(ada_done, h * PIECES + (j + 1))
                            sp.dma_start(w_ada[:, j, :, :], ada_w[ds(l, 1), :, ds(g * (PIECES * CH) + j * CH, CH)].rearrange("o (k p) n -> p (o k) n", p=P)) \
                                .then_inc(ada_in[j], 16)

            @block.tensor
            def _(pe):
                pe.sem_inc(s_done, 2)
                pe.sem_inc(ada_done, PIECES)
                pe.wait_ge(c_ready, 1)
                with pe.Fori(0, PEER_H) as h:
                    pe.wait_ge(loaded, h * 64 + 64)
                    for c in range(2):
                        pe.wait_ge(s_copied, h * 2 + (c + 1))
                        for t in range(NT):
                            last = nc.tensor.matmul(psum[:, c, t * NK:(t + 1) * NK], qs[:, c, t * P:(t + 1) * P], ks[:, c, :], start=True, stop=True)
                        last.then_inc(s_done, 1)
                    for j in range(PIECES):
                        pe.wait_ge(ada_in[j], h * 16 + 16)
                        pe.wait_ge(rows_ready, h * PIECES + (j + 1))
                        for k in range(KD):
                            last = nc.tensor.matmul(psum[0:1, 2 + j, :], cT[:, k:k + 1], w_ada[:, j, k, :], start=k == 0, stop=k == KD - 1)
                        last.then_inc(ada_done, 1)

            @block.vector
            def _(dve):
                dve.sem_inc(s_copied, 2)
                dve.sem_inc(stored, 16 * NT)

                def best16(link, values, spare, v, i):
                    def each(op):
                        for t in range(NT):
                            ins = op(t)
                        link(ins)
                    each(lambda t: nc.vector.max(v[:, t, 0:8], values[:, t, :]))
                    each(lambda t: nc.vector.max_index(i[:, t, 0:8], v[:, t, 0:8], values[:, t, :]))
                    each(lambda t: nc.vector.match_replace(spare[:, t, :], v[:, t, 0:8], values[:, t, :], NEG))
                    each(lambda t: nc.vector.max(v[:, t, 8:16], spare[:, t, :]))
                    each(lambda t: nc.vector.max_index(i[:, t, 8:16], v[:, t, 8:16], spare[:, t, :]))

                flat = lambda ap: ap.rearrange("p t k -> p (t k)")
                pairs = lambda ap: ap.rearrange("p t (a b) -> p t a b", b=TOPK)
                over_a = lambda ap: ap.rearrange("p t (o b) -> p t o b", o=1).broadcast_to([P, NT, TOPK, TOPK])
                eq_rows = eq[:, :, :, :].rearrange("p t a b -> p (t a) b")
                with dve.Fori(0, PEER_H) as h:
                    dve.sem_clear(dve_order)
                    link = chain(dve, dve_order)
                    for c in range(2):
                        dve.wait_ge(s_done, h * 2 + (c + 3))
                        link(nc.vector.tensor_copy(sc[:, c, :, :].rearrange("p t k -> p (t k)"), psum[:, c, :]))
                        dve.sem_inc(s_copied, 1)
                        best16(link, sc[:, c, :, :], sc2[:, :, :], val[:, c, :, :], idx[:, c, :, :])
                        link(nc.vector.tensor_copy(idxf[:, c, :, :], idx[:, c, :, :]))
                    link(nc.vector.tensor_tensor(pairs(cand[:, :, :]), bc_last(flat(val[:, 0, :, :]), TOPK).rearrange("p (t a) b -> p t a b", a=TOPK),
                                                 over_a(val[:, 1, :, :]), ALU.add))
                    best16(link, cand[:, :, :], cand2[:, :, :], top[:, :, :], pos[:, :, :])
                    nc.vector.tensor_scalar(posx[:, 0, :, :], pos[:, :, :], 4, None, ALU.logical_shift_right)
                    link(nc.vector.tensor_scalar(posx[:, 1, :, :], pos[:, :, :], 15, None, ALU.bitwise_and))
                    link(nc.vector.tensor_copy(posf[:, :, :, :], posx[:, :, :, :]))
                    dve.wait_ge(stored, h * (16 * NT) + 16 * NT)
                    for t in range(NT):
                        ins = nc.vector.tensor_scalar(res[:, t, 2, :], top[:, t, :], top[:, t, 0:1], None, ALU.subtract)
                    ins.then_inc(diff_ready, 1)
                    for c in range(2):
                        link(nc.vector.tensor_tensor(eq_rows, bc_last(flat(posf[:, c, :, :]), TOPK), bc_mid(iota16, NT * TOPK), ALU.is_equal))
                        link(nc.vector.tensor_tensor(eq[:, :, :, :], eq[:, :, :, :], over_a(idxf[:, c, :, :]), ALU.mult))
                        link(nc.vector.tensor_reduce(res[:, :, c, :], eq[:, :, :, :], AX, ALU.add))
                    dve.wait_ge(exp_ready, h + 1)
                    link(nc.vector.tensor_reduce(sums[:, :], res[:, :, 2, :], AX, ALU.add))
                    link(nc.vector.reciprocal(sums[:, :], sums[:, :]))
                    link(nc.vector.tensor_tensor(res[:, :, 2, :], res[:, :, 2, :], bc_last(sums[:, :], TOPK), ALU.mult))
                    dve.sem_inc(res_ready, 1)

            @block.scalar
            def _(act):
                act.sem_inc(rows_ready, PIECES)
                act.sem_inc(rows_out, 16)
                act.wait_ge(c_in, 16)
                nc.scalar.activation(cT[:, :], cT[:, :], ACT.Silu).then_inc(c_ready, 1)
                with act.Fori(0, LAYERS) as l:
                    with act.Fori(0, GROUP) as g:
                        h = l * GROUP + g
                        act.wait_ge(rows_out, h * 16 + 16)
                        for j in range(PIECES):
                            act.wait_ge(ada_done, h * PIECES + (PIECES + 1 + j))
                            nc.scalar.copy(rows[0:1, j, :], psum[0:1, 2 + j, :]).then_inc(rows_ready, 1)
                        act.wait_ge(rows_ready, h * PIECES + 2 * PIECES)
                        act.dma_start(mods[ds(l, 1), 0, ds(g * (PIECES * CH), PIECES * CH)].rearrange("o (j n) -> o j n", n=CH), rows[:, :, :]).then_inc(rows_out, 16)
                        act.wait_ge(diff_ready, h + 1)
                        nc.scalar.activation(res[:, :, 2, :], res[:, :, 2, :], ACT.Exp).then_inc(exp_ready, 1)
                        act.wait_ge(res_ready, h + 1)
                        for t in range(NT):
                            act.dma_start(sel[t * P:(t + 1) * P, :, ds(h * TOPK, TOPK)], res[:, t, :, :]).then_inc(stored, 16)
                act.wait_ge(stored, 16 * NT * (PEER_H + 1))
                act.wait_ge(rows_out, 16 * PEER_H + 16)


def peer_gates(nc, tag, psum, selT, iota128, gates):
    TB = 4
    NB = P // TB
    G = 2 * TB
    with ExitStack() as ctx:
        sb = lambda m, s: ctx.enter_context(nc.sbuf_tensor(f"{tag}_{m}", s, F32))
        gbuf = sb("g", [P, NK, P])
        cols, oh1, oh2 = sb("cols", [P, 2, 3, G]), sb("oh1", [P, 2, G, NK]), sb("oh2", [P, 2, G, NK])
        (oh_ready, g_done, ev_a, stored, dve_order) = ctx.enter_context(stage_sems(
            nc, *[f"{tag}_{s}" for s in ("oh", "gd", "eva", "out", "dve")]))
        with nc.Block() as block:
            @block.sync
            def _(sp):
                sp.sem_inc(stored, 16)
                with sp.Fori(0, NT) as t:
                    sp.wait_ge(ev_a, t * NB + (NB + 4))
                    sp.dma_start(gates[ds(t, 1), :, :, :].rearrange("o p i t -> p (o i) t"), gbuf[:, :, :]).then_inc(stored, 16)
                sp.wait_ge(stored, 16 * NT + 16)

            @block.vector
            def _(dve):
                dve.sem_inc(g_done, 4)
                with dve.Fori(0, T // (2 * G)) as i:
                    dve.sem_clear(dve_order)
                    for v in range(2):
                        dve.wait_ge(g_done, i * 4 + (v * 2 + 2))
                        nc.vector.tensor_copy(cols[:, v, :, :], selT[:, :, ds(i * 2 * G + v * G, G)]).then_inc(dve_order, 1)
                        dve.wait_ge(dve_order, v + 1)
                        nc.vector.tensor_tensor(oh2[:, v, :, :], bc_mid(iota128, G), bc_last(cols[:, v, 1, :], NK), ALU.is_equal)
                        for b in range(G):
                            ins = nc.vector.tensor_scalar(oh1[:, v, b, :], iota128, cols[:, v, 0, b:b + 1], cols[:, v, 2, b:b + 1], ALU.is_equal, ALU.mult)
                        ins.then_inc(oh_ready, 1)

            @block.tensor
            def _(pe):
                with pe.Fori(0, T // (2 * G)) as i:
                    for v in range(2):
                        pe.wait_ge(oh_ready, i * 2 + (v + 1))
                        for half in range(2):
                            pe.wait_ge(ev_a, i * 4 + (v * 2 + half + 1))
                            for b in range(TB):
                                last = nc.tensor.matmul(psum[:, v * 2 + half, b * NK:(b + 1) * NK], oh2[:, v, half * TB + b, :], oh1[:, v, half * TB + b, :],
                                                        start=True, stop=True)
                            last.then_inc(g_done, 1)

            @block.scalar
            def _(act):
                act.sem_inc(ev_a, 4)
                with act.Fori(0, NT) as t:
                    act.wait_ge(stored, t * 16 + 16)
                    with act.Fori(0, NB // 4) as i:
                        for u in range(4):
                            act.wait_ge(g_done, t * NB + i * 4 + (u + 5))
                            nc.scalar.copy(gbuf[:, :, ds(i * 4 * TB + u * TB, TB)].rearrange("p i t -> p t i"),
                                           psum[:, u, :].rearrange("p (t i) -> p t i", i=NK)).then_inc(ev_a, 1)


def moe_dense(nc, tag, psum, halves, acc, n, w_a, w_out, w_b, token_w):
    FB = CH // P
    with ExitStack() as ctx:
        sb = lambda m, s: ctx.enter_context(nc.sbuf_tensor(f"{tag}_{m}", s, F32))
        wa, wo = sb("wa", [P, 2, KD, CH]), sb("wo", [P, 2, FB, D])
        wb, xT = sb("wb", [P, 2, KD, CH]), sb("x", [P, KD, T])
        nl, hid = sb("nl", [P, 2, T]), sb("hid", [P, 2, FB, T])
        (in0, in1, a_done, nl_ready, hid_ready, o_done, acc_done, dve_order, joined) = ctx.enter_context(stage_sems(
            nc, *[f"{tag}_{s}" for s in ("in0", "in1", "adone", "nl", "hid", "odone", "acc", "dve", "joined")]))
        loaded = (in0, in1)
        per_load = 48
        with nc.Block() as block:
            @block.sync
            def _(sp):
                with sp.Fori(0, n // 2) as i:
                    for u in range(2):
                        e = i * 2 + u
                        sp.wait_ge(o_done, e * 8 + 8)
                        sp.dma_start(wa[:, u, :, :], w_a(e)).then_inc(loaded[u], 16)
                        sp.dma_start(wb[:, u, :, :], w_b(e)).then_inc(loaded[u], 16)
                        sp.dma_start(wo[:, u, :, :], w_out(e)).then_inc(loaded[u], 16)

            @block.tensor
            def _(pe):
                pe.sem_inc(o_done, 16)
                pe.wait_ge(joined, 1)
                with pe.Fori(0, n // 2) as i:
                    for u in range(2):
                        e = i * 2 + u
                        pe.wait_ge(loaded[u], i * per_load + per_load)
                        for f in range(FB):
                            pe.wait_ge(hid_ready, e * FB + (f + 1))
                            for bank, w in ((f % 2, wa), (2 + f % 2, wb)):
                                for k in range(KD):
                                    last = nc.tensor.matmul(psum[:, bank, :], w[:, u, k, f * P:(f + 1) * P], xT[:, k, :], start=k == 0, stop=k == KD - 1)
                            last.then_inc(a_done, 1)
                        pe.wait_ge(hid_ready, e * FB + (FB + 2))
                        for j in range(8):
                            pe.wait_ge(acc_done, e * 8 + (j + 1))
                            for f in range(FB):
                                last = nc.tensor.matmul(psum[:, 4 + j % 4, :], hid[:, u, f, j // 2 * P:(j // 2 + 1) * P],
                                                        wo[:, u, f, j % 2 * CH:(j % 2 + 1) * CH], start=f == 0, stop=f == FB - 1)
                            last.then_inc(o_done, 1)

            @block.scalar
            def _(act):
                with act.Fori(0, n // 2) as i:
                    for u in range(2):
                        e = i * 2 + u
                        for f in range(FB):
                            act.wait_ge(a_done, e * FB + (f + 1))
                            act.wait_ge(hid_ready, e * FB + (f + 1))
                            nc.scalar.activation(nl[:, f % 2, :], psum[:, f % 2, :], ACT.Silu).then_inc(nl_ready, 1)

            @block.vector
            def _(dve):
                dve.sem_inc(hid_ready, 2)
                dve.sem_inc(acc_done, 4)
                nc.vector.tensor_tensor(xT[:, :, :], halves[0][:, :, :].bitcast(F32), halves[1][:, :, :].bitcast(F32), ALU.add).then_inc(joined, 1)
                nc.vector.memset(acc[:, :, :], 0.0).then_inc(dve_order, 1)
                dve.wait_ge(dve_order, 1)
                with dve.Fori(0, n // 2) as i:
                    for u in range(2):
                        e = i * 2 + u
                        for f in range(FB):
                            dve.wait_ge(nl_ready, e * FB + (f + 1))
                            nc.vector.tensor_tensor(hid[:, u, f, :], nl[:, f % 2, :], psum[:, 2 + f % 2, :], ALU.mult).then_inc(hid_ready, 1)
                        for j in range(8):
                            dve.wait_ge(o_done, e * 8 + (j + 17))
                            dst = acc[:, j // 2, j % 2 * CH:(j % 2 + 1) * CH]
                            dve.wait_ge(acc_done, e * 8 + (j + 4))
                            nc.vector.scalar_tensor_tensor(out=dst, in0=psum[:, 4 + j % 4, :], scalar=token_w[:, j // 2, ds(e, 1)],
                                                           in1=dst, op0=ALU.mult, op1=ALU.add).then_inc(acc_done, 1)


def peer_experts(nc, tag, psum, x, acc, down, up, gates):
    FB = CH // P
    n = N_EXP1 // CH
    with ExitStack() as ctx:
        sb = lambda m, s, d=F32: ctx.enter_context(nc.sbuf_tensor(f"{tag}_{m}", s, d))
        raw_d, raw_u, gt = sb("rawd", [P, KD, CH]), sb("rawu", [P, FB, D]), sb("gt", [P, 2, NT, FB, P])
        d_high, d_low = sb("dh", [P, KD, CH], F32R), sb("dl", [P, KD, CH], F32R)
        u_high, u_low = sb("uh", [P, FB, D], F32R), sb("ul", [P, FB, D], F32R)
        nl, h_high, h_low = sb("nl", [P, 2, T]), sb("hh", [P, FB, T], F32R), sb("hl", [P, FB, T], F32R)
        (d_in, u_in, g_in0, g_in1, dh_ready, dl_ready, uh_ready, ul_ready, a_done, nl_ready, prod_ready, hh_ready, hl_ready, o_done, acc_done, dve_order) = \
            ctx.enter_context(stage_sems(nc, *[f"{tag}_{s}" for s in (
                "din", "uin", "gin0", "gin1", "dhr", "dlr", "uhr", "ulr", "adone", "nl", "prod", "hhr", "hlr", "odone", "acc", "dve")]))
        g_in = (g_in0, g_in1)
        by_tile = lambda ap: ap.rearrange("p (t q) -> p t q", q=P)
        with nc.Block() as block:
            @block.sync
            def _(sp):
                with sp.Fori(0, n // 2) as i:
                    for v in range(2):
                        e = i * 2 + v
                        sp.wait_ge(dl_ready, e + 1)
                        sp.dma_start(raw_d[:, :, :], down[:, :, ds(e * CH, CH)]).then_inc(d_in, 16)
                        sp.wait_ge(hl_ready, e * FB + 1)
                        for t in range(NT):
                            sp.dma_start(gt[:, v, t, :, :], gates[t, :, ds(e * FB, FB), :]).then_inc(g_in[v], 16)
                        sp.wait_ge(ul_ready, e + 1)
                        sp.dma_start(raw_u[:, :, :], up[:, ds(e * FB, FB), :]).then_inc(u_in, 16)

            @block.tensor
            def _(pe):
                pe.sem_inc(a_done, FB)
                pe.sem_inc(o_done, 8)
                with pe.Fori(0, n) as e:
                    pe.wait_ge(dl_ready, e + 2)
                    for f in range(FB):
                        pe.wait_ge(nl_ready, e * FB + (f + 1))
                        for k in range(KD):
                            last = times(nc, psum[:, f, :], [w[:, k, f * P:(f + 1) * P] for w in (d_high, d_low)], [v[:, k, :] for v in x],
                                         k == 0, k == KD - 1)
                        last.then_inc(a_done, 1)
                    pe.wait_ge(ul_ready, e + 2)
                    for j in range(8):
                        pe.wait_ge(acc_done, e * 8 + (j + 1))
                        for f in range(FB):
                            if j == 0:
                                pe.wait_ge(hl_ready, e * FB + (FB + f + 1))
                            last = times(nc, psum[:, 4 + j % 4, :], [h[:, f, j // 2 * P:(j // 2 + 1) * P] for h in (h_high, h_low)],
                                         [w[:, f, j % 2 * CH:(j % 2 + 1) * CH] for w in (u_high, u_low)], f == 0, f == FB - 1)
                        last.then_inc(o_done, 1)

            @block.scalar
            def _(act):
                act.sem_inc(nl_ready, FB)

                def down_high(e):
                    act.wait_ge(d_in, e * 16 + 16)
                    act.wait_ge(a_done, e * FB + FB)
                    nc.scalar.copy(d_high[:, :, :], raw_d[:, :, :]).then_inc(dh_ready, 1)

                def block_of(e, is_last):
                    act.wait_ge(u_in, e * 16 + 16)
                    act.wait_ge(o_done, e * 8 + 8)
                    nc.scalar.copy(u_high[:, :, :], raw_u[:, :, :]).then_inc(uh_ready, 1)
                    for f in range(FB):
                        act.wait_ge(a_done, e * FB + (FB + f + 1))
                        act.wait_ge(hl_ready, e * FB + (f + 3))
                        nc.scalar.activation(nl[:, f % 2, :], psum[:, f, :], ACT.Gelu).then_inc(nl_ready, 1)
                        act.wait_ge(prod_ready, e * FB + (f + 1))
                        nc.scalar.copy(h_high[:, f, :], nl[:, f % 2, :]).then_inc(hh_ready, 1)
                    if not is_last:
                        down_high(e + 1)

                down_high(0)
                with act.Fori(0, n - 1) as e:
                    block_of(e, False)
                block_of(n - 1, True)

            @block.vector
            def _(dve):
                dve.sem_inc(dl_ready, 1)
                dve.sem_inc(ul_ready, 1)
                dve.sem_inc(hl_ready, FB)
                dve.sem_inc(acc_done, 4)
                nc.vector.memset(acc[:, :, :], 0.0).then_inc(dve_order, 1)
                dve.wait_ge(dve_order, 1)

                def down_low(e):
                    dve.wait_ge(dh_ready, e + 1)
                    nc.vector.tensor_tensor(d_low[:, :, :], raw_d[:, :, :], d_high[:, :, :].bitcast(F32), ALU.subtract).then_inc(dl_ready, 1)

                def block_of(e, v, turn, is_last):
                    dve.wait_ge(uh_ready, e + 1)
                    nc.vector.tensor_tensor(u_low[:, :, :], raw_u[:, :, :], u_high[:, :, :].bitcast(F32), ALU.subtract).then_inc(ul_ready, 1)
                    dve.wait_ge(g_in[v], turn * (16 * NT) + 16 * NT)
                    for f in range(FB):
                        dve.wait_ge(nl_ready, e * FB + (FB + f + 1))
                        nc.vector.tensor_tensor(by_tile(nl[:, f % 2, :]), by_tile(nl[:, f % 2, :]), gt[:, v, :, f, :], ALU.mult).then_inc(prod_ready, 1)
                        dve.wait_ge(hh_ready, e * FB + (f + 1))
                        nc.vector.tensor_tensor(h_low[:, f, :], nl[:, f % 2, :], h_high[:, f, :].bitcast(F32), ALU.subtract).then_inc(hl_ready, 1)
                    if not is_last:
                        down_low(e + 1)
                    for j in range(8):
                        dve.wait_ge(o_done, e * 8 + (j + 9))
                        dve.wait_ge(acc_done, e * 8 + (j + 4))
                        dst = acc[:, j // 2, j % 2 * CH:(j % 2 + 1) * CH]
                        nc.vector.tensor_tensor(dst, psum[:, 4 + j % 4, :], dst, ALU.add).then_inc(acc_done, 1)

                down_low(0)
                with dve.Fori(0, n // 2 - 1) as i:
                    for v in range(2):
                        block_of(i * 2 + v, v, i, False)
                block_of(n - 2, 0, n // 2 - 1, False)
                block_of(n - 1, 1, n // 2 - 1, True)


def adaptive_bias(nc, tag, b, mods):
    row = mods.rearrange("l o (p n) -> p (l o) n", p=P)
    with ExitStack() as ctx:
        m_sb, b_sb = (ctx.enter_context(nc.sbuf_tensor(f"{tag}_{m}", [P, LAYERS, 6 * D // P], F32)) for m in "mb")
        xin, added, stored = ctx.enter_context(stage_sems(nc, f"{tag}_in", f"{tag}_add", f"{tag}_out"))
        with nc.Block() as block:
            @block.sync
            def _(sp):
                sp.dma_start(m_sb[:, :, :], row).then_inc(xin, 16)
                sp.dma_start(b_sb[:, :, :], b.rearrange("l (p n) -> p l n", p=P)).then_inc(xin, 16)
                sp.wait_ge(added, 1)
                sp.dma_start(row, m_sb[:, :, :]).then_inc(stored, 16)
                sp.wait_ge(stored, 16)

            @block.vector
            def _(dve):
                dve.wait_ge(xin, 32)
                nc.vector.tensor_tensor(m_sb[:, :, :], m_sb[:, :, :], b_sb[:, :, :], ALU.add).then_inc(added, 1)


def fox_prep(nc, tag, psum, tri, proj, fb, qa, ka):
    H, DH = 4, 128
    root = DH ** 0.5
    with ExitStack() as ctx:
        sb = lambda m, s: ctx.enter_context(nc.sbuf_tensor(f"{tag}_{m}", s, F32))
        q, k = sb("q", [P, NT, H, DH + 2]), sb("k", [P, NT, H, DH + 2])
        ff, fbs, e, lf, ones = sb("ff", [P, NT, H]), sb("fb", [P, H]), sb("e", [P, NT, H]), sb("lf", [P, NT, H]), sb("ones", [P, P])
        (xin, qk_in, abs_ready, ln_ready, lf_ready, cum_done, ext_ready, stored, dve_order, act_order) = ctx.enter_context(stage_sems(
            nc, *[f"{tag}_{s}" for s in ("in", "qkin", "abs", "ln", "lf", "cum", "ext", "out", "dve", "act")]))
        tiled_heads = lambda a, t: a[t * P:(t + 1) * P, :].rearrange("p (h d) -> p h d", h=H)
        with nc.Block() as block:
            @block.sync
            def _(sp):
                sp.dma_start(ff[:, :, :], tiled(proj)[:, :, FF:FF + H]).then_inc(xin, 16)
                sp.dma_start(fbs[:, :], row_bc(fb)).then_inc(xin, 16)
                for t in range(NT):
                    sp.dma_start(q[:, t, :, 0:DH], tiled_heads(proj[:, FQ:FQ + H * DH], t)).then_inc(qk_in, 16)
                    sp.dma_start(k[:, t, :, 0:DH], tiled_heads(proj[:, FK:FK + H * DH], t)).then_inc(qk_in, 16)
                sp.wait_ge(qk_in, 32 * NT)
                sp.wait_ge(ext_ready, 1)
                for t in range(NT):
                    sp.dma_start(qa[t * P:(t + 1) * P, :, :], q[:, t, :, :]).then_inc(stored, 16)
                    sp.dma_start(ka[t * P:(t + 1) * P, :, :], k[:, t, :, :]).then_inc(stored, 16)
                sp.wait_ge(stored, 32 * NT)

            @block.vector
            def _(dve):
                link = chain(dve, dve_order)
                link(nc.vector.memset(ones[:, :], 1.0))
                dve.wait_ge(xin, 32)
                link(nc.vector.tensor_tensor(ff[:, :, :], ff[:, :, :], bc_mid(fbs[:, :], NT), ALU.add))
                link(nc.vector.tensor_scalar(e[:, :, :], ff[:, :, :], -1.0, None, ALU.mult))
                nc.vector.tensor_tensor(e[:, :, :], e[:, :, :], ff[:, :, :], ALU.min).then_inc(abs_ready, 1)
                dve.wait_ge(ln_ready, 1)
                nc.vector.scalar_tensor_tensor(out=lf[:, :, :], in0=ff[:, :, :], scalar=0.0, in1=e[:, :, :], op0=ALU.min, op1=ALU.subtract).then_inc(lf_ready, 1)
                dve.wait_ge(cum_done, 1)
                cum = psum[:, 0, 0:NT * H].rearrange("p (t h) -> p t h", h=H)
                link(nc.vector.tensor_scalar(q[:, :, :, DH], cum, root, None, ALU.mult))
                link(nc.vector.tensor_scalar(k[:, :, :, DH + 1], cum, -root, None, ALU.mult))
                link(nc.vector.memset(q[:, :, :, DH + 1], 1.0))
                link(nc.vector.memset(k[:, :, :, DH], 1.0))
                dve.sem_inc(ext_ready, 1)

            @block.scalar
            def _(act):
                link = chain(act, act_order)
                act.wait_ge(abs_ready, 1)
                link(nc.scalar.activation(e[:, :, :], e[:, :, :], ACT.Exp))
                nc.scalar.activation(e[:, :, :], e[:, :, :], ACT.Ln, bias=1.0).then_inc(ln_ready, 1)

            @block.tensor
            def _(pe):
                pe.wait_ge(lf_ready, 1)
                for t in range(NT):
                    for j in range(t + 1):
                        last = nc.tensor.matmul(psum[:, 0, t * H:(t + 1) * H], tri[:, :] if j == t else ones[:, :], lf[:, j, :], start=j == 0, stop=j == t)
                last.then_inc(cum_done, 1)


def copy_pieces(nc, tag, pairs):
    with ExitStack() as ctx:
        (copied,) = ctx.enter_context(stage_sems(nc, f"{tag}_cp"))
        with nc.Block() as block:
            @block.sync
            def _(sp):
                for dst, src in pairs:
                    sp.dma_start(dst, src).then_inc(copied, 16)
                sp.wait_ge(copied, 16 * len(pairs))


def retention(nc, tag, psum, ident, q, k, v, consts, o):
    H, DK, DV = 4, 64, 128
    dmask_d, decay_d = consts
    with ExitStack() as ctx:
        sb = lambda m, s: ctx.enter_context(nc.sbuf_tensor(f"{tag}_{m}", s, F32))
        dm, dec = sb("dm", [P, H * P]), sb("dec", [P, 3, H])
        qs, ks, vs = sb("q", [P, NT, H * DK]), sb("k", [P, NT, H * DK]), sb("v", [P, NT, H * DV])
        qT, kT, sT, kd = sb("qT", [DK, NT, H * P]), sb("kT", [DK, NT, H * P]), sb("sT", [P, NT, H * P]), sb("kd", [P, NT, H * DK])
        state, ob = sb("state", [DK, H * DV]), sb("ob", [P, NT, H * DV])
        hv = lambda ap: ap.rearrange("p (h d) -> p h d", h=H)
        (consts_in, qk_in, v_in, tr_done, q_ev, k_ev, s_done, s_ready, mm_done, o_ready, stored, dve_order) = ctx.enter_context(stage_sems(
            nc, *[f"{tag}_{s}" for s in ("cin", "qkin", "vin", "tr", "qev", "kev", "sd", "sr", "mm", "or", "out", "dve")]))
        with nc.Block() as block:
            @block.sync
            def _(sp):
                sp.dma_start(qs[:, :, :], tiled(q)).then_inc(qk_in, 16)
                sp.dma_start(ks[:, :, :], tiled(k)).then_inc(qk_in, 16)
                sp.dma_start(dm[:, :], dmask_d).then_inc(consts_in, 16)
                sp.dma_start(dec[:, :, :].rearrange("p a h -> p (a h)"), decay_d).then_inc(consts_in, 16)
                sp.dma_start(vs[:, :, :], tiled(v)).then_inc(v_in, 16)
                for c in range(NT):
                    sp.wait_ge(o_ready, c + 1)
                    sp.dma_start(o[c * P:(c + 1) * P, :], ob[:, c, :]).then_inc(stored, 16)
                sp.wait_ge(stored, 16 * NT)

            @block.tensor
            def _(pe):
                def products(c):
                    pe.wait_ge(q_ev, c + 1)
                    pe.wait_ge(k_ev, c + 1)
                    if c:
                        pe.wait_ge(s_ready, c)
                    for h in range(H):
                        last = nc.tensor.matmul(psum[:, 2, h * P:(h + 1) * P], kT[:, c, h * P:(h + 1) * P], qT[:, c, h * P:(h + 1) * P], start=True, stop=True)
                    last.then_inc(s_done, 1)

                pe.wait_ge(qk_in, 32)
                for c in range(NT):
                    if c:
                        pe.wait_ge(q_ev, c)
                        pe.wait_ge(k_ev, c)
                    take_bank(nc, psum[:, 0, 0:P], ident)
                    for h in range(H):
                        nc.tensor.transpose(psum[0:DK, 0, h * P:(h + 1) * P], qs[:, c, h * DK:(h + 1) * DK], ident[:, :])
                        last = nc.tensor.transpose(psum[0:DK, 1, h * P:(h + 1) * P], ks[:, c, h * DK:(h + 1) * DK], ident[:, :])
                    last.then_inc(tr_done, 1)
                    if c:
                        products(c - 1)
                products(NT - 1)
                pe.wait_ge(v_in, 16)
                for c in range(NT):
                    pe.wait_ge(s_ready, c + 1)
                    if c:
                        pe.wait_ge(o_ready, c)
                    for h in range(H):
                        nc.tensor.matmul(psum[0:DK, 5, h * DV:(h + 1) * DV], kd[:, c, h * DK:(h + 1) * DK], vs[:, c, h * DV:(h + 1) * DV], start=True, stop=True)
                        nc.tensor.matmul(psum[:, 3, h * DV:(h + 1) * DV], sT[:, c, h * P:(h + 1) * P], vs[:, c, h * DV:(h + 1) * DV], start=True, stop=True)
                        last = nc.tensor.matmul(psum[:, 4, h * DV:(h + 1) * DV], qT[:, c, h * P:(h + 1) * P], state[:, h * DV:(h + 1) * DV], start=True, stop=True)
                    last.then_inc(mm_done, 1)

            @block.scalar
            def _(act):
                for c in range(NT):
                    act.wait_ge(tr_done, c + 1)
                    nc.scalar.copy(qT[:, c, :], psum[0:DK, 0, :]).then_inc(q_ev, 1)

            @block.vector
            def _(dve):
                link = chain(dve, dve_order)
                nc.vector.memset(state[:, :], 0.0)

                def decayed(c):
                    dve.wait_ge(s_done, c + 1)
                    nc.vector.tensor_tensor(sT[:, c, :], psum[:, 2, :], dm[:, :], ALU.mult).then_inc(s_ready, 1)

                for c in range(NT):
                    dve.wait_ge(tr_done, c + 1)
                    nc.vector.tensor_copy(kT[:, c, :], psum[0:DK, 1, :]).then_inc(k_ev, 1)
                    if c == 0:
                        dve.wait_ge(consts_in, 32)
                    nc.vector.tensor_tensor(hv(kd[:, c, :]), hv(ks[:, c, :]), bc_last(dec[:, 1, :], DK), ALU.mult)
                    if c:
                        decayed(c - 1)
                decayed(NT - 1)
                for c in range(NT):
                    dve.wait_ge(mm_done, c + 1)
                    nc.vector.tensor_tensor(hv(state[:, :]), hv(state[:, :]), bc_last(dec[0:DK, 2, :], DV), ALU.mult)
                    link(nc.vector.tensor_tensor(hv(ob[:, c, :]), hv(psum[:, 4, :]), bc_last(dec[:, 0, :], DV), ALU.mult))
                    nc.vector.tensor_tensor(ob[:, c, :], ob[:, c, :], psum[:, 3, :], ALU.add)
                    nc.vector.tensor_tensor(state[:, :], state[:, :], psum[0:DK, 5, :], ALU.add).then_inc(o_ready, 1)


def retention_gate_norm(nc, tag, o, g, out):
    H, DV = 4, 128
    W = H * DV
    with ExitStack() as ctx:
        sb = lambda m, s: ctx.enter_context(nc.sbuf_tensor(f"{tag}_{m}", s, F32))
        ys, gs, sq = sb("y", [P, NT, W]), sb("g", [P, NT, W]), sb("sq", [P, NT, W])
        mean, var, rt, tp = sb("mean", [P, NT, H]), sb("var", [P, NT, H]), sb("rt", [P, NT, H]), sb("tp", [P, NT, H])
        xin, silu_ready, var_ready, root_ready, dve_order, y_ready, stored = ctx.enter_context(stage_sems(
            nc, *[f"{tag}_{s}" for s in ("in", "silu", "var", "root", "dve", "y", "out")]))
        grp = lambda ap: ap.rearrange("p t (g d) -> p (t g) d", g=H)
        flat = lambda ap: ap[:, :, :].rearrange("p t g -> p (t g)")
        with nc.Block() as block:
            @block.sync
            def _(sp):
                sp.dma_start(gs[:, :, :], tiled(g)).then_inc(xin, 16)
                sp.dma_start(ys[:, :, :], tiled(o)).then_inc(xin, 16)
                for t in range(NT):
                    sp.wait_ge(y_ready, t + 1)
                    sp.dma_start(out[t * P:(t + 1) * P, :], ys[:, t, :]).then_inc(stored, 16)
                sp.wait_ge(stored, 16 * NT)

            @block.scalar
            def _(act):
                act.wait_ge(xin, 32)
                nc.scalar.activation(gs[:, :, :], gs[:, :, :], ACT.Silu).then_inc(silu_ready, 1)
                act.wait_ge(var_ready, 1)
                nc.scalar.activation(rt[:, :, :], var[:, :, :], ACT.Sqrt).then_inc(root_ready, 1)

            @block.vector
            def _(dve):
                link = chain(dve, dve_order)
                dve.wait_ge(xin, 32)
                link(nc.vector.tensor_reduce(flat(mean), grp(ys[:, :, :]), AX, ALU.add))
                link(nc.vector.tensor_scalar(mean[:, :, :], mean[:, :, :], 1.0 / DV, None, ALU.mult))
                link(nc.vector.tensor_tensor(grp(ys[:, :, :]), grp(ys[:, :, :]), bc_last(flat(mean), DV), ALU.subtract))
                link(nc.vector.tensor_tensor(sq[:, :, :], ys[:, :, :], ys[:, :, :], ALU.mult))
                link(nc.vector.tensor_reduce(flat(var), grp(sq[:, :, :]), AX, ALU.add))
                nc.vector.tensor_scalar(var[:, :, :], var[:, :, :], 1.0 / DV, EPS, ALU.mult, ALU.add).then_inc(var_ready, 1)
                dve.wait_ge(silu_ready, 1)
                dve.wait_ge(root_ready, 1)
                refined_root(nc, link, rt[:, :, :], var[:, :, :], tp[:, :, :])
                link(nc.vector.tensor_tensor(gs[:, :, :], gs[:, :, :], ys[:, :, :], ALU.mult))
                for t in range(NT):
                    tile = lambda ap: ap[:, t, :].rearrange("p (g d) -> p g d", g=H)
                    nc.vector.tensor_tensor(tile(ys), tile(gs), bc_last(rt[:, t, :], DV), ALU.mult).then_inc(y_ready, 1)


def moe_route(nc, tag, psum, tri, logits, bias, iota, token_w, pair_w, pair_row, crowded):
    W = N_GRP + N_EXPERTS
    iota8 = iota[:, 0:8]
    with ExitStack() as ctx:
        sb = lambda m, s, d=F32: ctx.enter_context(nc.sbuf_tensor(f"{tag}_{m}", s, d))
        lg, bs = sb("lg", [P, NT, W]), sb("bs", [P, W])
        gl, gtop, gi, gif, goh = sb("gl", [P, NT, 8]), sb("gtop", [P, NT, 8]), sb("gi", [P, NT, 8], U32), sb("gif", [P, NT, 8]), sb("goh", [P, NT, 8])
        tmp, ing, etop, ei, eif = sb("tmp", [P, N_GRP, 8]), sb("ing", [P, NT, 8]), sb("etop", [P, NT, 8]), sb("ei", [P, NT, 8], U32), sb("eif", [P, NT, 8])
        s1, s2, wsel, wj = sb("s1", [P, NT]), sb("s2", [P, NT]), sb("wsel", [P, NT, 8]), sb("wj", [P, NT, 8])
        oh, sel, ones = sb("oh", [P, 2, NT, N_EXPERTS]), sb("sel", [P, NT, N_EXPERTS]), sb("ones", [P, P])
        base, rank, rowf, most = sb("base", [P, N_EXPERTS]), sb("rank", [P, NT, N_EXPERTS]), sb("rowf", [P, NT, 2]), sb("most", [P, 1])
        xin, diff_ready, exp_ready, sel_ready, rank_done, dve_order = ctx.enter_context(stage_sems(
            nc, *[f"{tag}_{s}" for s in ("in", "diff", "exp", "sel", "rank", "dve")]))
        by_group = lambda ap: ap.rearrange("p (g j) -> p g j", g=N_GRP)
        with nc.Block() as block:
            @block.sync
            def _(sp):
                sp.dma_start(lg[:, :, :], tiled(logits)).then_inc(xin, 16)
                sp.dma_start(bs[:, :], row_bc(bias)).then_inc(xin, 16)

            @block.tensor
            def _(pe):
                pe.wait_ge(sel_ready, 1)
                for t in range(NT):
                    for j in range(t + 1):
                        nc.tensor.matmul(psum[:, 0, t * N_EXPERTS:(t + 1) * N_EXPERTS], tri[:, :] if j == t else ones[:, :], sel[:, j, :],
                                         start=j == 0, stop=j == t)
                for j in range(NT):
                    last = nc.tensor.matmul(psum[:, 0, NT * N_EXPERTS:(NT + 1) * N_EXPERTS], ones[:, :], sel[:, j, :], start=j == 0, stop=j == NT - 1)
                last.then_inc(rank_done, 1)

            @block.vector
            def _(dve):
                link = chain(dve, dve_order)
                link(nc.vector.memset(ones[:, :], 1.0))
                link(nc.vector.memset(gl[:, :, :], NEG))
                link(nc.vector.tensor_scalar(base[:, :], iota[:, 0:N_EXPERTS], float(P), None, ALU.mult))
                dve.wait_ge(xin, 32)
                link(nc.vector.tensor_tensor(lg[:, :, :], lg[:, :, :], bc_mid(bs[:, :], NT), ALU.add))
                link(nc.vector.tensor_copy(gl[:, :, 0:N_GRP], lg[:, :, 0:N_GRP]))
                for t in range(NT):
                    link(nc.vector.max(gtop[:, t, :], gl[:, t, :]))
                    link(nc.vector.max_index(gi[:, t, :], gtop[:, t, :], gl[:, t, :]))
                link(nc.vector.tensor_copy(gif[:, :, :], gi[:, :, :]))
                for t in range(NT):
                    link(nc.vector.tensor_scalar(goh[:, t, :], iota8, gif[:, t, 0:1], None, ALU.is_equal))
                    link(nc.vector.tensor_tensor(tmp[:, :, :], by_group(lg[:, t, N_GRP:W]), bc_last(goh[:, t, 0:N_GRP], EPG), ALU.mult))
                    link(nc.vector.tensor_reduce(ing[:, t, :], tmp[:, :, :].rearrange("p g j -> p j g"), AX, ALU.add))
                    link(nc.vector.max(etop[:, t, :], ing[:, t, :]))
                    link(nc.vector.max_index(ei[:, t, :], etop[:, t, :], ing[:, t, :]))
                    link(nc.vector.tensor_scalar(gl[:, t, 0:N_GRP], gl[:, t, 0:N_GRP], gtop[:, t, 0:1], None, ALU.subtract))
                    link(nc.vector.tensor_scalar(wsel[:, t, :], etop[:, t, :], etop[:, t, 0:1], None, ALU.subtract))
                link(nc.vector.tensor_copy(eif[:, :, :], ei[:, :, :]))
                dve.sem_inc(diff_ready, 1)
                for c in range(2):
                    for t in range(NT):
                        link(nc.vector.tensor_scalar(wj[:, t, :], iota8, eif[:, t, c:c + 1], None, ALU.is_equal))
                        link(nc.vector.tensor_tensor(by_group(oh[:, c, t, :]), bc_last(goh[:, t, 0:N_GRP], EPG), bc_mid(wj[:, t, :], N_GRP), ALU.mult))
                link(nc.vector.tensor_tensor(sel[:, :, :], oh[:, 0, :, :], oh[:, 1, :, :], ALU.add))
                dve.sem_inc(sel_ready, 1)
                dve.wait_ge(exp_ready, 1)
                link(nc.vector.tensor_reduce(s1[:, :], gl[:, :, 0:N_GRP], AX, ALU.add))
                link(nc.vector.reciprocal(s1[:, :], s1[:, :]))
                link(nc.vector.tensor_reduce(s2[:, :], wsel[:, :, :], AX, ALU.add))
                link(nc.vector.reciprocal(s2[:, :], s2[:, :]))
                link(nc.vector.tensor_tensor(wsel[:, :, :], wsel[:, :, :], bc_last(s2[:, :], 8), ALU.mult))
                link(nc.vector.tensor_reduce(s2[:, :], wsel[:, :, 0:2], AX, ALU.add))
                link(nc.vector.reciprocal(s2[:, :], s2[:, :]))
                link(nc.vector.tensor_tensor(s2[:, :], s2[:, :], s1[:, :], ALU.mult))
                link(nc.vector.tensor_tensor(pair_w[:, :, :], wsel[:, :, 0:2], bc_last(s2[:, :], 2), ALU.mult))
                dve.wait_ge(rank_done, 1)
                link(nc.vector.tensor_tensor(rank[:, :, :], psum[:, 0, 0:NT * N_EXPERTS].rearrange("p (t e) -> p t e", t=NT), bc_mid(base[:, :], NT), ALU.add))
                link(nc.vector.tensor_reduce(most[:, :], psum[:, 0, NT * N_EXPERTS:(NT + 1) * N_EXPERTS], AX, ALU.max))
                link(nc.vector.tensor_scalar(crowded[:, :], most[:, :], float(P), None, ALU.is_gt))
                for c in range(2):
                    link(nc.vector.tensor_tensor(sel[:, :, :], oh[:, c, :, :], rank[:, :, :], ALU.mult))
                    link(nc.vector.tensor_reduce(rowf[:, :, c], sel[:, :, :], AX, ALU.add))
                    link(nc.vector.tensor_tensor(oh[:, c, :, :], oh[:, c, :, :], bc_last(pair_w[:, :, c], N_EXPERTS), ALU.mult))
                link(nc.vector.tensor_scalar(pair_row[:, :, :], rowf[:, :, :], -1.0, None, ALU.add))
                link(nc.vector.tensor_tensor(token_w[:, :, :], oh[:, 0, :, :], oh[:, 1, :, :], ALU.add))

            @block.scalar
            def _(act):
                act.wait_ge(diff_ready, 1)
                nc.scalar.activation(gl[:, :, 0:N_GRP], gl[:, :, 0:N_GRP], ACT.Exp)
                nc.scalar.activation(wsel[:, :, :], wsel[:, :, :], ACT.Exp).then_inc(exp_ready, 1)


def moe_slots(nc, tag, psum, ident, tokens, pair_row, table, slot_token):
    with ExitStack() as ctx:
        sb = lambda m, s, d: ctx.enter_context(nc.sbuf_tensor(f"{tag}_{m}", s, d))
        zero, rows, rows_f = sb("zero", [N_EXPERTS, P], I32), sb("rows", [N_EXPERTS, P], I32), sb("rowsf", [N_EXPERTS, P], F32)
        zero_ready, cleared, scattered, rows_in, rows_ready, turned = ctx.enter_context(stage_sems(
            nc, *[f"{tag}_{s}" for s in ("zero", "clr", "sc", "rin", "rr", "turn")]))
        table_v = table.rearrange("(e s) o -> e (s o)", e=N_EXPERTS)
        with nc.Block() as block:
            @block.sync
            def _(sp):
                sp.wait_ge(zero_ready, 1)
                sp.dma_start(table_v, zero[:, :]).then_inc(cleared, 16)
                sp.wait_ge(scattered, 16 * 2 * NT)
                sp.dma_start(rows[:, :], table_v).then_inc(rows_in, 16)

            @block.gpsimd
            def _(pool):
                pool.wait_ge(cleared, 16)
                for t in range(NT):
                    for c in range(2):
                        pool.indirect_dma_start(out=table[:, :], out_offset=bass.IndirectOffsetOnAxis(ap=pair_row[:, t, c:c + 1], axis=0),
                                                in_=tokens[:, t:t + 1], in_offset=None).then_inc(scattered, 16)

            @block.vector
            def _(dve):
                nc.vector.memset(zero[:, :], 0).then_inc(zero_ready, 1)
                dve.wait_ge(rows_in, 16)
                nc.vector.tensor_copy(rows_f[:, :], rows[:, :]).then_inc(rows_ready, 1)
                dve.wait_ge(turned, 1)
                nc.vector.tensor_copy(slot_token[:, :], psum[:, 0, 0:N_EXPERTS])

            @block.tensor
            def _(pe):
                pe.wait_ge(rows_ready, 1)
                nc.tensor.transpose(psum[:, 0, 0:N_EXPERTS], rows_f[:, :], ident[0:N_EXPERTS, 0:N_EXPERTS]).then_inc(turned, 1)


def moe_experts(nc, tag, psum, ident, x, slot_token, w_a, w_b, w_out, y, col_ready):
    FB = D_EXP // P
    n = N_EXPERTS
    with ExitStack() as ctx:
        sb = lambda m, s, d=F32: ctx.enter_context(nc.sbuf_tensor(f"{tag}_{m}", s, d))
        wa, wb, wo = sb("wa", [P, 2, KD, CH]), sb("wb", [P, 2, KD, CH]), sb("wo", [P, 2, FB, D])
        rows, xg, hidT, y_sb = sb("rows", [P, 2, D]), sb("xg", [P, 2, KD, P]), sb("hidT", [P, FB, P]), sb("y", [P, 2, D])
        nl, hid = sb("nl", [P, D_EXP]), sb("hid", [P, D_EXP])
        col0, col1 = sb("col0", [P, 1], U32), sb("col1", [P, 1], U32)
        (in0, in1, rows0, rows1, x_turned, xg_ready, gu_done, nl_ready, hid_ready, h_turned, hT_ready, o_done, y_ready, out0, out1) = \
            ctx.enter_context(stage_sems(nc, *[f"{tag}_{s}" for s in (
                "in0", "in1", "rows0", "rows1", "xt", "xg", "gu", "nl", "hid", "ht", "hTr", "od", "yr", "out0", "out1")]))
        loaded, rows_in, stored, cols = (in0, in1), (rows0, rows1), (out0, out1), (col0, col1)
        with nc.Block() as block:
            @block.sync
            def _(sp):
                with sp.Fori(0, n // 2) as i:
                    for u in range(2):
                        e = i * 2 + u
                        sp.wait_ge(gu_done, e + 1)
                        sp.dma_start(wa[:, u, :, :], w_a(e)).then_inc(loaded[u], 16)
                        sp.dma_start(wb[:, u, :, :], w_b(e)).then_inc(loaded[u], 16)
                        sp.wait_ge(o_done, e + 1)
                        sp.dma_start(wo[:, u, :, :], w_out(e)).then_inc(loaded[u], 16)

            @block.gpsimd
            def _(pool):
                with pool.Fori(0, n // 2) as i:
                    for u in range(2):
                        pool.sem_clear(col_ready)
                        pool.wait_ge(x_turned, i * 2 + (u + 1))
                        nc.gpsimd.tensor_copy(cols[u][:, :], slot_token[:, ds(i * 2 + u, 1)]).then_inc(col_ready, 1)
                        pool.wait_ge(col_ready, 1)
                        pool.indirect_dma_start(out=rows[:, u, :], out_offset=None, in_=x[:, :],
                                                in_offset=bass.IndirectOffsetOnAxis(ap=cols[u][:, :], axis=0)).then_inc(rows_in[u], 16)

            @block.tensor
            def _(pe):
                pe.sem_inc(o_done, 2)
                pe.sem_inc(gu_done, 2)
                pe.sem_inc(x_turned, 2)

                def turn_rows(u, turn, evacuated, half):
                    if half == 0:
                        pe.wait_ge(rows_in[u], turn * 16 + 16)
                        pe.wait_ge(xg_ready, evacuated)
                    for k in range(half * KD // 2, (half + 1) * KD // 2):
                        last = nc.tensor.transpose(psum[:, k // 4, k % 4 * P:(k % 4 + 1) * P], rows[:, u, k * P:(k + 1) * P], ident[:, :])
                    if half == 1:
                        last.then_inc(x_turned, 1)

                def expert(e, u, turn, is_last):
                    pe.wait_ge(xg_ready, e * 2 + 4)
                    pe.wait_ge(loaded[u], turn * 48 + 48)
                    pe.wait_ge(hid_ready, e + 1)
                    for bank, w in ((2, wa), (3, wb)):
                        for k in range(KD):
                            last = nc.tensor.matmul(psum[:, bank, :], xg[:, u, k, :], w[:, u, k, :], start=k == 0, stop=k == KD - 1)
                    last.then_inc(gu_done, 1)
                    if not is_last:
                        turn_rows(1 - u, turn + u, e * 2 + 4, 0)
                    pe.wait_ge(hid_ready, e + 2)
                    for f in range(FB):
                        last = nc.tensor.transpose(psum[:, 4, f * P:(f + 1) * P], hid[:, f * P:(f + 1) * P], ident[:, :])
                    last.then_inc(h_turned, 1)
                    if not is_last:
                        turn_rows(1 - u, turn + u, e * 2 + 4, 1)
                    pe.wait_ge(hT_ready, e + 1)
                    pe.wait_ge(y_ready, e + 1)
                    for half in range(2):
                        for f in range(FB):
                            last = nc.tensor.matmul(psum[:, 5 + half, :], hidT[:, f, :], wo[:, u, f, half * CH:(half + 1) * CH], start=f == 0, stop=f == FB - 1)
                    last.then_inc(o_done, 1)

                turn_rows(0, 0, 2, 0)
                turn_rows(0, 0, 2, 1)
                with pe.Fori(0, n // 2 - 1) as i:
                    for u in range(2):
                        expert(i * 2 + u, u, i, False)
                expert(n - 2, 0, n // 2 - 1, False)
                expert(n - 1, 1, n // 2 - 1, True)

            @block.scalar
            def _(act):
                act.sem_inc(xg_ready, 2)
                act.sem_inc(out0, 16)
                act.sem_inc(out1, 16)

                def take_rows(u, e):
                    act.wait_ge(x_turned, e + 3)
                    for b in range(2):
                        nc.scalar.copy(xg[:, u, b * 4:(b + 1) * 4, :], psum[:, b, :].rearrange("p (k s) -> p k s", s=P)).then_inc(xg_ready, 1)

                def expert(e, u, turn, is_last):
                    act.wait_ge(gu_done, e + 3)
                    nc.scalar.activation(nl[:, :], psum[:, 2, :], ACT.Silu).then_inc(nl_ready, 1)
                    act.wait_ge(h_turned, e + 1)
                    nc.scalar.copy(hidT[:, :, :], psum[:, 4, :].rearrange("p (f s) -> p f s", s=P)).then_inc(hT_ready, 1)
                    if not is_last:
                        take_rows(1 - u, e + 1)
                    act.wait_ge(y_ready, e + 2)
                    act.dma_start(y[ds(e * P, P), :], y_sb[:, u, :]).then_inc(stored[u], 16)

                take_rows(0, 0)
                with act.Fori(0, n // 2 - 1) as i:
                    for u in range(2):
                        expert(i * 2 + u, u, i, False)
                expert(n - 2, 0, n // 2 - 1, False)
                expert(n - 1, 1, n // 2 - 1, True)
                act.wait_ge(out0, n // 2 * 16 + 16)
                act.wait_ge(out1, n // 2 * 16 + 16)

            @block.vector
            def _(dve):
                dve.sem_inc(hid_ready, 1)
                dve.sem_inc(y_ready, 1)
                with dve.Fori(0, n // 2) as i:
                    for u in range(2):
                        e = i * 2 + u
                        dve.wait_ge(nl_ready, e + 1)
                        nc.vector.tensor_tensor(hid[:, :], nl[:, :], psum[:, 3, :], ALU.mult).then_inc(hid_ready, 1)
                        dve.wait_ge(o_done, e + 3)
                        dve.wait_ge(stored[u], i * 16 + 16)
                        for half in range(2):
                            last = nc.vector.tensor_copy(y_sb[:, u, half * CH:(half + 1) * CH], psum[:, 5 + half, :])
                        last.then_inc(y_ready, 1)


def moe_collect(nc, tag, y, pair_row, pair_w, acc):
    with ExitStack() as ctx:
        rows = ctx.enter_context(nc.sbuf_tensor(f"{tag}_rows", [P, NT, 2, D], F32))
        rows_in, dve_order = ctx.enter_context(stage_sems(nc, f"{tag}_in", f"{tag}_dve"))
        with nc.Block() as block:
            @block.gpsimd
            def _(pool):
                for t in range(NT):
                    for c in range(2):
                        pool.indirect_dma_start(out=rows[:, t, c, :], out_offset=None, in_=y[:, :],
                                                in_offset=bass.IndirectOffsetOnAxis(ap=pair_row[:, t, c:c + 1], axis=0)).then_inc(rows_in, 16)

            @block.vector
            def _(dve):
                link = chain(dve, dve_order)
                dve.wait_ge(rows_in, 32 * NT)
                for t in range(NT):
                    link(nc.vector.tensor_scalar(acc[:, t, :], rows[:, t, 0, :], pair_w[:, t, 0:1], None, ALU.mult))
                    link(nc.vector.scalar_tensor_tensor(out=acc[:, t, :], in0=rows[:, t, 1, :], scalar=pair_w[:, t, 1:2], in1=acc[:, t, :],
                                                        op0=ALU.mult, op1=ALU.add))


def build(nc, a, out):
    dram = lambda name, shape: nc.dram_tensor(name, shape, F32, kind="Internal").ap()
    with ExitStack() as ctx:
        sb = lambda m, s: ctx.enter_context(nc.sbuf_tensor(m, s, F32))
        psum = ctx.enter_context(nc.psum_tensor("psum", [P, 8, CH], F32))
        ident, tri, iota = sb("ident", [P, P]), sb("tri", [P, P]), sb("iota", [P, P])
        tokens = ctx.enter_context(nc.sbuf_tensor("tokens", [P, NT], I32))
        h = sb("h", [P, NT, D])
        xT = [ctx.enter_context(nc.sbuf_tensor(n, [P, KD, T], F32R)) for n in ("xT_high", "xT_low")]
        with ExitStack() as st:
            (cin,) = st.enter_context(stage_sems(nc, "consts_in"))
            with nc.Block() as block:
                @block.sync
                def _(sp):
                    sp.dma_start(ident[:, :], a["c_ident"]).then_inc(cin, 16)
                    sp.dma_start(tri[:, :], a["c_tri"]).then_inc(cin, 16)
                    sp.dma_start(iota[:, :], a["c_iota"]).then_inc(cin, 16)
                    sp.dma_start(h[:, :, :], tiled(a["x"][0])).then_inc(cin, 16)
                    sp.dma_start(tokens[:, :], a["c_tokens"]).then_inc(cin, 16)
                    sp.wait_ge(cin, 80)

        u_gain = a["norm_mix_w"][0]
        proj = dram("proj", [T, IN_W])
        xbcT, convT, conv_tok = dram("xbcT", [XBC, T]), dram("convT", [XBC, T]), dram("conv_tok", [T, XBC])
        w_in = a["w_in"][0]
        linear(nc, "lz", psum, xT, KD, w_in[:, 0:D], proj[:, 0:D], D,
               before=NormTurn(nc, "n1", psum, ident, h, u_gain, xT))
        linear(nc, "lx", psum, xT, KD, w_in[:, OFF_XBC:OFF_DT], xbcT, XBC, feature_major=True)
        linear(nc, "ldt", psum, xT, KD, w_in[:, OFF_DT:OFF_DQ], proj[:, OFF_DT:OFF_DQ], OFF_DQ - OFF_DT)
        dt, da, y_raw, y_ssd = dram("dt", [T, HEADS]), dram("da", [T, HEADS]), dram("y_raw", [T, D]), dram("y_ssd", [T, D])
        conv_silu(nc, "cv", psum, ident, xbcT, a["taps"], convT, conv_tok)
        ssd_dt(nc, "sdt", proj[:, OFF_DT:OFF_DQ], a["ssd_dt_bias"][0], a["ssd_a_log"][0], dt, da)
        ssd_scan(nc, "ssd", psum, tri, convT, conv_tok, dt, da, a["ssd_d"][0], y_raw, xT, w_in[:, OFF_DQ:IN_W], proj[:, OFF_DQ:IN_W])
        ssd_gate_norm(nc, "sgn", y_raw, proj[:, 0:D], a["ssd_norm_w"][0], y_ssd)

        qd, kd, od, lse = dram("qd", [T, 12, HD]), dram("kd", [T, 12, HD]), dram("od", [T, 12, HD]), dram("lse", [T, 12])
        with ExitStack() as st:
            cos = st.enter_context(nc.sbuf_tensor("cos1", [P, NT, 8], F32))
            sin = st.enter_context(nc.sbuf_tensor("sin1", [P, NT, 8], F32))
            rope_tables(nc, "rt1", a["positions"][0], a["c_inv1"], 8, cos, sin)
            prep_only(nc, HeadPrep(nc, "pdq", proj[:, OFF_DQ:OFF_DK], qd, 12, HD, a["dil_q_norm_w"][0], cos, sin, 16),
                      HeadPrep(nc, "pdk", proj[:, OFF_DK:OFF_DV], kd, 12, HD, a["dil_k_norm_w"][0], cos, sin, 16))
        vd = proj[:, OFF_DV:OFF_MQ].rearrange("t (h d) -> t h d", d=HD)
        for g in range(DIL):
            hs = slice(g * 4, g * 4 + 4)
            span = (lambda qt: (max(0, qt - 1), qt + 1)) if g == 0 else (lambda qt: (0, qt + 1))
            attention(nc, f"da{g}", psum, ident, qd[:, hs, :], kd[:, hs, :], vd[:, hs, :], od[:, hs, :], [HD], HD, HD ** -0.5, NT,
                      mask=a["c_mask"][g], span=span, lse=lse[:, hs])
        y_dil = dram("y_dil", [T, 4 * HD])
        dil_combine(nc, "dc", od.rearrange("t h d -> t (h d)"), lse, y_dil)

        MT = N_MEM // P
        MHD = MEM_W // 4
        mkv, mk, mqn, y_mem = dram("mkv", [N_MEM, 2 * MEM_W]), dram("mk", [N_MEM, 4, MHD]), dram("mqn", [T, 4, MHD]), dram("y_mem", [T, 4, MHD])
        with ExitStack() as st:
            mem = st.enter_context(nc.sbuf_tensor("mem_sb", [P, MT, D], F32))
            memT = [st.enter_context(nc.sbuf_tensor(f"memT_{h}", [P, KD, N_MEM], F32R)) for h in ("high", "low")]
            (min_,) = st.enter_context(stage_sems(nc, "mem_in"))
            with nc.Block() as block:
                @block.sync
                def _(sp):
                    sp.dma_start(mem[:, :, :], tiled(a["mem"][0])).then_inc(min_, 16)
                    sp.wait_ge(min_, 16)
            linear(nc, "lm", psum, memT, KD, a["w_mem_kv"][0], mkv, 2 * MEM_W, tiles=MT,
                   before=NormTurn(nc, "nm", psum, ident, mem, a["mem_norm_w"][0], memT, tiles=MT))
        prep_only(nc, HeadPrep(nc, "pmk", mkv[:, 0:MEM_W], mk, 4, MHD, a["mem_k_norm_w"][0]),
                  HeadPrep(nc, "pmq", proj[:, OFF_MQ:OFF_GATE], mqn, 4, MHD, a["mem_q_norm_w"][0]))
        mv = mkv[:, MEM_W:2 * MEM_W].rearrange("t (h d) -> t h d", d=MHD)
        attention(nc, "ma", psum, ident, mqn, mk, mv, y_mem, [P, MHD - P], MHD, MHD ** -0.5, MT)

        with ExitStack() as st:
            merged = st.enter_context(nc.sbuf_tensor("merged", [P, NT, D], F32))
            for i, (y, width, w) in enumerate(((y_ssd, D, a["w_ssd_br"][0]), (y_dil, 4 * HD, a["w_dil_br"][0]),
                                               (y_mem.rearrange("t h d -> t (h d)"), MEM_W, a["w_mem_br"][0]))):
                linear(nc, f"bl{i}", psum, xT, width // P, w, None, D,
                       before=LoadTurn(nc, f"bt{i}", psum, ident, y, xT, width),
                       into=GatedSum(nc, f"bg{i}", merged, proj[:, OFF_GATE + i * D:OFF_GATE + (i + 1) * D], None, i == 0))
            linear(nc, "ml", psum, xT, KD, a["w_out"][0], None, D,
                   before=HeldTurn(nc, "mt", psum, ident, merged, xT, D), into=Sum(nc, "ms", h))

        qT, sel, gates = dram("peer_qT", [2 * P * PEER_H, T]), dram("peer_sel", [T, 3, P]), dram("peer_gates", [NT, NK, NK, P])
        linear(nc, "pq", psum, xT, KD, a["peer_w_query"][0], qT, 2 * P * PEER_H, feature_major=True,
               before=NormTurn(nc, "n2", psum, ident, h, a["norm_ffn_w"][0], xT))
        mods = dram("mods", [LAYERS, 1, 6 * D])
        peer_route(nc, "pr", psum, qT, a["keysT"], iota[:, 0:TOPK], sel, a["c_2"][0], a["ada_w_2"], mods)
        with ExitStack() as st:
            selT = st.enter_context(nc.sbuf_tensor("selT", [P, 3, T], F32))
            with ExitStack() as turn:
                halves = [turn.enter_context(nc.sbuf_tensor(f"selT_{h}", [P, 3, T], F32R)) for h in ("high", "low")]
                turn_only(nc, LoadTurn(nc, "pst", psum, ident, sel.rearrange("t a k -> t (a k)"), halves, 3 * P))
                join_halves(nc, "psj", halves, selT)
            peer_gates(nc, "pg", psum, selT, iota[:, :], gates)

        def add_acc(tag, acc, gate=None):
            with ExitStack() as st:
                gs = st.enter_context(nc.sbuf_tensor(f"{tag}_g", [P, D], F32))
                gin, order = st.enter_context(stage_sems(nc, f"{tag}_gin", f"{tag}_ord"))
                with nc.Block() as block:
                    @block.sync
                    def _(sp):
                        if gate is not None:
                            sp.dma_start(gs[:, :], row_bc(gate)).then_inc(gin, 16)

                    @block.vector
                    def _(dve):
                        link = chain(dve, order)
                        if gate is not None:
                            dve.wait_ge(gin, 16)
                        for t in range(NT):
                            if gate is not None:
                                link(nc.vector.tensor_tensor(acc[:, t, :], acc[:, t, :], gs[:, :], ALU.mult))
                            link(nc.vector.tensor_tensor(h[:, t, :], h[:, t, :], acc[:, t, :], ALU.add))

        downT = a["downT"].rearrange("(k p) e -> p k e", p=P)
        up = a["peer_up"][0].rearrange("(f p) d -> p f d", p=P)
        with ExitStack() as st:
            acc = st.enter_context(nc.sbuf_tensor("peer_acc", [P, NT, D], F32))
            peer_experts(nc, "pf", psum, xT, acc, downT, up, gates)
            add_acc("pa", acc)

        adaptive_bias(nc, "ada", a["ada_b_2"], mods)
        cos = sb("cos2", [P, NT, 32])
        sin = sb("sin2", [P, NT, 32])
        rope_tables(nc, "rt2", a["positions_2"][0], a["c_inv2"], 32, cos, sin)
        proj2, gates2, h2 = dram("proj2", [T, D_IN2]), dram("gates2", [T, 3 * D]), None
        rq, rk, ro, ya = dram("rq", [T, 4, 64]), dram("rk", [T, 4, 64]), dram("ro", [T, 512]), dram("ya", [T, 512])
        qa, ka, yb = dram("qa", [T, 4, 130]), dram("ka", [T, 4, 130]), dram("yb", [T, 4, 128])
        qh, qr, kvh, kp, kc, yc = (dram("qh", [T, 768]), dram("qr", [T, 4, 192]), dram("kvh", [T, 1024]), dram("kp", [T, 1, 64]),
                                   dram("kc", [T, 4, 192]), dram("yc", [T, 4, 128]))
        logits, h_norm, y_exp = dram("logits", [T, 36]), dram("h_norm", [T, D]), dram("y_exp", [N_EXPERTS * P, D])
        table = nc.dram_tensor("table", [N_EXPERTS * P, 1], I32, kind="Internal").ap()
        causal = lambda qt: (0, qt + 1)
        for l in range(LAYERS):
            mod = [mods[l][0, i * D:(i + 1) * D] for i in range(6)]
            linear(nc, f"i{l}", psum, xT, KD, a["w_in_2"][l], proj2, D_IN2,
                   before=NormTurn(nc, f"m{l}", psum, ident, h, a["norm1_g_2"][l], xT, shift=mod[0], scale=mod[1]))
            linear(nc, f"g{l}", psum, xT, KD, a["gate_w_2"][l], gates2, 3 * D,
                   beside=[HeadPrep(nc, f"rq{l}", proj2[:, RQ:RK], rq, 4, 64, None, cos, sin, 64),
                           HeadPrep(nc, f"rk{l}", proj2[:, RK:RV], rk, 4, 64, None, cos, sin, 64),
                           HeadPrep(nc, f"hk{l}", proj2[:, MKR:D_IN2], kp, 1, 64, None, cos, sin, 64)])
            retention(nc, f"re{l}", psum, ident, rq.rearrange("t h d -> t (h d)"), rk.rearrange("t h d -> t (h d)"), proj2[:, RV:RG],
                      (a["c_dmask"], a["c_decay"]), ro)
            retention_gate_norm(nc, f"rn{l}", ro, proj2[:, RG:FQ], ya)
            fox_prep(nc, f"fp{l}", psum, tri, proj2, a["fox_fb_2"][l], qa, ka)
            fv = proj2[:, FV:FF].rearrange("t (h d) -> t h d", h=4)
            attention(nc, f"fa{l}", psum, ident, qa, ka, fv, yb, [P, 2], P, P ** -0.5, NT, mask=a["c_mask"][3], span=causal)
            with ExitStack() as st:
                lat = st.enter_context(nc.sbuf_tensor(f"lat{l}", [P, NT, 384], F32))
                latT = [st.enter_context(nc.sbuf_tensor(f"latT{l}_{h}", [P, 2, T], F32R)) for h in ("high", "low")]
                (lin,) = st.enter_context(stage_sems(nc, f"lat_in{l}"))
                with nc.Block() as block:
                    @block.sync
                    def _(sp):
                        sp.dma_start(lat[:, :, :], tiled(proj2)[:, :, MQ2:MKR]).then_inc(lin, 16)
                        sp.wait_ge(lin, 16)
                linear(nc, f"lq{l}", psum, latT, 2, a["mla_wq_up_2"][l], qh, 768,
                       before=NormTurn(nc, f"nq{l}", psum, ident, lat[:, :, 0:256], a["mla_q_norm_g_2"][l], latT, width=256))
                linear(nc, f"lk{l}", psum, latT, 1, a["mla_wkv_up_2"][l], kvh, 1024,
                       before=NormTurn(nc, f"nk{l}", psum, ident, lat[:, :, 256:384], a["mla_kv_norm_g_2"][l], latT, width=128),
                       beside=[HeadPrep(nc, f"hq{l}", qh, qr, 4, 192, None, cos, sin, 64, 128)])
            kv = kvh.rearrange("t (h d) -> t h d", h=4)
            copy_pieces(nc, f"kc{l}", [(kc[:, :, 0:P], kv[:, :, 0:P])] + [(kc[:, i:i + 1, P:P + 64], kp) for i in range(4)])
            attention(nc, f"la{l}", psum, ident, qr, kc, kv[:, :, P:2 * P], yc, [P, 64], P, 192 ** -0.5, NT, mask=a["c_mask"][3], span=causal)
            with ExitStack() as st:
                merged = st.enter_context(nc.sbuf_tensor(f"merged{l}", [P, NT, D], F32))
                for i, y in enumerate((ya, yb.rearrange("t h d -> t (h d)"), yc.rearrange("t h d -> t (h d)"))):
                    linear(nc, f"bl{l}{i}", psum, xT, 4, a["branch_w_2"][l, i], None, D,
                           before=LoadTurn(nc, f"bt{l}{i}", psum, ident, y, xT, 512),
                           into=GatedSum(nc, f"bg{l}{i}", merged, gates2[:, i * D:(i + 1) * D], a["gate_b_2"][l][i * D:(i + 1) * D], i == 0))
                linear(nc, f"ml{l}", psum, xT, KD, a["out_w_2"][l], None, D,
                       before=HeldTurn(nc, f"mt{l}", psum, ident, merged, xT, D), into=ScaledSum(nc, f"ms{l}", h, mod[2]))
            linear(nc, f"rl{l}", psum, xT, KD, a["router_w"][l], logits, 36,
                   before=NormTurn(nc, f"k{l}", psum, ident, h, a["norm2_g_2"][l], xT, shift=mod[3], scale=mod[4], keep=h_norm))
            with ExitStack() as st:
                sbt = lambda m, s, d=F32: st.enter_context(nc.sbuf_tensor(f"{m}{l}", s, d))
                token_w, acc = sbt("token_w", [P, NT, N_EXPERTS]), sbt("moe_acc", [P, NT, D])
                pair_w, pair_row = sbt("pair_w", [P, NT, 2]), sbt("pair_row", [P, NT, 2], U32)
                crowded, slot_token = sbt("crowded", [P, 1], I32), sbt("slot_token", [P, N_EXPERTS], U32)
                moe_route(nc, f"mr{l}", psum, tri, logits, a["router_b"][l], iota, token_w, pair_w, pair_row, crowded)
                w1, w3 = (a[n][l].rearrange("e (k p) f -> p (e k) f", p=P) for n in ("exp_w1_2", "exp_w3_2"))
                w2 = a["exp_w2_2"][l].rearrange("e (f p) d -> p (e f) d", p=P)
                take_w1, take_w3 = (lambda e: w1[:, ds(e * KD, KD), :]), (lambda e: w3[:, ds(e * KD, KD), :])
                take_w2 = lambda e: w2[:, ds(e * 4, 4), :]
                (col_ready,) = st.enter_context(stage_sems(nc, f"col{l}"))
                over = nc.values_load(crowded[0:1, 0:1], min_val=0, max_val=1)
                with nc.If(over == 1):
                    moe_dense(nc, f"mf{l}", psum, xT, acc, N_EXPERTS, take_w1, take_w2, take_w3, token_w)
                with nc.Else():
                    moe_slots(nc, f"ms{l}", psum, ident, tokens, pair_row, table, slot_token)
                    moe_experts(nc, f"me{l}", psum, ident, h_norm, slot_token, take_w1, take_w3, take_w2, y_exp, col_ready)
                    moe_collect(nc, f"mc{l}", y_exp, pair_row, pair_w, acc)
                add_acc(f"aa{l}", acc, gate=mod[5])

        turn_only(nc, NormTurn(nc, "nf", psum, ident, h, a["final_g_2"], xT, keep=out[0]))


_INPUTS = ("x", "mem", "positions", "norm_mix_w", "w_in", "ssd_dt_bias", "ssd_a_log", "ssd_d", "ssd_norm_w", "dil_q_norm_w",
           "dil_k_norm_w", "mem_norm_w", "w_mem_kv", "mem_q_norm_w", "mem_k_norm_w", "w_ssd_br", "w_dil_br", "w_mem_br", "w_out",
           "norm_ffn_w", "peer_w_query", "peer_up", "c_2", "positions_2", "ada_w_2", "ada_b_2", "norm1_g_2", "norm2_g_2",
           "w_in_2", "fox_fb_2", "mla_q_norm_g_2", "mla_wq_up_2", "mla_kv_norm_g_2", "mla_wkv_up_2", "gate_w_2", "gate_b_2",
           "branch_w_2", "out_w_2", "exp_w1_2", "exp_w3_2", "exp_w2_2", "final_g_2")


def shape_constants():
    f = np.float32
    i = np.arange(P)
    t = np.arange(T)
    dist = t[:, None] - t[None, :]
    seen = [(dist >= 0) & (dist <= 128), (dist >= 0) & (dist % 4 == 0), (dist >= 0) & (dist % 16 == 0), dist >= 0]
    log_gamma = np.log1p(-np.exp2(-5.0 - np.arange(4)))
    rel = i[None, :] - i[:, None]
    dmask = np.where(rel[:, None, :] >= 0, np.exp(log_gamma[None, :, None] * np.maximum(rel, 0)[:, None, :]), 0.0) * 64 ** -0.5
    decay = np.stack([np.exp(log_gamma[None, :] * (i[:, None] + 1.0)), np.exp(log_gamma[None, :] * (P - 1.0 - i[:, None])) * 64 ** -0.5,
                      np.broadcast_to(np.exp(log_gamma * P), (P, 4))], axis=1)
    return {
        "c_ident": np.eye(P, dtype=f), "c_tri": (i[:, None] <= i[None, :]).astype(f),
        "c_iota": np.broadcast_to(np.arange(P, dtype=f), (P, P)).copy(),
        "c_mask": np.stack([np.where(s, 0.0, NEG) for s in seen]).astype(f),
        "c_inv1": np.exp(f(-math.log(500000.0)) * f(2.0 / 16) * np.arange(8, dtype=f)).astype(f),
        "c_inv2": (10000.0 ** (-np.arange(0, 64, 2) / 64.0)).astype(f),
        "c_tokens": (i[:, None] + P * np.arange(NT)[None, :]).astype(np.int32),
        "c_dmask": dmask.reshape(P, 4 * P).astype(f), "c_decay": decay.reshape(P, 12).astype(f),
    }


def kernel(**inputs):
    import concourse.bacc as bacc
    from concourse.bass_utils import run_bass_kernel_spmd

    arrays = {n: np.ascontiguousarray(inputs[n]) for n in _INPUTS}
    arrays["taps"] = np.ascontiguousarray(np.concatenate([inputs["ssd_conv_w"][0], inputs["ssd_conv_b"]], axis=0).T)
    arrays["keysT"] = np.ascontiguousarray(np.transpose(inputs["peer_sub_keys"][0], (0, 1, 3, 2)).reshape(2 * P * PEER_H, NK))
    arrays["downT"] = np.ascontiguousarray(inputs["peer_down"][0].T)
    arrays["router_w"] = np.ascontiguousarray(np.concatenate([inputs["router_grp_w_2"], inputs["router_exp_w_2"]], axis=2))
    arrays["router_b"] = np.ascontiguousarray(np.concatenate([inputs["router_grp_b_2"], inputs["router_exp_b_2"]], axis=1))
    arrays.update(shape_constants())

    nc = bacc.Bacc("TRN2", target_bir_lowering=False, num_devices=1)
    aps = {n: nc.dram_tensor(f"in_{n}", v.shape, mybir.dt.from_np(v.dtype), kind="ExternalInput").ap() for n, v in arrays.items()}
    out = nc.dram_tensor("out_0", (1, T, D), F32, kind="ExternalOutput").ap()
    build(nc, aps, out)
    result = run_bass_kernel_spmd(nc, [{f"in_{n}": v for n, v in arrays.items()}], core_ids=[0])
    return result.results[0]["out_0"]
```
